# Optimizing a Trainium2 kernel written in Bass

```python
import math
import jax
import jax.numpy as jnp
from jax import lax
import numpy as np

D_MODEL = 1024
BATCH = 1
SEQ = 1024
DEPTH = 1
DEC_BATCH = 8
DEC_SEQ = 4
PAST_LEN = 512
PAGE_SIZE = 128

MIX_WIDTH = D_MODEL
GDN_WIDTH = MIX_WIDTH // 2
GDN_HEADS = 4
GDN_DK = GDN_WIDTH // GDN_HEADS
GDN_DV = GDN_WIDTH // GDN_HEADS
GDN_CONV = 4
GDN_CHUNK = 64
DIFF_WIDTH = MIX_WIDTH - GDN_WIDTH
DIFF_HEADS = 4
DIFF_DV = DIFF_WIDTH // DIFF_HEADS
DIFF_DQK = DIFF_DV // 2
Q_BLOCK = 128
D_FF = 2816
FFN_CONV = 3
EPS = 1e-6

COL_GDN_Z = 3 * GDN_WIDTH
COL_GDN_B = 4 * GDN_WIDTH
COL_GDN_A = COL_GDN_B + GDN_HEADS
COL_DIFF = COL_GDN_A + GDN_HEADS
IN_COLS = COL_DIFF + 3 * DIFF_WIDTH

kernel_name = 'hybrid_gdn_diffattn_step'

def _rmsnorm(x, g):
    xf = x.astype(jnp.float32)
    xf = xf * lax.rsqrt(jnp.mean(xf * xf, axis=-1, keepdims=True) + EPS)
    return xf.astype(x.dtype) * g.astype(x.dtype)

def _l2norm(x):
    xf = x.astype(jnp.float32)
    return (xf * lax.rsqrt(jnp.sum(xf * xf, axis=-1, keepdims=True) + EPS)).astype(x.dtype)

def _causal_dwconv(x, buf, w, b=None):
    width = w.shape[0]
    L = x.shape[1]
    xp = jnp.concatenate([buf.astype(x.dtype), x], axis=1)
    y = xp[:, 0:L] * w[0]
    for j in range(1, width):
        y = y + xp[:, j:j + L] * w[j]
    if b is not None:
        y = y + b
    return y, xp[:, L:]

def _to_chunks(t, n, c):
    t = t.reshape(t.shape[0], n, c, *t.shape[2:])
    return jnp.moveaxis(t, (1, 3), (0, 2))

def _gated_delta_chunked(q, k, v, g, beta, S0):
    B, L, H, DK = q.shape
    DV = v.shape[-1]
    f32 = jnp.float32
    C = min(GDN_CHUNK, L)
    pad = (-L) % C
    n = (L + pad) // C

    def prep(t):
        t = t.astype(f32)
        return _to_chunks(jnp.pad(t, [(0, 0), (0, pad)] + [(0, 0)] * (t.ndim - 2)), n, C)

    qc, kc, vc, gc, bc = prep(q), prep(k), prep(v), prep(g), prep(beta)
    gcum = jnp.cumsum(gc, axis=-1)
    idx = jnp.arange(C)
    causal = idx[:, None] >= idx[None, :]
    decay = jnp.exp(jnp.where(causal, gcum[..., :, None] - gcum[..., None, :], -jnp.inf))
    kb = kc * bc[..., None]
    m = jnp.einsum('nbhik,nbhjk->nbhij', kb, kc) * decay
    a = jnp.where(idx[:, None] > idx[None, :], m, 0.0) + jnp.eye(C, dtype=f32)
    rhs = jnp.concatenate([vc * bc[..., None], kb * jnp.exp(gcum)[..., None]], axis=-1)
    sol = lax.linalg.triangular_solve(a, rhs, left_side=True, lower=True, unit_diagonal=True)
    u, w = sol[..., :DV], sol[..., DV:]

    def step(S, inp):
        q_i, k_i, u_i, w_i, g_i, d_i = inp
        v_new = u_i - jnp.einsum('bhck,bhkv->bhcv', w_i, S)
        intra = jnp.einsum('bhik,bhjk->bhij', q_i, k_i) * d_i
        o_i = (jnp.einsum('bhck,bhkv->bhcv', q_i * jnp.exp(g_i)[..., None], S)
               + jnp.einsum('bhij,bhjv->bhiv', intra, v_new))
        g_last = g_i[..., -1]
        S = (S * jnp.exp(g_last)[..., None, None]
             + jnp.einsum('bhck,bhcv->bhkv', k_i * jnp.exp(g_last[..., None] - g_i)[..., None], v_new))
        return S, o_i

    S_final, o = lax.scan(step, S0.astype(f32), (qc, kc, u, w, gcum, decay))
    o = jnp.transpose(o, (1, 0, 3, 2, 4)).reshape(B, n * C, H, DV)[:, :L]
    return o, S_final

def _diff_attention(q, k, v, lam, past_len):
    B, L = q.shape[0], q.shape[1]
    T = k.shape[1]
    H, DV = v.shape[2], v.shape[3]
    k_pos = jnp.arange(T)
    scale = DIFF_DQK ** -0.5

    def attend(qb, q_pos):
        s = jnp.einsum('bqhcd,bthcd->bhcqt', qb, k).astype(jnp.float32) * scale
        s = jnp.where(k_pos[None, :] <= q_pos[:, None], s, -jnp.inf)
        p = jax.nn.softmax(s, axis=-1)
        amap = p[:, :, 0] - lam * p[:, :, 1]
        return jnp.einsum('bhqt,bthv->bqhv', amap.astype(v.dtype), v)

    q_pos = past_len + jnp.arange(L)
    if L % Q_BLOCK == 0 and L > Q_BLOCK:
        nb = L // Q_BLOCK
        qb = jnp.moveaxis(q.reshape(B, nb, Q_BLOCK, H, 2, DIFF_DQK), 1, 0)
        pb = q_pos.reshape(nb, Q_BLOCK)
        o = lax.map(lambda xs: attend(xs[0], xs[1]), (qb, pb))
        return jnp.moveaxis(o, 0, 1).reshape(B, L, H, DV)
    return attend(q, q_pos)

def _hybrid_layer(x, gdn_conv_buf, gdn_S0, past_k, past_v, ffn_buf, wl, lam_init):
    (attn_norm_g, w_in, gdn_conv_w, gdn_A_log, gdn_dt_bias, gdn_out_norm_g,
     diff_q_norm_g, diff_k_norm_g, lq1, lk1, lq2, lk2, diff_subln_g, w_out,
     ffn_norm_g, w_up, ffn_conv_w, ffn_conv_b, w_down) = wl
    f32 = jnp.float32
    B, L, _ = x.shape
    P = past_k.shape[1]
    xn = _rmsnorm(x, attn_norm_g)
    proj = xn @ w_in

    qkv, new_gdn_conv = _causal_dwconv(proj[..., :COL_GDN_Z], gdn_conv_buf, gdn_conv_w)
    qkv = jax.nn.silu(qkv)
    gq = _l2norm(qkv[..., :GDN_WIDTH].reshape(B, L, GDN_HEADS, GDN_DK)) * (GDN_DK ** -0.5)
    gk = _l2norm(qkv[..., GDN_WIDTH:2 * GDN_WIDTH].reshape(B, L, GDN_HEADS, GDN_DK))
    gv = qkv[..., 2 * GDN_WIDTH:].reshape(B, L, GDN_HEADS, GDN_DV)
    z = proj[..., COL_GDN_Z:COL_GDN_B].reshape(B, L, GDN_HEADS, GDN_DV)
    beta = jax.nn.sigmoid(proj[..., COL_GDN_B:COL_GDN_A].astype(f32))
    g = -jnp.exp(gdn_A_log.astype(f32)) * jax.nn.softplus(
        proj[..., COL_GDN_A:COL_DIFF].astype(f32) + gdn_dt_bias.astype(f32))
    o_g, new_S = _gated_delta_chunked(gq, gk, gv, g, beta, gdn_S0)
    o_g = (_rmsnorm(o_g.astype(x.dtype), gdn_out_norm_g) * jax.nn.silu(z)).reshape(B, L, GDN_WIDTH)

    d = proj[..., COL_DIFF:]
    dq = _rmsnorm(d[..., :DIFF_WIDTH].reshape(B, L, DIFF_HEADS, 2, DIFF_DQK), diff_q_norm_g)
    dk = _rmsnorm(d[..., DIFF_WIDTH:2 * DIFF_WIDTH].reshape(B, L, DIFF_HEADS, 2, DIFF_DQK), diff_k_norm_g)
    dv = d[..., 2 * DIFF_WIDTH:].reshape(B, L, DIFF_HEADS, DIFF_DV)
    new_k = dk.reshape(B, L, DIFF_HEADS, 2 * DIFF_DQK)
    keys = jnp.concatenate([past_k.astype(x.dtype), new_k], axis=1).reshape(B, P + L, DIFF_HEADS, 2, DIFF_DQK)
    vals = jnp.concatenate([past_v.astype(x.dtype), dv], axis=1)
    lam = (jnp.exp(jnp.sum(lq1.astype(f32) * lk1.astype(f32)))
           - jnp.exp(jnp.sum(lq2.astype(f32) * lk2.astype(f32))) + lam_init)
    o_d = _diff_attention(dq, keys, vals, lam, P)
    o_d = (_rmsnorm(o_d, diff_subln_g) * (1.0 - lam_init)).reshape(B, L, DIFF_WIDTH)

    h = x + jnp.concatenate([o_g, o_d], axis=-1) @ w_out

    hn = _rmsnorm(h, ffn_norm_g)
    u, new_ffn = _causal_dwconv(hn @ w_up, ffn_buf, ffn_conv_w, ffn_conv_b)
    y = h + (jax.nn.silu(u[..., :D_FF]) * u[..., D_FF:]) @ w_down
    return y, new_gdn_conv, new_S, new_k, dv, new_ffn

def setup_inputs(seed: int = 0) -> dict:
    key = jax.random.key(seed)
    ks = jax.random.split(key, 32)
    f32 = jnp.float32
    n_pages = PAST_LEN // PAGE_SIZE
    n_pool = (DEC_BATCH * n_pages * 5) // 4

    def nrm(k, shape, scale):
        return jax.random.normal(k, shape, f32) * scale

    dt = jnp.exp(jax.random.uniform(ks[12], (DEPTH, GDN_HEADS), f32, math.log(1e-3), math.log(1e-1)))
    return {
        'x_prompt': nrm(ks[0], (BATCH, SEQ, D_MODEL), 1.0),
        'x_sample': nrm(ks[1], (DEC_BATCH, DEC_SEQ, D_MODEL), 1.0),
        'state_gdn_conv': nrm(ks[2], (DEPTH, DEC_BATCH, GDN_CONV - 1, 3 * GDN_WIDTH), 1.0),
        'state_gdn_S': nrm(ks[3], (DEPTH, DEC_BATCH, GDN_HEADS, GDN_DK, GDN_DV), 0.1),
        'cache_k': nrm(ks[4], (DEPTH, n_pool, PAGE_SIZE, DIFF_HEADS, 2 * DIFF_DQK), 1.0),
        'cache_v': nrm(ks[5], (DEPTH, n_pool, PAGE_SIZE, DIFF_HEADS, DIFF_DV), 1.0),
        'page_table': jax.random.permutation(ks[6], n_pool)[:DEC_BATCH * n_pages]
                      .reshape(DEC_BATCH, n_pages).astype(jnp.int32),
        'state_ffn_conv': nrm(ks[7], (DEPTH, DEC_BATCH, FFN_CONV - 1, 2 * D_FF), 1.0),
        'attn_norm_g': 1.0 + nrm(ks[8], (DEPTH, D_MODEL), 0.02),
        'w_in': nrm(ks[9], (DEPTH, D_MODEL, IN_COLS), D_MODEL ** -0.5),
        'gdn_conv_w': nrm(ks[10], (DEPTH, GDN_CONV, 3 * GDN_WIDTH), GDN_CONV ** -0.5),
        'gdn_A_log': jnp.log(jax.random.uniform(ks[11], (DEPTH, GDN_HEADS), f32, 1.0, 16.0)),
        'gdn_dt_bias': dt + jnp.log(-jnp.expm1(-dt)),
        'gdn_out_norm_g': 1.0 + nrm(ks[13], (DEPTH, GDN_DV), 0.02),
        'diff_q_norm_g': 1.0 + nrm(ks[14], (DEPTH, DIFF_DQK), 0.02),
        'diff_k_norm_g': 1.0 + nrm(ks[15], (DEPTH, DIFF_DQK), 0.02),
        'diff_lambda_q1': nrm(ks[16], (DEPTH, DIFF_DQK), 0.1),
        'diff_lambda_k1': nrm(ks[17], (DEPTH, DIFF_DQK), 0.1),
        'diff_lambda_q2': nrm(ks[18], (DEPTH, DIFF_DQK), 0.1),
        'diff_lambda_k2': nrm(ks[19], (DEPTH, DIFF_DQK), 0.1),
        'diff_subln_g': 1.0 + nrm(ks[20], (DEPTH, DIFF_DV), 0.02),
        'w_out': nrm(ks[21], (DEPTH, MIX_WIDTH, D_MODEL), MIX_WIDTH ** -0.5),
        'ffn_norm_g': 1.0 + nrm(ks[22], (DEPTH, D_MODEL), 0.02),
        'w_up': nrm(ks[23], (DEPTH, D_MODEL, 2 * D_FF), D_MODEL ** -0.5),
        'ffn_conv_w': nrm(ks[24], (DEPTH, FFN_CONV, 2 * D_FF), FFN_CONV ** -0.5),
        'ffn_conv_b': nrm(ks[25], (DEPTH, 2 * D_FF), 0.01),
        'w_down': nrm(ks[26], (DEPTH, D_FF, D_MODEL), D_FF ** -0.5),
    }

def reference(x_prompt, x_sample, state_gdn_conv, state_gdn_S, cache_k, cache_v, page_table,
              state_ffn_conv, attn_norm_g, w_in, gdn_conv_w, gdn_A_log, gdn_dt_bias,
              gdn_out_norm_g, diff_q_norm_g, diff_k_norm_g, diff_lambda_q1, diff_lambda_k1,
              diff_lambda_q2, diff_lambda_k2, diff_subln_g, w_out, ffn_norm_g, w_up,
              ffn_conv_w, ffn_conv_b, w_down):
    B = x_prompt.shape[0]
    Bd = x_sample.shape[0]
    dt = x_prompt.dtype
    n_pages = page_table.shape[1]
    past_len = n_pages * cache_k.shape[2]
    hp, hs = x_prompt, x_sample
    pc, pS, pk, pv, pf = [], [], [], [], []
    sc, sS, sk, sv, sf = [], [], [], [], []
    for l in range(DEPTH):
        wl = (attn_norm_g[l], w_in[l], gdn_conv_w[l], gdn_A_log[l], gdn_dt_bias[l],
              gdn_out_norm_g[l], diff_q_norm_g[l], diff_k_norm_g[l], diff_lambda_q1[l],
              diff_lambda_k1[l], diff_lambda_q2[l], diff_lambda_k2[l], diff_subln_g[l],
              w_out[l], ffn_norm_g[l], w_up[l], ffn_conv_w[l], ffn_conv_b[l], w_down[l])
        lam_init = 0.8 - 0.6 * math.exp(-0.3 * l)
        hp, c1, S1, k1, v1, f1 = _hybrid_layer(
            hp,
            jnp.zeros((B, GDN_CONV - 1, 3 * GDN_WIDTH), dt),
            jnp.zeros((B, GDN_HEADS, GDN_DK, GDN_DV), jnp.float32),
            jnp.zeros((B, 0, DIFF_HEADS, 2 * DIFF_DQK), dt),
            jnp.zeros((B, 0, DIFF_HEADS, DIFF_DV), dt),
            jnp.zeros((B, FFN_CONV - 1, 2 * D_FF), dt),
            wl, lam_init)
        past_k = cache_k[l][page_table].reshape(Bd, past_len, DIFF_HEADS, 2 * DIFF_DQK)
        past_v = cache_v[l][page_table].reshape(Bd, past_len, DIFF_HEADS, DIFF_DV)
        hs, c2, S2, k2, v2, f2 = _hybrid_layer(
            hs, state_gdn_conv[l], state_gdn_S[l], past_k, past_v, state_ffn_conv[l], wl, lam_init)
        pc.append(c1); pS.append(S1); pk.append(k1); pv.append(v1); pf.append(f1)
        sc.append(c2); sS.append(S2); sk.append(k2); sv.append(v2); sf.append(f2)
    return (hp, hs, jnp.stack(pc), jnp.stack(pS), jnp.stack(pk), jnp.stack(pv), jnp.stack(pf),
            jnp.stack(sc), jnp.stack(sS), jnp.stack(sk), jnp.stack(sv), jnp.stack(sf))


_drawn_inputs = setup_inputs


def setup_inputs(seed=0):
    import zlib

    import numpy as np

    out = dict(_drawn_inputs(seed))
    spreads = {}
    factors = {'gdn_out_norm_g': 7.084,
     'diff_q_norm_g': 5.553,
     'diff_k_norm_g': 3.032,
     'diff_subln_g': 5.825,
     'ffn_norm_g': 2.81,
     'ffn_conv_b': 8.0}
    for name, (base, spread) in spreads.items():
        noise = np.random.default_rng([zlib.crc32(name.encode()), seed]).standard_normal(out[name].shape)
        drawn = base * np.exp(spread * noise) if base else spread * noise
        out[name] = jnp.asarray(drawn.astype(out[name].dtype))
    for name, factor in factors.items():
        out[name] = (out[name] * factor).astype(out[name].dtype)
    return out
```

```python
from contextlib import ExitStack

import concourse.bass as bass
from concourse import mybir

F32 = mybir.dt.float32
F32R = mybir.dt.float32r
BF16 = mybir.dt.bfloat16
I32 = mybir.dt.int32
ALU = mybir.AluOpType
ACT = mybir.ActivationFunctionType
AX = mybir.AxisListType

P = 128
D = 1024
KT = D // P
SEQ = 1024
NB = 8
NL = 4
NS = NB * NL
T = SEQ + NS
NG = 3
TG = T // NG
H = 4
DH = 128
HALF = 64
GW = H * DH
CG = 4
CF = 3
FF = 2816
FT = FF // P
COL_BA = 4 * GW
COL_DIFF = COL_BA + 2 * H
PAGE = 128
NPG = 4
PAST = NPG * PAGE
EPS = 1e-6
NEG = -1e30
LAM_INIT = 0.8 - 0.6
NLEV = 7
NT = SEQ // P
CREDIT = 2

G_PAD, F_PAD = CG - 1, CF - 1
G_SAMPLE, F_SAMPLE = G_PAD + SEQ, F_PAD + SEQ
G_BUF = G_SAMPLE + NB * (G_PAD + NL)
F_BUF = F_SAMPLE + NB * (F_PAD + NL)
G_OUT, F_OUT = G_BUF - G_PAD, F_BUF - F_PAD
G_TAIL = G_PAD * (1 + NB)
F_TAIL = F_PAD * (1 + NB)


def done(n):
    return n + 1 + CREDIT


def levels_done(turn, level, levels=NLEV):
    return levels * turn + (level + 1)


def r32(ap):
    return ap.bitcast(F32)


def over(ap, axis, shape):
    return ap.unsqueeze(axis).to_broadcast(shape)


def samples(buf, start, pad, lo, n):
    return buf[:, start:start + NB * (pad + NL)].rearrange("p (b c) -> p b c", b=NB)[:, :, lo:lo + n]


def project_tile(nc, psum, w_hi, w_lo, x_hi, x_lo, cols=P):
    for k in range(KT):
        for i, (w, x) in enumerate(((w_hi, x_hi), (w_hi, x_lo), (w_lo, x_hi))):
            for g in range(NG):
                mm = nc.tensor.matmul(psum[0:cols, g, 0:TG], w[:, k, 0:cols], x[:, k, g * TG:(g + 1) * TG],
                                      start=(k == 0 and i == 0), stop=(k == KT - 1 and i == 2))
    return mm


class Memory:

    def __init__(self, nc):
        self.nc, self.stack = nc, ExitStack()

    def sb(self, name, shape, dt=F32):
        return self.stack.enter_context(self.nc.sbuf_tensor(name, shape, dt))

    def ps(self, name, shape, dt=F32):
        return self.stack.enter_context(self.nc.psum_tensor(name, shape, dt))

    def free(self):
        self.stack.close()


def hybrid_step(nc, i, o):
    held = []

    def sem(name):
        held.append(nc.alloc_semaphore(name=name))
        return held[-1]

    def phase(step, *args):
        step(nc, *args, sem)
        nc.clear_and_free_semaphores(held)
        nc.all_engine_barrier()
        held.clear()

    x_scratch = nc.dram_tensor("x_scratch", (P, KT, T), F32, kind="Internal").ap()
    z_scratch = nc.dram_tensor("z_scratch", (P, H, T), F32, kind="Internal").ap()

    keep = Memory(nc)
    c = {
        "ident": keep.sb("ident", [P, P]),
        "ones": keep.sb("ones", [P, P]),
        "halves": keep.sb("halves", [P, P]),
        "cols": keep.sb("cols", [P, 2 * KT]),
        "gain": keep.sb("gain", [P, 4]),
        "neglam": keep.sb("neglam", [P, 1]),
        "eps": keep.sb("eps", [P, 1]),
        "pages": keep.sb("pages", [1, NB * NPG], I32),
        "gtail": keep.sb("gtail", [P, 3 * H, G_TAIL]),
        "gcol": keep.sb("gcol", [P, 3 * H, NB * G_PAD + CG]),
    }
    feat = keep.sb("feat", [P, 5 * H, T])
    ba = keep.sb("ba", [P, NT + 1, 2 * H])
    x_split = Memory(nc)
    x_hi = x_split.sb("x_hi", [P, KT, T], F32R)
    x_lo = x_split.sb("x_lo", [P, KT, T], F32R)

    phase(setup_and_input_norm, i, c, feat, x_hi, x_lo, x_scratch)
    phase(input_projection, i, o, c, feat, ba, x_hi, x_lo, z_scratch)
    x_split.free()

    head_out = feat[:, 0:2 * H, :]
    phase(head_norms, i, o, c, feat, ba)
    phase(delta_prompt, i, o, c, feat, ba, head_out)
    phase(delta_sample, i, o, c, feat, ba, head_out)
    phase(attention_prompt, i, o, c, feat, head_out)
    phase(attention_sample, i, o, c, feat, head_out)
    hT = feat[:, 3 * H:5 * H, :]
    x_split = Memory(nc)
    x_hi = x_split.sb("hn_hi", [P, KT, T], F32R)
    x_lo = x_split.sb("hn_lo", [P, KT, T], F32R)
    phase(head_gate, c, hT, feat[:, 2 * H:3 * H, :], head_out, x_hi, x_lo, x_scratch, z_scratch)
    phase(output_projection, i, hT, x_hi, x_lo)
    phase(middle_norm, c, hT, x_hi, x_lo)
    phase(gated_mlp, i, o, c, feat, hT, x_hi, x_lo)
    x_split.free()
    phase(write_output, o, c, hT)
    keep.free()


def ln_rows(ap):
    return ap.rearrange("a (k p) -> (a k) p", p=P)


def norm_emitters(nc, src, hi, lo, g_cols, c, m, sem, name, psum):
    square = [m.sb(f"{name}_square{s}", [P, T]) for s in range(2)]
    rstd = m.sb(f"{name}_rstd", [P, T])
    value = [m.sb(f"{name}_value{s}", [P, T]) for s in range(2)]
    squared, summed, root_done = sem(f"{name}_squared"), sem(f"{name}_summed"), sem(f"{name}_root")
    rstd_done, value_done, hi_done, lo_done = (sem(f"{name}_{x}") for x in ("rstd_done", "value_done", "hi_done", "lo_done"))

    def on_scalar(act):
        nc.scalar.preload_act_table(ACT.Sqrt)
        for k in range(KT):
            if k >= 2:
                act.wait_ge(summed, k - 1)
            nc.scalar.activation(square[k % 2][:, :], src[:, k, :], ACT.Square).then_inc(squared, 1)
        act.wait_ge(summed, KT)
        nc.scalar.activation(rstd[:, :].rearrange("p (g t) -> p g t", g=NG), psum[:, :, 0:TG], ACT.Sqrt,
                             bias=c["eps"][:, 0:1], scale=1.0).then_inc(root_done, 1)
        for k in range(KT):
            act.wait_ge(value_done, k + 1)
            nc.scalar.activation(hi[:, k, :], value[k % 2][:, :], ACT.Copy).then_inc(hi_done, 1)

    def on_tensor(pe):
        for k in range(KT):
            pe.wait_ge(squared, k + 1)
            for g in range(NG):
                mm = nc.tensor.matmul(psum[:, g, 0:TG], c["ones"][:, :], square[k % 2][:, g * TG:(g + 1) * TG],
                                      start=(k == 0), stop=(k == KT - 1))
            mm.then_inc(summed, 1)

    def on_vector(dve):
        dve.wait_ge(root_done, 1)
        nc.vector.reciprocal(rstd[:, :], rstd[:, :]).then_inc(rstd_done, 1)
        dve.wait_ge(rstd_done, 1)
        for k in range(KT):
            if k >= 2:
                dve.wait_ge(lo_done, k - 1)
            nc.vector.scalar_tensor_tensor(out=value[k % 2][:, :], in0=src[:, k, :], scalar=g_cols[:, k:k + 1],
                                           in1=rstd[:, :], op0=ALU.mult, op1=ALU.mult).then_inc(value_done, 1)
            if k >= 1:
                split_low(k - 1, dve)
        split_low(KT - 1, dve)

    def split_low(k, dve):
        dve.wait_ge(hi_done, k + 1)
        nc.vector.tensor_tensor(lo[:, k, :], value[k % 2][:, :], r32(hi[:, k, :]), ALU.subtract).then_inc(lo_done, 1)

    return on_scalar, on_tensor, on_vector


def setup_and_input_norm(nc, i, c, feat, x_hi, x_lo, x_scratch, sem):
    m = Memory(nc)
    xT = feat[:, 0:KT, :]
    x_in = [m.sb(f"x_in{s}", [P, D]) for s in range(2)]
    rows = m.sb("rows", [20, P])
    state_rows = m.sb("state_rows", [NB * G_PAD + CG, 3 * GW])
    lam = m.sb("lam", [P, 4, HALF])
    lam_sum = m.sb("lam_sum", [P, 4])
    lam_prod = m.sb("lam_prod", [P, 2, HALF])
    turned = [m.ps(f"turned{s}", [P, KT, P]) for s in range(2)]
    total = m.ps("total", [P, NG, 512])

    params_in, x_loaded = sem("params_in"), [sem(f"x_loaded{s}") for s in range(2)]
    x_turned, x_kept = sem("x_turned"), [sem(f"x_kept{s}") for s in range(2)]
    consts_zero, consts = sem("consts_zero"), sem("consts")
    turned_cols, cols_kept, scratch_out = sem("turned_cols"), sem("cols_kept"), sem("x_scratch_out")
    lam_step = sem("lam_step")
    lam_exp = sem("lam_exp")
    n_act, n_pe, n_dve = norm_emitters(nc, xT, x_hi, x_lo, c["cols"][:, 0:KT], c, m, sem, "xn", total)

    with nc.Block() as block:
        @block.sync
        def _(sp):
            sp.dma_start(x_in[0][:, :], i["x_prompt"][0, 0:P, :]).then_inc(x_loaded[0], 16)
            sp.dma_start(x_in[1][:, :], i["x_prompt"][0, P:2 * P, :]).then_inc(x_loaded[1], 16)
            prompt_rows = i["x_prompt"].rearrange("a t d -> (a t) d")
            with sp.Fori(1, NT // 2) as it:
                for s in range(2):
                    sp.wait_ge(x_turned, 2 * it + s - 1)
                    sp.dma_start(x_in[s][:, :], prompt_rows[bass.ds(it * (2 * P) + s * P, P), :]).then_inc(x_loaded[s], 16)
            sp.wait_ge(x_turned, NT - 1)
            sp.dma_start(x_in[0][0:NS, :], i["x_sample"].rearrange("b l d -> (b l) d")).then_inc(x_loaded[0], 16)
            sp.wait_ge(x_kept[0], NT // 2 + 2)
            sp.wait_ge(x_kept[1], NT // 2 + 1)
            sp.dma_start(x_scratch, xT).then_inc(scratch_out, 16)
            sp.wait_ge(scratch_out, 16)

        @block.gpsimd
        def _(pool):
            pool.memset(c["ident"][:, :], 0.0).then_inc(consts_zero, 1)
            pool.memset(c["ones"][:, :], 1.0).then_inc(consts_zero, 1)
            pool.memset(c["halves"][:, :], 1.0).then_inc(consts_zero, 1)
            pool.memset(c["eps"][:, :], D * EPS).then_inc(consts_zero, 1)
            pool.wait_ge(consts_zero, 4)
            pool.affine_select(out=c["ident"][:, :], in_=c["ident"][:, :], compare_op=ALU.not_equal, fill=1.0, base=0,
                               pattern=[[-1, P]], channel_multiplier=1).then_inc(consts, 1)
            hv = c["halves"][:, :].rearrange("p (a b) -> p a b", a=2)
            pool.affine_select(out=hv, in_=hv, compare_op=ALU.is_ge, fill=0.0, base=0,
                               pattern=[[-HALF, 2], [0, HALF]], channel_multiplier=1).then_inc(consts, 1)
            pool.wait_ge(consts, 2)
            pool.affine_select(out=hv, in_=hv, compare_op=ALU.is_ge, fill=0.0, base=HALF - 1,
                               pattern=[[HALF, 2], [0, HALF]], channel_multiplier=-1).then_inc(consts, 1)

        @block.scalar
        def _(act):
            n = 0
            for dst, src in (
                (rows[0:KT, :], ln_rows(i["attn_norm_g"])),
                (rows[KT:2 * KT, :], ln_rows(i["ffn_norm_g"])),
                (rows[16:17, :], i["gdn_out_norm_g"]),
                (rows[17:18, :], i["diff_subln_g"]),
                (rows[18:19, 0:HALF], i["diff_q_norm_g"]),
                (rows[18:19, HALF:P], i["diff_q_norm_g"]),
                (rows[19:20, 0:HALF], i["diff_k_norm_g"]),
                (rows[19:20, HALF:P], i["diff_k_norm_g"]),
                (state_rows[0:NB * G_PAD, :], i["state_gdn_conv"].rearrange("a b r w -> (a b r) w")),
                (state_rows[NB * G_PAD:NB * G_PAD + CG, :], i["gdn_conv_w"].rearrange("a r w -> (a r) w")),
                (lam[:, 0, :], i["diff_lambda_q1"].to_broadcast([P, HALF])),
                (lam[:, 1, :], i["diff_lambda_k1"].to_broadcast([P, HALF])),
                (lam[:, 2, :], i["diff_lambda_q2"].to_broadcast([P, HALF])),
                (lam[:, 3, :], i["diff_lambda_k2"].to_broadcast([P, HALF])),
                (c["pages"][:, :], i["page_table"].rearrange("(o b) n -> o (b n)", o=1)),
            ):
                nc.scalar.dma_start(dst, src).then_inc(params_in, 16)
                n += 1
            nc.scalar.preload_act_table(ACT.Copy)
            act.sem_inc(x_kept[0], 1)
            with act.Fori(0, NT // 2) as it:
                act.wait_ge(x_turned, 2 * it + 1)
                nc.scalar.copy(xT[:, :, bass.ds(it * (2 * P), P)], turned[0][:, :, :]).then_inc(x_kept[0], 1)
            act.wait_ge(x_turned, NT + 1)
            nc.scalar.copy(xT[:, :, SEQ:T], turned[0][:, :, 0:NS]).then_inc(x_kept[0], 1)
            act.wait_ge(lam_step, 2)
            nc.scalar.activation(lam_sum[:, 2:4], lam_sum[:, 0:2], ACT.Exp).then_inc(lam_exp, 1)
            act.wait_ge(x_kept[0], NT // 2 + 2)
            act.wait_ge(x_kept[1], NT // 2 + 1)
            n_act(act)

        @block.tensor
        def _(pe):
            pe.wait_ge(consts, 3)
            with pe.Fori(0, NT // 2) as it:
                for s in range(2):
                    pe.wait_ge(x_loaded[s], 16 * it + 16)
                    pe.wait_ge(x_kept[s], it + 1)
                    for k in range(KT):
                        mm = nc.tensor.transpose(turned[s][:, k, :], x_in[s][:, k * P:(k + 1) * P], c["ident"][:, :])
                    mm.then_inc(x_turned, 1)
            pe.wait_ge(x_loaded[0], 16 * (NT // 2 + 1))
            pe.wait_ge(x_kept[0], NT // 2 + 1)
            for k in range(KT):
                mm = nc.tensor.transpose(turned[0][:, k, 0:NS], x_in[0][0:NS, k * P:(k + 1) * P], c["ident"][0:NS, 0:NS])
            mm.then_inc(x_turned, 1)
            pe.wait_ge(params_in, 16 * 15)
            pe.wait_ge(x_kept[1], NT // 2 + 1)
            nr = NB * G_PAD + CG
            for j in range(3 * H):
                nc.tensor.transpose(turned[1][:, :, :].rearrange("p a b -> p (a b)")[:, j * nr:(j + 1) * nr],
                                    state_rows[:, j * P:(j + 1) * P], c["ident"][0:nr, 0:nr])
            nc.tensor.transpose(turned[1][:, KT - 1, 0:20], rows[:, :], c["ident"][0:20, 0:20]).then_inc(turned_cols, 1)
            n_pe(pe)

        @block.vector
        def _(dve):
            dve.sem_inc(x_kept[1], 1)
            dve.wait_ge(params_in, 16 * 15)
            for j in range(2):
                nc.vector.tensor_tensor_reduce(out=lam_prod[:, j, :], in0=lam[:, 2 * j, :], in1=lam[:, 2 * j + 1, :], scale=1.0,
                                               scalar=0.0, op0=ALU.mult, op1=ALU.add,
                                               accum_out=lam_sum[:, j:j + 1]).then_inc(lam_step, 1)
            with dve.Fori(0, NT // 2) as it:
                dve.wait_ge(x_turned, 2 * it + 2)
                nc.vector.tensor_copy(xT[:, :, bass.ds(it * (2 * P) + P, P)], turned[1][:, :, :]).then_inc(x_kept[1], 1)
            dve.wait_ge(turned_cols, 1)
            nr = NB * G_PAD + CG
            nc.vector.tensor_copy(c["gcol"][:, :, :].rearrange("p a b -> p (a b)"),
                                  turned[1][:, :, :].rearrange("p a b -> p (a b)")[:, 0:3 * H * nr]).then_inc(cols_kept, 1)
            nc.vector.tensor_scalar(c["cols"][:, :], turned[1][:, KT - 1, 0:2 * KT], D ** 0.5, None,
                                    ALU.mult).then_inc(cols_kept, 1)
            for j, scale in enumerate((DH ** 0.5, (1.0 - LAM_INIT) * DH ** 0.5, 1.0, HALF ** 0.5)):
                nc.vector.tensor_scalar(c["gain"][:, j:j + 1], turned[1][:, KT - 1, 2 * KT + j:2 * KT + j + 1], scale, None,
                                        ALU.mult).then_inc(cols_kept, 1)
            dve.wait_ge(lam_exp, 1)
            nc.vector.tensor_tensor(c["neglam"][:, :], lam_sum[:, 3:4], lam_sum[:, 2:3], ALU.subtract).then_inc(lam_step, 1)
            dve.wait_ge(lam_step, 3)
            nc.vector.tensor_scalar(c["neglam"][:, :], c["neglam"][:, :], LAM_INIT, None, ALU.subtract)
            dve.wait_ge(cols_kept, 6)
            n_dve(dve)
    m.free()


def input_projection(nc, i, o, c, feat, ba, x_hi, x_lo, z_scratch, sem):
    m = Memory(nc)
    raw = [m.sb(f"win_raw{s}", [P, KT, P]) for s in range(2)]
    w_hi = [m.sb(f"win_hi{s}", [P, KT, P], F32R) for s in range(2)]
    w_lo = [m.sb(f"win_lo{s}", [P, KT, P], F32R) for s in range(2)]
    buf = m.sb("conv_buf", [P, 4, G_BUF])
    pre = [buf[:, s, :] for s in range(2)]
    acc = [buf[:, 2 + s, :] for s in range(2)]
    psum = [m.ps(f"proj{s}", [P, NG, 512]) for s in range(2)]
    small = m.ps("proj_small", [P, 2, 512])

    NGDN, NZ, ND, NV = 3 * H, H, 2 * H, H
    Z0, D0, V0 = NGDN, NGDN + NZ, NGDN + NZ + ND
    NTILE = V0 + NV

    loaded = [sem(f"win_loaded{s}") for s in range(2)]
    split_hi, split_lo = sem("win_split_hi"), sem("win_split_lo")
    projected, evacuated = sem("win_projected"), sem("win_evacuated")
    state_put, tail_kept = sem("g_state_put"), sem("g_tail_kept")
    tap0, taps, activated = sem("g_tap0"), sem("g_taps"), sem("g_activated")
    pads = sem("g_pads")
    z_out = [sem(f"z_out{s}") for s in range(2)]
    ba_loaded, ba_split, ba_projected, ba_kept, ba_turned = (sem(f"ba_{x}") for x in ("loaded", "split", "projected", "kept", "turned"))
    tail_turned, tail_rows, tail_out = sem("g_tail_turned"), sem("g_tail_rows"), sem("g_tail_out")
    v_turned, v_kept, v_out = sem("v_turned"), sem("v_kept"), [sem(f"v_out{s}") for s in range(2)]

    w = i["w_in"][0].rearrange("(k p) n -> p k n", p=P)
    ba_raw = m.sb("ba_raw", [P, KT, 2 * H])
    ba_hi = m.sb("ba_hi", [P, KT, 2 * H], F32R)
    ba_lo = m.sb("ba_lo", [P, KT, 2 * H], F32R)
    tail_tok = raw[0][0:G_TAIL, :, :].rearrange("p a b -> p (a b)")
    tail_tok2 = raw[1][0:G_TAIL, :, :].rearrange("p a b -> p (a b)")
    v_tok = [raw[s][:, 4:8, :].rearrange("p a b -> p (a b)") for s in range(2)]
    tail_tok3 = m.sb("tail_tok3", [G_TAIL, 512])
    ba_T = m.sb("ba_T", [2 * H, T])
    v_ps = [small[:, 1, :], psum[0][:, 0, :]]

    def pairs(eng, first, last, body):
        with eng.Fori(first // 2, last // 2) as it:
            for s in range(2):
                body(2 * it + s, s)

    with nc.Block() as block:
        @block.sync
        def _(sp):
            def load(n, s, col):
                if not isinstance(n, int) or n >= 2:
                    sp.wait_ge(split_lo, done(n - 2))
                sp.dma_start(raw[s][:, :, :], w[:, :, bass.ds(col, P)]).then_inc(loaded[s], 16)

            load(0, 0, 0)
            load(1, 1, P)
            sp.dma_start(ba_raw[:, :, :], w[:, :, COL_BA:COL_DIFF]).then_inc(ba_loaded, 16)
            with sp.Fori(1, Z0 // 2) as it:
                for s in range(2):
                    load(2 * it + s, s, it * (2 * P) + s * P)
            with sp.Fori(Z0 // 2, D0 // 2) as it:
                for s in range(2):
                    load(2 * it + s, s, it * (2 * P) + s * P)
            with sp.Fori(D0 // 2, NTILE // 2) as it:
                for s in range(2):
                    load(2 * it + s, s, it * (2 * P) + (s * P + 2 * H))
            for a, src in ((0, tail_tok[:, 0:512]), (1, tail_tok2[:, 0:512])):
                sp.wait_ge(tail_rows, a + 1)
                sp.dma_start(o["gdn_conv_prompt"][0, 0, :, a * 512:(a + 1) * 512], src[0:G_PAD, :]).then_inc(tail_out, 16)
                sp.dma_start(o["gdn_conv_sample"][0].rearrange("b r w -> (b r) w")[:, a * 512:(a + 1) * 512],
                             src[G_PAD:G_TAIL, :]).then_inc(tail_out, 16)
            sp.wait_ge(tail_rows, 3)
            sp.dma_start(o["gdn_conv_prompt"][0, 0, :, 1024:1536], tail_tok3[0:G_PAD, :]).then_inc(tail_out, 16)
            sp.dma_start(o["gdn_conv_sample"][0].rearrange("b r w -> (b r) w")[:, 1024:1536],
                         tail_tok3[G_PAD:G_TAIL, :]).then_inc(tail_out, 16)
            for t in range(NT + 1):
                sp.wait_ge(v_kept, t + 1)
                if t < NT:
                    sp.dma_start(o["v_prompt"].rearrange("a b t h d -> (a b t) (h d)")[t * P:(t + 1) * P, :],
                                 v_tok[t % 2]).then_inc(v_out[t % 2], 16)
                else:
                    sp.dma_start(o["v_sample"].rearrange("a b l h d -> (a b l) (h d)"), v_tok[t % 2][0:NS, :]).then_inc(v_out[t % 2], 16)
            sp.wait_ge(tail_out, 16 * 6)
            sp.wait_ge(v_out[0], 16 * (NT // 2 + 1))
            sp.wait_ge(v_out[1], 16 * (NT // 2))

        @block.gpsimd
        def _(pool):
            pool.sem_inc(state_put, CREDIT)
            pool.sem_inc(tail_kept, CREDIT)
            for s in range(2):
                pool.memset(pre[s][:, 0:G_PAD], 0.0).then_inc(pads, 1)

            def body(n, s):
                pool.wait_ge(taps, done(n - 2))
                nc.gpsimd.tensor_copy(samples(pre[s], G_SAMPLE, G_PAD, 0, G_PAD),
                                      c["gcol"][:, bass.ds(n, 1), 0:NB * G_PAD].rearrange("p o (b r) -> p (o b) r", r=G_PAD)
                                      ).then_inc(state_put, 1)
                pool.wait_ge(evacuated, done(n))
                nc.gpsimd.tensor_copy(c["gtail"][:, bass.ds(n, 1), 0:G_PAD], pre[s][:, SEQ:SEQ + G_PAD].unsqueeze(1))
                nc.gpsimd.tensor_copy(c["gtail"][:, bass.ds(n, 1), G_PAD:G_TAIL].rearrange("p o (b r) -> p (o b) r", r=G_PAD),
                                      samples(pre[s], G_SAMPLE, G_PAD, NL, G_PAD)).then_inc(tail_kept, 1)

            pairs(pool, 0, Z0, body)

        @block.scalar
        def _(act):
            act.sem_inc(split_hi, CREDIT)
            act.sem_inc(evacuated, CREDIT)
            act.sem_inc(tap0, CREDIT)
            act.sem_inc(activated, CREDIT)
            nc.scalar.preload_act_table(ACT.Silu)

            def high(n, s):
                act.wait_ge(loaded[s], high_loaded(n, s))
                act.wait_ge(projected, done(n - 2))
                nc.scalar.activation(w_hi[s][:, :, :], raw[s][:, :, :], ACT.Copy).then_inc(split_hi, 1)

            def high_loaded(n, s):
                return 8 * (n - s) + 16

            def drain_gdn(n, s):
                act.wait_ge(projected, done(n))
                act.wait_ge(taps, done(n - 2))
                act.wait_ge(tail_kept, done(n - 2))
                nc.scalar.copy(pre[s][:, G_PAD:G_PAD + 2 * TG].rearrange("p (g t) -> p g t", g=2), psum[s][:, 0:2, 0:TG])
                nc.scalar.copy(pre[s][:, G_PAD + 2 * TG:G_SAMPLE], psum[s][:, 2, 0:TG - NS])
                nc.scalar.copy(samples(pre[s], G_SAMPLE, G_PAD, G_PAD, NL),
                               psum[s][:, 2, TG - NS:TG].rearrange("p (b l) -> p b l", b=NB)).then_inc(evacuated, 1)
                act.wait_ge(evacuated, done(n))
                act.wait_ge(state_put, done(n))
                nc.scalar.activation(acc[s][:, 0:G_OUT], pre[s][:, 0:G_OUT], ACT.Copy,
                                     scale=c["gcol"][:, bass.ds(n, 1), NB * G_PAD:NB * G_PAD + 1].rearrange("p o r -> p (o r)")
                                     ).then_inc(tap0, 1)
                act.wait_ge(taps, done(n))
                nc.scalar.activation(feat[:, bass.ds(n, 1), 0:SEQ].rearrange("p o t -> p (o t)"), acc[s][:, 0:SEQ], ACT.Silu)
                nc.scalar.activation(feat[:, bass.ds(n, 1), SEQ:T].rearrange("p o (b l) -> p (o b) l", b=NB),
                                     samples(acc[s], G_SAMPLE, G_PAD, 0, NL), ACT.Silu).then_inc(activated, 1)

            def drain_z(n, s):
                act.wait_ge(projected, done(n))
                if n - Z0 >= 2:
                    act.wait_ge(z_out[s], 16)
                nc.scalar.activation(acc[s][:, 0:T].rearrange("p (g t) -> p g t", g=NG), psum[s][:, :, 0:TG],
                                     ACT.Silu).then_inc(evacuated, 1)
                act.wait_ge(evacuated, done(n))
                nc.scalar.dma_start(z_scratch[:, n - Z0, :], acc[s][:, 0:T]).then_inc(z_out[s], 16)

            def drain_diff(n, s):
                act.wait_ge(projected, done(n))
                nc.scalar.copy(feat[:, bass.ds(n - NZ, 1), :].rearrange("p o (g t) -> p (o g) t", g=NG),
                               psum[s][:, :, 0:TG]).then_inc(evacuated, 1)

            def drain_v(n, s):
                act.wait_ge(projected, done(n))
                if n == V0:
                    act.wait_ge(taps, done(Z0 - 1))
                    act.wait_ge(tail_kept, done(Z0 - 1))
                if n == V0 + 2:
                    act.wait_ge(z_out[0], 32)
                    act.wait_ge(z_out[1], 32)
                nc.scalar.copy(buf[:, n - V0, 0:T].rearrange("p (g t) -> p g t", g=NG), psum[s][:, :, 0:TG]).then_inc(evacuated, 1)

            high(0, 0)
            act.wait_ge(ba_loaded, 16)
            nc.scalar.activation(ba_hi[:, :, :], ba_raw[:, :, :], ACT.Copy).then_inc(ba_split, 1)

            def gdn_tile(n, s):
                high(n + 1, 1 - s)
                drain_gdn(n, s)

            def diff_tile(n, s):
                high(n + 1, 1 - s)
                drain_diff(n, s)

            pairs(act, 0, Z0, gdn_tile)
            for n in range(Z0, D0):
                high(n + 1, 1 - n % 2)
                drain_z(n, n % 2)
            pairs(act, D0, V0, diff_tile)
            for n in range(V0, NTILE):
                if n + 1 < NTILE:
                    high(n + 1, 1 - n % 2)
                drain_v(n, n % 2)
            act.wait_ge(ba_projected, 1)
            nc.scalar.copy(ba_T[:, :].rearrange("p (g t) -> p g t", g=NG), psum[0][0:2 * H, :, 0:TG]).then_inc(ba_kept, 1)

        @block.vector
        def _(dve):
            dve.sem_inc(split_lo, CREDIT)
            dve.sem_inc(taps, CREDIT)
            step = sem("g_tap_step")
            dve.sem_inc(step, 2 * CREDIT)

            def low(n, s):
                dve.wait_ge(split_hi, done(n))
                nc.vector.tensor_tensor(w_lo[s][:, :, :], raw[s][:, :, :], r32(w_hi[s][:, :, :]),
                                        ALU.subtract).then_inc(split_lo, 1)

            def gdn_tile(n, s):
                low(n + 1, 1 - s)
                dve.wait_ge(tap0, done(n))
                for j in range(1, CG):
                    if j >= 2:
                        dve.wait_ge(step, 2 * n + (2 * CREDIT + j - 1))
                    ins = nc.vector.scalar_tensor_tensor(
                        out=acc[s][:, 0:G_OUT], in0=pre[s][:, j:j + G_OUT],
                        scalar=c["gcol"][:, bass.ds(n, 1), NB * G_PAD + j:NB * G_PAD + j + 1].rearrange("p o r -> p (o r)"),
                        in1=acc[s][:, 0:G_OUT], op0=ALU.mult, op1=ALU.add)
                    ins.then_inc(step if j < CG - 1 else taps, 1)

            low(0, 0)
            dve.wait_ge(ba_split, 1)
            nc.vector.tensor_tensor(ba_lo[:, :, :], ba_raw[:, :, :], r32(ba_hi[:, :, :]), ALU.subtract).then_inc(ba_split, 1)
            pairs(dve, 0, Z0, gdn_tile)
            pairs(dve, Z0, V0, lambda n, s: low(n + 1, 1 - s))
            for n in range(V0, NTILE - 1):
                low(n + 1, 1 - n % 2)
            dve.wait_ge(ba_turned, 1)
            nc.vector.tensor_copy(ba[:, 0:NT, :], small[:, 0, 0:NT * 2 * H].rearrange("p (t c) -> p t c", c=2 * H))
            nc.vector.tensor_copy(ba[0:NS, NT, :], small[0:NS, 0, NT * 2 * H:(NT + 1) * 2 * H]).then_inc(ba_turned, 1)
            for a, dst in enumerate((tail_tok[:, 0:512], tail_tok2[:, 0:512], tail_tok3[:, :])):
                dve.wait_ge(tail_turned, a + 1)
                nc.vector.tensor_copy(dst, psum[1][0:G_TAIL, a, :]).then_inc(tail_rows, 1)
            for t in range(NT + 1):
                dve.wait_ge(v_turned, t + 1)
                if t >= 2:
                    dve.wait_ge(v_out[t % 2], 16 * (t // 2))
                n = P if t < NT else NS
                nc.vector.tensor_copy(v_tok[t % 2][0:n, :], v_ps[t % 2][0:n, :]).then_inc(v_kept, 1)

        @block.tensor
        def _(pe):
            pe.sem_inc(projected, CREDIT)

            def tile(n, s):
                pe.wait_ge(split_lo, done(n))
                pe.wait_ge(evacuated, done(n - 2))
                project_tile(nc, psum[s], w_hi[s], w_lo[s], x_hi, x_lo).then_inc(projected, 1)

            pairs(pe, 0, NTILE, tile)
            pe.wait_ge(ba_split, 2)
            pe.wait_ge(evacuated, done(NTILE - 2))
            project_tile(nc, psum[0], ba_hi, ba_lo, x_hi, x_lo, 2 * H).then_inc(ba_projected, 1)
            pe.wait_ge(ba_kept, 1)
            for t in range(NT + 1):
                n = P if t < NT else NS
                mm = nc.tensor.transpose(small[0:n, 0, t * 2 * H:(t + 1) * 2 * H], ba_T[:, t * P:t * P + n],
                                         c["ident"][0:2 * H, 0:2 * H])
            mm.then_inc(ba_turned, 1)
            pe.wait_ge(tail_kept, done(Z0 - 1))
            pe.wait_ge(evacuated, done(NTILE - 1))
            for j in range(3 * H):
                mm = nc.tensor.transpose(psum[1][0:G_TAIL, j // 4, (j % 4) * P:(j % 4 + 1) * P], c["gtail"][:, j, :],
                                         c["ident"][:, :])
                if j % 4 == 3:
                    mm.then_inc(tail_turned, 1)
            for t in range(NT + 1):
                n = P if t < NT else NS
                if t >= 2:
                    pe.wait_ge(v_kept, t - 1)
                for h in range(H):
                    mm = nc.tensor.transpose(v_ps[t % 2][0:n, h * P:(h + 1) * P], buf[:, h, t * P:t * P + n], c["ident"][:, :])
                mm.then_inc(v_turned, 1)
    m.free()


def head_scales(nc, m, sem, name, tiles, total, eps_of):
    n = len(tiles)
    R = tiles[-1][2] + (2 if tiles[-1][1] else 1)
    square = [m.sb(f"{name}_square{x}", [P, T]) for x in range(2)]
    strip = m.sb(f"{name}_strip", [P, 2, 2 * R])
    spread_by = m.sb(f"{name}_spread_by", [R, n, P])
    spread_r = m.sb(f"{name}_spread_r", [R, n, P], F32R)
    eps = m.sb(f"{name}_eps", [R, 1])
    rows = m.sb(f"{name}_rows", [R, T])
    hi, lo = m.sb(f"{name}_rows_hi", [R, T], F32R), m.sb(f"{name}_rows_lo", [R, T], F32R)
    zeroed, made, spread_made = sem(f"{name}_zeroed"), sem(f"{name}_made"), sem(f"{name}_spread_made")
    squared, summed, root_done, inverted, hi_done, lo_done = (
        sem(f"{name}_{x}") for x in ("squared", "summed", "root", "inverted", "rows_hi", "rows_lo"))
    halved = [t for t in range(n) if tiles[t][1]]
    whole = n - len(halved)

    def on_pool(pool):
        pool.memset(strip[:, :, :], 0.0).then_inc(zeroed, 1)
        pool.memset(spread_by[:, :, :], 1.0).then_inc(zeroed, 1)
        k = 2
        for first, value in eps_of:
            pool.memset(eps[0:first, :], value).then_inc(zeroed, 1)
            k += 1
            pool.wait_ge(zeroed, k)
        for j, ones in enumerate((strip[:, 0, R - 1:R], strip[0:HALF, 1, R - 1:R], strip[HALF:P, 1, R:R + 1])):
            if j:
                pool.wait_ge(made, j)
            pool.memset(ones, 1.0).then_inc(made, 1)
        pool.wait_ge(made, 3)
        views = []
        if whole:
            views.append((spread_by[:, 0:whole, :], 0, [[-1, whole], [0, P]]))
        if halved:
            views.append((spread_by[:, whole:n, :].rearrange("r t (x f) -> r (t x) f", x=2), -tiles[whole][2],
                          [[-1, 2 * (n - whole)], [0, HALF]]))
        for v, base, pattern in views:
            pool.affine_select(out=v, in_=v, compare_op=ALU.is_equal, fill=0.0, base=base, pattern=pattern,
                               channel_multiplier=1).then_inc(spread_made, 1)

    def on_scalar(act):
        nc.scalar.preload_act_table(ACT.Sqrt)
        for t in range(0, n):
            if t >= 2:
                act.wait_ge(summed, t - 1)
            nc.scalar.activation(square[t % 2][:, :], tiles[t][0], ACT.Square).then_inc(squared, 1)
        act.wait_ge(summed, n)
        act.wait_ge(zeroed, 2 + len(eps_of))
        nc.scalar.activation(rows[:, :].rearrange("p (g t) -> p g t", g=NG), total[0:R, :, 0:TG], ACT.Sqrt, bias=eps[:, :],
                             scale=1.0).then_inc(root_done, 1)
        act.wait_ge(inverted, 1)
        nc.scalar.copy(hi[:, :], rows[:, :]).then_inc(hi_done, 1)

    def on_tensor(pe):
        pe.wait_ge(made, 3)
        for t, (_, two, row) in enumerate(tiles):
            pe.wait_ge(squared, t + 1)
            for g in range(NG):
                mm = nc.tensor.matmul(total[0:R, g, 0:TG], strip[:, 1 if two else 0, R - 1 - row:2 * R - 1 - row],
                                      square[t % 2][:, g * TG:(g + 1) * TG], start=(t == 0), stop=(t == n - 1))
            mm.then_inc(summed, 1)
        pe.wait_ge(lo_done, 2)

    def on_vector(dve):
        dve.wait_ge(spread_made, (1 if whole else 0) + (1 if halved else 0))
        nc.vector.tensor_copy(spread_r[:, :, :], spread_by[:, :, :]).then_inc(lo_done, 1)
        dve.wait_ge(root_done, 1)
        nc.vector.reciprocal(rows[:, :], rows[:, :]).then_inc(inverted, 1)
        dve.wait_ge(hi_done, 1)
        nc.vector.tensor_tensor(lo[:, :], rows[:, :], r32(hi[:, :]), ALU.subtract).then_inc(lo_done, 1)

    def spread(t, psum):
        for g in range(NG):
            for k, part in enumerate((hi, lo)):
                mm = nc.tensor.matmul(psum[:, g, 0:TG], spread_r[:, t, :], part[:, g * TG:(g + 1) * TG], start=(k == 0), stop=(k == 1))
        return mm

    return on_pool, on_scalar, on_tensor, on_vector, spread


def head_norms(nc, i, o, c, feat, ba, sem):
    m = Memory(nc)
    k_tok = [m.sb(f"k_tok{s}", [P, GW]) for s in range(2)]
    a_pos = m.sb("a_pos", [P, NT + 1, H])
    a_neg = m.sb("a_neg", [P, NT + 1, H])
    dt_bias = m.sb("dt_bias", [P, H])
    a_log = m.sb("a_log", [P, H])
    psum = [m.ps(f"h_scale{s}", [P, NG, 512]) for s in range(2)]
    k_ps = m.ps("k_ps", [P, 2, 512])

    spread_done, normed = sem("h_spread"), sem("h_normed")
    k_turned, k_kept, k_out = sem("k_turned"), sem("k_kept"), [sem(f"k_out{s}") for s in range(2)]
    rate_in, gate_act, gate_dve = sem("rate_in"), sem("gate_act"), sem("gate_dve")

    order = [(j, j, DH ** -0.5) for j in range(H)] + [(j, j, 1.0) for j in range(H, 2 * H)]
    order += [(3 * H + j, 2 * H + 2 * j, c["gain"][:, 2 + j // H:3 + j // H]) for j in range(2 * H)]
    n_pool, n_act, n_pe, n_dve, spread = head_scales(
        nc, m, sem, "h", [(feat[:, j, :], j >= 3 * H, row) for j, row, _ in order], psum[1],
        ((6 * H, HALF * EPS), (2 * H, EPS)))

    with nc.Block() as block:
        @block.sync
        def _(sp):
            sp.dma_start(dt_bias[:, :], i["gdn_dt_bias"].to_broadcast([P, H])).then_inc(rate_in, 16)
            sp.dma_start(a_log[:, :], i["gdn_A_log"].to_broadcast([P, H])).then_inc(rate_in, 16)
            for t in range(NT + 1):
                sp.wait_ge(k_kept, t + 1)
                if t < NT:
                    sp.dma_start(o["k_prompt"].rearrange("a b t h d -> (a b t) (h d)")[t * P:(t + 1) * P, :],
                                 k_tok[t % 2][:, :]).then_inc(k_out[t % 2], 16)
                else:
                    sp.dma_start(o["k_sample"].rearrange("a b l h d -> (a b l) (h d)"), k_tok[t % 2][0:NS, :]).then_inc(k_out[t % 2], 16)
            sp.wait_ge(k_out[0], 16 * (NT // 2 + 1))
            sp.wait_ge(k_out[1], 16 * (NT // 2))

        @block.gpsimd
        def _(pool):
            n_pool(pool)

        @block.scalar
        def _(act):
            n_act(act)
            nc.scalar.activation(ba[:, 0:NT, 0:H], ba[:, 0:NT, 0:H], ACT.Sigmoid).then_inc(gate_act, 1)
            nc.scalar.activation(ba[0:NS, NT, 0:H], ba[0:NS, NT, 0:H], ACT.Sigmoid).then_inc(gate_act, 1)
            act.wait_ge(rate_in, 32)
            nc.scalar.activation(a_log[:, :], a_log[:, :], ACT.Exp).then_inc(gate_act, 1)
            act.wait_ge(gate_dve, 4)
            nc.scalar.activation(a_neg[:, :, :], a_neg[:, :, :], ACT.Exp).then_inc(gate_act, 1)
            act.wait_ge(gate_act, 4)
            nc.scalar.activation(a_neg[:, :, :], a_neg[:, :, :], ACT.Ln, bias=c["ones"][:, 0:1], scale=1.0).then_inc(gate_act, 1)

        @block.tensor
        def _(pe):
            n_pe(pe)
            for t in range(4 * H):
                if t >= 2:
                    pe.wait_ge(normed, t - 1)
                spread(t, psum[t % 2]).then_inc(spread_done, 1)
            pe.wait_ge(normed, 4 * H)
            for t in range(NT + 1):
                n = P if t < NT else NS
                if t >= 2:
                    pe.wait_ge(k_kept, t - 1)
                for h in range(H):
                    mm = nc.tensor.transpose(k_ps[0:n, t % 2, h * P:(h + 1) * P], feat[:, 4 * H + h, t * P:t * P + n],
                                             c["ident"][:, :])
                mm.then_inc(k_turned, 1)

        @block.vector
        def _(dve):
            dve.wait_ge(rate_in, 32)
            a = ba[:, :, H:2 * H]
            nc.vector.memset(a_pos[:, NT, :], 0.0).then_inc(gate_dve, 1)
            bias = over(dt_bias[:, :], 1, [P, NT, H])
            nc.vector.tensor_tensor(a_pos[:, 0:NT, :], ba[:, 0:NT, H:2 * H], bias, ALU.add).then_inc(gate_dve, 1)
            dve.wait_ge(gate_dve, 2)
            nc.vector.tensor_tensor(a_pos[0:NS, NT, :], ba[0:NS, NT, H:2 * H], dt_bias[0:NS, :], ALU.add).then_inc(gate_dve, 1)
            dve.wait_ge(gate_dve, 3)
            nc.vector.scalar_tensor_tensor(out=a_neg[:, :, :], in0=a_pos[:, :, :], scalar=-1.0, in1=a_pos[:, :, :],
                                           op0=ALU.mult, op1=ALU.min).then_inc(gate_dve, 1)

            n_dve(dve)
            for t, (j, _, gain) in enumerate(order):
                dve.wait_ge(spread_done, t + 1)
                x = feat[:, j, :].rearrange("p (g t) -> p g t", g=NG)
                nc.vector.scalar_tensor_tensor(out=x, in0=x, scalar=gain, in1=psum[t % 2][:, :, 0:TG], op0=ALU.mult,
                                               op1=ALU.mult).then_inc(normed, 1)
            for t in range(NT + 1):
                n = P if t < NT else NS
                dve.wait_ge(k_turned, t + 1)
                if t >= 2:
                    dve.wait_ge(k_out[t % 2], 16 * (t // 2))
                nc.vector.tensor_copy(k_tok[t % 2][0:n, :], k_ps[0:n, t % 2, :]).then_inc(k_kept, 1)
            dve.wait_ge(gate_act, 5)
            nc.vector.scalar_tensor_tensor(out=a_pos[:, :, :], in0=a_pos[:, :, :], scalar=0.0, in1=a_neg[:, :, :],
                                           op0=ALU.max, op1=ALU.add).then_inc(gate_dve, 1)
            dve.wait_ge(gate_dve, 5)
            nc.vector.scalar_tensor_tensor(out=a, in0=a_pos[:, :, :], scalar=-1.0, in1=over(a_log[:, :], 1, [P, NT + 1, H]),
                                           op0=ALU.mult, op1=ALU.mult)
    m.free()


def chunk_masks(nc, m, sem, n, name):
    up = m.sb(f"{name}_up", [n, n])
    far = m.sb(f"{name}_far", [n, n])
    zeroed, ready = sem(f"{name}_zeroed"), sem(f"{name}_ready")

    def emit(pool):
        blocks = n // NL if n == NS else 1
        width = n // blocks
        pool.memset(up[:, :], 1.0).then_inc(zeroed, 1)
        pool.memset(far[:, :], 0.0).then_inc(zeroed, 1)
        pool.wait_ge(zeroed, 2)
        k = 0
        for t, fill in ((up, 0.0), (far, NEG)):
            v = t[:, :].rearrange("p (b l) -> p b l", b=blocks)
            pool.affine_select(out=v, in_=v, compare_op=ALU.is_ge, fill=fill, base=0, pattern=[[width, blocks], [1, width]],
                               channel_multiplier=-1).then_inc(ready, 1)
            k += 1
            if blocks > 1:
                pool.wait_ge(ready, k)
                pool.affine_select(out=v, in_=v, compare_op=ALU.is_ge, fill=fill, base=0,
                                   pattern=[[-width, blocks], [0, width]], channel_multiplier=1).then_inc(ready, 1)
                k += 1
        return k
    return up, far, ready, emit


def level_masks(pool, mask, levels, n, made):
    pool.memset(mask, 0.0).then_inc(made, 1)
    pool.wait_ge(made, 1)
    k = 1
    for level in range(levels):
        b = 1 << level
        v = mask[:, level, :].rearrange("p (a c) -> p a c", c=2 * b)[:, :, 0:b]
        pool.memset(v, 1.0).then_inc(made, 1)
        k += 1
        pool.wait_ge(made, k)
        pool.affine_select(out=v, in_=v, compare_op=ALU.is_ge, fill=0.0, base=-b, pattern=[[-2 * b, n // (2 * b)], [0, b]],
                           channel_multiplier=1).then_inc(made, 1)
        k += 1
        pool.wait_ge(made, k)
        pool.affine_select(out=v, in_=v, compare_op=ALU.is_ge, fill=0.0, base=2 * b - 1,
                           pattern=[[2 * b, n // (2 * b)], [0, b]], channel_multiplier=-1).then_inc(made, 1)
        k += 1
    return k


def delta_prompt(nc, i, o, c, feat, ba, head_out, sem):
    m = Memory(nc)

    def per_slot(name, shape):
        return [m.sb(f"{name}{s}", shape) for s in range(2)]

    W4 = [P, H, P]
    kv = per_slot("c_kv", [P, 2 * H, P])
    row_g, row_b, e_row, ET = (per_slot(n, W4) for n in ("c_row_g", "c_row_b", "c_e_row", "c_ET"))
    AT, PT, kbg, kdec, vb = (per_slot(n, W4) for n in ("c_AT", "c_PT", "c_kbg", "c_kdec", "c_vb"))
    D, DT, M, qg, u, wT, vn = (per_slot(n, W4) for n in ("c_D", "c_DT", "c_M", "c_qg", "c_u", "c_wT", "c_vn"))
    gcum, eg, beg, beta = (per_slot(n, [P, H]) for n in ("c_gcum", "c_eg", "c_beg", "c_beta"))
    S = per_slot("c_S", W4)
    S_dec = m.sb("c_S_dec", W4)
    mask = m.sb("c_mask", [P, NLEV, P])
    up, far, masks_ready, emit_masks = chunk_masks(nc, m, sem, P, "c")
    bank = [[m.ps(f"c_bank{s}{b}", [P, 512]) for b in range(4)] for s in range(2)]

    def heads(ap):
        return ap.rearrange("p (h t) -> p h t", h=H)

    names = ("staged rows_g rows_b identity_put beta_put R_ready B_ready KK_ready KQ_ready C_ready gcum_ready e_row_ready eg_ready arg_ready "
             "ET_ready KE_ready AT_ready PT_ready kt_turned vt_turned beg_ready kbg_ready kdec_ready vb_ready qg_ready "
             "u_product w_product u_kept w_kept wS_ready vn_ready o_ready S_product decayed S_done o_kept").split()
    S_ = {n: sem("c_" + n) for n in names}
    M_product, M_kept, D_product, D_kept, DT_kept = (
        [sem(f"c_{n}{s}") for s in range(2)] for n in ("M_product", "M_kept", "D_product", "D_kept", "DT_kept"))
    mask_made, S_zero, S_out = sem("c_mask_made"), sem("c_S_zero"), sem("c_S_out")
    owner = {"pool": "staged rows_g rows_b identity_put beta_put beg_ready qg_ready",
             "tensor": "C_ready R_ready B_ready KK_ready KQ_ready kt_turned vt_turned u_product w_product wS_ready o_ready S_product",
             "scalar": "gcum_ready e_row_ready eg_ready ET_ready u_kept w_kept o_kept",
             "vector": "arg_ready KE_ready AT_ready PT_ready kbg_ready kdec_ready vb_ready vn_ready decayed S_done"}

    def credit(eng, who):
        for n in owner[who].split():
            eng.sem_inc(S_[n], CREDIT)

    n_mask = 1 + 3 * NLEV

    def odd_even(ap, level, odd):
        b = 1 << level
        return ap.rearrange("p h (a c) -> p (h a) c", c=2 * b)[:, :, odd * b:(odd + 1) * b]

    with nc.Block() as block:
        @block.sync
        def _(sp):
            sp.wait_ge(S_["S_done"], done(NT - 1))
            sp.dma_start(o["gdn_S_prompt"][0, 0].rearrange("h k v -> k h v"), S[0][:, :, :]).then_inc(S_out, 16)
            sp.wait_ge(S_out, 16)

        @block.gpsimd
        def _(pool):
            credit(pool, "pool")
            pool.memset(S[0][:, :, :], 0.0).then_inc(S_zero, 1)
            k = emit_masks(pool)
            level_masks(pool, mask[:, :, :], NLEV, P, mask_made)
            pool.wait_ge(masks_ready, k)
            with pool.Fori(0, NT // 2) as it:
                for s in range(2):
                    n = 2 * it + s
                    pool.wait_ge(S_["S_done"], done(n - 2))
                    pool.wait_ge(S_["o_kept"], done(n - 2))
                    for t in (D[s], DT[s]):
                        ins = nc.gpsimd.tensor_tensor(t[:, :, :], over(c["ident"][:, :], 1, W4), over(c["ident"][:, :], 1, W4), ALU.mult)
                    ins.then_inc(S_["identity_put"], 1)
                    nc.gpsimd.tensor_tensor(row_g[s][:, :, :], over(up[:, :], 1, W4),
                                            over(ba[:, bass.ds(n, 1), H:2 * H].rearrange("p o h -> p (o h)"), 2, W4),
                                            ALU.mult).then_inc(S_["rows_g"], 1)
                    nc.gpsimd.tensor_tensor(row_b[s][:, :, :], over(c["ident"][:, :], 1, W4),
                                            over(ba[:, bass.ds(n, 1), 0:H].rearrange("p o h -> p (o h)"), 2, W4),
                                            ALU.mult).then_inc(S_["rows_b"], 1)
                    nc.gpsimd.tensor_copy(kv[s][:, :, :], feat[:, H:3 * H, bass.ds(n * P, P)]).then_inc(S_["staged"], 1)
                    nc.gpsimd.tensor_copy(beta[s][:, :], ba[:, bass.ds(n, 1), 0:H].rearrange("p o h -> p (o h)")
                                          ).then_inc(S_["beta_put"], 1)
                for s in range(2):
                    n = 2 * it + s
                    pool.wait_ge(S_["beta_put"], done(n))
                    pool.wait_ge(S_["eg_ready"], done(n))
                    pool.wait_ge(S_["e_row_ready"], done(n))
                    nc.gpsimd.tensor_tensor(beg[s][:, :], eg[s][:, :], beta[s][:, :], ALU.mult).then_inc(S_["beg_ready"], 1)
                    nc.gpsimd.tensor_tensor(qg[s][:, :, :], feat[:, 0:H, bass.ds(n * P, P)], e_row[s][:, :, :],
                                            ALU.mult).then_inc(S_["qg_ready"], 1)

        @block.tensor
        def _(pe):
            credit(pe, "tensor")
            pe.wait_ge(masks_ready, 2)
            with pe.Fori(0, NT // 2) as it:
                for s in range(2):
                    n = 2 * it + s
                    b = bank[s]
                    pe.wait_ge(S_["rows_g"], done(n))
                    nc.tensor.matmul(b[3][:, 0:H], up[:, :], ba[:, bass.ds(n, 1), H:2 * H].rearrange("p o h -> p (o h)"),
                                     start=True, stop=True).then_inc(S_["C_ready"], 1)
                    nc.tensor.matmul(b[0][:, :], c["ones"][:, :], row_g[s][:, :, :], start=True, stop=True
                                     ).then_inc(S_["R_ready"], 1)
                    pe.wait_ge(S_["rows_b"], done(n))
                    nc.tensor.matmul(b[1][:, :], c["ones"][:, :], row_b[s][:, :, :], start=True, stop=True
                                     ).then_inc(S_["B_ready"], 1)
                    pe.wait_ge(S_["staged"], done(n))
                    for h in range(H):
                        mm = nc.tensor.matmul(b[2][:, h * P:(h + 1) * P], kv[s][:, h, :], kv[s][:, h, :], start=True, stop=True)
                    mm.then_inc(S_["KK_ready"], 1)
                    pe.wait_ge(S_["gcum_ready"], done(n))
                    for h in range(H):
                        mm = nc.tensor.matmul(b[3][:, h * P:(h + 1) * P], kv[s][:, h, :],
                                              feat[:, h, bass.ds(n * P, P)], start=True, stop=True)
                    mm.then_inc(S_["KQ_ready"], 1)
                for s in range(2):
                    n = 2 * it + s
                    b = bank[s]
                    pe.wait_ge(S_["e_row_ready"], done(n))
                    for h in range(H):
                        mm = nc.tensor.transpose(b[0][:, h * P:(h + 1) * P], kv[s][:, h, :], c["ident"][:, :])
                    mm.then_inc(S_["kt_turned"], 1)
                    pe.wait_ge(S_["AT_ready"], done(n))
                    for h in range(H):
                        mm = nc.tensor.transpose(b[1][:, h * P:(h + 1) * P], kv[s][:, H + h, :], c["ident"][:, :])
                    mm.then_inc(S_["vt_turned"], 1)
                for level in range(NLEV):
                    for s in range(2):
                        n = 2 * it + s
                        if level == 0:
                            pe.wait_ge(S_["AT_ready"], done(n))
                            pe.wait_ge(S_["identity_put"], done(n))
                        else:
                            pe.wait_ge(D_kept[s], levels_done(it, level - 1, NLEV - 1))
                        for h in range(H):
                            mm = nc.tensor.matmul(bank[s][2][:, h * P:(h + 1) * P], AT[s][:, h, :], D[s][:, h, :],
                                                  start=True, stop=True)
                        mm.then_inc(M_product[s], 1)
                    for s in range(2):
                        n = 2 * it + s
                        pe.wait_ge(M_kept[s], levels_done(it, level))
                        if level == 0:
                            pe.wait_ge(S_["PT_ready"], done(n))
                        else:
                            pe.wait_ge(DT_kept[s], levels_done(it, level - 1))
                        for h in range(H):
                            if level < NLEV - 1:
                                nc.tensor.matmul(bank[s][3][:, h * HALF:(h + 1) * HALF], DT[s][:, h, :],
                                                 odd_even(M[s][:, h:h + 1, :], level, 0), start=True, stop=True)
                            mm = nc.tensor.matmul(bank[s][3][:, (H + h) * HALF:(H + h + 1) * HALF], M[s][:, h, :],
                                                  odd_even(DT[s][:, h:h + 1, :], level, 1), start=True, stop=True)
                        mm.then_inc(D_product[s], 1)
                for s in range(2):
                    n = 2 * it + s
                    b = bank[s]
                    pe.wait_ge(DT_kept[s], levels_done(it, NLEV - 1))
                    pe.wait_ge(S_["vb_ready"], done(n))
                    for h in range(H):
                        mm = nc.tensor.matmul(b[0][:, h * P:(h + 1) * P], DT[s][:, h, :], vb[s][:, h, :], start=True, stop=True)
                    mm.then_inc(S_["u_product"], 1)
                    for h in range(H):
                        mm = nc.tensor.matmul(b[1][:, h * P:(h + 1) * P], kbg[s][:, h, :], DT[s][:, h, :], start=True, stop=True)
                    mm.then_inc(S_["w_product"], 1)
                for s in range(2):
                    n = 2 * it + s
                    b = bank[s]
                    pe.wait_ge(S_["w_kept"], done(n))
                    pe.wait_ge(S_["S_done"], done(n - 1))
                    for h in range(H):
                        mm = nc.tensor.matmul(b[2][:, h * P:(h + 1) * P], wT[s][:, h, :], S[s][:, h, :], start=True, stop=True)
                    mm.then_inc(S_["wS_ready"], 1)
                    pe.wait_ge(S_["vn_ready"], done(n))
                    pe.wait_ge(S_["u_kept"], done(n))
                    for h in range(H):
                        mm = nc.tensor.matmul(b[0][:, h * P:(h + 1) * P], kdec[s][:, h, :], vn[s][:, h, :], start=True, stop=True)
                    mm.then_inc(S_["S_product"], 1)
                    pe.wait_ge(S_["qg_ready"], done(n))
                    for h in range(H):
                        nc.tensor.matmul(b[3][:, h * P:(h + 1) * P], S[s][:, h, :], qg[s][:, h, :], start=True, stop=False)
                        mm = nc.tensor.matmul(b[3][:, h * P:(h + 1) * P], vn[s][:, h, :], PT[s][:, h, :], start=False, stop=True)
                    mm.then_inc(S_["o_ready"], 1)

        @block.scalar
        def _(act):
            credit(act, "scalar")
            nc.scalar.preload_act_table(ACT.Exp)
            with act.Fori(0, NT // 2) as it:
                for s in range(2):
                    n = 2 * it + s
                    b = bank[s]
                    act.wait_ge(S_["C_ready"], done(n))
                    nc.scalar.copy(gcum[s][:, :], b[3][:, 0:H]).then_inc(S_["gcum_ready"], 1)
                    act.wait_ge(S_["gcum_ready"], done(n))
                    nc.scalar.activation(eg[s][:, :], gcum[s][:, :], ACT.Exp).then_inc(S_["eg_ready"], 1)
                    act.wait_ge(S_["arg_ready"], done(n))
                    nc.scalar.activation(ET[s][:, :, :], ET[s][:, :, :], ACT.Exp).then_inc(S_["ET_ready"], 1)
                    nc.scalar.activation(e_row[s][:, :, :], heads(b[0][:, :]), ACT.Exp).then_inc(S_["e_row_ready"], 1)
                for s in range(2):
                    n = 2 * it + s
                    act.wait_ge(S_["w_product"], done(n))
                    nc.scalar.copy(wT[s][:, :, :], heads(bank[s][1][:, :])).then_inc(S_["w_kept"], 1)
                    nc.scalar.copy(u[s][:, :, :], heads(bank[s][0][:, :])).then_inc(S_["u_kept"], 1)
                for s in range(2):
                    n = 2 * it + s
                    act.wait_ge(S_["o_ready"], done(n))
                    nc.scalar.copy(head_out[:, 0:H, bass.ds(n * P, P)], heads(bank[s][3][:, :])).then_inc(S_["o_kept"], 1)

        @block.vector
        def _(dve):
            credit(dve, "vector")
            dve.wait_ge(masks_ready, 2)
            dve.wait_ge(mask_made, n_mask)
            dve.wait_ge(S_zero, 1)
            with dve.Fori(0, NT // 2) as it:
                for s in range(2):
                    n = 2 * it + s
                    b = bank[s]
                    dve.wait_ge(S_["R_ready"], done(n))
                    dve.wait_ge(S_["gcum_ready"], done(n))
                    for h in range(H):
                        ins = nc.vector.scalar_tensor_tensor(
                            out=ET[s][:, h, :], in0=b[0][:, h * P:(h + 1) * P], scalar=gcum[s][:, h:h + 1], in1=far[:, :],
                            op0=ALU.subtract, op1=ALU.add)
                    ins.then_inc(S_["arg_ready"], 1)
                    dve.wait_ge(S_["KK_ready"], done(n))
                    dve.wait_ge(S_["ET_ready"], done(n))
                    nc.vector.tensor_tensor(AT[s][:, :, :], heads(b[2][:, :]), ET[s][:, :, :], ALU.mult).then_inc(S_["KE_ready"], 1)
                    dve.wait_ge(S_["KE_ready"], done(n))
                    dve.wait_ge(S_["B_ready"], done(n))
                    nc.vector.tensor_tensor(AT[s][:, :, :], heads(b[1][:, :]), AT[s][:, :, :], ALU.mult).then_inc(S_["AT_ready"], 1)
                    dve.wait_ge(S_["KQ_ready"], done(n))
                    nc.vector.tensor_tensor(PT[s][:, :, :], heads(b[3][:, :]), ET[s][:, :, :], ALU.mult).then_inc(S_["PT_ready"], 1)

                def token_major(s):
                    n = 2 * it + s
                    b = bank[s]
                    dve.wait_ge(S_["kt_turned"], done(n))
                    dve.wait_ge(S_["beg_ready"], done(n))
                    nc.vector.tensor_tensor(kbg[s][:, :, :], heads(b[0][:, :]), over(beg[s][:, :], 2, W4), ALU.mult
                                            ).then_inc(S_["kbg_ready"], 1)
                    nc.vector.tensor_tensor(kdec[s][:, :, :], heads(b[0][:, :]),
                                            ET[s][:, :, P - 1:P].to_broadcast(W4), ALU.mult).then_inc(S_["kdec_ready"], 1)
                    dve.wait_ge(S_["vt_turned"], done(n))
                    nc.vector.tensor_tensor(vb[s][:, :, :], heads(b[1][:, :]),
                                            over(ba[:, bass.ds(n, 1), 0:H].rearrange("p o h -> p (o h)"), 2, W4),
                                            ALU.mult).then_inc(S_["vb_ready"], 1)

                for level in range(NLEV):
                    for s in range(2):
                        n = 2 * it + s
                        dve.wait_ge(M_product[s], levels_done(it, level))
                        nc.vector.tensor_tensor(M[s][:, :, :], heads(bank[s][2][:, :]), over(mask[:, level, :], 1, W4),
                                                ALU.mult).then_inc(M_kept[s], 1)
                    if level == 0:
                        token_major(0)
                        token_major(1)
                    for s in range(2):
                        n = 2 * it + s
                        dve.wait_ge(D_product[s], levels_done(it, level))
                        b = 1 << level
                        if level < NLEV - 1:
                            d = odd_even(D[s][:, :, :], level, 0)
                            nc.vector.tensor_tensor(d, d, bank[s][3][:, 0:H * HALF].rearrange("p (a b) -> p a b", b=b),
                                                    ALU.subtract).then_inc(D_kept[s], 1)
                        d = odd_even(DT[s][:, :, :], level, 1)
                        nc.vector.tensor_tensor(d, d, bank[s][3][:, H * HALF:2 * H * HALF].rearrange("p (a b) -> p a b", b=b),
                                                ALU.subtract).then_inc(DT_kept[s], 1)
                for s in range(2):
                    n = 2 * it + s
                    b = bank[s]
                    dve.wait_ge(S_["e_row_ready"], done(n))
                    dve.wait_ge(S_["S_done"], done(n - 1))
                    nc.vector.tensor_tensor(S_dec[:, :, :], S[s][:, :, :], e_row[s][:, :, P - 1:P].to_broadcast(W4),
                                            ALU.mult).then_inc(S_["decayed"], 1)
                    dve.wait_ge(S_["wS_ready"], done(n))
                    dve.wait_ge(S_["u_kept"], done(n))
                    nc.vector.tensor_tensor(vn[s][:, :, :], u[s][:, :, :], heads(b[2][:, :]), ALU.subtract
                                            ).then_inc(S_["vn_ready"], 1)
                    dve.wait_ge(S_["S_product"], done(n))
                    dve.wait_ge(S_["decayed"], done(n))
                    nc.vector.tensor_tensor(S[1 - s][:, :, :], heads(b[0][:, :]), S_dec[:, :, :], ALU.add
                                            ).then_inc(S_["S_done"], 1)
    m.free()


def delta_sample(nc, i, o, c, feat, ba, head_out, sem):
    m = Memory(nc)
    R, C = [NS, H, NS], [NS, H, DH]
    LEV = 2
    row_g, row_b, ET, AT, PT, D, DT, M = (m.sb(f"s_{n}", R) for n in ("row_g", "row_b", "ET", "AT", "PT", "D", "DT", "M"))
    kbg, kdec, vb, vn = (m.sb(f"s_{n}", C) for n in ("kbg", "kdec", "vb", "vn"))
    e_row = m.sb("s_e_row", [P, H, NS])
    wq = m.sb("s_wq", [P, H, NB, 2 * NL])
    uT, vnT, qS = (m.sb(f"s_{n}", [P, H, NS]) for n in ("uT", "vnT", "qS"))
    gcum, eg, beg, dec = (m.sb(f"s_{n}", [NS, H]) for n in ("gcum", "eg", "beg", "dec"))
    state = m.sb("s_state", [P, NB * H, DH])
    own = m.sb("s_own", [NS, NB])
    spread = m.sb("s_spread", [NS, NB, DH])
    mask = m.sb("s_mask", [NS, LEV, NS])
    up, far, masks_ready, emit_masks = chunk_masks(nc, m, sem, NS, "s")
    bank = [m.ps(f"s_bank{b}", [P, 512]) for b in range(6)]
    wide = m.ps("s_wide", [P, NB, DH])

    state_in, state_out = sem("s_state_in"), sem("s_state_out")
    own_made, mask_made, rows_ready, to_pe, pe_done = (sem(f"s_{n}") for n in ("own_made", "mask_made", "rows_ready", "to_pe", "pe_done"))
    act_done, dve_done, q_put, identity_put = sem("s_act_done"), sem("s_dve_done"), sem("s_q_put"), sem("s_identity_put")
    PE = {n: k + 1 for k, n in enumerate("gcum row beta KK KQ k_turned v_turned M0 D0 M1 D1 u w wqS vn_turned o S0 S1 S2 S3".split())}
    SC = {n: k + 1 for k, n in enumerate("gcum eg e_row ET u w qS".split())}
    DV = {n: k + 1 for k, n in enumerate(
        "arg dec KE AT PT beg kbg kdec vb M0 D0 DT0 M1 DT1 vnT vn o "
        "spread0 decay0 S0 spread1 decay1 S1 spread2 decay2 S2 spread3 decay3 S3".split())}

    def cols(ap, n=NS, rows=NS):
        return ap[0:rows, 0:H * n].rearrange("p (h t) -> p h t", h=H)

    def pairs_of(ap, level, odd):
        b = 1 << level
        return ap.rearrange("p h (a c) -> p (h a) c", c=2 * b)[:, :, odd * b:(odd + 1) * b]

    b_gate = ba[0:NS, NT, 0:H]
    g_gate = ba[0:NS, NT, H:2 * H]
    q, k, v = (feat[:, x * H:(x + 1) * H, SEQ:T] for x in range(3))

    with nc.Block() as block:
        @block.sync
        def _(sp):
            sp.dma_start(state[:, :, :], i["state_gdn_S"][0].rearrange("b h k v -> k (b h) v")).then_inc(state_in, 16)
            sp.wait_ge(dve_done, DV["S3"])
            sp.dma_start(o["gdn_S_sample"][0].rearrange("b h k v -> k (b h) v"), state[:, :, :]).then_inc(state_out, 16)
            sp.wait_ge(state_out, 16)

        @block.gpsimd
        def _(pool):
            kk = emit_masks(pool)
            level_masks(pool, mask[:, :, :], LEV, NS, mask_made)
            pool.memset(own[:, :], 1.0).then_inc(own_made, 1)
            pool.wait_ge(own_made, 1)
            pool.affine_select(out=own[:, :], in_=own[:, :], compare_op=ALU.is_ge, fill=0.0, base=0, pattern=[[-NL, NB]],
                               channel_multiplier=1).then_inc(own_made, 1)
            pool.wait_ge(own_made, 2)
            pool.affine_select(out=own[:, :], in_=own[:, :], compare_op=ALU.is_ge, fill=0.0, base=NL - 1, pattern=[[NL, NB]],
                               channel_multiplier=-1).then_inc(own_made, 1)
            pool.wait_ge(masks_ready, kk)
            nc.gpsimd.tensor_tensor(row_g[:, :, :], over(up[:, :], 1, R), over(g_gate, 2, R), ALU.mult).then_inc(rows_ready, 1)
            nc.gpsimd.tensor_tensor(row_b[:, :, :], over(c["ident"][0:NS, 0:NS], 1, R), over(b_gate, 2, R), ALU.mult
                                    ).then_inc(rows_ready, 1)
            for t in (D, DT):
                nc.gpsimd.tensor_copy(t[:, :, :], over(c["ident"][0:NS, 0:NS], 1, R)).then_inc(identity_put, 1)
            pool.wait_ge(act_done, SC["e_row"])
            nc.gpsimd.tensor_tensor(wq[:, :, :, NL:2 * NL], q.rearrange("p h (b l) -> p h b l", b=NB),
                                    e_row[:, :, :].rearrange("p h (b l) -> p h b l", b=NB), ALU.mult).then_inc(q_put, 1)

        @block.tensor
        def _(pe):
            pe.wait_ge(rows_ready, 2)
            nc.tensor.matmul(bank[3][0:NS, 0:H], up[:, :], g_gate, start=True, stop=True).then_inc(pe_done, 1)
            ones = c["ones"][0:NS, :]
            nc.tensor.matmul(bank[0][:, 0:H * NS], ones, row_g[:, :, :], start=True, stop=True).then_inc(pe_done, 1)
            nc.tensor.matmul(bank[1][0:NS, 0:H * NS], ones[:, 0:NS], row_b[:, :, :], start=True, stop=True).then_inc(pe_done, 1)
            for h in range(H):
                mm = nc.tensor.matmul(cols(bank[2])[:, h, :], k[:, h, :], k[:, h, :], start=True, stop=True)
            mm.then_inc(pe_done, 1)
            pe.wait_ge(act_done, SC["gcum"])
            for h in range(H):
                mm = nc.tensor.matmul(cols(bank[3])[:, h, :], k[:, h, :], q[:, h, :], start=True, stop=True)
            mm.then_inc(pe_done, 1)
            for x, b in ((k, 4), (v, 5)):
                for h in range(H):
                    mm = nc.tensor.transpose(bank[b][0:NS, h * DH:(h + 1) * DH], x[:, h, :], c["ident"][:, :])
                mm.then_inc(pe_done, 1)
            pe.wait_ge(identity_put, 2)
            for level in range(LEV):
                pe.wait_ge(dve_done, DV["PT"] if level == 0 else DV["D0"])
                for h in range(H):
                    mm = nc.tensor.matmul(cols(bank[2])[:, h, :], AT[:, h, :], D[:, h, :], start=True, stop=True)
                mm.then_inc(pe_done, 1)
                pe.wait_ge(dve_done, DV[f"M{level}"])
                half = NS // 2
                for h in range(H):
                    if level < LEV - 1:
                        nc.tensor.matmul(bank[3][0:NS, h * half:(h + 1) * half], DT[:, h, :],
                                         pairs_of(M[:, h:h + 1, :], level, 0), start=True, stop=True)
                    mm = nc.tensor.matmul(bank[3][0:NS, (H + h) * half:(H + h + 1) * half], M[:, h, :],
                                          pairs_of(DT[:, h:h + 1, :], level, 1), start=True, stop=True)
                mm.then_inc(pe_done, 1)
            pe.wait_ge(dve_done, DV["DT1"])
            for h in range(H):
                mm = nc.tensor.matmul(cols(bank[0], NS, P)[:, h, :], vb[:, h, :], DT[:, h, :], start=True, stop=True)
            mm.then_inc(pe_done, 1)
            for h in range(H):
                mm = nc.tensor.matmul(bank[1][:, h * NS:(h + 1) * NS], kbg[:, h, :], DT[:, h, :], start=True, stop=True)
            mm.then_inc(pe_done, 1)
            pe.wait_ge(act_done, SC["w"])
            pe.wait_ge(q_put, 1)
            pe.wait_ge(state_in, 16)
            for b in range(NB):
                for h in range(H):
                    at = (h * NB + b) * 2 * NL
                    mm = nc.tensor.matmul(bank[2][:, at:at + 2 * NL], state[:, b * H + h, :], wq[:, h, b, :], start=True, stop=True)
            mm.then_inc(pe_done, 1)
            pe.wait_ge(dve_done, DV["vnT"])
            for h in range(H):
                mm = nc.tensor.transpose(bank[4][0:NS, h * DH:(h + 1) * DH], vnT[:, h, :], c["ident"][:, :])
            mm.then_inc(pe_done, 1)
            pe.wait_ge(dve_done, DV["vn"])
            for h in range(H):
                mm = nc.tensor.matmul(bank[5][:, h * NS:(h + 1) * NS], vn[:, h, :], PT[:, h, :], start=True, stop=True)
            mm.then_inc(pe_done, 1)
            for h in range(H):
                pe.wait_ge(dve_done, DV[f"spread{h}"])
                for g in range(2):
                    mm = nc.tensor.matmul(wide[:, g * 4:g * 4 + 4, :], kdec[:, h, :], spread[:, g * 4:g * 4 + 4, :],
                                          start=True, stop=True)
                mm.then_inc(pe_done, 1)

        @block.scalar
        def _(act):
            act.wait_ge(pe_done, PE["gcum"])
            nc.scalar.copy(gcum[:, :], bank[3][0:NS, 0:H]).then_inc(act_done, 1)
            act.wait_ge(act_done, SC["gcum"])
            nc.scalar.activation(eg[:, :], gcum[:, :], ACT.Exp).then_inc(act_done, 1)
            act.wait_ge(pe_done, PE["row"])
            nc.scalar.activation(e_row[:, :, :], cols(bank[0], NS, P), ACT.Exp).then_inc(act_done, 1)
            act.wait_ge(dve_done, DV["arg"])
            nc.scalar.activation(ET[:, :, :], ET[:, :, :], ACT.Exp).then_inc(act_done, 1)
            act.wait_ge(pe_done, PE["w"])
            nc.scalar.copy(uT[:, :, :], cols(bank[0], NS, P)).then_inc(act_done, 1)
            nc.scalar.copy(wq[:, :, :, 0:NL], cols(bank[1], NS, P).rearrange("p h (b l) -> p h b l", b=NB)).then_inc(act_done, 1)
            act.wait_ge(dve_done, DV["vnT"])
            nc.scalar.copy(qS[:, :, :].rearrange("p h (b l) -> p (h b) l", b=NB),
                           bank[2][:, 0:2 * H * NS].rearrange("p (a l) -> p a l", l=2 * NL)[:, :, NL:2 * NL]).then_inc(act_done, 1)

        @block.vector
        def _(dve):
            dve.wait_ge(masks_ready, 4)
            dve.wait_ge(mask_made, 1 + 3 * LEV)
            dve.wait_ge(act_done, SC["e_row"])
            for h in range(H):
                ins = nc.vector.scalar_tensor_tensor(out=ET[:, h, :], in0=cols(bank[0])[:, h, :], scalar=gcum[:, h:h + 1],
                                                     in1=far[:, :], op0=ALU.subtract, op1=ALU.add)
            ins.then_inc(dve_done, 1)
            dve.wait_ge(act_done, SC["ET"])
            nc.vector.tensor_reduce(out=dec[:, :], in_=ET[:, :, :].rearrange("p h (b l) -> p h b l", b=NB)[:, :, :, NL - 1],
                                    axis=AX.X, op=ALU.add).then_inc(dve_done, 1)
            dve.wait_ge(pe_done, PE["KK"])
            nc.vector.tensor_tensor(AT[:, :, :], cols(bank[2]), ET[:, :, :], ALU.mult).then_inc(dve_done, 1)
            dve.wait_ge(dve_done, DV["KE"])
            nc.vector.tensor_tensor(AT[:, :, :], cols(bank[1]), AT[:, :, :], ALU.mult).then_inc(dve_done, 1)
            dve.wait_ge(pe_done, PE["KQ"])
            nc.vector.tensor_tensor(PT[:, :, :], cols(bank[3]), ET[:, :, :], ALU.mult).then_inc(dve_done, 1)
            nc.vector.tensor_tensor(beg[:, :], eg[:, :], b_gate, ALU.mult).then_inc(dve_done, 1)
            dve.wait_ge(pe_done, PE["v_turned"])
            dve.wait_ge(dve_done, DV["beg"])
            nc.vector.tensor_tensor(kbg[:, :, :], cols(bank[4], DH), over(beg[:, :], 2, C), ALU.mult).then_inc(dve_done, 1)
            nc.vector.tensor_tensor(kdec[:, :, :], cols(bank[4], DH), over(dec[:, :], 2, C), ALU.mult).then_inc(dve_done, 1)
            nc.vector.tensor_tensor(vb[:, :, :], cols(bank[5], DH), over(b_gate, 2, C), ALU.mult).then_inc(dve_done, 1)
            for level in range(LEV):
                dve.wait_ge(pe_done, PE[f"M{level}"])
                nc.vector.tensor_tensor(M[:, :, :], cols(bank[2]), over(mask[:, level, :], 1, R), ALU.mult).then_inc(dve_done, 1)
                dve.wait_ge(pe_done, PE[f"D{level}"])
                half, b = NS // 2, 1 << level
                if level < LEV - 1:
                    d = pairs_of(D[:, :, :], level, 0)
                    nc.vector.tensor_tensor(d, d, bank[3][0:NS, 0:H * half].rearrange("p (a b) -> p a b", b=b),
                                            ALU.subtract).then_inc(dve_done, 1)
                d = pairs_of(DT[:, :, :], level, 1)
                nc.vector.tensor_tensor(d, d, bank[3][0:NS, H * half:2 * H * half].rearrange("p (a b) -> p a b", b=b),
                                        ALU.subtract).then_inc(dve_done, 1)
            dve.wait_ge(pe_done, PE["wqS"])
            dve.wait_ge(act_done, SC["u"])
            nc.vector.tensor_tensor(vnT[:, :, :].rearrange("p h (b l) -> p (h b) l", b=NB),
                                    uT[:, :, :].rearrange("p h (b l) -> p (h b) l", b=NB),
                                    bank[2][:, 0:2 * H * NS].rearrange("p (a l) -> p a l", l=2 * NL)[:, :, 0:NL],
                                    ALU.subtract).then_inc(dve_done, 1)
            dve.wait_ge(pe_done, PE["vn_turned"])
            nc.vector.tensor_copy(vn[:, :, :], cols(bank[4], DH)).then_inc(dve_done, 1)
            dve.wait_ge(pe_done, PE["o"])
            dve.wait_ge(act_done, SC["qS"])
            nc.vector.tensor_tensor(head_out[:, 0:H, SEQ:T], cols(bank[5], NS, P), qS[:, :, :], ALU.add).then_inc(dve_done, 1)
            dve.wait_ge(state_in, 16)
            for h in range(H):
                dve.wait_ge(dve_done, DV["vn"])
                if h:
                    dve.wait_ge(pe_done, PE[f"S{h - 1}"])
                nc.vector.tensor_tensor(spread[:, :, :], over(vn[:, h, :], 1, [NS, NB, DH]), over(own[:, :], 2, [NS, NB, DH]),
                                        ALU.mult).then_inc(dve_done, 1)
                mine = state[:, :, :].rearrange("p (b h) v -> p b h v", h=H)[:, :, h, :]
                last = e_row[:, h, :].rearrange("p (b l) -> p b l", b=NB)[:, :, NL - 1:NL]
                nc.vector.tensor_tensor(mine, mine, last.to_broadcast([P, NB, DH]), ALU.mult).then_inc(dve_done, 1)
                dve.wait_ge(pe_done, PE[f"S{h}"])
                dve.wait_ge(dve_done, DV[f"decay{h}"])
                nc.vector.tensor_tensor(mine, wide[:, :, :], mine, ALU.add).then_inc(dve_done, 1)
    m.free()


def attention_prompt(nc, i, o, c, feat, head_out, sem):
    m = Memory(nc)
    qk = [m.sb(f"a_qk{s}", [P, 2, SEQ]) for s in range(2)]
    v = [m.sb(f"a_v{s}", [P, NT, DH]) for s in range(2)]
    e = [[m.sb(f"a_e{s}{x}", [P, SEQ]) for x in range(2)] for s in range(2)]
    amapT = [m.sb(f"a_mapT{s}", [P, NT, P]) for s in range(2)]
    nmax, total, inv, w2 = (m.sb(f"a_{n}", [P, 2, 2]) for n in ("nmax", "total", "inv", "w2"))
    ident16 = m.sb("a_ident16", [P, P], BF16)
    far16 = m.sb("a_far16", [P, P], BF16)
    score = [m.ps(f"a_score{x}", [P, SEQ]) for x in range(2)]
    turned = m.ps("a_turned", [P, 2, 4, P])
    out = [m.ps(f"a_out{s}", [P, 512]) for s in range(2)]

    v_in = [sem(f"a_v_in{s}") for s in range(2)]
    made, made2 = sem("a_made"), sem("a_masks")
    qk_staged = sem("a_qk_staged")
    scored, maxed, expd = ([sem(f"a_{n}{x}") for x in range(2)] for n in ("scored", "maxed", "expd"))
    inverted, weighted, scaled, mapped = (sem(f"a_{n}") for n in ("inverted", "weighted", "scaled", "mapped"))
    block_turned, multiplied, out_kept = sem("a_block_turned"), sem("a_multiplied"), sem("a_out_kept")
    half_kept = [sem(f"a_half_kept{x}") for x in range(2)]

    units = [(hh, qb) for hh in range(2) for qb in range(NT)]
    NU = len(units)
    groups, g_of = [], {}
    for u, (hh, qb) in enumerate(units):
        for g in range((qb + 4) // 4):
            g_of[(u, g)] = len(groups)
            groups.append((u, g, min(4, qb + 1 - 4 * g)))
    NGR = len(groups)
    assert NGR % 2 == 0
    v_rows = o["v_prompt"].rearrange("a b (n p) h d -> p (a b n) h d", p=P)

    with nc.Block() as block:
        @block.sync
        def _(sp):
            sp.dma_start(v[0][:, :, :], v_rows[:, :, 0, :]).then_inc(v_in[0], 16)
            sp.dma_start(v[1][:, :, :], v_rows[:, :, 1, :]).then_inc(v_in[1], 16)
            for s in range(2):
                sp.wait_ge(multiplied, (s + 1) * NT + CREDIT)
                sp.dma_start(v[s][:, :, :], v_rows[:, :, 2 + s, :]).then_inc(v_in[s], 16)

        @block.gpsimd
        def _(pool):
            pool.sem_inc(qk_staged, CREDIT)
            pool.memset(ident16[:, :], 0.0).then_inc(made, 1)
            pool.memset(far16[:, :], 0.0).then_inc(made, 1)
            pool.wait_ge(made, 2)
            pool.affine_select(out=ident16[:, :], in_=ident16[:, :], compare_op=ALU.not_equal, fill=1.0, base=0,
                               pattern=[[-1, P]], channel_multiplier=1).then_inc(made2, 1)
            pool.affine_select(out=far16[:, :], in_=far16[:, :], compare_op=ALU.is_ge, fill=NEG, base=0,
                               pattern=[[-1, P]], channel_multiplier=1).then_inc(made2, 1)
            for h in range(H):
                if h >= 2:
                    pool.wait_ge(multiplied, (h - 1) * NT + CREDIT)
                nc.gpsimd.tensor_copy(qk[h % 2][:, 0, :], feat[:, 3 * H + h, 0:SEQ])
                nc.gpsimd.tensor_copy(qk[h % 2][:, 1, :], feat[:, 4 * H + h, 0:SEQ]).then_inc(qk_staged, 1)

        @block.tensor
        def _(pe):
            pe.sem_inc(multiplied, CREDIT)
            pe.wait_ge(made2, 2)

            def scores(it, u):
                hh, qb = units[u]
                if qb == 0:
                    pe.wait_ge(qk_staged, done(2 * it + hh))
                for x in range(2):
                    pe.wait_ge(expd[x], NU * it + (u + 1))
                    lo = x * HALF
                    q = qk[hh][lo:lo + HALF, 0, qb * P:(qb + 1) * P]
                    n = (qb + 1) * P
                    for k0 in range(0, n - P, 512):
                        k1 = min(n - P, k0 + 512)
                        nc.tensor.matmul(score[x][:, k0:k1], q, qk[hh][lo:lo + HALF, 1, k0:k1], start=True, stop=True)
                    nc.tensor.matmul(score[x][:, n - P:n], q, qk[hh][lo:lo + HALF, 1, n - P:n], start=True, stop=False)
                    mm = nc.tensor.matmul(score[x][:, n - P:n], ident16[:, :], far16[:, :], start=False, stop=True)
                    mm.then_inc(scored[x], 1)

            def turn_and_multiply(it, u):
                hh, qb = units[u]
                pe.wait_ge(mapped, NU * it + (u + 1))
                for g in range((qb + 4) // 4):
                    k = g_of[(u, g)]
                    pe.wait_ge(half_kept[k % 2], (NGR // 2) * it + (k // 2 + 1))
                    for j in range(groups[k][2]):
                        mm = nc.tensor.transpose(turned[:, k % 2, j, :], e[u % 2][0][:, (4 * g + j) * P:(4 * g + j + 1) * P],
                                                 c["ident"][:, :])
                    mm.then_inc(block_turned, 1)
                if qb == 0:
                    pe.wait_ge(v_in[hh], 16 * it + 16)
                pe.wait_ge(out_kept, NU * it + (u + 1))
                for g in range((qb + 4) // 4):
                    k = g_of[(u, g)]
                    pe.wait_ge(half_kept[k % 2], (NGR // 2) * it + (k // 2 + 2))
                    for j in range(groups[k][2]):
                        b = 4 * g + j
                        mm = nc.tensor.matmul(out[u % 2][:, 0:P], v[hh][:, b, :], amapT[u % 2][:, b, :], start=(b == 0), stop=(b == qb))
                mm.then_inc(multiplied, 1)

            with pe.Fori(0, H // 2) as it:
                scores(it, 0)
                for u in range(NU):
                    if u + 1 < NU:
                        scores(it, u + 1)
                    turn_and_multiply(it, u)

        def copy_group(nc_copy, eng, it, k):
            u, g, blocks = groups[k]
            eng.wait_ge(block_turned, NGR * it + (k + 1))
            nc_copy(amapT[u % 2][:, 4 * g:4 * g + blocks, :], turned[:, k % 2, 0:blocks, :]).then_inc(half_kept[k % 2], 1)

        @block.scalar
        def _(act):
            act.sem_inc(expd[0], 1)
            act.sem_inc(expd[1], 1)
            act.sem_inc(half_kept[0], 1)
            act.sem_inc(out_kept, 2)
            nc.scalar.preload_act_table(ACT.Exp)

            def exps(it, u):
                hh, qb = units[u]
                n = (qb + 1) * P
                act.wait_ge(multiplied, NU * it + (u + 1))
                for x in range(2):
                    act.wait_ge(maxed[x], NU * it + (u + 1))
                    nc.scalar.activation(e[u % 2][x][:, 0:n], score[x][:, 0:n], ACT.Exp, bias=nmax[:, u % 2, x:x + 1], scale=1.0,
                                         accum_out=total[:, u % 2, x:x + 1]).then_inc(expd[x], 1)

            def rest(it, u):
                hh, qb = units[u]
                for g in range((qb + 4) // 4):
                    if g_of[(u, g)] % 2 == 0:
                        copy_group(nc.scalar.copy, act, it, g_of[(u, g)])
                act.wait_ge(multiplied, NU * it + (u + 1 + CREDIT))
                nc.scalar.copy(head_out[:, bass.ds(2 * it + (H + hh), 1), qb * P:(qb + 1) * P].rearrange("p o t -> p (o t)"),
                               out[u % 2][:, 0:P]).then_inc(out_kept, 1)

            with act.Fori(0, H // 2) as it:
                exps(it, 0)
                for u in range(NU):
                    if u + 1 < NU:
                        exps(it, u + 1)
                    rest(it, u)
            act.wait_ge(v_in[0], 32)
            act.wait_ge(v_in[1], 32)

        @block.vector
        def _(dve):
            dve.sem_inc(half_kept[1], 1)

            def maxes(it, u):
                hh, qb = units[u]
                n = (qb + 1) * P
                for x in range(2):
                    dve.wait_ge(scored[x], NU * it + (u + 1))
                    nc.vector.tensor_reduce(out=nmax[:, u % 2, x:x + 1], in_=score[x][:, 0:n], axis=AX.X, op=ALU.max, negate=True
                                            ).then_inc(maxed[x], 1)

            def difference(it, u):
                hh, qb = units[u]
                n = (qb + 1) * P
                s = u % 2
                for x in range(2):
                    dve.wait_ge(expd[x], NU * it + (u + 2))
                nc.vector.reciprocal(inv[:, s, :], total[:, s, :]).then_inc(inverted, 1)
                dve.wait_ge(inverted, NU * it + (u + 1))
                nc.vector.tensor_scalar(e[s][0][:, 0:n], e[s][0][:, 0:n], inv[:, s, 0:1], None, ALU.mult).then_inc(scaled, 1)
                nc.vector.tensor_tensor(w2[:, s, 0:1], inv[:, s, 1:2], c["neglam"][:, :], ALU.mult).then_inc(weighted, 1)
                dve.wait_ge(scaled, NU * it + (u + 1))
                dve.wait_ge(weighted, NU * it + (u + 1))
                nc.vector.scalar_tensor_tensor(out=e[s][0][:, 0:n], in0=e[s][1][:, 0:n], scalar=w2[:, s, 0:1],
                                               in1=e[s][0][:, 0:n], op0=ALU.mult, op1=ALU.add).then_inc(mapped, 1)

            with dve.Fori(0, H // 2) as it:
                maxes(it, 0)
                for u in range(NU):
                    difference(it, u)
                    if u + 1 < NU:
                        maxes(it, u + 1)
                    hh, qb = units[u]
                    for g in range((qb + 4) // 4):
                        if g_of[(u, g)] % 2 == 1:
                            copy_group(nc.vector.tensor_copy, dve, it, g_of[(u, g)])
    m.free()


def attention_sample(nc, i, o, c, feat, head_out, sem):
    m = Memory(nc)
    RW = 2 * NL
    NR = H * RW
    key_in = [m.sb(f"p_key{s}", [P, NPG, GW]) for s in range(2)]
    val_in = [m.sb(f"p_val{s}", [P, NPG, GW]) for s in range(2)]
    v_new = m.sb("p_v_new", [NS, GW])
    keyT = [m.sb(f"p_keyT{s}", [P, H, PAST]) for s in range(2)]
    q_pad = [m.sb(f"p_q{s}", [P, H * (NR + RW)]) for s in range(2)]
    e = [m.sb(f"p_e{s}", [NR, PAST + NS]) for s in range(2)]
    fresh = [m.sb(f"p_fresh{s}", [NR, NS]) for s in range(2)]
    mapT = [m.sb(f"p_mapT{s}", [P, NPG, H * NL]) for s in range(2)]
    mapT_new = [m.sb(f"p_mapTn{s}", [NS, H * NL]) for s in range(2)]
    stat = [m.sb(f"p_stat{s}", [NR, 8]) for s in range(2)]
    maskT = m.sb("p_maskT", [NS, NB, NR])
    mask = m.sb("p_mask", [NR, NB, NS])
    sign_row = m.sb("p_sign_row", [1, NR])
    sign = m.sb("p_sign", [NR, 1])
    key_ps = m.ps("p_key_ps", [P, H, PAST])
    score = m.ps("p_score", [P, 512])
    fresh_ps = m.ps("p_fresh_ps", [P, 512])
    turned = m.ps("p_turned", [P, 512])
    out = m.ps("p_out", [P, 512])

    k_in, v_in = ([sem(f"p_{n}{s}") for s in range(2)] for n in ("k_in", "v_in"))
    vn_in, made, setup_ps, setup_sb = sem("p_vn_in"), sem("p_made"), sem("p_setup_ps"), sem("p_setup_sb")
    names = "key_turned key_kept q_put scored masked past_max maxed e_past e_fresh summed inverse weight weighted map_turned map_kept multiplied out_kept"
    S_ = {n: sem("p_" + n) for n in names.split()}
    owner = {"tensor": "key_turned scored map_turned multiplied", "gpsimd": "q_put", "scalar": "key_kept e_past e_fresh out_kept",
             "vector": "masked past_max maxed summed inverse weight weighted map_kept"}

    def credit(eng, who):
        for n in owner[who].split():
            eng.sem_inc(S_[n], CREDIT)

    pool_k = i["cache_k"][0].rearrange("n p h d -> n p (h d)")
    pool_v = i["cache_v"][0].rearrange("n p h d -> n p (h d)")
    n_pool = i["cache_k"].shape[1]

    with nc.Block() as block:
        @block.sync
        def _(sp):
            sp.dma_start(v_new[:, :], o["v_sample"].rearrange("a b l h d -> (a b l) (h d)")).then_inc(vn_in, 16)

            def load(b, s):
                for j in range(NPG):
                    page = sp.value_load(c["pages"][0:1, bass.ds(b * NPG + j, 1)], min_val=0, max_val=n_pool - 1)
                    sp.dma_start(key_in[s][:, j, :], pool_k[bass.ds(page, 1)].rearrange("o p w -> (o p) w")).then_inc(k_in[s], 16)
                    sp.dma_start(val_in[s][:, j, :], pool_v[bass.ds(page, 1)].rearrange("o p w -> (o p) w")).then_inc(v_in[s], 16)

            load(0, 0)
            load(1, 1)
            with sp.Fori(1, NB // 2) as it:
                for s in range(2):
                    b = 2 * it + s
                    sp.wait_ge(S_["key_turned"], done(b - 2))
                    sp.wait_ge(S_["multiplied"], done(b - 2))
                    load(b, s)

        @block.gpsimd
        def _(pool):
            credit(pool, "gpsimd")
            for t in (q_pad[0][:, :], q_pad[1][:, :], maskT[:, :, :]):
                pool.memset(t, 0.0).then_inc(made, 1)
            pool.wait_ge(made, 3)
            v = maskT[:, :, :].rearrange("p b (g l) -> p b g l", l=NL)
            pool.affine_select(out=v, in_=v, compare_op=ALU.is_ge, fill=NEG, base=0,
                               pattern=[[-NL, NB], [0, NR // NL], [0, NL]], channel_multiplier=1).then_inc(made, 1)
            pool.wait_ge(made, 4)
            pool.affine_select(out=v, in_=v, compare_op=ALU.is_ge, fill=NEG, base=0,
                               pattern=[[NL, NB], [0, NR // NL], [1, NL]], channel_multiplier=-1).then_inc(made, 1)
            rows = sign_row[:, :].rearrange("p (h x l) -> p h x l", h=H, x=2)
            pool.memset(rows[:, :, 0, :], 1.0).then_inc(made, 1)
            nc.gpsimd.tensor_copy(rows[:, :, 1, :], over(c["neglam"][0:1, 0:1], 2, [1, H, NL])).then_inc(made, 1)
            with pool.Fori(0, NB // 2) as it:
                for s in range(2):
                    b = 2 * it + s
                    pool.wait_ge(S_["scored"], done(b - 2))
                    for x in range(2):
                        lo = x * HALF
                        dst = q_pad[s][lo:lo + HALF, :].rearrange("p (h r) -> p h r", h=H)[:, :, x * NL:(x + 1) * NL]
                        ins = nc.gpsimd.tensor_copy(dst, feat[lo:lo + HALF, 3 * H:4 * H, bass.ds(b * NL + SEQ, NL)])
                    ins.then_inc(S_["q_put"], 1)

        @block.tensor
        def _(pe):
            credit(pe, "tensor")
            pe.wait_ge(made, 7)
            for b in range(NB):
                mm = nc.tensor.transpose(score[0:NR, b * NS:(b + 1) * NS], maskT[:, b, :], c["ident"][0:NS, 0:NS])
            nc.tensor.matmul(fresh_ps[0:NR, 0:1], sign_row[:, :], c["ones"][0:1, 0:1], start=True, stop=True).then_inc(setup_ps, 1)
            pe.wait_ge(vn_in, 16)

            def turn_keys(b, s, first):
                pe.wait_ge(k_in[s], NPG * 8 * (b - s) + NPG * 16)
                pe.wait_ge(S_["key_kept"], done(b - 1))
                for h in range(H):
                    for j in range(NPG):
                        mm = nc.tensor.transpose(key_ps[:, h, j * PAGE:(j + 1) * PAGE], key_in[s][:, j, h * DH:(h + 1) * DH],
                                                 c["ident"][:, :])
                mm.then_inc(S_["key_turned"], 1)

            def attend(b, s):
                pe.wait_ge(S_["key_kept"], done(b))
                pe.wait_ge(S_["q_put"], done(b))
                pe.wait_ge(S_["e_fresh"], done(b - 1))
                for h in range(H):
                    nc.tensor.matmul(score[0:NR, :], q_pad[s][:, h * NR:(h + 1) * NR], keyT[s][:, h, :], start=(h == 0), stop=(h == H - 1))
                for h in range(H):
                    mm = nc.tensor.matmul(fresh_ps[0:NR, 0:NS], q_pad[s][:, h * NR:(h + 1) * NR], feat[:, 4 * H + h, SEQ:T], start=(h == 0),
                                          stop=(h == H - 1))
                mm.then_inc(S_["scored"], 1)
                pe.wait_ge(S_["weighted"], done(b))
                pe.wait_ge(S_["map_kept"], done(b - 1))
                for j in range(NPG):
                    nc.tensor.matmul(turned[:, j * NR:(j + 1) * NR], e[s][:, j * PAGE:(j + 1) * PAGE], c["ident"][0:NR, 0:NR],
                                     start=True, stop=True)
                nc.tensor.matmul(turned[0:NS, NPG * NR:(NPG + 1) * NR], e[s][:, PAST:PAST + NS], c["ident"][0:NR, 0:NR],
                                 start=True, stop=True).then_inc(S_["map_turned"], 1)
                pe.wait_ge(v_in[s], NPG * 8 * (b - s) + NPG * 16)
                pe.wait_ge(S_["map_kept"], done(b))
                pe.wait_ge(S_["out_kept"], done(b - 1))
                for h in range(H):
                    at = slice(h * NL, (h + 1) * NL)
                    for j in range(NPG):
                        nc.tensor.matmul(out[:, at], val_in[s][:, j, h * DH:(h + 1) * DH], mapT[s][:, j, at], start=(j == 0), stop=False)
                    mm = nc.tensor.matmul(out[:, at], v_new[:, h * DH:(h + 1) * DH], mapT_new[s][:, at], start=False, stop=True)
                mm.then_inc(S_["multiplied"], 1)

            pe.wait_ge(setup_sb, 2)
            with pe.Fori(0, NB // 2) as it:
                turn_keys(2 * it, 0, True)
                turn_keys(2 * it + 1, 1, False)
                attend(2 * it, 0)
                attend(2 * it + 1, 1)

        @block.scalar
        def _(act):
            credit(act, "scalar")
            nc.scalar.preload_act_table(ACT.Exp)

            def keys(b, s):
                act.wait_ge(S_["key_turned"], done(b))
                act.wait_ge(S_["scored"], done(b - 2))
                nc.scalar.copy(keyT[s][:, :, :], key_ps[:, :, :]).then_inc(S_["key_kept"], 1)

            def attend(b, s):
                act.wait_ge(S_["maxed"], done(b))
                nc.scalar.activation(e[s][:, 0:PAST], score[0:NR, :], ACT.Exp, bias=stat[s][:, 2:3], scale=1.0,
                                     accum_out=stat[s][:, 3:4]).then_inc(S_["e_past"], 1)
                nc.scalar.activation(e[s][:, PAST:PAST + NS], fresh[s][:, :], ACT.Exp, bias=stat[s][:, 2:3], scale=1.0,
                                     accum_out=stat[s][:, 4:5]).then_inc(S_["e_fresh"], 1)
                act.wait_ge(S_["multiplied"], done(b))
                nc.scalar.copy(head_out[:, H:2 * H, bass.ds(b * NL + SEQ, NL)],
                               out[:, 0:H * NL].rearrange("p (h l) -> p h l", h=H)).then_inc(S_["out_kept"], 1)

            with act.Fori(0, NB // 2) as it:
                keys(2 * it, 0)
                keys(2 * it + 1, 1)
                attend(2 * it, 0)
                attend(2 * it + 1, 1)

        @block.vector
        def _(dve):
            credit(dve, "vector")
            dve.wait_ge(setup_ps, 1)
            nc.vector.tensor_copy(mask[:, :, :].rearrange("p b k -> p (b k)"), score[0:NR, 0:NB * NS]).then_inc(setup_sb, 1)
            nc.vector.tensor_copy(sign[:, :], fresh_ps[0:NR, 0:1]).then_inc(setup_sb, 1)
            dve.wait_ge(setup_sb, 2)
            with dve.Fori(0, NB // 2) as it:
                for s in range(2):
                    b = 2 * it + s
                    dve.wait_ge(S_["scored"], done(b))
                    nc.vector.tensor_tensor(fresh[s][:, :], fresh_ps[0:NR, 0:NS],
                                            mask[:, bass.ds(b, 1), :].rearrange("p o k -> p (o k)"), ALU.add).then_inc(S_["masked"], 1)
                    nc.vector.tensor_reduce(out=stat[s][:, 0:1], in_=score[0:NR, :], axis=AX.X, op=ALU.max)
                    dve.wait_ge(S_["masked"], done(b))
                    nc.vector.tensor_reduce(out=stat[s][:, 1:2], in_=fresh[s][:, :], axis=AX.X, op=ALU.max).then_inc(S_["past_max"], 1)
                    dve.wait_ge(S_["past_max"], done(b))
                    nc.vector.tensor_reduce(out=stat[s][:, 2:3], in_=stat[s][:, 0:2], axis=AX.X, op=ALU.max, negate=True
                                            ).then_inc(S_["maxed"], 1)
                    dve.wait_ge(S_["e_fresh"], done(b))
                    nc.vector.tensor_tensor(stat[s][:, 5:6], stat[s][:, 3:4], stat[s][:, 4:5], ALU.add).then_inc(S_["summed"], 1)
                    dve.wait_ge(S_["summed"], done(b))
                    nc.vector.reciprocal(stat[s][:, 6:7], stat[s][:, 5:6]).then_inc(S_["inverse"], 1)
                    dve.wait_ge(S_["inverse"], done(b))
                    nc.vector.tensor_tensor(stat[s][:, 7:8], stat[s][:, 6:7], sign[:, :], ALU.mult).then_inc(S_["weight"], 1)
                    dve.wait_ge(S_["weight"], done(b))
                    nc.vector.tensor_scalar(e[s][:, :], e[s][:, :], stat[s][:, 7:8], None, ALU.mult).then_inc(S_["weighted"], 1)
                    dve.wait_ge(S_["map_turned"], done(b))
                    nc.vector.tensor_reduce(out=mapT[s][:, :, :].rearrange("p j (h l) -> p (j h) l", h=H),
                                            in_=turned[:, 0:NPG * NR].rearrange("p (a x l) -> p a l x", x=2, l=NL), axis=AX.X,
                                            op=ALU.add)
                    nc.vector.tensor_reduce(out=mapT_new[s][:, :].rearrange("p (h l) -> p h l", h=H),
                                            in_=turned[0:NS, NPG * NR:(NPG + 1) * NR].rearrange("p (a x l) -> p a l x", x=2, l=NL),
                                            axis=AX.X, op=ALU.add).then_inc(S_["map_kept"], 1)
    m.free()


def head_gate(nc, c, hT, zT, head_out, hi, lo, x_scratch, z_scratch, sem):
    m = Memory(nc)
    psum = [m.ps(f"o_scale{s}", [P, NG, 512]) for s in range(2)]
    spread_done, normed, gated, hi_done, lo_done, x_in, z_in = (
        sem(f"o_{x}") for x in ("spread", "normed", "gated", "hi", "lo", "x_in", "z_in"))
    n_pool, n_act, n_pe, n_dve, spread = head_scales(
        nc, m, sem, "o", [(head_out[:, t, :], False, t) for t in range(2 * H)], psum[1], ((2 * H, DH * EPS),))

    with nc.Block() as block:
        @block.sync
        def _(sp):
            sp.dma_start(zT, z_scratch).then_inc(z_in, 16)
            sp.dma_start(hT, x_scratch).then_inc(x_in, 16)
            sp.wait_ge(x_in, 16)

        @block.gpsimd
        def _(pool):
            n_pool(pool)

        @block.scalar
        def _(act):
            n_act(act)
            for t in range(2 * H):
                if t < H:
                    act.wait_ge(gated, t + 1)
                else:
                    act.wait_ge(normed, t + 1)
                nc.scalar.copy(hi[:, t, :], head_out[:, t, :]).then_inc(hi_done, 1)

        @block.tensor
        def _(pe):
            n_pe(pe)
            for t in range(2 * H):
                if t >= 2:
                    pe.wait_ge(normed, t - 1)
                spread(t, psum[t % 2]).then_inc(spread_done, 1)

        @block.vector
        def _(dve):
            def low(t):
                dve.wait_ge(hi_done, t + 1)
                nc.vector.tensor_tensor(lo[:, t, :], head_out[:, t, :], r32(hi[:, t, :]), ALU.subtract).then_inc(lo_done, 1)

            n_dve(dve)
            dve.wait_ge(z_in, 16)
            for t in range(2 * H):
                dve.wait_ge(spread_done, t + 1)
                x = head_out[:, t, :].rearrange("p (g t) -> p g t", g=NG)
                nc.vector.scalar_tensor_tensor(out=x, in0=x, scalar=c["gain"][:, t // H:t // H + 1], in1=psum[t % 2][:, :, 0:TG],
                                               op0=ALU.mult, op1=ALU.mult).then_inc(normed, 1)
                if t < H:
                    dve.wait_ge(normed, t + 1)
                    nc.vector.tensor_tensor(head_out[:, t, :], head_out[:, t, :], zT[:, t, :], ALU.mult).then_inc(gated, 1)
                if t >= 1:
                    low(t - 1)
            low(2 * H - 1)
    m.free()


def output_projection(nc, i, hT, x_hi, x_lo, sem):
    m = Memory(nc)
    raw = [m.sb(f"wo_raw{s}", [P, KT, P]) for s in range(2)]
    w_hi = [m.sb(f"wo_hi{s}", [P, KT, P], F32R) for s in range(2)]
    w_lo = [m.sb(f"wo_lo{s}", [P, KT, P], F32R) for s in range(2)]
    psum = [m.ps(f"wo_ps{s}", [P, NG, 512]) for s in range(2)]
    loaded = [sem(f"wo_loaded{s}") for s in range(2)]
    split_hi, split_lo, projected, added = (sem(f"wo_{x}") for x in ("split_hi", "split_lo", "projected", "added"))
    w = i["w_out"][0].rearrange("(k p) n -> p k n", p=P)

    with nc.Block() as block:
        @block.sync
        def _(sp):
            sp.dma_start(raw[0][:, :, :], w[:, :, 0:P]).then_inc(loaded[0], 16)
            sp.dma_start(raw[1][:, :, :], w[:, :, P:2 * P]).then_inc(loaded[1], 16)
            with sp.Fori(1, KT // 2) as it:
                for s in range(2):
                    sp.wait_ge(split_lo, done(2 * it + s - 2))
                    sp.dma_start(raw[s][:, :, :], w[:, :, bass.ds(it * (2 * P) + s * P, P)]).then_inc(loaded[s], 16)

        @block.scalar
        def _(act):
            act.sem_inc(split_hi, CREDIT)
            with act.Fori(0, KT // 2) as it:
                for s in range(2):
                    act.wait_ge(loaded[s], 16 * it + 16)
                    act.wait_ge(projected, done(2 * it + s - 2))
                    nc.scalar.copy(w_hi[s][:, :, :], raw[s][:, :, :]).then_inc(split_hi, 1)

        @block.tensor
        def _(pe):
            pe.sem_inc(projected, CREDIT)
            with pe.Fori(0, KT // 2) as it:
                for s in range(2):
                    pe.wait_ge(split_lo, done(2 * it + s))
                    pe.wait_ge(added, done(2 * it + s - 2))
                    project_tile(nc, psum[s], w_hi[s], w_lo[s], x_hi, x_lo).then_inc(projected, 1)

        @block.vector
        def _(dve):
            dve.sem_inc(split_lo, CREDIT)
            dve.sem_inc(added, CREDIT)

            def low(n, s):
                dve.wait_ge(split_hi, done(n))
                nc.vector.tensor_tensor(w_lo[s][:, :, :], raw[s][:, :, :], r32(w_hi[s][:, :, :]), ALU.subtract
                                        ).then_inc(split_lo, 1)

            def add(n, s):
                dve.wait_ge(projected, done(n))
                h = hT[:, bass.ds(n, 1), :].rearrange("p o (g t) -> p (o g) t", g=NG)
                nc.vector.tensor_tensor(h, psum[s][:, :, 0:TG], h, ALU.add).then_inc(added, 1)

            low(0, 0)
            low(1, 1)
            with dve.Fori(0, KT // 2 - 1) as it:
                for s in range(2):
                    add(2 * it + s, s)
                    low(2 * it + (s + 2), s)
            add(KT - 2, 0)
            add(KT - 1, 1)
    m.free()


def middle_norm(nc, c, hT, hi, lo, sem):
    m = Memory(nc)
    total = m.ps("hn_total", [P, NG, 512])
    n_act, n_pe, n_dve = norm_emitters(nc, hT, hi, lo, c["cols"][:, KT:2 * KT], c, m, sem, "hn", total)
    with nc.Block() as block:
        @block.scalar
        def _(act):
            n_act(act)

        @block.tensor
        def _(pe):
            n_pe(pe)

        @block.vector
        def _(dve):
            n_dve(dve)
    m.free()


def gated_mlp(nc, i, o, c, feat, hT, x_hi, x_lo, sem):
    m = Memory(nc)
    w_hi = [m.sb(f"up_hi{s}", [P, KT, P], F32R) for s in range(2)]
    w_lo = [m.sb(f"up_lo{s}", [P, KT, P], F32R) for s in range(2)]
    d_hi, d_lo = m.sb("dn_hi", [P, 2, D], F32R), m.sb("dn_lo", [P, 2, D], F32R)
    spare = feat[:, 0:3 * H, :].rearrange("p a t -> p (a t)")
    pre = [spare[:, s * F_BUF:(s + 1) * F_BUF] for s in range(2)]
    acc = [spare[:, (2 + s) * F_BUF:(3 + s) * F_BUF] for s in range(2)]
    prod = spare[:, 4 * F_BUF:4 * F_BUF + T]
    NRW = NB * F_PAD + CF + 1
    at = 5 * F_BUF
    col = spare[:, at:at + 2 * FT * NRW].rearrange("p (j r) -> p j r", r=NRW)
    at += 2 * FT * NRW
    tail = spare[:, at:at + 2 * FT * F_TAIL].rearrange("p (j r) -> p j r", r=F_TAIL)
    at += 2 * FT * F_TAIL
    raw = []
    for s in range(2):
        raw.append(spare[:, at:at + D].rearrange("p (k f) -> p k f", k=KT))
        at += D
    raw_d = spare[:, at:at + 2 * D].rearrange("p (x d) -> p x d", x=2)
    at += 2 * D
    Q = 11
    rows = spare[0:NRW, at:at + Q * P]
    tail_tok = m.sb("f_tail_tok", [F_TAIL, 4 * P])
    g_hi, g_lo = m.sb("f_g_hi", [P, 2, T], F32R), m.sb("f_g_lo", [P, 2, T], F32R)
    psum = [m.ps(f"f_up{s}", [P, NG, 512]) for s in range(2)]
    down = [m.ps(f"f_down{s}", [P, 512]) for s in range(2)]

    loaded = [sem(f"up_loaded{s}") for s in range(2)]
    d_loaded, rows_in, rows_turned, rows_kept = sem("dn_loaded"), sem("f_rows_in"), sem("f_rows_turned"), sem("f_rows_kept")
    pads, state_put, tail_kept = sem("f_pads"), sem("f_state_put"), sem("f_tail_kept")
    split_hi, split_lo = sem("up_split_hi"), sem("up_split_lo")
    projected, evacuated, tap0, tap1, taps = (sem(f"f_{x}") for x in ("projected", "evacuated", "tap0", "tap1", "taps"))
    activated, gated, gate_hi, gate_lo = (sem(f"f_{x}") for x in ("activated", "gated", "gate_hi", "gate_lo"))
    d_split_hi, d_split_lo, partial, summed = (sem(f"dn_{x}") for x in ("split_hi", "split_lo", "partial", "summed"))
    tail_turned, tail_rows, tail_out = sem("f_tail_turned"), sem("f_tail_rows"), sem("f_tail_out")

    w = i["w_up"][0].rearrange("(k p) n -> p k n", p=P)
    w_d = i["w_down"][0]
    NU = KT * NG

    with nc.Block() as block:
        @block.sync
        def _(sp):
            for q in range(4):
                if q:
                    sp.wait_ge(rows_turned, q)
                a, b = q * Q * P, (q + 1) * Q * P
                sp.dma_start(rows[0:NB * F_PAD, :], i["state_ffn_conv"][0].rearrange("b r w -> (b r) w")[:, a:b]).then_inc(rows_in, 16)
                sp.dma_start(rows[NB * F_PAD:NB * F_PAD + CF, :], i["ffn_conv_w"][0, :, a:b]).then_inc(rows_in, 16)
                sp.dma_start(rows[NB * F_PAD + CF:NRW, :], i["ffn_conv_b"][:, a:b]).then_inc(rows_in, 16)
                if q == 0:
                    sp.dma_start(raw[0], w[:, :, 0:P]).then_inc(loaded[0], 16)
                    sp.dma_start(raw[1], w[:, :, FF:FF + P]).then_inc(loaded[1], 16)
                    sp.dma_start(raw_d, w_d[0:2 * P, :].rearrange("(x p) d -> p x d", x=2)).then_inc(d_loaded, 16)

            def load_pair(p):
                for s in range(2):
                    sp.wait_ge(split_lo, done(2 * p + s - 2))
                    sp.dma_start(raw[s], w[:, :, bass.ds(p * P + s * FF, P)]).then_inc(loaded[s], 16)

            load_pair(1)
            with sp.Fori(1, FT // 2) as it:
                sp.wait_ge(d_split_lo, it)
                sp.dma_start(raw_d, w_d[bass.ds(it * (2 * P), 2 * P), :].rearrange("(x p) d -> p x d", x=2)).then_inc(d_loaded, 16)
                load_pair(2 * it)
                load_pair(2 * it + 1)
            for q in range(2 * FT // 4):
                sp.wait_ge(tail_rows, q + 1)
                a, b = q * 4 * P, (q + 1) * 4 * P
                sp.dma_start(o["ffn_conv_prompt"][0, 0, :, a:b], tail_tok[0:F_PAD, :]).then_inc(tail_out, 16)
                sp.dma_start(o["ffn_conv_sample"][0].rearrange("b r w -> (b r) w")[:, a:b], tail_tok[F_PAD:F_TAIL, :]
                             ).then_inc(tail_out, 16)
            sp.wait_ge(tail_out, 16 * 2 * (2 * FT // 4))

        @block.gpsimd
        def _(pool):
            pool.sem_inc(state_put, CREDIT)
            pool.sem_inc(tail_kept, CREDIT)
            for s in range(2):
                pool.memset(pre[s][:, 0:F_PAD], 0.0).then_inc(pads, 1)
            pool.wait_ge(rows_kept, 4)
            with pool.Fori(0, FT) as it:
                for s in range(2):
                    n, j = 2 * it + s, it + s * FT
                    pool.wait_ge(taps, done(n - 2))
                    nc.gpsimd.tensor_copy(samples(pre[s], F_SAMPLE, F_PAD, 0, F_PAD),
                                          col[:, bass.ds(j, 1), 0:NB * F_PAD].rearrange("p o (b r) -> p (o b) r", r=F_PAD)
                                          ).then_inc(state_put, 1)
                for s in range(2):
                    n, j = 2 * it + s, it + s * FT
                    pool.wait_ge(evacuated, done(n))
                    nc.gpsimd.tensor_copy(tail[:, bass.ds(j, 1), 0:F_PAD], pre[s][:, SEQ:SEQ + F_PAD].unsqueeze(1))
                    nc.gpsimd.tensor_copy(tail[:, bass.ds(j, 1), F_PAD:F_TAIL].rearrange("p o (b r) -> p (o b) r", r=F_PAD),
                                          samples(pre[s], F_SAMPLE, F_PAD, NL, F_PAD)).then_inc(tail_kept, 1)

        @block.scalar
        def _(act):
            act.sem_inc(split_hi, CREDIT)
            act.sem_inc(evacuated, CREDIT)
            act.sem_inc(tap0, CREDIT)
            nc.scalar.preload_act_table(ACT.Silu)

            def high(n, turn, s):
                act.wait_ge(loaded[s], 16 * turn + 16)
                act.wait_ge(projected, done(n - 2))
                nc.scalar.copy(w_hi[s][:, :, :], raw[s]).then_inc(split_hi, 1)

            def drain(p, s):
                n = 2 * p + s
                act.wait_ge(projected, done(n))
                act.wait_ge(taps, done(n - 2))
                act.wait_ge(tail_kept, done(n - 2))
                nc.scalar.copy(pre[s][:, F_PAD:F_PAD + 2 * TG].rearrange("p (g t) -> p g t", g=2), psum[s][:, 0:2, 0:TG])
                nc.scalar.copy(pre[s][:, F_PAD + 2 * TG:F_SAMPLE], psum[s][:, 2, 0:TG - NS])
                nc.scalar.copy(samples(pre[s], F_SAMPLE, F_PAD, F_PAD, NL),
                               psum[s][:, 2, TG - NS:TG].rearrange("p (b l) -> p b l", b=NB)).then_inc(evacuated, 1)

            def first_tap(p, s):
                n, j = 2 * p + s, p + s * FT
                act.wait_ge(evacuated, done(n))
                act.wait_ge(state_put, done(n))
                act.wait_ge(gated, p + 1)
                nc.scalar.activation(
                    acc[s][:, 0:F_OUT], pre[s][:, 0:F_OUT], ACT.Identity,
                    scale=col[:, bass.ds(j, 1), NB * F_PAD:NB * F_PAD + 1].rearrange("p o r -> p (o r)"),
                    bias=col[:, bass.ds(j, 1), NRW - 1:NRW].rearrange("p o r -> p (o r)")).then_inc(tap0, 1)

            def pair(p, last=False):
                drain(p, 0)
                if not last:
                    high(2 * p + 2, p + 1, 0)
                first_tap(p, 0)
                act.wait_ge(taps, done(2 * p))
                nc.scalar.activation(acc[0][:, 0:F_OUT], acc[0][:, 0:F_OUT], ACT.Silu).then_inc(activated, 1)
                drain(p, 1)
                if not last:
                    high(2 * p + 3, p + 1, 1)
                first_tap(p, 1)

            def gate_high(p, x):
                act.wait_ge(gated, p + 2)
                nc.scalar.copy(g_hi[:, x, :], prod).then_inc(gate_hi, 1)

            def turn(it, last=False):
                pair(2 * it)
                act.wait_ge(d_loaded, 16 * it + 16)
                act.wait_ge(partial, NU * it + 1)
                nc.scalar.copy(d_hi[:, :, :], raw_d).then_inc(d_split_hi, 1)
                gate_high(2 * it, 0)
                pair(2 * it + 1, last)
                gate_high(2 * it + 1, 1)

            high(0, 0, 0)
            high(1, 0, 1)
            act.wait_ge(pads, 2)
            with act.Fori(0, FT // 2 - 1) as it:
                turn(it)
            turn(FT // 2 - 1, last=True)

        @block.vector
        def _(dve):
            for x in (split_lo, taps, tap1):
                dve.sem_inc(x, CREDIT)
            dve.sem_inc(gate_lo, 1)
            dve.sem_inc(gated, 1)
            dve.sem_inc(summed, 2)

            def low(n, s):
                dve.wait_ge(split_hi, done(n))
                nc.vector.tensor_tensor(w_lo[s][:, :, :], raw[s], r32(w_hi[s][:, :, :]), ALU.subtract
                                        ).then_inc(split_lo, 1)

            def tap(p, s, t):
                n, j = 2 * p + s, p + s * FT
                dve.wait_ge(tap0 if t == 1 else tap1, done(n))
                nc.vector.scalar_tensor_tensor(
                    out=acc[s][:, 0:F_OUT], in0=pre[s][:, t:t + F_OUT],
                    scalar=col[:, bass.ds(j, 1), NB * F_PAD + t:NB * F_PAD + t + 1].rearrange("p o r -> p (o r)"),
                    in1=acc[s][:, 0:F_OUT], op0=ALU.mult, op1=ALU.add).then_inc(tap1 if t == 1 else taps, 1)

            def add_partials(it, u0, u1):
                for u in range(u0, u1):
                    dve.wait_ge(partial, NU * it + (u + 2))
                    h = hT[:, u // NG, (u % NG) * TG:(u % NG + 1) * TG]
                    nc.vector.tensor_tensor(h, down[u % 2][:, 0:TG], h, ALU.add).then_inc(summed, 1)

            def gate(p):
                dve.wait_ge(activated, p + 1)
                dve.wait_ge(taps, done(2 * p + 1))
                dve.wait_ge(gate_lo, p + 1)
                nc.vector.tensor_tensor(prod[:, 0:SEQ], acc[0][:, 0:SEQ], acc[1][:, 0:SEQ], ALU.mult)
                nc.vector.tensor_tensor(prod[:, SEQ:T].rearrange("p (b l) -> p b l", b=NB), samples(acc[0], F_SAMPLE, F_PAD, 0, NL),
                                        samples(acc[1], F_SAMPLE, F_PAD, 0, NL), ALU.mult).then_inc(gated, 1)

            def gate_low(p, x):
                dve.wait_ge(gate_hi, p + 1)
                nc.vector.tensor_tensor(g_lo[:, x, :], prod, r32(g_hi[:, x, :]), ALU.subtract).then_inc(gate_lo, 1)

            def turn(it, before=None, last=False):
                add = (lambda u0, u1: add_partials(before, u0, u1)) if before is not None else (lambda u0, u1: None)
                a, b = 2 * it, 2 * it + 1
                tap(a, 0, 1)
                tap(a, 0, 2)
                low(2 * a + 2, 0)
                add(0, 4)
                tap(a, 1, 1)
                add(4, 6)
                tap(a, 1, 2)
                add(6, 8)
                low(2 * a + 3, 1)
                add(8, 10)
                gate(a)
                add(10, NU)
                gate_low(a, 0)
                dve.wait_ge(d_split_hi, it + 1)
                nc.vector.tensor_tensor(d_lo[:, :, :], raw_d, r32(d_hi[:, :, :]), ALU.subtract).then_inc(d_split_lo, 1)
                tap(b, 0, 1)
                tap(b, 0, 2)
                if not last:
                    low(2 * b + 2, 0)
                tap(b, 1, 1)
                tap(b, 1, 2)
                if not last:
                    low(2 * b + 3, 1)
                gate(b)
                gate_low(b, 1)

            for q in range(4):
                dve.wait_ge(rows_turned, q + 1)
                nc.vector.tensor_copy(col[:, q * Q:(q + 1) * Q, :].rearrange("p j r -> p (j r)"),
                                      psum[0][:, q % 2, 0:Q * NRW]).then_inc(rows_kept, 1)
            low(0, 0)
            low(1, 1)
            dve.wait_ge(rows_kept, 4)
            turn(0)
            with dve.Fori(1, FT // 2 - 1) as it:
                turn(it, it - 1)
            turn(FT // 2 - 1, FT // 2 - 2, last=True)
            add_partials(FT // 2 - 1, 0, NU)
            for q in range(2 * FT // 4):
                dve.wait_ge(tail_turned, q + 1)
                if q:
                    dve.wait_ge(tail_out, 32 * q)
                nc.vector.tensor_copy(tail_tok[:, :], psum[q % 2][0:F_TAIL, 0, :]).then_inc(tail_rows, 1)

        @block.tensor
        def _(pe):
            pe.sem_inc(projected, CREDIT)
            pe.sem_inc(partial, 1)
            for q in range(4):
                pe.wait_ge(rows_in, 48 * (q + 1))
                if q >= 2:
                    pe.wait_ge(rows_kept, q - 1)
                for j in range(Q):
                    mm = nc.tensor.transpose(psum[0][:, q % 2, j * NRW:(j + 1) * NRW], rows[:, j * P:(j + 1) * P],
                                             c["ident"][0:NRW, 0:NRW])
                mm.then_inc(rows_turned, 1)
            pe.wait_ge(rows_kept, 4)

            def up(p):
                for s in range(2):
                    n = 2 * p + s
                    pe.wait_ge(split_lo, done(n))
                    pe.wait_ge(evacuated, done(n - 2))
                    project_tile(nc, psum[s], w_hi[s], w_lo[s], x_hi, x_lo).then_inc(projected, 1)

            def down_product(it):
                pe.wait_ge(d_split_lo, it + 1)
                pe.wait_ge(gate_lo, 2 * it + 3)
                for u in range(NU):
                    t, g = u // NG, u % NG
                    pe.wait_ge(summed, NU * it + (u + 1))
                    for k, (a, b) in enumerate(((d_hi, g_hi), (d_hi, g_lo), (d_lo, g_hi))):
                        for x in range(2):
                            mm = nc.tensor.matmul(down[u % 2][:, 0:TG], a[:, x, t * P:(t + 1) * P], b[:, x, g * TG:(g + 1) * TG],
                                                  start=(k + x == 0), stop=(k == 2 and x == 1))
                    mm.then_inc(partial, 1)

            up(0)
            up(1)
            with pe.Fori(1, FT // 2) as it:
                up(2 * it)
                down_product(it - 1)
                up(2 * it + 1)
            down_product(FT // 2 - 1)
            pe.wait_ge(tail_kept, done(2 * FT - 1))
            pe.wait_ge(evacuated, done(2 * FT - 1))
            for q in range(2 * FT // 4):
                if q >= 2:
                    pe.wait_ge(tail_rows, q - 1)
                for j in range(4):
                    mm = nc.tensor.transpose(psum[q % 2][0:F_TAIL, 0, j * P:(j + 1) * P], tail[:, 4 * q + j, :], c["ident"][:, :])
                mm.then_inc(tail_turned, 1)
    m.free()


def write_output(nc, o, c, hT, sem):
    m = Memory(nc)
    y = [m.sb(f"y{s}", [P, D]) for s in range(2)]
    turned = [m.ps(f"y_ps{s}", [P, KT, P]) for s in range(2)]
    y_turned, y_kept, y_out = sem("y_turned"), sem("y_kept"), [sem(f"y_out{s}") for s in range(2)]
    prompt = o["y_prompt"].rearrange("a t d -> (a t) d")
    sample = o["y_sample"].rearrange("b l d -> (b l) d")

    with nc.Block() as block:
        @block.sync
        def _(sp):
            for t in range(NT + 1):
                sp.wait_ge(y_kept, 2 * t + 2)
                if t < NT:
                    sp.dma_start(prompt[t * P:(t + 1) * P, :], y[t % 2][:, :]).then_inc(y_out[t % 2], 16)
                else:
                    sp.dma_start(sample, y[t % 2][0:NS, :]).then_inc(y_out[t % 2], 16)
            sp.wait_ge(y_out[0], 16 * (NT // 2 + 1))
            sp.wait_ge(y_out[1], 16 * (NT // 2))

        @block.tensor
        def _(pe):
            for t in range(NT + 1):
                n = P if t < NT else NS
                if t >= 2:
                    pe.wait_ge(y_kept, 2 * (t - 1))
                for k in range(KT):
                    mm = nc.tensor.transpose(turned[t % 2][0:n, k, :], hT[:, k, t * P:t * P + n], c["ident"][:, :])
                mm.then_inc(y_turned, 1)

        @block.vector
        def _(dve):
            for t in range(NT + 1):
                n = P if t < NT else NS
                dve.wait_ge(y_turned, t + 1)
                if t >= 2:
                    dve.wait_ge(y_out[t % 2], 16 * (t // 2))
                for half in range(2):
                    k = slice(half * KT // 2, (half + 1) * KT // 2)
                    nc.vector.tensor_copy(y[t % 2][0:n, :].rearrange("p (k d) -> p k d", k=KT)[:, k, :],
                                          turned[t % 2][0:n, k, :]).then_inc(y_kept, 1)
    m.free()


_INS = ['x_prompt', 'x_sample', 'state_gdn_conv', 'state_gdn_S', 'cache_k', 'cache_v', 'page_table', 'state_ffn_conv',
        'attn_norm_g', 'w_in', 'gdn_conv_w', 'gdn_A_log', 'gdn_dt_bias', 'gdn_out_norm_g', 'diff_q_norm_g', 'diff_k_norm_g',
        'diff_lambda_q1', 'diff_lambda_k1', 'diff_lambda_q2', 'diff_lambda_k2', 'diff_subln_g', 'w_out', 'ffn_norm_g',
        'w_up', 'ffn_conv_w', 'ffn_conv_b', 'w_down']
_OUTS = [('y_prompt', (1, SEQ, D)), ('y_sample', (NB, NL, D)), ('gdn_conv_prompt', (1, 1, G_PAD, 3 * GW)),
         ('gdn_S_prompt', (1, 1, H, DH, DH)), ('k_prompt', (1, 1, SEQ, H, DH)), ('v_prompt', (1, 1, SEQ, H, DH)),
         ('ffn_conv_prompt', (1, 1, F_PAD, 2 * FF)), ('gdn_conv_sample', (1, NB, G_PAD, 3 * GW)),
         ('gdn_S_sample', (1, NB, H, DH, DH)), ('k_sample', (1, NB, NL, H, DH)), ('v_sample', (1, NB, NL, H, DH)),
         ('ffn_conv_sample', (1, NB, F_PAD, 2 * FF))]


def kernel(**inputs):
    import numpy as _np
    import concourse.bacc as _bacc
    from concourse import mybir as _mybir
    from concourse.bass_utils import run_bass_kernel_spmd as _run

    nc = _bacc.Bacc("TRN2", target_bir_lowering=False, num_devices=1)
    arrays, ins, outs = {}, {}, {}
    for name in _INS:
        a = _np.ascontiguousarray(inputs[name])
        arrays[f"in_{name}"] = a
        ins[name] = nc.dram_tensor(f"in_{name}", a.shape, _mybir.dt.from_np(a.dtype), kind="ExternalInput").ap()
    for name, shape in _OUTS:
        outs[name] = nc.dram_tensor(f"out_{name}", shape, F32, kind="ExternalOutput").ap()
    hybrid_step(nc, ins, outs)
    r = _run(nc, [arrays], core_ids=[0])
    return tuple(r.results[0][f"out_{name}"] for name, _ in _OUTS)
```

```python
from contextlib import ExitStack

import concourse.bass as bass
from concourse import mybir

F32 = mybir.dt.float32
F32R = mybir.dt.float32r
BF16 = mybir.dt.bfloat16
I32 = mybir.dt.int32
ALU = mybir.AluOpType
ACT = mybir.ActivationFunctionType
AX = mybir.AxisListType

P = 128
D = 1024
KT = D // P
SEQ = 1024
NB = 8
NL = 4
NS = NB * NL
T = SEQ + NS
NG = 3
TG = T // NG
H = 4
DH = 128
HALF = 64
GW = H * DH
CG = 4
CF = 3
FF = 2816
FT = FF // P
COL_BA = 4 * GW
COL_DIFF = COL_BA + 2 * H
PAGE = 128
NPG = 4
PAST = NPG * PAGE
EPS = 1e-6
NEG = -1e30
LAM_INIT = 0.8 - 0.6
NLEV = 7
NT = SEQ // P
CREDIT = 2

G_PAD, F_PAD = CG - 1, CF - 1
G_SAMPLE, F_SAMPLE = G_PAD + SEQ, F_PAD + SEQ
G_BUF = G_SAMPLE + NB * (G_PAD + NL)
F_BUF = F_SAMPLE + NB * (F_PAD + NL)
G_OUT, F_OUT = G_BUF - G_PAD, F_BUF - F_PAD
G_TAIL = G_PAD * (1 + NB)
F_TAIL = F_PAD * (1 + NB)


def done(n):
    return n + 1 + CREDIT


def levels_done(turn, level, levels=NLEV):
    return levels * turn + (level + 1)


def r32(ap):
    return ap.bitcast(F32)


def over(ap, axis, shape):
    return ap.unsqueeze(axis).to_broadcast(shape)


def samples(buf, start, pad, lo, n):
    return buf[:, start:start + NB * (pad + NL)].rearrange("p (b c) -> p b c", b=NB)[:, :, lo:lo + n]


def project_tile(nc, psum, w_hi, w_lo, x_hi, x_lo, cols=P, before=None):
    for k in range(KT):
        if before is not None:
            before(k)
        for i, (w, x) in enumerate(((w_hi, x_hi), (w_hi, x_lo), (w_lo, x_hi))):
            for g in range(NG):
                mm = nc.tensor.matmul(psum[0:cols, g, 0:TG], w[:, k, 0:cols], x[:, k, g * TG:(g + 1) * TG],
                                      start=(k == 0 and i == 0), stop=(k == KT - 1 and i == 2))
    return mm


class Memory:

    def __init__(self, nc):
        self.nc, self.stack = nc, ExitStack()

    def sb(self, name, shape, dt=F32):
        return self.stack.enter_context(self.nc.sbuf_tensor(name, shape, dt))

    def ps(self, name, shape, dt=F32):
        return self.stack.enter_context(self.nc.psum_tensor(name, shape, dt))

    def free(self):
        self.stack.close()


def hybrid_step(nc, i, o):
    held = []

    def sem(name):
        held.append(nc.alloc_semaphore(name=name))
        return held[-1]

    def phase(step, *args):
        step(nc, *args, sem)
        nc.clear_and_free_semaphores(held)
        nc.all_engine_barrier()
        held.clear()

    x_scratch = nc.dram_tensor("x_scratch", (P, KT, T), F32, kind="Internal").ap()
    z_scratch = nc.dram_tensor("z_scratch", (P, H, T), F32, kind="Internal").ap()

    keep = Memory(nc)
    c = {
        "ident": keep.sb("ident", [P, P]),
        "ones": keep.sb("ones", [P, P]),
        "halves": keep.sb("halves", [P, P]),
        "cols": keep.sb("cols", [P, 2 * KT]),
        "gain": keep.sb("gain", [P, 4]),
        "neglam": keep.sb("neglam", [P, 1]),
        "eps": keep.sb("eps", [P, 1]),
        "pages": keep.sb("pages", [1, NB * NPG], I32),
        "gtail": keep.sb("gtail", [P, 3 * H, G_TAIL]),
        "gcol": keep.sb("gcol", [P, 3 * H, NB * G_PAD + CG]),
    }
    feat = keep.sb("feat", [P, 5 * H, T])
    ba = keep.sb("ba", [P, NT + 1, 2 * H])
    x_split = Memory(nc)
    x_hi = x_split.sb("x_hi", [P, KT, T], F32R)
    x_lo = x_split.sb("x_lo", [P, KT, T], F32R)

    phase(setup_and_input_norm, i, c, feat, x_hi, x_lo, x_scratch)
    phase(input_projection, i, o, c, feat, ba, x_hi, x_lo, z_scratch)
    x_split.free()

    head_out = feat[:, 0:2 * H, :]
    phase(head_norms, i, o, c, feat, ba)
    phase(delta_prompt, i, o, c, feat, ba, head_out)
    phase(delta_sample, i, o, c, feat, ba, head_out)
    phase(attention_prompt, i, o, c, feat, head_out)
    phase(attention_sample, i, o, c, feat, head_out)
    hT = feat[:, 3 * H:5 * H, :]
    x_split = Memory(nc)
    x_hi = x_split.sb("hn_hi", [P, KT, T], F32R)
    x_lo = x_split.sb("hn_lo", [P, KT, T], F32R)
    phase(head_gate, c, hT, feat[:, 2 * H:3 * H, :], head_out, x_hi, x_lo, x_scratch, z_scratch)
    sumsq = feat[:, 3, :]
    phase(output_projection, i, hT, x_hi, x_lo, sumsq)
    phase(gated_mlp, i, o, c, feat, hT, x_hi, x_lo, sumsq)
    x_split.free()
    keep.free()


def ln_rows(ap):
    return ap.rearrange("a (k p) -> (a k) p", p=P)


def norm_emitters(nc, src, hi, lo, g_cols, c, m, sem, name, psum):
    square = [m.sb(f"{name}_square{s}", [P, T]) for s in range(2)]
    rstd = m.sb(f"{name}_rstd", [P, T])
    value = [m.sb(f"{name}_value{s}", [P, T]) for s in range(2)]
    squared, summed, root_done = sem(f"{name}_squared"), sem(f"{name}_summed"), sem(f"{name}_root")
    rstd_done, value_done, hi_done, lo_done = (sem(f"{name}_{x}") for x in ("rstd_done", "value_done", "hi_done", "lo_done"))

    def on_scalar(act):
        nc.scalar.preload_act_table(ACT.Sqrt)
        for k in range(KT):
            if k >= 2:
                act.wait_ge(summed, k - 1)
            nc.scalar.activation(square[k % 2][:, :], src[:, k, :], ACT.Square).then_inc(squared, 1)
        act.wait_ge(summed, KT)
        nc.scalar.activation(rstd[:, :].rearrange("p (g t) -> p g t", g=NG), psum[:, :, 0:TG], ACT.Sqrt,
                             bias=c["eps"][:, 0:1], scale=1.0).then_inc(root_done, 1)
        for k in range(KT):
            act.wait_ge(value_done, k + 1)
            nc.scalar.activation(hi[:, k, :], value[k % 2][:, :], ACT.Copy).then_inc(hi_done, 1)

    def on_tensor(pe):
        for k in range(KT):
            pe.wait_ge(squared, k + 1)
            for g in range(NG):
                mm = nc.tensor.matmul(psum[:, g, 0:TG], c["ones"][:, :], square[k % 2][:, g * TG:(g + 1) * TG],
                                      start=(k == 0), stop=(k == KT - 1))
            mm.then_inc(summed, 1)

    def on_vector(dve):
        dve.wait_ge(root_done, 1)
        nc.vector.reciprocal(rstd[:, :], rstd[:, :]).then_inc(rstd_done, 1)
        dve.wait_ge(rstd_done, 1)
        for k in range(KT):
            if k >= 2:
                dve.wait_ge(lo_done, k - 1)
            nc.vector.scalar_tensor_tensor(out=value[k % 2][:, :], in0=src[:, k, :], scalar=g_cols[:, k:k + 1],
                                           in1=rstd[:, :], op0=ALU.mult, op1=ALU.mult).then_inc(value_done, 1)
            if k >= 1:
                split_low(k - 1, dve)
        split_low(KT - 1, dve)

    def split_low(k, dve):
        dve.wait_ge(hi_done, k + 1)
        nc.vector.tensor_tensor(lo[:, k, :], value[k % 2][:, :], r32(hi[:, k, :]), ALU.subtract).then_inc(lo_done, 1)

    return on_scalar, on_tensor, on_vector


def setup_and_input_norm(nc, i, c, feat, x_hi, x_lo, x_scratch, sem):
    m = Memory(nc)
    xT = feat[:, 0:KT, :]
    x_in = [m.sb(f"x_in{s}", [P, D]) for s in range(2)]
    rows = m.sb("rows", [20, P])
    state_rows = m.sb("state_rows", [NB * G_PAD + CG, 3 * GW])
    lam = m.sb("lam", [P, 4, HALF])
    lam_sum = m.sb("lam_sum", [P, 4])
    lam_prod = m.sb("lam_prod", [P, 2, HALF])
    turned = [m.ps(f"turned{s}", [P, KT, P]) for s in range(2)]
    total = m.ps("total", [P, NG, 512])

    params_in, x_loaded = sem("params_in"), [sem(f"x_loaded{s}") for s in range(2)]
    x_turned, x_kept = sem("x_turned"), [sem(f"x_kept{s}") for s in range(2)]
    consts_zero, consts = sem("consts_zero"), sem("consts")
    turned_cols, cols_kept, scratch_out = sem("turned_cols"), sem("cols_kept"), sem("x_scratch_out")
    lam_step = sem("lam_step")
    lam_exp = sem("lam_exp")
    n_act, n_pe, n_dve = norm_emitters(nc, xT, x_hi, x_lo, c["cols"][:, 0:KT], c, m, sem, "xn", total)

    with nc.Block() as block:
        @block.sync
        def _(sp):
            sp.dma_start(x_in[0][:, :], i["x_prompt"][0, 0:P, :]).then_inc(x_loaded[0], 16)
            sp.dma_start(x_in[1][:, :], i["x_prompt"][0, P:2 * P, :]).then_inc(x_loaded[1], 16)
            prompt_rows = i["x_prompt"].rearrange("a t d -> (a t) d")
            with sp.Fori(1, NT // 2) as it:
                for s in range(2):
                    sp.wait_ge(x_turned, 2 * it + s - 1)
                    sp.dma_start(x_in[s][:, :], prompt_rows[bass.ds(it * (2 * P) + s * P, P), :]).then_inc(x_loaded[s], 16)
            sp.wait_ge(x_turned, NT - 1)
            sp.dma_start(x_in[0][0:NS, :], i["x_sample"].rearrange("b l d -> (b l) d")).then_inc(x_loaded[0], 16)
            sp.wait_ge(x_kept[0], NT // 2 + 2)
            sp.wait_ge(x_kept[1], NT // 2 + 1)
            sp.dma_start(x_scratch, xT).then_inc(scratch_out, 16)
            sp.wait_ge(scratch_out, 16)

        @block.gpsimd
        def _(pool):
            pool.memset(c["ident"][:, :], 0.0).then_inc(consts_zero, 1)
            pool.memset(c["ones"][:, :], 1.0).then_inc(consts_zero, 1)
            pool.memset(c["halves"][:, :], 1.0).then_inc(consts_zero, 1)
            pool.memset(c["eps"][:, :], D * EPS).then_inc(consts_zero, 1)
            pool.wait_ge(consts_zero, 4)
            pool.affine_select(out=c["ident"][:, :], in_=c["ident"][:, :], compare_op=ALU.not_equal, fill=1.0, base=0,
                               pattern=[[-1, P]], channel_multiplier=1).then_inc(consts, 1)
            hv = c["halves"][:, :].rearrange("p (a b) -> p a b", a=2)
            pool.affine_select(out=hv, in_=hv, compare_op=ALU.is_ge, fill=0.0, base=0,
                               pattern=[[-HALF, 2], [0, HALF]], channel_multiplier=1).then_inc(consts, 1)
            pool.wait_ge(consts, 2)
            pool.affine_select(out=hv, in_=hv, compare_op=ALU.is_ge, fill=0.0, base=HALF - 1,
                               pattern=[[HALF, 2], [0, HALF]], channel_multiplier=-1).then_inc(consts, 1)

        @block.scalar
        def _(act):
            n = 0
            for dst, src in (
                (rows[0:KT, :], ln_rows(i["attn_norm_g"])),
                (rows[KT:2 * KT, :], ln_rows(i["ffn_norm_g"])),
                (rows[16:17, :], i["gdn_out_norm_g"]),
                (rows[17:18, :], i["diff_subln_g"]),
                (rows[18:19, 0:HALF], i["diff_q_norm_g"]),
                (rows[18:19, HALF:P], i["diff_q_norm_g"]),
                (rows[19:20, 0:HALF], i["diff_k_norm_g"]),
                (rows[19:20, HALF:P], i["diff_k_norm_g"]),
                (state_rows[0:NB * G_PAD, :], i["state_gdn_conv"].rearrange("a b r w -> (a b r) w")),
                (state_rows[NB * G_PAD:NB * G_PAD + CG, :], i["gdn_conv_w"].rearrange("a r w -> (a r) w")),
                (lam[:, 0, :], i["diff_lambda_q1"].to_broadcast([P, HALF])),
                (lam[:, 1, :], i["diff_lambda_k1"].to_broadcast([P, HALF])),
                (lam[:, 2, :], i["diff_lambda_q2"].to_broadcast([P, HALF])),
                (lam[:, 3, :], i["diff_lambda_k2"].to_broadcast([P, HALF])),
                (c["pages"][:, :], i["page_table"].rearrange("(o b) n -> o (b n)", o=1)),
            ):
                nc.scalar.dma_start(dst, src).then_inc(params_in, 16)
                n += 1
            nc.scalar.preload_act_table(ACT.Copy)
            act.sem_inc(x_kept[0], 1)
            with act.Fori(0, NT // 2) as it:
                act.wait_ge(x_turned, 2 * it + 1)
                nc.scalar.copy(xT[:, :, bass.ds(it * (2 * P), P)], turned[0][:, :, :]).then_inc(x_kept[0], 1)
            act.wait_ge(x_turned, NT + 1)
            nc.scalar.copy(xT[:, :, SEQ:T], turned[0][:, :, 0:NS]).then_inc(x_kept[0], 1)
            act.wait_ge(lam_step, 2)
            nc.scalar.activation(lam_sum[:, 2:4], lam_sum[:, 0:2], ACT.Exp).then_inc(lam_exp, 1)
            act.wait_ge(x_kept[0], NT // 2 + 2)
            act.wait_ge(x_kept[1], NT // 2 + 1)
            n_act(act)

        @block.tensor
        def _(pe):
            pe.wait_ge(consts, 3)
            with pe.Fori(0, NT // 2) as it:
                for s in range(2):
                    pe.wait_ge(x_loaded[s], 16 * it + 16)
                    pe.wait_ge(x_kept[s], it + 1)
                    for k in range(KT):
                        mm = nc.tensor.transpose(turned[s][:, k, :], x_in[s][:, k * P:(k + 1) * P], c["ident"][:, :])
                    mm.then_inc(x_turned, 1)
            pe.wait_ge(x_loaded[0], 16 * (NT // 2 + 1))
            pe.wait_ge(x_kept[0], NT // 2 + 1)
            for k in range(KT):
                mm = nc.tensor.transpose(turned[0][:, k, 0:NS], x_in[0][0:NS, k * P:(k + 1) * P], c["ident"][0:NS, 0:NS])
            mm.then_inc(x_turned, 1)
            pe.wait_ge(params_in, 16 * 15)
            pe.wait_ge(x_kept[1], NT // 2 + 1)
            nr = NB * G_PAD + CG
            for j in range(3 * H):
                nc.tensor.transpose(turned[1][:, :, :].rearrange("p a b -> p (a b)")[:, j * nr:(j + 1) * nr],
                                    state_rows[:, j * P:(j + 1) * P], c["ident"][0:nr, 0:nr])
            nc.tensor.transpose(turned[1][:, KT - 1, 0:20], rows[:, :], c["ident"][0:20, 0:20]).then_inc(turned_cols, 1)
            n_pe(pe)

        @block.vector
        def _(dve):
            dve.sem_inc(x_kept[1], 1)
            dve.wait_ge(params_in, 16 * 15)
            for j in range(2):
                nc.vector.tensor_tensor_reduce(out=lam_prod[:, j, :], in0=lam[:, 2 * j, :], in1=lam[:, 2 * j + 1, :], scale=1.0,
                                               scalar=0.0, op0=ALU.mult, op1=ALU.add,
                                               accum_out=lam_sum[:, j:j + 1]).then_inc(lam_step, 1)
            with dve.Fori(0, NT // 2) as it:
                dve.wait_ge(x_turned, 2 * it + 2)
                nc.vector.tensor_copy(xT[:, :, bass.ds(it * (2 * P) + P, P)], turned[1][:, :, :]).then_inc(x_kept[1], 1)
            dve.wait_ge(turned_cols, 1)
            nr = NB * G_PAD + CG
            nc.vector.tensor_copy(c["gcol"][:, :, :].rearrange("p a b -> p (a b)"),
                                  turned[1][:, :, :].rearrange("p a b -> p (a b)")[:, 0:3 * H * nr]).then_inc(cols_kept, 1)
            nc.vector.tensor_scalar(c["cols"][:, :], turned[1][:, KT - 1, 0:2 * KT], D ** 0.5, None,
                                    ALU.mult).then_inc(cols_kept, 1)
            for j, scale in enumerate((DH ** 0.5, (1.0 - LAM_INIT) * DH ** 0.5, 1.0, HALF ** 0.5)):
                nc.vector.tensor_scalar(c["gain"][:, j:j + 1], turned[1][:, KT - 1, 2 * KT + j:2 * KT + j + 1], scale, None,
                                        ALU.mult).then_inc(cols_kept, 1)
            dve.wait_ge(lam_exp, 1)
            nc.vector.tensor_tensor(c["neglam"][:, :], lam_sum[:, 3:4], lam_sum[:, 2:3], ALU.subtract).then_inc(lam_step, 1)
            dve.wait_ge(lam_step, 3)
            nc.vector.tensor_scalar(c["neglam"][:, :], c["neglam"][:, :], LAM_INIT, None, ALU.subtract)
            dve.wait_ge(cols_kept, 6)
            n_dve(dve)
    m.free()


def input_projection(nc, i, o, c, feat, ba, x_hi, x_lo, z_scratch, sem):
    m = Memory(nc)
    raw = [m.sb(f"win_raw{s}", [P, KT, P]) for s in range(2)]
    w_hi = [m.sb(f"win_hi{s}", [P, KT, P], F32R) for s in range(2)]
    w_lo = [m.sb(f"win_lo{s}", [P, KT, P], F32R) for s in range(2)]
    buf = m.sb("conv_buf", [P, 4, G_BUF])
    pre = [buf[:, s, :] for s in range(2)]
    acc = [buf[:, 2 + s, :] for s in range(2)]
    psum = [m.ps(f"proj{s}", [P, NG, 512]) for s in range(2)]
    small = m.ps("proj_small", [P, 2, 512])

    NGDN, NZ, ND, NV = 3 * H, H, 2 * H, H
    Z0, D0, V0 = NGDN, NGDN + NZ, NGDN + NZ + ND
    NTILE = V0 + NV

    loaded = [sem(f"win_loaded{s}") for s in range(2)]
    split_hi, split_lo = sem("win_split_hi"), sem("win_split_lo")
    projected, evacuated = sem("win_projected"), sem("win_evacuated")
    state_put, tail_kept = sem("g_state_put"), sem("g_tail_kept")
    tap0, taps, activated = sem("g_tap0"), sem("g_taps"), sem("g_activated")
    pads = sem("g_pads")
    z_out = [sem(f"z_out{s}") for s in range(2)]
    ba_loaded, ba_split, ba_projected, ba_kept, ba_turned = (sem(f"ba_{x}") for x in ("loaded", "split", "projected", "kept", "turned"))
    tail_turned, tail_rows, tail_out = sem("g_tail_turned"), sem("g_tail_rows"), sem("g_tail_out")
    v_turned, v_kept, v_out = sem("v_turned"), sem("v_kept"), [sem(f"v_out{s}") for s in range(2)]

    w = i["w_in"][0].rearrange("(k p) n -> p k n", p=P)
    ba_raw = m.sb("ba_raw", [P, KT, 2 * H])
    ba_hi = m.sb("ba_hi", [P, KT, 2 * H], F32R)
    ba_lo = m.sb("ba_lo", [P, KT, 2 * H], F32R)
    tail_tok = raw[0][0:G_TAIL, :, :].rearrange("p a b -> p (a b)")
    tail_tok2 = raw[1][0:G_TAIL, :, :].rearrange("p a b -> p (a b)")
    v_tok = [raw[s][:, 4:8, :].rearrange("p a b -> p (a b)") for s in range(2)]
    tail_tok3 = m.sb("tail_tok3", [G_TAIL, 512])
    ba_T = m.sb("ba_T", [2 * H, T])
    v_ps = [small[:, 1, :], psum[0][:, 0, :]]

    def pairs(eng, first, last, body):
        with eng.Fori(first // 2, last // 2) as it:
            for s in range(2):
                body(2 * it + s, s)

    with nc.Block() as block:
        @block.sync
        def _(sp):
            def load(n, s, col):
                if not isinstance(n, int) or n >= 2:
                    sp.wait_ge(split_lo, done(n - 2))
                sp.dma_start(raw[s][:, :, :], w[:, :, bass.ds(col, P)]).then_inc(loaded[s], 16)

            load(0, 0, 0)
            load(1, 1, P)
            sp.dma_start(ba_raw[:, :, :], w[:, :, COL_BA:COL_DIFF]).then_inc(ba_loaded, 16)
            with sp.Fori(1, Z0 // 2) as it:
                for s in range(2):
                    load(2 * it + s, s, it * (2 * P) + s * P)
            with sp.Fori(Z0 // 2, D0 // 2) as it:
                for s in range(2):
                    load(2 * it + s, s, it * (2 * P) + s * P)
            with sp.Fori(D0 // 2, NTILE // 2) as it:
                for s in range(2):
                    load(2 * it + s, s, it * (2 * P) + (s * P + 2 * H))
            for a, src in ((0, tail_tok[:, 0:512]), (1, tail_tok2[:, 0:512])):
                sp.wait_ge(tail_rows, a + 1)
                sp.dma_start(o["gdn_conv_prompt"][0, 0, :, a * 512:(a + 1) * 512], src[0:G_PAD, :]).then_inc(tail_out, 16)
                sp.dma_start(o["gdn_conv_sample"][0].rearrange("b r w -> (b r) w")[:, a * 512:(a + 1) * 512],
                             src[G_PAD:G_TAIL, :]).then_inc(tail_out, 16)
            sp.wait_ge(tail_rows, 3)
            sp.dma_start(o["gdn_conv_prompt"][0, 0, :, 1024:1536], tail_tok3[0:G_PAD, :]).then_inc(tail_out, 16)
            sp.dma_start(o["gdn_conv_sample"][0].rearrange("b r w -> (b r) w")[:, 1024:1536],
                         tail_tok3[G_PAD:G_TAIL, :]).then_inc(tail_out, 16)
            for t in range(NT + 1):
                sp.wait_ge(v_kept, t + 1)
                if t < NT:
                    sp.dma_start(o["v_prompt"].rearrange("a b t h d -> (a b t) (h d)")[t * P:(t + 1) * P, :],
                                 v_tok[t % 2]).then_inc(v_out[t % 2], 16)
                else:
                    sp.dma_start(o["v_sample"].rearrange("a b l h d -> (a b l) (h d)"), v_tok[t % 2][0:NS, :]).then_inc(v_out[t % 2], 16)
            sp.wait_ge(tail_out, 16 * 6)
            sp.wait_ge(v_out[0], 16 * (NT // 2 + 1))
            sp.wait_ge(v_out[1], 16 * (NT // 2))

        @block.gpsimd
        def _(pool):
            pool.sem_inc(state_put, CREDIT)
            pool.sem_inc(tail_kept, CREDIT)
            for s in range(2):
                pool.memset(pre[s][:, 0:G_PAD], 0.0).then_inc(pads, 1)

            def body(n, s):
                pool.wait_ge(taps, done(n - 2))
                nc.gpsimd.tensor_copy(samples(pre[s], G_SAMPLE, G_PAD, 0, G_PAD),
                                      c["gcol"][:, bass.ds(n, 1), 0:NB * G_PAD].rearrange("p o (b r) -> p (o b) r", r=G_PAD)
                                      ).then_inc(state_put, 1)
                pool.wait_ge(evacuated, done(n))
                nc.gpsimd.tensor_copy(c["gtail"][:, bass.ds(n, 1), 0:G_PAD], pre[s][:, SEQ:SEQ + G_PAD].unsqueeze(1))
                nc.gpsimd.tensor_copy(c["gtail"][:, bass.ds(n, 1), G_PAD:G_TAIL].rearrange("p o (b r) -> p (o b) r", r=G_PAD),
                                      samples(pre[s], G_SAMPLE, G_PAD, NL, G_PAD)).then_inc(tail_kept, 1)

            pairs(pool, 0, Z0, body)

        @block.scalar
        def _(act):
            act.sem_inc(split_hi, CREDIT)
            act.sem_inc(evacuated, CREDIT)
            act.sem_inc(tap0, CREDIT)
            act.sem_inc(activated, CREDIT)
            nc.scalar.preload_act_table(ACT.Silu)

            def high(n, s):
                act.wait_ge(loaded[s], high_loaded(n, s))
                act.wait_ge(projected, done(n - 2))
                nc.scalar.activation(w_hi[s][:, :, :], raw[s][:, :, :], ACT.Copy).then_inc(split_hi, 1)

            def high_loaded(n, s):
                return 8 * (n - s) + 16

            def drain_gdn(n, s):
                act.wait_ge(projected, done(n))
                act.wait_ge(taps, done(n - 2))
                act.wait_ge(tail_kept, done(n - 2))
                nc.scalar.copy(pre[s][:, G_PAD:G_PAD + 2 * TG].rearrange("p (g t) -> p g t", g=2), psum[s][:, 0:2, 0:TG])
                nc.scalar.copy(pre[s][:, G_PAD + 2 * TG:G_SAMPLE], psum[s][:, 2, 0:TG - NS])
                nc.scalar.copy(samples(pre[s], G_SAMPLE, G_PAD, G_PAD, NL),
                               psum[s][:, 2, TG - NS:TG].rearrange("p (b l) -> p b l", b=NB)).then_inc(evacuated, 1)
                act.wait_ge(evacuated, done(n))
                act.wait_ge(state_put, done(n))
                nc.scalar.activation(acc[s][:, 0:G_OUT], pre[s][:, 0:G_OUT], ACT.Copy,
                                     scale=c["gcol"][:, bass.ds(n, 1), NB * G_PAD:NB * G_PAD + 1].rearrange("p o r -> p (o r)")
                                     ).then_inc(tap0, 1)
                act.wait_ge(taps, done(n))
                nc.scalar.activation(feat[:, bass.ds(n, 1), 0:SEQ].rearrange("p o t -> p (o t)"), acc[s][:, 0:SEQ], ACT.Silu)
                nc.scalar.activation(feat[:, bass.ds(n, 1), SEQ:T].rearrange("p o (b l) -> p (o b) l", b=NB),
                                     samples(acc[s], G_SAMPLE, G_PAD, 0, NL), ACT.Silu).then_inc(activated, 1)

            def drain_z(n, s):
                act.wait_ge(projected, done(n))
                if n - Z0 >= 2:
                    act.wait_ge(z_out[s], 16)
                nc.scalar.activation(acc[s][:, 0:T].rearrange("p (g t) -> p g t", g=NG), psum[s][:, :, 0:TG],
                                     ACT.Silu).then_inc(evacuated, 1)
                act.wait_ge(evacuated, done(n))
                nc.scalar.dma_start(z_scratch[:, n - Z0, :], acc[s][:, 0:T]).then_inc(z_out[s], 16)

            def drain_diff(n, s):
                act.wait_ge(projected, done(n))
                nc.scalar.copy(feat[:, bass.ds(n - NZ, 1), :].rearrange("p o (g t) -> p (o g) t", g=NG),
                               psum[s][:, :, 0:TG]).then_inc(evacuated, 1)

            def drain_v(n, s):
                act.wait_ge(projected, done(n))
                if n == V0:
                    act.wait_ge(taps, done(Z0 - 1))
                    act.wait_ge(tail_kept, done(Z0 - 1))
                if n == V0 + 2:
                    act.wait_ge(z_out[0], 32)
                    act.wait_ge(z_out[1], 32)
                nc.scalar.copy(buf[:, n - V0, 0:T].rearrange("p (g t) -> p g t", g=NG), psum[s][:, :, 0:TG]).then_inc(evacuated, 1)

            high(0, 0)
            act.wait_ge(ba_loaded, 16)
            nc.scalar.activation(ba_hi[:, :, :], ba_raw[:, :, :], ACT.Copy).then_inc(ba_split, 1)

            def gdn_tile(n, s):
                high(n + 1, 1 - s)
                drain_gdn(n, s)

            def diff_tile(n, s):
                high(n + 1, 1 - s)
                drain_diff(n, s)

            pairs(act, 0, Z0, gdn_tile)
            for n in range(Z0, D0):
                high(n + 1, 1 - n % 2)
                drain_z(n, n % 2)
            pairs(act, D0, V0, diff_tile)
            for n in range(V0, NTILE):
                if n + 1 < NTILE:
                    high(n + 1, 1 - n % 2)
                drain_v(n, n % 2)
            act.wait_ge(ba_projected, 1)
            nc.scalar.copy(ba_T[:, :].rearrange("p (g t) -> p g t", g=NG), psum[0][0:2 * H, :, 0:TG]).then_inc(ba_kept, 1)

        @block.vector
        def _(dve):
            dve.sem_inc(split_lo, CREDIT)
            dve.sem_inc(taps, CREDIT)
            step = sem("g_tap_step")
            dve.sem_inc(step, 2 * CREDIT)

            def low(n, s):
                dve.wait_ge(split_hi, done(n))
                nc.vector.tensor_tensor(w_lo[s][:, :, :], raw[s][:, :, :], r32(w_hi[s][:, :, :]),
                                        ALU.subtract).then_inc(split_lo, 1)

            def gdn_tile(n, s):
                low(n + 1, 1 - s)
                dve.wait_ge(tap0, done(n))
                for j in range(1, CG):
                    if j >= 2:
                        dve.wait_ge(step, 2 * n + (2 * CREDIT + j - 1))
                    ins = nc.vector.scalar_tensor_tensor(
                        out=acc[s][:, 0:G_OUT], in0=pre[s][:, j:j + G_OUT],
                        scalar=c["gcol"][:, bass.ds(n, 1), NB * G_PAD + j:NB * G_PAD + j + 1].rearrange("p o r -> p (o r)"),
                        in1=acc[s][:, 0:G_OUT], op0=ALU.mult, op1=ALU.add)
                    ins.then_inc(step if j < CG - 1 else taps, 1)

            low(0, 0)
            dve.wait_ge(ba_split, 1)
            nc.vector.tensor_tensor(ba_lo[:, :, :], ba_raw[:, :, :], r32(ba_hi[:, :, :]), ALU.subtract).then_inc(ba_split, 1)
            pairs(dve, 0, Z0, gdn_tile)
            pairs(dve, Z0, V0, lambda n, s: low(n + 1, 1 - s))
            for n in range(V0, NTILE - 1):
                low(n + 1, 1 - n % 2)
            dve.wait_ge(ba_turned, 1)
            nc.vector.tensor_copy(ba[:, 0:NT, :], small[:, 0, 0:NT * 2 * H].rearrange("p (t c) -> p t c", c=2 * H))
            nc.vector.tensor_copy(ba[0:NS, NT, :], small[0:NS, 0, NT * 2 * H:(NT + 1) * 2 * H]).then_inc(ba_turned, 1)
            for a, dst in enumerate((tail_tok[:, 0:512], tail_tok2[:, 0:512], tail_tok3[:, :])):
                dve.wait_ge(tail_turned, a + 1)
                nc.vector.tensor_copy(dst, psum[1][0:G_TAIL, a, :]).then_inc(tail_rows, 1)
            for t in range(NT + 1):
                dve.wait_ge(v_turned, t + 1)
                if t >= 2:
                    dve.wait_ge(v_out[t % 2], 16 * (t // 2))
                n = P if t < NT else NS
                nc.vector.tensor_copy(v_tok[t % 2][0:n, :], v_ps[t % 2][0:n, :]).then_inc(v_kept, 1)

        @block.tensor
        def _(pe):
            pe.sem_inc(projected, CREDIT)

            def tile(n, s):
                pe.wait_ge(split_lo, done(n))
                pe.wait_ge(evacuated, done(n - 2))
                project_tile(nc, psum[s], w_hi[s], w_lo[s], x_hi, x_lo).then_inc(projected, 1)

            pairs(pe, 0, NTILE, tile)
            pe.wait_ge(ba_split, 2)
            pe.wait_ge(evacuated, done(NTILE - 2))
            project_tile(nc, psum[0], ba_hi, ba_lo, x_hi, x_lo, 2 * H).then_inc(ba_projected, 1)
            pe.wait_ge(ba_kept, 1)
            for t in range(NT + 1):
                n = P if t < NT else NS
                mm = nc.tensor.transpose(small[0:n, 0, t * 2 * H:(t + 1) * 2 * H], ba_T[:, t * P:t * P + n],
                                         c["ident"][0:2 * H, 0:2 * H])
            mm.then_inc(ba_turned, 1)
            pe.wait_ge(tail_kept, done(Z0 - 1))
            pe.wait_ge(evacuated, done(NTILE - 1))
            for j in range(3 * H):
                mm = nc.tensor.transpose(psum[1][0:G_TAIL, j // 4, (j % 4) * P:(j % 4 + 1) * P], c["gtail"][:, j, :],
                                         c["ident"][:, :])
                if j % 4 == 3:
                    mm.then_inc(tail_turned, 1)
            for t in range(NT + 1):
                n = P if t < NT else NS
                if t >= 2:
                    pe.wait_ge(v_kept, t - 1)
                for h in range(H):
                    mm = nc.tensor.transpose(v_ps[t % 2][0:n, h * P:(h + 1) * P], buf[:, h, t * P:t * P + n], c["ident"][:, :])
                mm.then_inc(v_turned, 1)
    m.free()


def head_scales(nc, m, sem, name, tiles, total, eps_of):
    n = len(tiles)
    R = tiles[-1][2] + (2 if tiles[-1][1] else 1)
    square = [m.sb(f"{name}_square{x}", [P, T]) for x in range(2)]
    strip = m.sb(f"{name}_strip", [P, 2, 2 * R])
    spread_by = m.sb(f"{name}_spread_by", [R, n, P])
    spread_r = m.sb(f"{name}_spread_r", [R, n, P], F32R)
    eps = m.sb(f"{name}_eps", [R, 1])
    rows = m.sb(f"{name}_rows", [R, T])
    hi, lo = m.sb(f"{name}_rows_hi", [R, T], F32R), m.sb(f"{name}_rows_lo", [R, T], F32R)
    zeroed, made, spread_made = sem(f"{name}_zeroed"), sem(f"{name}_made"), sem(f"{name}_spread_made")
    squared, summed, root_done, inverted, hi_done, lo_done = (
        sem(f"{name}_{x}") for x in ("squared", "summed", "root", "inverted", "rows_hi", "rows_lo"))
    halved = [t for t in range(n) if tiles[t][1]]
    whole = n - len(halved)

    def on_pool(pool):
        pool.memset(strip[:, :, :], 0.0).then_inc(zeroed, 1)
        pool.memset(spread_by[:, :, :], 1.0).then_inc(zeroed, 1)
        k = 2
        for first, value in eps_of:
            pool.memset(eps[0:first, :], value).then_inc(zeroed, 1)
            k += 1
            pool.wait_ge(zeroed, k)
        for j, ones in enumerate((strip[:, 0, R - 1:R], strip[0:HALF, 1, R - 1:R], strip[HALF:P, 1, R:R + 1])):
            if j:
                pool.wait_ge(made, j)
            pool.memset(ones, 1.0).then_inc(made, 1)
        pool.wait_ge(made, 3)
        views = []
        if whole:
            views.append((spread_by[:, 0:whole, :], 0, [[-1, whole], [0, P]]))
        if halved:
            views.append((spread_by[:, whole:n, :].rearrange("r t (x f) -> r (t x) f", x=2), -tiles[whole][2],
                          [[-1, 2 * (n - whole)], [0, HALF]]))
        for v, base, pattern in views:
            pool.affine_select(out=v, in_=v, compare_op=ALU.is_equal, fill=0.0, base=base, pattern=pattern,
                               channel_multiplier=1).then_inc(spread_made, 1)

    def on_scalar(act):
        nc.scalar.preload_act_table(ACT.Sqrt)
        for t in range(0, n):
            if t >= 2:
                act.wait_ge(summed, t - 1)
            nc.scalar.activation(square[t % 2][:, :], tiles[t][0], ACT.Square).then_inc(squared, 1)
        act.wait_ge(summed, n)
        act.wait_ge(zeroed, 2 + len(eps_of))
        nc.scalar.activation(rows[:, :].rearrange("p (g t) -> p g t", g=NG), total[0:R, :, 0:TG], ACT.Sqrt, bias=eps[:, :],
                             scale=1.0).then_inc(root_done, 1)
        act.wait_ge(inverted, 1)
        nc.scalar.copy(hi[:, :], rows[:, :]).then_inc(hi_done, 1)

    def on_tensor(pe):
        pe.wait_ge(made, 3)
        for t, (_, two, row) in enumerate(tiles):
            pe.wait_ge(squared, t + 1)
            for g in range(NG):
                mm = nc.tensor.matmul(total[0:R, g, 0:TG], strip[:, 1 if two else 0, R - 1 - row:2 * R - 1 - row],
                                      square[t % 2][:, g * TG:(g + 1) * TG], start=(t == 0), stop=(t == n - 1))
            mm.then_inc(summed, 1)
        pe.wait_ge(lo_done, 2)

    def on_vector(dve):
        dve.wait_ge(spread_made, (1 if whole else 0) + (1 if halved else 0))
        nc.vector.tensor_copy(spread_r[:, :, :], spread_by[:, :, :]).then_inc(lo_done, 1)
        dve.wait_ge(root_done, 1)
        nc.vector.reciprocal(rows[:, :], rows[:, :]).then_inc(inverted, 1)
        dve.wait_ge(hi_done, 1)
        nc.vector.tensor_tensor(lo[:, :], rows[:, :], r32(hi[:, :]), ALU.subtract).then_inc(lo_done, 1)

    def spread(t, psum):
        for g in range(NG):
            for k, part in enumerate((hi, lo)):
                mm = nc.tensor.matmul(psum[:, g, 0:TG], spread_r[:, t, :], part[:, g * TG:(g + 1) * TG], start=(k == 0), stop=(k == 1))
        return mm

    return on_pool, on_scalar, on_tensor, on_vector, spread


def head_norms(nc, i, o, c, feat, ba, sem):
    m = Memory(nc)
    k_tok = [m.sb(f"k_tok{s}", [P, GW]) for s in range(2)]
    a_pos = m.sb("a_pos", [P, NT + 1, H])
    a_neg = m.sb("a_neg", [P, NT + 1, H])
    dt_bias = m.sb("dt_bias", [P, H])
    a_log = m.sb("a_log", [P, H])
    psum = [m.ps(f"h_scale{s}", [P, NG, 512]) for s in range(2)]
    k_ps = m.ps("k_ps", [P, 2, 512])

    spread_done, normed = sem("h_spread"), sem("h_normed")
    k_turned, k_kept, k_out = sem("k_turned"), sem("k_kept"), [sem(f"k_out{s}") for s in range(2)]
    rate_in, gate_act, gate_dve = sem("rate_in"), sem("gate_act"), sem("gate_dve")

    order = [(j, j, DH ** -0.5) for j in range(H)] + [(j, j, 1.0) for j in range(H, 2 * H)]
    order += [(3 * H + j, 2 * H + 2 * j, c["gain"][:, 2 + j // H:3 + j // H]) for j in range(2 * H)]
    n_pool, n_act, n_pe, n_dve, spread = head_scales(
        nc, m, sem, "h", [(feat[:, j, :], j >= 3 * H, row) for j, row, _ in order], psum[1],
        ((6 * H, HALF * EPS), (2 * H, EPS)))

    with nc.Block() as block:
        @block.sync
        def _(sp):
            sp.dma_start(dt_bias[:, :], i["gdn_dt_bias"].to_broadcast([P, H])).then_inc(rate_in, 16)
            sp.dma_start(a_log[:, :], i["gdn_A_log"].to_broadcast([P, H])).then_inc(rate_in, 16)
            for t in range(NT + 1):
                sp.wait_ge(k_kept, t + 1)
                if t < NT:
                    sp.dma_start(o["k_prompt"].rearrange("a b t h d -> (a b t) (h d)")[t * P:(t + 1) * P, :],
                                 k_tok[t % 2][:, :]).then_inc(k_out[t % 2], 16)
                else:
                    sp.dma_start(o["k_sample"].rearrange("a b l h d -> (a b l) (h d)"), k_tok[t % 2][0:NS, :]).then_inc(k_out[t % 2], 16)
            sp.wait_ge(k_out[0], 16 * (NT // 2 + 1))
            sp.wait_ge(k_out[1], 16 * (NT // 2))

        @block.gpsimd
        def _(pool):
            n_pool(pool)

        @block.scalar
        def _(act):
            n_act(act)
            nc.scalar.activation(ba[:, 0:NT, 0:H], ba[:, 0:NT, 0:H], ACT.Sigmoid).then_inc(gate_act, 1)
            nc.scalar.activation(ba[0:NS, NT, 0:H], ba[0:NS, NT, 0:H], ACT.Sigmoid).then_inc(gate_act, 1)
            act.wait_ge(rate_in, 32)
            nc.scalar.activation(a_log[:, :], a_log[:, :], ACT.Exp).then_inc(gate_act, 1)
            act.wait_ge(gate_dve, 4)
            nc.scalar.activation(a_neg[:, :, :], a_neg[:, :, :], ACT.Exp).then_inc(gate_act, 1)
            act.wait_ge(gate_act, 4)
            nc.scalar.activation(a_neg[:, :, :], a_neg[:, :, :], ACT.Ln, bias=c["ones"][:, 0:1], scale=1.0).then_inc(gate_act, 1)

        @block.tensor
        def _(pe):
            n_pe(pe)
            for t in range(4 * H):
                if t >= 2:
                    pe.wait_ge(normed, t - 1)
                spread(t, psum[t % 2]).then_inc(spread_done, 1)
            pe.wait_ge(normed, 4 * H)
            for t in range(NT + 1):
                n = P if t < NT else NS
                if t >= 2:
                    pe.wait_ge(k_kept, t - 1)
                for h in range(H):
                    mm = nc.tensor.transpose(k_ps[0:n, t % 2, h * P:(h + 1) * P], feat[:, 4 * H + h, t * P:t * P + n],
                                             c["ident"][:, :])
                mm.then_inc(k_turned, 1)

        @block.vector
        def _(dve):
            dve.wait_ge(rate_in, 32)
            a = ba[:, :, H:2 * H]
            nc.vector.memset(a_pos[:, NT, :], 0.0).then_inc(gate_dve, 1)
            bias = over(dt_bias[:, :], 1, [P, NT, H])
            nc.vector.tensor_tensor(a_pos[:, 0:NT, :], ba[:, 0:NT, H:2 * H], bias, ALU.add).then_inc(gate_dve, 1)
            dve.wait_ge(gate_dve, 2)
            nc.vector.tensor_tensor(a_pos[0:NS, NT, :], ba[0:NS, NT, H:2 * H], dt_bias[0:NS, :], ALU.add).then_inc(gate_dve, 1)
            dve.wait_ge(gate_dve, 3)
            nc.vector.scalar_tensor_tensor(out=a_neg[:, :, :], in0=a_pos[:, :, :], scalar=-1.0, in1=a_pos[:, :, :],
                                           op0=ALU.mult, op1=ALU.min).then_inc(gate_dve, 1)

            n_dve(dve)
            for t, (j, _, gain) in enumerate(order):
                dve.wait_ge(spread_done, t + 1)
                x = feat[:, j, :].rearrange("p (g t) -> p g t", g=NG)
                nc.vector.scalar_tensor_tensor(out=x, in0=x, scalar=gain, in1=psum[t % 2][:, :, 0:TG], op0=ALU.mult,
                                               op1=ALU.mult).then_inc(normed, 1)
            for t in range(NT + 1):
                n = P if t < NT else NS
                dve.wait_ge(k_turned, t + 1)
                if t >= 2:
                    dve.wait_ge(k_out[t % 2], 16 * (t // 2))
                nc.vector.tensor_copy(k_tok[t % 2][0:n, :], k_ps[0:n, t % 2, :]).then_inc(k_kept, 1)
            dve.wait_ge(gate_act, 5)
            nc.vector.scalar_tensor_tensor(out=a_pos[:, :, :], in0=a_pos[:, :, :], scalar=0.0, in1=a_neg[:, :, :],
                                           op0=ALU.max, op1=ALU.add).then_inc(gate_dve, 1)
            dve.wait_ge(gate_dve, 5)
            nc.vector.scalar_tensor_tensor(out=a, in0=a_pos[:, :, :], scalar=-1.0, in1=over(a_log[:, :], 1, [P, NT + 1, H]),
                                           op0=ALU.mult, op1=ALU.mult)
    m.free()


def chunk_masks(nc, m, sem, n, name):
    up = m.sb(f"{name}_up", [n, n])
    far = m.sb(f"{name}_far", [n, n])
    zeroed, ready = sem(f"{name}_zeroed"), sem(f"{name}_ready")

    def emit(pool):
        blocks = n // NL if n == NS else 1
        width = n // blocks
        pool.memset(up[:, :], 1.0).then_inc(zeroed, 1)
        pool.memset(far[:, :], 0.0).then_inc(zeroed, 1)
        pool.wait_ge(zeroed, 2)
        k = 0
        for t, fill in ((up, 0.0), (far, NEG)):
            v = t[:, :].rearrange("p (b l) -> p b l", b=blocks)
            pool.affine_select(out=v, in_=v, compare_op=ALU.is_ge, fill=fill, base=0, pattern=[[width, blocks], [1, width]],
                               channel_multiplier=-1).then_inc(ready, 1)
            k += 1
            if blocks > 1:
                pool.wait_ge(ready, k)
                pool.affine_select(out=v, in_=v, compare_op=ALU.is_ge, fill=fill, base=0,
                                   pattern=[[-width, blocks], [0, width]], channel_multiplier=1).then_inc(ready, 1)
                k += 1
        return k
    return up, far, ready, emit


def level_masks(pool, mask, levels, n, made):
    pool.memset(mask, 0.0).then_inc(made, 1)
    pool.wait_ge(made, 1)
    k = 1
    for level in range(levels):
        b = 1 << level
        v = mask[:, level, :].rearrange("p (a c) -> p a c", c=2 * b)[:, :, 0:b]
        pool.memset(v, 1.0).then_inc(made, 1)
        k += 1
        pool.wait_ge(made, k)
        pool.affine_select(out=v, in_=v, compare_op=ALU.is_ge, fill=0.0, base=-b, pattern=[[-2 * b, n // (2 * b)], [0, b]],
                           channel_multiplier=1).then_inc(made, 1)
        k += 1
        pool.wait_ge(made, k)
        pool.affine_select(out=v, in_=v, compare_op=ALU.is_ge, fill=0.0, base=2 * b - 1,
                           pattern=[[2 * b, n // (2 * b)], [0, b]], channel_multiplier=-1).then_inc(made, 1)
        k += 1
    return k


def delta_prompt(nc, i, o, c, feat, ba, head_out, sem):
    m = Memory(nc)

    def per_slot(name, shape):
        return [m.sb(f"{name}{s}", shape) for s in range(2)]

    W4 = [P, H, P]
    kv = per_slot("c_kv", [P, 2 * H, P])
    row_g, row_b, e_row, ET = (per_slot(n, W4) for n in ("c_row_g", "c_row_b", "c_e_row", "c_ET"))
    AT, PT, kbg, kdec, vb = (per_slot(n, W4) for n in ("c_AT", "c_PT", "c_kbg", "c_kdec", "c_vb"))
    D, DT, M, qg, u, wT, vn = (per_slot(n, W4) for n in ("c_D", "c_DT", "c_M", "c_qg", "c_u", "c_wT", "c_vn"))
    gcum, eg, beg, beta = (per_slot(n, [P, H]) for n in ("c_gcum", "c_eg", "c_beg", "c_beta"))
    S = per_slot("c_S", W4)
    S_dec = m.sb("c_S_dec", W4)
    mask = m.sb("c_mask", [P, NLEV, P])
    up, far, masks_ready, emit_masks = chunk_masks(nc, m, sem, P, "c")
    bank = [[m.ps(f"c_bank{s}{b}", [P, 512]) for b in range(4)] for s in range(2)]

    def heads(ap):
        return ap.rearrange("p (h t) -> p h t", h=H)

    names = ("staged rows_g rows_b identity_put beta_put R_ready B_ready KK_ready KQ_ready C_ready gcum_ready e_row_ready eg_ready arg_ready "
             "ET_ready KE_ready AT_ready PT_ready kt_turned vt_turned beg_ready kbg_ready kdec_ready vb_ready qg_ready "
             "u_product w_product u_kept w_kept wS_ready vn_ready o_ready S_product decayed S_done o_kept").split()
    S_ = {n: sem("c_" + n) for n in names}
    M_product, M_kept, D_product, D_kept, DT_kept = (
        [sem(f"c_{n}{s}") for s in range(2)] for n in ("M_product", "M_kept", "D_product", "D_kept", "DT_kept"))
    mask_made, S_zero, S_out = sem("c_mask_made"), sem("c_S_zero"), sem("c_S_out")
    owner = {"pool": "staged rows_g rows_b identity_put beta_put beg_ready qg_ready",
             "tensor": "C_ready R_ready B_ready KK_ready KQ_ready kt_turned vt_turned u_product w_product wS_ready o_ready S_product",
             "scalar": "gcum_ready e_row_ready eg_ready ET_ready u_kept w_kept o_kept",
             "vector": "arg_ready KE_ready AT_ready PT_ready kbg_ready kdec_ready vb_ready vn_ready decayed S_done"}

    def credit(eng, who):
        for n in owner[who].split():
            eng.sem_inc(S_[n], CREDIT)

    n_mask = 1 + 3 * NLEV

    def odd_even(ap, level, odd):
        b = 1 << level
        return ap.rearrange("p h (a c) -> p (h a) c", c=2 * b)[:, :, odd * b:(odd + 1) * b]

    with nc.Block() as block:
        @block.sync
        def _(sp):
            sp.wait_ge(S_["S_done"], done(NT - 1))
            sp.dma_start(o["gdn_S_prompt"][0, 0].rearrange("h k v -> k h v"), S[0][:, :, :]).then_inc(S_out, 16)
            sp.wait_ge(S_out, 16)

        @block.gpsimd
        def _(pool):
            credit(pool, "pool")
            pool.memset(S[0][:, :, :], 0.0).then_inc(S_zero, 1)
            k = emit_masks(pool)
            level_masks(pool, mask[:, :, :], NLEV, P, mask_made)
            pool.wait_ge(masks_ready, k)
            with pool.Fori(0, NT // 2) as it:
                for s in range(2):
                    n = 2 * it + s
                    pool.wait_ge(S_["S_done"], done(n - 2))
                    pool.wait_ge(S_["o_kept"], done(n - 2))
                    for t in (D[s], DT[s]):
                        ins = nc.gpsimd.tensor_tensor(t[:, :, :], over(c["ident"][:, :], 1, W4), over(c["ident"][:, :], 1, W4), ALU.mult)
                    ins.then_inc(S_["identity_put"], 1)
                    nc.gpsimd.tensor_tensor(row_g[s][:, :, :], over(up[:, :], 1, W4),
                                            over(ba[:, bass.ds(n, 1), H:2 * H].rearrange("p o h -> p (o h)"), 2, W4),
                                            ALU.mult).then_inc(S_["rows_g"], 1)
                    nc.gpsimd.tensor_tensor(row_b[s][:, :, :], over(c["ident"][:, :], 1, W4),
                                            over(ba[:, bass.ds(n, 1), 0:H].rearrange("p o h -> p (o h)"), 2, W4),
                                            ALU.mult).then_inc(S_["rows_b"], 1)
                    nc.gpsimd.tensor_copy(kv[s][:, :, :], feat[:, H:3 * H, bass.ds(n * P, P)]).then_inc(S_["staged"], 1)
                    nc.gpsimd.tensor_copy(beta[s][:, :], ba[:, bass.ds(n, 1), 0:H].rearrange("p o h -> p (o h)")
                                          ).then_inc(S_["beta_put"], 1)
                for s in range(2):
                    n = 2 * it + s
                    pool.wait_ge(S_["beta_put"], done(n))
                    pool.wait_ge(S_["eg_ready"], done(n))
                    pool.wait_ge(S_["e_row_ready"], done(n))
                    nc.gpsimd.tensor_tensor(beg[s][:, :], eg[s][:, :], beta[s][:, :], ALU.mult).then_inc(S_["beg_ready"], 1)
                    nc.gpsimd.tensor_tensor(qg[s][:, :, :], feat[:, 0:H, bass.ds(n * P, P)], e_row[s][:, :, :],
                                            ALU.mult).then_inc(S_["qg_ready"], 1)

        @block.tensor
        def _(pe):
            credit(pe, "tensor")
            pe.wait_ge(masks_ready, 2)
            with pe.Fori(0, NT // 2) as it:
                for s in range(2):
                    n = 2 * it + s
                    b = bank[s]
                    pe.wait_ge(S_["rows_g"], done(n))
                    nc.tensor.matmul(b[3][:, 0:H], up[:, :], ba[:, bass.ds(n, 1), H:2 * H].rearrange("p o h -> p (o h)"),
                                     start=True, stop=True).then_inc(S_["C_ready"], 1)
                    nc.tensor.matmul(b[0][:, :], c["ones"][:, :], row_g[s][:, :, :], start=True, stop=True
                                     ).then_inc(S_["R_ready"], 1)
                    pe.wait_ge(S_["rows_b"], done(n))
                    nc.tensor.matmul(b[1][:, :], c["ones"][:, :], row_b[s][:, :, :], start=True, stop=True
                                     ).then_inc(S_["B_ready"], 1)
                    pe.wait_ge(S_["staged"], done(n))
                    for h in range(H):
                        mm = nc.tensor.matmul(b[2][:, h * P:(h + 1) * P], kv[s][:, h, :], kv[s][:, h, :], start=True, stop=True)
                    mm.then_inc(S_["KK_ready"], 1)
                    pe.wait_ge(S_["gcum_ready"], done(n))
                    for h in range(H):
                        mm = nc.tensor.matmul(b[3][:, h * P:(h + 1) * P], kv[s][:, h, :],
                                              feat[:, h, bass.ds(n * P, P)], start=True, stop=True)
                    mm.then_inc(S_["KQ_ready"], 1)
                for s in range(2):
                    n = 2 * it + s
                    b = bank[s]
                    pe.wait_ge(S_["e_row_ready"], done(n))
                    for h in range(H):
                        mm = nc.tensor.transpose(b[0][:, h * P:(h + 1) * P], kv[s][:, h, :], c["ident"][:, :])
                    mm.then_inc(S_["kt_turned"], 1)
                    pe.wait_ge(S_["AT_ready"], done(n))
                    for h in range(H):
                        mm = nc.tensor.transpose(b[1][:, h * P:(h + 1) * P], kv[s][:, H + h, :], c["ident"][:, :])
                    mm.then_inc(S_["vt_turned"], 1)
                for level in range(NLEV):
                    for s in range(2):
                        n = 2 * it + s
                        if level == 0:
                            pe.wait_ge(S_["AT_ready"], done(n))
                            pe.wait_ge(S_["identity_put"], done(n))
                        else:
                            pe.wait_ge(D_kept[s], levels_done(it, level - 1, NLEV - 1))
                        for h in range(H):
                            mm = nc.tensor.matmul(bank[s][2][:, h * P:(h + 1) * P], AT[s][:, h, :], D[s][:, h, :],
                                                  start=True, stop=True)
                        mm.then_inc(M_product[s], 1)
                    for s in range(2):
                        n = 2 * it + s
                        pe.wait_ge(M_kept[s], levels_done(it, level))
                        if level == 0:
                            pe.wait_ge(S_["PT_ready"], done(n))
                        else:
                            pe.wait_ge(DT_kept[s], levels_done(it, level - 1))
                        for h in range(H):
                            if level < NLEV - 1:
                                nc.tensor.matmul(bank[s][3][:, h * HALF:(h + 1) * HALF], DT[s][:, h, :],
                                                 odd_even(M[s][:, h:h + 1, :], level, 0), start=True, stop=True)
                            mm = nc.tensor.matmul(bank[s][3][:, (H + h) * HALF:(H + h + 1) * HALF], M[s][:, h, :],
                                                  odd_even(DT[s][:, h:h + 1, :], level, 1), start=True, stop=True)
                        mm.then_inc(D_product[s], 1)
                for s in range(2):
                    n = 2 * it + s
                    b = bank[s]
                    pe.wait_ge(DT_kept[s], levels_done(it, NLEV - 1))
                    pe.wait_ge(S_["vb_ready"], done(n))
                    for h in range(H):
                        mm = nc.tensor.matmul(b[0][:, h * P:(h + 1) * P], DT[s][:, h, :], vb[s][:, h, :], start=True, stop=True)
                    mm.then_inc(S_["u_product"], 1)
                    for h in range(H):
                        mm = nc.tensor.matmul(b[1][:, h * P:(h + 1) * P], kbg[s][:, h, :], DT[s][:, h, :], start=True, stop=True)
                    mm.then_inc(S_["w_product"], 1)
                for s in range(2):
                    n = 2 * it + s
                    b = bank[s]
                    pe.wait_ge(S_["w_kept"], done(n))
                    pe.wait_ge(S_["S_done"], done(n - 1))
                    for h in range(H):
                        mm = nc.tensor.matmul(b[2][:, h * P:(h + 1) * P], wT[s][:, h, :], S[s][:, h, :], start=True, stop=True)
                    mm.then_inc(S_["wS_ready"], 1)
                    pe.wait_ge(S_["vn_ready"], done(n))
                    pe.wait_ge(S_["u_kept"], done(n))
                    for h in range(H):
                        mm = nc.tensor.matmul(b[0][:, h * P:(h + 1) * P], kdec[s][:, h, :], vn[s][:, h, :], start=True, stop=True)
                    mm.then_inc(S_["S_product"], 1)
                    pe.wait_ge(S_["qg_ready"], done(n))
                    for h in range(H):
                        nc.tensor.matmul(b[3][:, h * P:(h + 1) * P], S[s][:, h, :], qg[s][:, h, :], start=True, stop=False)
                        mm = nc.tensor.matmul(b[3][:, h * P:(h + 1) * P], vn[s][:, h, :], PT[s][:, h, :], start=False, stop=True)
                    mm.then_inc(S_["o_ready"], 1)

        @block.scalar
        def _(act):
            credit(act, "scalar")
            nc.scalar.preload_act_table(ACT.Exp)
            with act.Fori(0, NT // 2) as it:
                for s in range(2):
                    n = 2 * it + s
                    b = bank[s]
                    act.wait_ge(S_["C_ready"], done(n))
                    nc.scalar.copy(gcum[s][:, :], b[3][:, 0:H]).then_inc(S_["gcum_ready"], 1)
                    act.wait_ge(S_["gcum_ready"], done(n))
                    nc.scalar.activation(eg[s][:, :], gcum[s][:, :], ACT.Exp).then_inc(S_["eg_ready"], 1)
                    act.wait_ge(S_["arg_ready"], done(n))
                    nc.scalar.activation(ET[s][:, :, :], ET[s][:, :, :], ACT.Exp).then_inc(S_["ET_ready"], 1)
                    nc.scalar.activation(e_row[s][:, :, :], heads(b[0][:, :]), ACT.Exp).then_inc(S_["e_row_ready"], 1)
                for s in range(2):
                    n = 2 * it + s
                    act.wait_ge(S_["w_product"], done(n))
                    nc.scalar.copy(wT[s][:, :, :], heads(bank[s][1][:, :])).then_inc(S_["w_kept"], 1)
                    nc.scalar.copy(u[s][:, :, :], heads(bank[s][0][:, :])).then_inc(S_["u_kept"], 1)
                for s in range(2):
                    n = 2 * it + s
                    act.wait_ge(S_["o_ready"], done(n))
                    nc.scalar.copy(head_out[:, 0:H, bass.ds(n * P, P)], heads(bank[s][3][:, :])).then_inc(S_["o_kept"], 1)

        @block.vector
        def _(dve):
            credit(dve, "vector")
            dve.wait_ge(masks_ready, 2)
            dve.wait_ge(mask_made, n_mask)
            dve.wait_ge(S_zero, 1)
            with dve.Fori(0, NT // 2) as it:
                for s in range(2):
                    n = 2 * it + s
                    b = bank[s]
                    dve.wait_ge(S_["R_ready"], done(n))
                    dve.wait_ge(S_["gcum_ready"], done(n))
                    for h in range(H):
                        ins = nc.vector.scalar_tensor_tensor(
                            out=ET[s][:, h, :], in0=b[0][:, h * P:(h + 1) * P], scalar=gcum[s][:, h:h + 1], in1=far[:, :],
                            op0=ALU.subtract, op1=ALU.add)
                    ins.then_inc(S_["arg_ready"], 1)
                    dve.wait_ge(S_["KK_ready"], done(n))
                    dve.wait_ge(S_["ET_ready"], done(n))
                    nc.vector.tensor_tensor(AT[s][:, :, :], heads(b[2][:, :]), ET[s][:, :, :], ALU.mult).then_inc(S_["KE_ready"], 1)
                    dve.wait_ge(S_["KE_ready"], done(n))
                    dve.wait_ge(S_["B_ready"], done(n))
                    nc.vector.tensor_tensor(AT[s][:, :, :], heads(b[1][:, :]), AT[s][:, :, :], ALU.mult).then_inc(S_["AT_ready"], 1)
                    dve.wait_ge(S_["KQ_ready"], done(n))
                    nc.vector.tensor_tensor(PT[s][:, :, :], heads(b[3][:, :]), ET[s][:, :, :], ALU.mult).then_inc(S_["PT_ready"], 1)

                def token_major(s):
                    n = 2 * it + s
                    b = bank[s]
                    dve.wait_ge(S_["kt_turned"], done(n))
                    dve.wait_ge(S_["beg_ready"], done(n))
                    nc.vector.tensor_tensor(kbg[s][:, :, :], heads(b[0][:, :]), over(beg[s][:, :], 2, W4), ALU.mult
                                            ).then_inc(S_["kbg_ready"], 1)
                    nc.vector.tensor_tensor(kdec[s][:, :, :], heads(b[0][:, :]),
                                            ET[s][:, :, P - 1:P].to_broadcast(W4), ALU.mult).then_inc(S_["kdec_ready"], 1)
                    dve.wait_ge(S_["vt_turned"], done(n))
                    nc.vector.tensor_tensor(vb[s][:, :, :], heads(b[1][:, :]),
                                            over(ba[:, bass.ds(n, 1), 0:H].rearrange("p o h -> p (o h)"), 2, W4),
                                            ALU.mult).then_inc(S_["vb_ready"], 1)

                for level in range(NLEV):
                    for s in range(2):
                        n = 2 * it + s
                        dve.wait_ge(M_product[s], levels_done(it, level))
                        nc.vector.tensor_tensor(M[s][:, :, :], heads(bank[s][2][:, :]), over(mask[:, level, :], 1, W4),
                                                ALU.mult).then_inc(M_kept[s], 1)
                    if level == 0:
                        token_major(0)
                        token_major(1)
                    for s in range(2):
                        n = 2 * it + s
                        dve.wait_ge(D_product[s], levels_done(it, level))
                        b = 1 << level
                        if level < NLEV - 1:
                            d = odd_even(D[s][:, :, :], level, 0)
                            nc.vector.tensor_tensor(d, d, bank[s][3][:, 0:H * HALF].rearrange("p (a b) -> p a b", b=b),
                                                    ALU.subtract).then_inc(D_kept[s], 1)
                        d = odd_even(DT[s][:, :, :], level, 1)
                        nc.vector.tensor_tensor(d, d, bank[s][3][:, H * HALF:2 * H * HALF].rearrange("p (a b) -> p a b", b=b),
                                                ALU.subtract).then_inc(DT_kept[s], 1)
                for s in range(2):
                    n = 2 * it + s
                    b = bank[s]
                    dve.wait_ge(S_["e_row_ready"], done(n))
                    dve.wait_ge(S_["S_done"], done(n - 1))
                    nc.vector.tensor_tensor(S_dec[:, :, :], S[s][:, :, :], e_row[s][:, :, P - 1:P].to_broadcast(W4),
                                            ALU.mult).then_inc(S_["decayed"], 1)
                    dve.wait_ge(S_["wS_ready"], done(n))
                    dve.wait_ge(S_["u_kept"], done(n))
                    nc.vector.tensor_tensor(vn[s][:, :, :], u[s][:, :, :], heads(b[2][:, :]), ALU.subtract
                                            ).then_inc(S_["vn_ready"], 1)
                    dve.wait_ge(S_["S_product"], done(n))
                    dve.wait_ge(S_["decayed"], done(n))
                    nc.vector.tensor_tensor(S[1 - s][:, :, :], heads(b[0][:, :]), S_dec[:, :, :], ALU.add
                                            ).then_inc(S_["S_done"], 1)
    m.free()


def delta_sample(nc, i, o, c, feat, ba, head_out, sem):
    m = Memory(nc)
    R, C = [NS, H, NS], [NS, H, DH]
    LEV = 2
    row_g, row_b, ET, AT, PT, D, DT, M = (m.sb(f"s_{n}", R) for n in ("row_g", "row_b", "ET", "AT", "PT", "D", "DT", "M"))
    kbg, kdec, vb, vn = (m.sb(f"s_{n}", C) for n in ("kbg", "kdec", "vb", "vn"))
    e_row = m.sb("s_e_row", [P, H, NS])
    wq = m.sb("s_wq", [P, H, NB, 2 * NL])
    uT, vnT, qS = (m.sb(f"s_{n}", [P, H, NS]) for n in ("uT", "vnT", "qS"))
    gcum, eg, beg, dec = (m.sb(f"s_{n}", [NS, H]) for n in ("gcum", "eg", "beg", "dec"))
    state = m.sb("s_state", [P, NB * H, DH])
    own = m.sb("s_own", [NS, NB])
    spread = m.sb("s_spread", [NS, NB, DH])
    mask = m.sb("s_mask", [NS, LEV, NS])
    up, far, masks_ready, emit_masks = chunk_masks(nc, m, sem, NS, "s")
    bank = [m.ps(f"s_bank{b}", [P, 512]) for b in range(6)]
    wide = m.ps("s_wide", [P, NB, DH])

    state_in, state_out = sem("s_state_in"), sem("s_state_out")
    own_made, mask_made, rows_ready, to_pe, pe_done = (sem(f"s_{n}") for n in ("own_made", "mask_made", "rows_ready", "to_pe", "pe_done"))
    act_done, dve_done, q_put, identity_put = sem("s_act_done"), sem("s_dve_done"), sem("s_q_put"), sem("s_identity_put")
    PE = {n: k + 1 for k, n in enumerate("gcum row beta KK KQ k_turned v_turned M0 D0 M1 D1 u w wqS vn_turned o S0 S1 S2 S3".split())}
    SC = {n: k + 1 for k, n in enumerate("gcum eg e_row ET u w qS".split())}
    DV = {n: k + 1 for k, n in enumerate(
        "arg dec KE AT PT beg kbg kdec vb M0 D0 DT0 M1 DT1 vnT vn o "
        "spread0 decay0 S0 spread1 decay1 S1 spread2 decay2 S2 spread3 decay3 S3".split())}

    def cols(ap, n=NS, rows=NS):
        return ap[0:rows, 0:H * n].rearrange("p (h t) -> p h t", h=H)

    def pairs_of(ap, level, odd):
        b = 1 << level
        return ap.rearrange("p h (a c) -> p (h a) c", c=2 * b)[:, :, odd * b:(odd + 1) * b]

    b_gate = ba[0:NS, NT, 0:H]
    g_gate = ba[0:NS, NT, H:2 * H]
    q, k, v = (feat[:, x * H:(x + 1) * H, SEQ:T] for x in range(3))

    with nc.Block() as block:
        @block.sync
        def _(sp):
            sp.dma_start(state[:, :, :], i["state_gdn_S"][0].rearrange("b h k v -> k (b h) v")).then_inc(state_in, 16)
            sp.wait_ge(dve_done, DV["S3"])
            sp.dma_start(o["gdn_S_sample"][0].rearrange("b h k v -> k (b h) v"), state[:, :, :]).then_inc(state_out, 16)
            sp.wait_ge(state_out, 16)

        @block.gpsimd
        def _(pool):
            kk = emit_masks(pool)
            level_masks(pool, mask[:, :, :], LEV, NS, mask_made)
            pool.memset(own[:, :], 1.0).then_inc(own_made, 1)
            pool.wait_ge(own_made, 1)
            pool.affine_select(out=own[:, :], in_=own[:, :], compare_op=ALU.is_ge, fill=0.0, base=0, pattern=[[-NL, NB]],
                               channel_multiplier=1).then_inc(own_made, 1)
            pool.wait_ge(own_made, 2)
            pool.affine_select(out=own[:, :], in_=own[:, :], compare_op=ALU.is_ge, fill=0.0, base=NL - 1, pattern=[[NL, NB]],
                               channel_multiplier=-1).then_inc(own_made, 1)
            pool.wait_ge(masks_ready, kk)
            nc.gpsimd.tensor_tensor(row_g[:, :, :], over(up[:, :], 1, R), over(g_gate, 2, R), ALU.mult).then_inc(rows_ready, 1)
            nc.gpsimd.tensor_tensor(row_b[:, :, :], over(c["ident"][0:NS, 0:NS], 1, R), over(b_gate, 2, R), ALU.mult
                                    ).then_inc(rows_ready, 1)
            for t in (D, DT):
                nc.gpsimd.tensor_copy(t[:, :, :], over(c["ident"][0:NS, 0:NS], 1, R)).then_inc(identity_put, 1)
            pool.wait_ge(act_done, SC["e_row"])
            nc.gpsimd.tensor_tensor(wq[:, :, :, NL:2 * NL], q.rearrange("p h (b l) -> p h b l", b=NB),
                                    e_row[:, :, :].rearrange("p h (b l) -> p h b l", b=NB), ALU.mult).then_inc(q_put, 1)

        @block.tensor
        def _(pe):
            pe.wait_ge(rows_ready, 2)
            nc.tensor.matmul(bank[3][0:NS, 0:H], up[:, :], g_gate, start=True, stop=True).then_inc(pe_done, 1)
            ones = c["ones"][0:NS, :]
            nc.tensor.matmul(bank[0][:, 0:H * NS], ones, row_g[:, :, :], start=True, stop=True).then_inc(pe_done, 1)
            nc.tensor.matmul(bank[1][0:NS, 0:H * NS], ones[:, 0:NS], row_b[:, :, :], start=True, stop=True).then_inc(pe_done, 1)
            for h in range(H):
                mm = nc.tensor.matmul(cols(bank[2])[:, h, :], k[:, h, :], k[:, h, :], start=True, stop=True)
            mm.then_inc(pe_done, 1)
            pe.wait_ge(act_done, SC["gcum"])
            for h in range(H):
                mm = nc.tensor.matmul(cols(bank[3])[:, h, :], k[:, h, :], q[:, h, :], start=True, stop=True)
            mm.then_inc(pe_done, 1)
            for x, b in ((k, 4), (v, 5)):
                for h in range(H):
                    mm = nc.tensor.transpose(bank[b][0:NS, h * DH:(h + 1) * DH], x[:, h, :], c["ident"][:, :])
                mm.then_inc(pe_done, 1)
            pe.wait_ge(identity_put, 2)
            for level in range(LEV):
                pe.wait_ge(dve_done, DV["PT"] if level == 0 else DV["D0"])
                for h in range(H):
                    mm = nc.tensor.matmul(cols(bank[2])[:, h, :], AT[:, h, :], D[:, h, :], start=True, stop=True)
                mm.then_inc(pe_done, 1)
                pe.wait_ge(dve_done, DV[f"M{level}"])
                half = NS // 2
                for h in range(H):
                    if level < LEV - 1:
                        nc.tensor.matmul(bank[3][0:NS, h * half:(h + 1) * half], DT[:, h, :],
                                         pairs_of(M[:, h:h + 1, :], level, 0), start=True, stop=True)
                    mm = nc.tensor.matmul(bank[3][0:NS, (H + h) * half:(H + h + 1) * half], M[:, h, :],
                                          pairs_of(DT[:, h:h + 1, :], level, 1), start=True, stop=True)
                mm.then_inc(pe_done, 1)
            pe.wait_ge(dve_done, DV["DT1"])
            for h in range(H):
                mm = nc.tensor.matmul(cols(bank[0], NS, P)[:, h, :], vb[:, h, :], DT[:, h, :], start=True, stop=True)
            mm.then_inc(pe_done, 1)
            for h in range(H):
                mm = nc.tensor.matmul(bank[1][:, h * NS:(h + 1) * NS], kbg[:, h, :], DT[:, h, :], start=True, stop=True)
            mm.then_inc(pe_done, 1)
            pe.wait_ge(act_done, SC["w"])
            pe.wait_ge(q_put, 1)
            pe.wait_ge(state_in, 16)
            for b in range(NB):
                for h in range(H):
                    at = (h * NB + b) * 2 * NL
                    mm = nc.tensor.matmul(bank[2][:, at:at + 2 * NL], state[:, b * H + h, :], wq[:, h, b, :], start=True, stop=True)
            mm.then_inc(pe_done, 1)
            pe.wait_ge(dve_done, DV["vnT"])
            for h in range(H):
                mm = nc.tensor.transpose(bank[4][0:NS, h * DH:(h + 1) * DH], vnT[:, h, :], c["ident"][:, :])
            mm.then_inc(pe_done, 1)
            pe.wait_ge(dve_done, DV["vn"])
            for h in range(H):
                mm = nc.tensor.matmul(bank[5][:, h * NS:(h + 1) * NS], vn[:, h, :], PT[:, h, :], start=True, stop=True)
            mm.then_inc(pe_done, 1)
            for h in range(H):
                pe.wait_ge(dve_done, DV[f"spread{h}"])
                for g in range(2):
                    mm = nc.tensor.matmul(wide[:, g * 4:g * 4 + 4, :], kdec[:, h, :], spread[:, g * 4:g * 4 + 4, :],
                                          start=True, stop=True)
                mm.then_inc(pe_done, 1)

        @block.scalar
        def _(act):
            act.wait_ge(pe_done, PE["gcum"])
            nc.scalar.copy(gcum[:, :], bank[3][0:NS, 0:H]).then_inc(act_done, 1)
            act.wait_ge(act_done, SC["gcum"])
            nc.scalar.activation(eg[:, :], gcum[:, :], ACT.Exp).then_inc(act_done, 1)
            act.wait_ge(pe_done, PE["row"])
            nc.scalar.activation(e_row[:, :, :], cols(bank[0], NS, P), ACT.Exp).then_inc(act_done, 1)
            act.wait_ge(dve_done, DV["arg"])
            nc.scalar.activation(ET[:, :, :], ET[:, :, :], ACT.Exp).then_inc(act_done, 1)
            act.wait_ge(pe_done, PE["w"])
            nc.scalar.copy(uT[:, :, :], cols(bank[0], NS, P)).then_inc(act_done, 1)
            nc.scalar.copy(wq[:, :, :, 0:NL], cols(bank[1], NS, P).rearrange("p h (b l) -> p h b l", b=NB)).then_inc(act_done, 1)
            act.wait_ge(dve_done, DV["vnT"])
            nc.scalar.copy(qS[:, :, :].rearrange("p h (b l) -> p (h b) l", b=NB),
                           bank[2][:, 0:2 * H * NS].rearrange("p (a l) -> p a l", l=2 * NL)[:, :, NL:2 * NL]).then_inc(act_done, 1)

        @block.vector
        def _(dve):
            dve.wait_ge(masks_ready, 4)
            dve.wait_ge(mask_made, 1 + 3 * LEV)
            dve.wait_ge(act_done, SC["e_row"])
            for h in range(H):
                ins = nc.vector.scalar_tensor_tensor(out=ET[:, h, :], in0=cols(bank[0])[:, h, :], scalar=gcum[:, h:h + 1],
                                                     in1=far[:, :], op0=ALU.subtract, op1=ALU.add)
            ins.then_inc(dve_done, 1)
            dve.wait_ge(act_done, SC["ET"])
            nc.vector.tensor_reduce(out=dec[:, :], in_=ET[:, :, :].rearrange("p h (b l) -> p h b l", b=NB)[:, :, :, NL - 1],
                                    axis=AX.X, op=ALU.add).then_inc(dve_done, 1)
            dve.wait_ge(pe_done, PE["KK"])
            nc.vector.tensor_tensor(AT[:, :, :], cols(bank[2]), ET[:, :, :], ALU.mult).then_inc(dve_done, 1)
            dve.wait_ge(dve_done, DV["KE"])
            nc.vector.tensor_tensor(AT[:, :, :], cols(bank[1]), AT[:, :, :], ALU.mult).then_inc(dve_done, 1)
            dve.wait_ge(pe_done, PE["KQ"])
            nc.vector.tensor_tensor(PT[:, :, :], cols(bank[3]), ET[:, :, :], ALU.mult).then_inc(dve_done, 1)
            nc.vector.tensor_tensor(beg[:, :], eg[:, :], b_gate, ALU.mult).then_inc(dve_done, 1)
            dve.wait_ge(pe_done, PE["v_turned"])
            dve.wait_ge(dve_done, DV["beg"])
            nc.vector.tensor_tensor(kbg[:, :, :], cols(bank[4], DH), over(beg[:, :], 2, C), ALU.mult).then_inc(dve_done, 1)
            nc.vector.tensor_tensor(kdec[:, :, :], cols(bank[4], DH), over(dec[:, :], 2, C), ALU.mult).then_inc(dve_done, 1)
            nc.vector.tensor_tensor(vb[:, :, :], cols(bank[5], DH), over(b_gate, 2, C), ALU.mult).then_inc(dve_done, 1)
            for level in range(LEV):
                dve.wait_ge(pe_done, PE[f"M{level}"])
                nc.vector.tensor_tensor(M[:, :, :], cols(bank[2]), over(mask[:, level, :], 1, R), ALU.mult).then_inc(dve_done, 1)
                dve.wait_ge(pe_done, PE[f"D{level}"])
                half, b = NS // 2, 1 << level
                if level < LEV - 1:
                    d = pairs_of(D[:, :, :], level, 0)
                    nc.vector.tensor_tensor(d, d, bank[3][0:NS, 0:H * half].rearrange("p (a b) -> p a b", b=b),
                                            ALU.subtract).then_inc(dve_done, 1)
                d = pairs_of(DT[:, :, :], level, 1)
                nc.vector.tensor_tensor(d, d, bank[3][0:NS, H * half:2 * H * half].rearrange("p (a b) -> p a b", b=b),
                                        ALU.subtract).then_inc(dve_done, 1)
            dve.wait_ge(pe_done, PE["wqS"])
            dve.wait_ge(act_done, SC["u"])
            nc.vector.tensor_tensor(vnT[:, :, :].rearrange("p h (b l) -> p (h b) l", b=NB),
                                    uT[:, :, :].rearrange("p h (b l) -> p (h b) l", b=NB),
                                    bank[2][:, 0:2 * H * NS].rearrange("p (a l) -> p a l", l=2 * NL)[:, :, 0:NL],
                                    ALU.subtract).then_inc(dve_done, 1)
            dve.wait_ge(pe_done, PE["vn_turned"])
            nc.vector.tensor_copy(vn[:, :, :], cols(bank[4], DH)).then_inc(dve_done, 1)
            dve.wait_ge(pe_done, PE["o"])
            dve.wait_ge(act_done, SC["qS"])
            nc.vector.tensor_tensor(head_out[:, 0:H, SEQ:T], cols(bank[5], NS, P), qS[:, :, :], ALU.add).then_inc(dve_done, 1)
            dve.wait_ge(state_in, 16)
            for h in range(H):
                dve.wait_ge(dve_done, DV["vn"])
                if h:
                    dve.wait_ge(pe_done, PE[f"S{h - 1}"])
                nc.vector.tensor_tensor(spread[:, :, :], over(vn[:, h, :], 1, [NS, NB, DH]), over(own[:, :], 2, [NS, NB, DH]),
                                        ALU.mult).then_inc(dve_done, 1)
                mine = state[:, :, :].rearrange("p (b h) v -> p b h v", h=H)[:, :, h, :]
                last = e_row[:, h, :].rearrange("p (b l) -> p b l", b=NB)[:, :, NL - 1:NL]
                nc.vector.tensor_tensor(mine, mine, last.to_broadcast([P, NB, DH]), ALU.mult).then_inc(dve_done, 1)
                dve.wait_ge(pe_done, PE[f"S{h}"])
                dve.wait_ge(dve_done, DV[f"decay{h}"])
                nc.vector.tensor_tensor(mine, wide[:, :, :], mine, ALU.add).then_inc(dve_done, 1)
    m.free()


def attention_prompt(nc, i, o, c, feat, head_out, sem):
    m = Memory(nc)
    qk = [m.sb(f"a_qk{s}", [P, 2, SEQ]) for s in range(2)]
    v = [m.sb(f"a_v{s}", [P, NT, DH]) for s in range(2)]
    e = [[m.sb(f"a_e{s}{x}", [P, SEQ]) for x in range(2)] for s in range(2)]
    amapT = [m.sb(f"a_mapT{s}", [P, NT, P]) for s in range(2)]
    nmax, total, inv, w2 = (m.sb(f"a_{n}", [P, 2, 2]) for n in ("nmax", "total", "inv", "w2"))
    ident16 = m.sb("a_ident16", [P, P], BF16)
    far16 = m.sb("a_far16", [P, P], BF16)
    score = [m.ps(f"a_score{x}", [P, SEQ]) for x in range(2)]
    turned = m.ps("a_turned", [P, 2, 4, P])
    out = [m.ps(f"a_out{s}", [P, 512]) for s in range(2)]

    v_in = [sem(f"a_v_in{s}") for s in range(2)]
    made, made2 = sem("a_made"), sem("a_masks")
    qk_staged = sem("a_qk_staged")
    scored, maxed, expd = ([sem(f"a_{n}{x}") for x in range(2)] for n in ("scored", "maxed", "expd"))
    inverted, weighted, scaled, mapped = (sem(f"a_{n}") for n in ("inverted", "weighted", "scaled", "mapped"))
    block_turned, multiplied, out_kept = sem("a_block_turned"), sem("a_multiplied"), sem("a_out_kept")
    half_kept = [sem(f"a_half_kept{x}") for x in range(2)]

    units = [(hh, qb) for hh in range(2) for qb in range(NT)]
    NU = len(units)
    groups, g_of = [], {}
    for u, (hh, qb) in enumerate(units):
        for g in range((qb + 4) // 4):
            g_of[(u, g)] = len(groups)
            groups.append((u, g, min(4, qb + 1 - 4 * g)))
    NGR = len(groups)
    assert NGR % 2 == 0
    v_rows = o["v_prompt"].rearrange("a b (n p) h d -> p (a b n) h d", p=P)

    with nc.Block() as block:
        @block.sync
        def _(sp):
            sp.dma_start(v[0][:, :, :], v_rows[:, :, 0, :]).then_inc(v_in[0], 16)
            sp.dma_start(v[1][:, :, :], v_rows[:, :, 1, :]).then_inc(v_in[1], 16)
            for s in range(2):
                sp.wait_ge(multiplied, (s + 1) * NT + CREDIT)
                sp.dma_start(v[s][:, :, :], v_rows[:, :, 2 + s, :]).then_inc(v_in[s], 16)

        @block.gpsimd
        def _(pool):
            pool.sem_inc(qk_staged, CREDIT)
            pool.memset(ident16[:, :], 0.0).then_inc(made, 1)
            pool.memset(far16[:, :], 0.0).then_inc(made, 1)
            pool.wait_ge(made, 2)
            pool.affine_select(out=ident16[:, :], in_=ident16[:, :], compare_op=ALU.not_equal, fill=1.0, base=0,
                               pattern=[[-1, P]], channel_multiplier=1).then_inc(made2, 1)
            pool.affine_select(out=far16[:, :], in_=far16[:, :], compare_op=ALU.is_ge, fill=NEG, base=0,
                               pattern=[[-1, P]], channel_multiplier=1).then_inc(made2, 1)
            for h in range(H):
                if h >= 2:
                    pool.wait_ge(multiplied, (h - 1) * NT + CREDIT)
                nc.gpsimd.tensor_copy(qk[h % 2][:, 0, :], feat[:, 3 * H + h, 0:SEQ])
                nc.gpsimd.tensor_copy(qk[h % 2][:, 1, :], feat[:, 4 * H + h, 0:SEQ]).then_inc(qk_staged, 1)

        @block.tensor
        def _(pe):
            pe.sem_inc(multiplied, CREDIT)
            pe.wait_ge(made2, 2)

            def scores(it, u):
                hh, qb = units[u]
                if qb == 0:
                    pe.wait_ge(qk_staged, done(2 * it + hh))
                for x in range(2):
                    pe.wait_ge(expd[x], NU * it + (u + 1))
                    lo = x * HALF
                    q = qk[hh][lo:lo + HALF, 0, qb * P:(qb + 1) * P]
                    n = (qb + 1) * P
                    for k0 in range(0, n - P, 512):
                        k1 = min(n - P, k0 + 512)
                        nc.tensor.matmul(score[x][:, k0:k1], q, qk[hh][lo:lo + HALF, 1, k0:k1], start=True, stop=True)
                    nc.tensor.matmul(score[x][:, n - P:n], q, qk[hh][lo:lo + HALF, 1, n - P:n], start=True, stop=False)
                    mm = nc.tensor.matmul(score[x][:, n - P:n], ident16[:, :], far16[:, :], start=False, stop=True)
                    mm.then_inc(scored[x], 1)

            def turn_and_multiply(it, u):
                hh, qb = units[u]
                pe.wait_ge(mapped, NU * it + (u + 1))
                for g in range((qb + 4) // 4):
                    k = g_of[(u, g)]
                    pe.wait_ge(half_kept[k % 2], (NGR // 2) * it + (k // 2 + 1))
                    for j in range(groups[k][2]):
                        mm = nc.tensor.transpose(turned[:, k % 2, j, :], e[u % 2][0][:, (4 * g + j) * P:(4 * g + j + 1) * P],
                                                 c["ident"][:, :])
                    mm.then_inc(block_turned, 1)
                if qb == 0:
                    pe.wait_ge(v_in[hh], 16 * it + 16)
                pe.wait_ge(out_kept, NU * it + (u + 1))
                for g in range((qb + 4) // 4):
                    k = g_of[(u, g)]
                    pe.wait_ge(half_kept[k % 2], (NGR // 2) * it + (k // 2 + 2))
                    for j in range(groups[k][2]):
                        b = 4 * g + j
                        mm = nc.tensor.matmul(out[u % 2][:, 0:P], v[hh][:, b, :], amapT[u % 2][:, b, :], start=(b == 0), stop=(b == qb))
                mm.then_inc(multiplied, 1)

            with pe.Fori(0, H // 2) as it:
                scores(it, 0)
                for u in range(NU):
                    if u + 1 < NU:
                        scores(it, u + 1)
                    turn_and_multiply(it, u)

        def copy_group(nc_copy, eng, it, k):
            u, g, blocks = groups[k]
            eng.wait_ge(block_turned, NGR * it + (k + 1))
            nc_copy(amapT[u % 2][:, 4 * g:4 * g + blocks, :], turned[:, k % 2, 0:blocks, :]).then_inc(half_kept[k % 2], 1)

        @block.scalar
        def _(act):
            act.sem_inc(expd[0], 1)
            act.sem_inc(expd[1], 1)
            act.sem_inc(half_kept[0], 1)
            act.sem_inc(out_kept, 2)
            nc.scalar.preload_act_table(ACT.Exp)

            def exps(it, u):
                hh, qb = units[u]
                n = (qb + 1) * P
                act.wait_ge(multiplied, NU * it + (u + 1))
                for x in range(2):
                    act.wait_ge(maxed[x], NU * it + (u + 1))
                    nc.scalar.activation(e[u % 2][x][:, 0:n], score[x][:, 0:n], ACT.Exp, bias=nmax[:, u % 2, x:x + 1], scale=1.0,
                                         accum_out=total[:, u % 2, x:x + 1]).then_inc(expd[x], 1)

            def rest(it, u):
                hh, qb = units[u]
                for g in range((qb + 4) // 4):
                    if g_of[(u, g)] % 2 == 0:
                        copy_group(nc.scalar.copy, act, it, g_of[(u, g)])
                act.wait_ge(multiplied, NU * it + (u + 1 + CREDIT))
                nc.scalar.copy(head_out[:, bass.ds(2 * it + (H + hh), 1), qb * P:(qb + 1) * P].rearrange("p o t -> p (o t)"),
                               out[u % 2][:, 0:P]).then_inc(out_kept, 1)

            with act.Fori(0, H // 2) as it:
                exps(it, 0)
                for u in range(NU):
                    if u + 1 < NU:
                        exps(it, u + 1)
                    rest(it, u)
            act.wait_ge(v_in[0], 32)
            act.wait_ge(v_in[1], 32)

        @block.vector
        def _(dve):
            dve.sem_inc(half_kept[1], 1)

            def maxes(it, u):
                hh, qb = units[u]
                n = (qb + 1) * P
                for x in range(2):
                    dve.wait_ge(scored[x], NU * it + (u + 1))
                    nc.vector.tensor_reduce(out=nmax[:, u % 2, x:x + 1], in_=score[x][:, 0:n], axis=AX.X, op=ALU.max, negate=True
                                            ).then_inc(maxed[x], 1)

            def difference(it, u):
                hh, qb = units[u]
                n = (qb + 1) * P
                s = u % 2
                for x in range(2):
                    dve.wait_ge(expd[x], NU * it + (u + 2))
                nc.vector.reciprocal(inv[:, s, :], total[:, s, :]).then_inc(inverted, 1)
                dve.wait_ge(inverted, NU * it + (u + 1))
                nc.vector.tensor_scalar(e[s][0][:, 0:n], e[s][0][:, 0:n], inv[:, s, 0:1], None, ALU.mult).then_inc(scaled, 1)
                nc.vector.tensor_tensor(w2[:, s, 0:1], inv[:, s, 1:2], c["neglam"][:, :], ALU.mult).then_inc(weighted, 1)
                dve.wait_ge(scaled, NU * it + (u + 1))
                dve.wait_ge(weighted, NU * it + (u + 1))
                nc.vector.scalar_tensor_tensor(out=e[s][0][:, 0:n], in0=e[s][1][:, 0:n], scalar=w2[:, s, 0:1],
                                               in1=e[s][0][:, 0:n], op0=ALU.mult, op1=ALU.add).then_inc(mapped, 1)

            with dve.Fori(0, H // 2) as it:
                maxes(it, 0)
                for u in range(NU):
                    difference(it, u)
                    if u + 1 < NU:
                        maxes(it, u + 1)
                    hh, qb = units[u]
                    for g in range((qb + 4) // 4):
                        if g_of[(u, g)] % 2 == 1:
                            copy_group(nc.vector.tensor_copy, dve, it, g_of[(u, g)])
    m.free()


def attention_sample(nc, i, o, c, feat, head_out, sem):
    m = Memory(nc)
    NBT = 2
    SB = NB // NBT
    RW = 2 * NL
    NR = H * RW
    NK = 3
    key_in = [m.sb(f"p_key{s}", [P, NPG, GW]) for s in range(NK)]
    val_in = [m.sb(f"p_val{b}", [P, NPG, GW]) for b in range(NB)]
    v_new = m.sb("p_v_new", [NS, GW])
    keyT = [m.sb(f"p_keyT{s}", [P, H, PAST]) for s in range(2)]
    q_pad = [m.sb(f"p_q{t}", [P, H * (P + RW)]) for t in range(NBT)]
    e = [m.sb(f"p_e{t}", [P, PAST + NS]) for t in range(NBT)]
    fresh = [m.sb(f"p_fresh{t}", [P, NS]) for t in range(NBT)]
    mapT = [m.sb(f"p_mapT{t}", [P, NPG, P // 2]) for t in range(NBT)]
    mapT_new = [m.sb(f"p_mapTn{t}", [NS, P // 2]) for t in range(NBT)]
    stat = [m.sb(f"p_stat{t}", [P, 8]) for t in range(NBT)]
    maskT = m.sb("p_maskT", [NS, NBT, P])
    mask = m.sb("p_mask", [P, NBT, NS])
    sign_row = m.sb("p_sign_row", [1, P])
    sign = m.sb("p_sign", [P, 1])
    key_ps = m.ps("p_key_ps", [P, H, PAST])
    score = [m.ps(f"p_score{t}", [P, 512]) for t in range(NBT)]
    fresh_ps = [m.ps(f"p_fresh_ps{t}", [P, 512]) for t in range(NBT)]

    k_in, vn_in = [sem(f"p_k_in{s}") for s in range(NK)], sem("p_vn_in")
    v_in = [sem(f"p_v_in{b}") for b in range(NB)]
    made, setup_ps, setup_sb, q_put = sem("p_made"), sem("p_setup_ps"), sem("p_setup_sb"), sem("p_q_put")
    key_turned, key_kept = ([sem(f"p_{n}{x}") for x in range(2)] for n in ("key_turned", "key_kept"))
    scored, fresh_scored, masked, max_parts, maxed, expd, summed, inverse, weight, weighted, map_turned, map_kept, multiplied, out_kept = (
        sem("p_" + n) for n in ("scored fresh_scored masked max_parts maxed expd summed inverse weight weighted map_turned "
                                "map_kept multiplied out_kept").split())

    pool_k = i["cache_k"][0].rearrange("n p h d -> n p (h d)")
    pool_v = i["cache_v"][0].rearrange("n p h d -> n p (h d)")
    n_pool = i["cache_k"].shape[1]

    def load(queue, dst, src, b, signal):
        for j in range(NPG):
            page = queue.value_load(c["pages"][0:1, b * NPG + j:b * NPG + j + 1], min_val=0, max_val=n_pool - 1)
            queue.dma_start(dst[:, j, :], src[bass.ds(page, 1)].rearrange("o p w -> (o p) w")).then_inc(signal, 16)

    with nc.Block() as block:
        @block.sync
        def _(sp):
            sp.dma_start(v_new[:, :], o["v_sample"].rearrange("a b l h d -> (a b l) (h d)")).then_inc(vn_in, 16)
            for b in range(NB):
                if b >= NK:
                    sp.wait_ge(key_turned[1], b - NK + 1)
                load(sp, key_in[b % NK], pool_k, b, k_in[b % NK])

        @block.gpsimd
        def _(pool):
            for t in (q_pad[0][:, :], q_pad[1][:, :], maskT[:, :, :]):
                pool.memset(t, 0.0).then_inc(made, 1)
            pool.wait_ge(made, 3)
            for t in range(NBT):
                for x in range(2):
                    lo = x * HALF
                    dst = q_pad[t][lo:lo + HALF, :].rearrange("p (h r) -> p h r", h=H)[:, :, 0:P].rearrange(
                        "p h (s r) -> p h s r", s=SB)[:, :, :, x * NL:(x + 1) * NL]
                    src = feat[lo:lo + HALF, 3 * H:4 * H, SEQ + t * SB * NL:SEQ + (t + 1) * SB * NL]
                    ins = nc.gpsimd.tensor_copy(dst, src.rearrange("p h (s l) -> p h s l", s=SB))
                ins.then_inc(q_put, 1)
            v = maskT[:, :, :].rearrange("p t (s g l) -> p (t s) g l", s=SB, l=NL)
            pool.affine_select(out=v, in_=v, compare_op=ALU.is_ge, fill=NEG, base=0,
                               pattern=[[-NL, NB], [0, NR // NL], [0, NL]], channel_multiplier=1).then_inc(made, 1)
            pool.wait_ge(made, 4)
            pool.affine_select(out=v, in_=v, compare_op=ALU.is_ge, fill=NEG, base=0,
                               pattern=[[NL, NB], [0, NR // NL], [1, NL]], channel_multiplier=-1).then_inc(made, 1)
            rows = sign_row[:, :].rearrange("p (a x l) -> p a x l", x=2, l=NL)
            pool.memset(rows[:, :, 0, :], 1.0).then_inc(made, 1)
            nc.gpsimd.tensor_copy(rows[:, :, 1, :], over(c["neglam"][0:1, 0:1], 2, [1, P // RW, NL])).then_inc(made, 1)
            for b in range(NB):
                load(pool, val_in[b], pool_v, b, v_in[b])

        @block.tensor
        def _(pe):
            pe.wait_ge(made, 7)
            for t in range(NBT):
                nc.tensor.transpose(fresh_ps[1][:, t * NS:(t + 1) * NS], maskT[:, t, :], c["ident"][0:NS, 0:NS])
            nc.tensor.matmul(fresh_ps[0][:, 0:1], sign_row[:, :], c["ones"][0:1, 0:1], start=True, stop=True).then_inc(setup_ps, 1)

            def turn_keys(b):
                s = b % NK
                pe.wait_ge(k_in[s], NPG * 16 * (b // NK + 1))
                for x in range(2):
                    if b:
                        pe.wait_ge(key_kept[x], b)
                    for h in (2 * x, 2 * x + 1):
                        for j in range(NPG):
                            mm = nc.tensor.transpose(key_ps[:, h, j * PAGE:(j + 1) * PAGE], key_in[s][:, j, h * DH:(h + 1) * DH],
                                                     c["ident"][:, :])
                    mm.then_inc(key_turned[x], 1)

            def score_keys(b):
                t, r = b // SB, (b % SB) * NR
                for x in range(2):
                    pe.wait_ge(key_kept[x], b + 1)
                pe.wait_ge(q_put, t + 1)
                for h in range(H):
                    mm = nc.tensor.matmul(score[t][r:r + NR, :], q_pad[t][:, h * P + r:h * P + r + NR], keyT[b % 2][:, h, :],
                                          start=(h == 0), stop=(h == H - 1))
                mm.then_inc(scored, 1)

            def score_fresh(t):
                pe.wait_ge(setup_sb, 2)
                for h in range(H):
                    mm = nc.tensor.matmul(fresh_ps[t][:, 0:NS], q_pad[t][:, h * P:(h + 1) * P], feat[:, 4 * H + h, SEQ:T],
                                          start=(h == 0), stop=(h == H - 1))
                mm.then_inc(fresh_scored, 1)

            def turn_map(t):
                pe.wait_ge(weighted, t + 1)
                for j in range(NPG):
                    nc.tensor.transpose(key_ps[:, t, j * P:(j + 1) * P], e[t][:, j * PAGE:(j + 1) * PAGE], c["ident"][:, :])
                nc.tensor.transpose(score[t][0:NS, 0:P], e[t][:, PAST:PAST + NS], c["ident"][:, :]).then_inc(map_turned, 1)

            def multiply(t):
                pe.wait_ge(map_kept, t + 1)
                for s in range(SB):
                    b = t * SB + s
                    pe.wait_ge(v_in[b], NPG * 16)
                    for h in range(H):
                        at = slice((s * H + h) * NL, (s * H + h + 1) * NL)
                        for j in range(NPG):
                            nc.tensor.matmul(key_ps[:, NBT + t, at], val_in[b][:, j, h * DH:(h + 1) * DH], mapT[t][:, j, at],
                                             start=(j == 0), stop=False)
                        mm = nc.tensor.matmul(key_ps[:, NBT + t, at], v_new[:, h * DH:(h + 1) * DH], mapT_new[t][:, at],
                                              start=False, stop=True)
                mm.then_inc(multiplied, 1)

            turn_keys(0)
            for b in range(NB):
                if b + 1 < NB:
                    turn_keys(b + 1)
                score_keys(b)
                if b % SB == SB - 1:
                    score_fresh(b // SB)
            pe.wait_ge(vn_in, 16)
            for t in range(NBT):
                turn_map(t)
                multiply(t)

        @block.scalar
        def _(act):
            nc.scalar.preload_act_table(ACT.Exp)

            def exps(t):
                act.wait_ge(maxed, t + 1)
                nc.scalar.activation(e[t][:, 0:PAST], score[t][:, :], ACT.Exp, bias=stat[t][:, 2:3], scale=1.0,
                                     accum_out=stat[t][:, 3:4])
                nc.scalar.activation(e[t][:, PAST:PAST + NS], fresh[t][:, :], ACT.Exp, bias=stat[t][:, 2:3], scale=1.0,
                                     accum_out=stat[t][:, 4:5]).then_inc(expd, 1)

            for b in range(NB):
                act.wait_ge(key_turned[0], b + 1)
                if b >= 2:
                    act.wait_ge(scored, b - 1)
                nc.scalar.copy(keyT[b % 2][:, 0:2, :], key_ps[:, 0:2, :]).then_inc(key_kept[0], 1)
                if b == SB:
                    exps(0)
            exps(1)
            for t in range(NBT):
                act.wait_ge(multiplied, t + 1)
                nc.scalar.copy(head_out[:, H:2 * H, SEQ + t * SB * NL:SEQ + (t + 1) * SB * NL].rearrange("p h (s l) -> p h s l", s=SB),
                               key_ps[:, NBT + t, 0:P // 2].rearrange("p (s h l) -> p h s l", s=SB, h=H)).then_inc(out_kept, 1)

        @block.vector
        def _(dve):
            dve.wait_ge(setup_ps, 1)
            nc.vector.tensor_copy(mask[:, :, :].rearrange("p t k -> p (t k)"), fresh_ps[1][:, 0:NBT * NS]).then_inc(setup_sb, 1)
            nc.vector.tensor_copy(sign[:, :], fresh_ps[0][:, 0:1]).then_inc(setup_sb, 1)

            def maxes(t):
                dve.wait_ge(fresh_scored, t + 1)
                nc.vector.tensor_tensor(fresh[t][:, :], fresh_ps[t][:, 0:NS], mask[:, t, :], ALU.add).then_inc(masked, 1)
                nc.vector.tensor_reduce(out=stat[t][:, 0:1], in_=score[t][:, :], axis=AX.X, op=ALU.max)
                dve.wait_ge(masked, t + 1)
                nc.vector.tensor_reduce(out=stat[t][:, 1:2], in_=fresh[t][:, :], axis=AX.X, op=ALU.max).then_inc(max_parts, 1)
                dve.wait_ge(max_parts, t + 1)
                nc.vector.tensor_reduce(out=stat[t][:, 2:3], in_=stat[t][:, 0:2], axis=AX.X, op=ALU.max, negate=True).then_inc(maxed, 1)

            def weigh(t):
                dve.wait_ge(expd, t + 1)
                nc.vector.tensor_tensor(stat[t][:, 5:6], stat[t][:, 3:4], stat[t][:, 4:5], ALU.add).then_inc(summed, 1)
                dve.wait_ge(summed, t + 1)
                nc.vector.reciprocal(stat[t][:, 6:7], stat[t][:, 5:6]).then_inc(inverse, 1)
                dve.wait_ge(inverse, t + 1)
                nc.vector.tensor_tensor(stat[t][:, 7:8], stat[t][:, 6:7], sign[:, :], ALU.mult).then_inc(weight, 1)
                dve.wait_ge(weight, t + 1)
                nc.vector.tensor_scalar(e[t][:, :], e[t][:, :], stat[t][:, 7:8], None, ALU.mult).then_inc(weighted, 1)

            def add_maps(t):
                dve.wait_ge(map_turned, t + 1)
                nc.vector.tensor_reduce(out=mapT[t][:, :, :].rearrange("p j (a l) -> p (j a) l", l=NL),
                                        in_=key_ps[:, t, :].rearrange("p (a x l) -> p a l x", x=2, l=NL), axis=AX.X, op=ALU.add)
                nc.vector.tensor_reduce(out=mapT_new[t][:, :].rearrange("p (a l) -> p a l", l=NL),
                                        in_=score[t][0:NS, 0:P].rearrange("p (a x l) -> p a l x", x=2, l=NL), axis=AX.X, op=ALU.add
                                        ).then_inc(map_kept, 1)

            for b in range(NB):
                dve.wait_ge(key_turned[1], b + 1)
                if b >= 2:
                    dve.wait_ge(scored, b - 1)
                nc.vector.tensor_copy(keyT[b % 2][:, 2:4, :], key_ps[:, 2:4, :]).then_inc(key_kept[1], 1)
                if b == SB:
                    maxes(0)
                if b == SB + 1:
                    weigh(0)
            maxes(1)
            weigh(1)
            for t in range(NBT):
                add_maps(t)
    m.free()


def head_gate(nc, c, hT, zT, head_out, hi, lo, x_scratch, z_scratch, sem):
    m = Memory(nc)
    psum = [m.ps(f"o_scale{s}", [P, NG, 512]) for s in range(2)]
    spread_done, normed, gated, hi_done, lo_done, x_in, z_in = (
        sem(f"o_{x}") for x in ("spread", "normed", "gated", "hi", "lo", "x_in", "z_in"))
    n_pool, n_act, n_pe, n_dve, spread = head_scales(
        nc, m, sem, "o", [(head_out[:, t, :], False, t) for t in range(2 * H)], psum[1], ((2 * H, DH * EPS),))

    with nc.Block() as block:
        @block.sync
        def _(sp):
            sp.dma_start(zT, z_scratch).then_inc(z_in, 16)
            sp.dma_start(hT, x_scratch).then_inc(x_in, 16)
            sp.wait_ge(x_in, 16)

        @block.gpsimd
        def _(pool):
            n_pool(pool)

        @block.scalar
        def _(act):
            n_act(act)
            for t in range(2 * H):
                if t < H:
                    act.wait_ge(gated, t + 1)
                else:
                    act.wait_ge(normed, t + 1)
                nc.scalar.copy(hi[:, t, :], head_out[:, t, :]).then_inc(hi_done, 1)

        @block.tensor
        def _(pe):
            n_pe(pe)
            for t in range(2 * H):
                if t >= 2:
                    pe.wait_ge(normed, t - 1)
                spread(t, psum[t % 2]).then_inc(spread_done, 1)

        @block.vector
        def _(dve):
            def low(t):
                dve.wait_ge(hi_done, t + 1)
                nc.vector.tensor_tensor(lo[:, t, :], head_out[:, t, :], r32(hi[:, t, :]), ALU.subtract).then_inc(lo_done, 1)

            n_dve(dve)
            dve.wait_ge(z_in, 16)
            for t in range(2 * H):
                dve.wait_ge(spread_done, t + 1)
                x = head_out[:, t, :].rearrange("p (g t) -> p g t", g=NG)
                nc.vector.scalar_tensor_tensor(out=x, in0=x, scalar=c["gain"][:, t // H:t // H + 1], in1=psum[t % 2][:, :, 0:TG],
                                               op0=ALU.mult, op1=ALU.mult).then_inc(normed, 1)
                if t < H:
                    dve.wait_ge(normed, t + 1)
                    nc.vector.tensor_tensor(head_out[:, t, :], head_out[:, t, :], zT[:, t, :], ALU.mult).then_inc(gated, 1)
                if t >= 1:
                    low(t - 1)
            low(2 * H - 1)
    m.free()


def output_projection(nc, i, hT, x_hi, x_lo, sumsq, sem):
    m = Memory(nc)
    raw = [m.sb(f"wo_raw{s}", [P, KT, P]) for s in range(2)]
    w_hi = [m.sb(f"wo_hi{s}", [P, KT, P], F32R) for s in range(2)]
    w_lo = [m.sb(f"wo_lo{s}", [P, KT, P], F32R) for s in range(2)]
    psum = [m.ps(f"wo_ps{s}", [P, NG, 512]) for s in range(2)]
    square = [m.sb(f"wo_square{s}", [P, T]) for s in range(2)]
    sum_zero, squared, gathered = sem("wo_sum_zero"), sem("wo_squared"), sem("wo_gathered")
    loaded = [sem(f"wo_loaded{s}") for s in range(2)]
    split_hi, split_lo, projected, added = (sem(f"wo_{x}") for x in ("split_hi", "split_lo", "projected", "added"))
    w = i["w_out"][0].rearrange("(k p) n -> p k n", p=P)

    with nc.Block() as block:
        @block.sync
        def _(sp):
            sp.dma_start(raw[0][:, :, :], w[:, :, 0:P]).then_inc(loaded[0], 16)
            sp.dma_start(raw[1][:, :, :], w[:, :, P:2 * P]).then_inc(loaded[1], 16)
            with sp.Fori(1, KT // 2) as it:
                for s in range(2):
                    sp.wait_ge(split_lo, done(2 * it + s - 2))
                    sp.dma_start(raw[s][:, :, :], w[:, :, bass.ds(it * (2 * P) + s * P, P)]).then_inc(loaded[s], 16)

        @block.scalar
        def _(act):
            act.sem_inc(split_hi, CREDIT)
            act.sem_inc(squared, CREDIT)

            def high(n, s):
                act.wait_ge(loaded[s], 8 * (n - s) + 16)
                act.wait_ge(projected, done(n - 2))
                nc.scalar.copy(w_hi[s][:, :, :], raw[s][:, :, :]).then_inc(split_hi, 1)

            def square_of(n, s):
                act.wait_ge(added, done(n))
                act.wait_ge(gathered, done(n - 2))
                nc.scalar.activation(square[s][:, :], hT[:, bass.ds(n, 1), :].rearrange("p o t -> p (o t)"), ACT.Square
                                     ).then_inc(squared, 1)

            high(0, 0)
            high(1, 1)
            with act.Fori(0, KT // 2 - 1) as it:
                for s in range(2):
                    square_of(2 * it + s, s)
                    high(2 * it + (s + 2), s)
            square_of(KT - 2, 0)
            square_of(KT - 1, 1)

        @block.gpsimd
        def _(pool):
            pool.memset(sumsq, 0.0).then_inc(sum_zero, 1)

        @block.tensor
        def _(pe):
            pe.sem_inc(projected, CREDIT)
            with pe.Fori(0, KT // 2) as it:
                for s in range(2):
                    pe.wait_ge(split_lo, done(2 * it + s))
                    pe.wait_ge(added, done(2 * it + s - 2))
                    project_tile(nc, psum[s], w_hi[s], w_lo[s], x_hi, x_lo).then_inc(projected, 1)

        @block.vector
        def _(dve):
            dve.sem_inc(split_lo, CREDIT)
            dve.sem_inc(added, CREDIT)

            def low(n, s):
                dve.wait_ge(split_hi, done(n))
                nc.vector.tensor_tensor(w_lo[s][:, :, :], raw[s][:, :, :], r32(w_hi[s][:, :, :]), ALU.subtract
                                        ).then_inc(split_lo, 1)

            def add(n, s):
                dve.wait_ge(projected, done(n))
                h = hT[:, bass.ds(n, 1), :].rearrange("p o (g t) -> p (o g) t", g=NG)
                nc.vector.tensor_tensor(h, psum[s][:, :, 0:TG], h, ALU.add).then_inc(added, 1)

            def gather(n, s):
                dve.wait_ge(squared, done(n))
                dve.wait_ge(gathered, done(n - 1))
                nc.vector.tensor_tensor(sumsq, sumsq, square[s][:, :], ALU.add).then_inc(gathered, 1)

            dve.sem_inc(gathered, CREDIT)
            low(0, 0)
            low(1, 1)
            dve.wait_ge(sum_zero, 1)
            with dve.Fori(0, KT // 2 - 1) as it:
                for s in range(2):
                    add(2 * it + s, s)
                    low(2 * it + (s + 2), s)
                    gather(2 * it + s, s)
            for s in range(2):
                add(KT - 2 + s, s)
            for s in range(2):
                gather(KT - 2 + s, s)
    m.free()


def gated_mlp(nc, i, o, c, feat, hT, x_hi, x_lo, sumsq, sem):
    m = Memory(nc)
    w_hi = [m.sb(f"up_hi{s}", [P, KT, P], F32R) for s in range(2)]
    w_lo = [m.sb(f"up_lo{s}", [P, KT, P], F32R) for s in range(2)]
    d_hi, d_lo = m.sb("dn_hi", [P, 2, D], F32R), m.sb("dn_lo", [P, 2, D], F32R)
    spare = feat[:, 0:3 * H, :].rearrange("p a t -> p (a t)")
    pre = [spare[:, s * F_BUF:(s + 1) * F_BUF] for s in range(2)]
    acc = [spare[:, (2 + s) * F_BUF:(3 + s) * F_BUF] for s in range(2)]
    prod = spare[:, 4 * F_BUF:4 * F_BUF + T]
    NRW = NB * F_PAD + CF + 1
    at = 4 * F_BUF + T
    col = spare[:, at:at + 2 * FT * NRW].rearrange("p (j r) -> p j r", r=NRW)
    at += 2 * FT * NRW
    tail = spare[:, at:at + 2 * FT * F_TAIL].rearrange("p (j r) -> p j r", r=F_TAIL)
    at += 2 * FT * F_TAIL
    raw = []
    for s in range(2):
        raw.append(spare[:, at:at + D].rearrange("p (k f) -> p k f", k=KT))
        at += D
    raw_d = spare[:, at:at + 2 * D].rearrange("p (x d) -> p x d", x=2)
    at += 2 * D
    Q = 11
    rows = spare[0:NRW, at:at + Q * P]
    tail_tok = spare[0:F_TAIL, at - 4 * D:at - 4 * D + 2 * FF]
    y = [spare[:, s * (NT + 1) * P:(s + 1) * (NT + 1) * P].rearrange("p (n d) -> p n d", d=P) for s in range(2)]
    g_hi, g_lo = m.sb("f_g_hi", [P, 2, T], F32R), m.sb("f_g_lo", [P, 2, T], F32R)
    psum = [m.ps(f"f_up{s}", [P, NG, 512]) for s in range(2)]
    root = prod
    value = [pre[s][:, F_PAD:F_PAD + T] for s in range(2)]
    down = [m.ps(f"f_down{s}", [P, 512]) for s in range(2)]

    loaded = [sem(f"up_loaded{s}") for s in range(2)]
    d_loaded, rows_in, rows_turned, rows_kept = sem("dn_loaded"), sem("f_rows_in"), sem("f_rows_turned"), sem("f_rows_kept")
    pads, state_put, tail_kept = sem("f_pads"), sem("f_state_put"), sem("f_tail_kept")
    split_hi, split_lo = sem("up_split_hi"), sem("up_split_lo")
    projected, evacuated, tap0, tap1, taps = (sem(f"f_{x}") for x in ("projected", "evacuated", "tap0", "tap1", "taps"))
    activated, gated, gate_hi, gate_lo = (sem(f"f_{x}") for x in ("activated", "gated", "gate_hi", "gate_lo"))
    d_split_hi, d_split_lo, partial, summed = (sem(f"dn_{x}") for x in ("split_hi", "split_lo", "partial", "summed"))
    tail_turned, tail_rows, tail_out = sem("f_tail_turned"), sem("f_tail_rows"), sem("f_tail_out")
    totalled, root_done, inverted, value_done, hi_done, lo_done = (
        sem(f"hn_{x}") for x in ("totalled", "root", "inverted", "value", "hi", "lo"))
    y_turned, y_kept, y_out = sem("y_turned"), sem("y_kept"), [sem(f"y_out{s}") for s in range(2)]

    w = i["w_up"][0].rearrange("(k p) n -> p k n", p=P)
    w_d = i["w_down"][0]
    NU = KT * NG
    NTG = 2 * FT // 4

    with nc.Block() as block:
        @block.sync
        def _(sp):
            sp.dma_start(raw[0], w[:, :, 0:P]).then_inc(loaded[0], 16)
            sp.dma_start(raw[1], w[:, :, FF:FF + P]).then_inc(loaded[1], 16)
            for q in range(4):
                if q:
                    sp.wait_ge(rows_turned, q)
                a, b = q * Q * P, (q + 1) * Q * P
                sp.dma_start(rows[0:NB * F_PAD, :], i["state_ffn_conv"][0].rearrange("b r w -> (b r) w")[:, a:b]).then_inc(rows_in, 16)
                sp.dma_start(rows[NB * F_PAD:NB * F_PAD + CF, :], i["ffn_conv_w"][0, :, a:b]).then_inc(rows_in, 16)
                sp.dma_start(rows[NB * F_PAD + CF:NRW, :], i["ffn_conv_b"][:, a:b]).then_inc(rows_in, 16)
            sp.dma_start(raw_d, w_d[0:2 * P, :].rearrange("(x p) d -> p x d", x=2)).then_inc(d_loaded, 16)

            def load_pair(p):
                for s in range(2):
                    sp.wait_ge(split_lo, done(2 * p + s - 2))
                    sp.dma_start(raw[s], w[:, :, bass.ds(p * P + s * FF, P)]).then_inc(loaded[s], 16)

            load_pair(1)
            with sp.Fori(1, FT // 2) as it:
                sp.wait_ge(d_split_lo, it)
                sp.dma_start(raw_d, w_d[bass.ds(it * (2 * P), 2 * P), :].rearrange("(x p) d -> p x d", x=2)).then_inc(d_loaded, 16)
                load_pair(2 * it)
                load_pair(2 * it + 1)
            sp.wait_ge(tail_rows, NTG)
            sp.dma_start(o["ffn_conv_prompt"].rearrange("a b r w -> (a b r) w"), tail_tok[0:F_PAD, :]).then_inc(tail_out, 16)
            sp.dma_start(o["ffn_conv_sample"].rearrange("a b r w -> (a b r) w"), tail_tok[F_PAD:F_TAIL, :]).then_inc(tail_out, 16)
            for t in range(KT):
                sp.wait_ge(y_kept, t + 1)
                cols = slice(t * P, (t + 1) * P)
                sp.dma_start(o["y_prompt"].rearrange("a (n p) d -> p (a n) d", p=P)[:, :, cols], y[t % 2][:, 0:NT, :]
                             ).then_inc(y_out[t % 2], 16)
                sp.dma_start(o["y_sample"].rearrange("b l d -> (b l) d")[:, cols], y[t % 2][0:NS, NT, :]).then_inc(y_out[t % 2], 16)
            sp.wait_ge(tail_out, 32)
            for s in range(2):
                sp.wait_ge(y_out[s], 32 * KT // 2)

        @block.gpsimd
        def _(pool):
            pool.sem_inc(state_put, CREDIT)
            pool.sem_inc(tail_kept, CREDIT)
            for s in range(2):
                pool.memset(pre[s][:, 0:F_PAD], 0.0).then_inc(pads, 1)
            pool.wait_ge(rows_kept, 4)
            with pool.Fori(0, FT) as it:
                for s in range(2):
                    n, j = 2 * it + s, it + s * FT
                    pool.wait_ge(taps, done(n - 2))
                    nc.gpsimd.tensor_copy(samples(pre[s], F_SAMPLE, F_PAD, 0, F_PAD),
                                          col[:, bass.ds(j, 1), 0:NB * F_PAD].rearrange("p o (b r) -> p (o b) r", r=F_PAD)
                                          ).then_inc(state_put, 1)
                for s in range(2):
                    n, j = 2 * it + s, it + s * FT
                    pool.wait_ge(evacuated, done(n))
                    nc.gpsimd.tensor_copy(tail[:, bass.ds(j, 1), 0:F_PAD], pre[s][:, SEQ:SEQ + F_PAD].unsqueeze(1))
                    nc.gpsimd.tensor_copy(tail[:, bass.ds(j, 1), F_PAD:F_TAIL].rearrange("p o (b r) -> p (o b) r", r=F_PAD),
                                          samples(pre[s], F_SAMPLE, F_PAD, NL, F_PAD)).then_inc(tail_kept, 1)

        @block.scalar
        def _(act):
            act.sem_inc(split_hi, CREDIT)
            act.sem_inc(evacuated, CREDIT)
            act.sem_inc(tap0, CREDIT)
            nc.scalar.preload_act_table(ACT.Sqrt)

            def high(n, turn, s):
                act.wait_ge(loaded[s], 16 * turn + 16)
                act.wait_ge(projected, done(n - 2))
                nc.scalar.copy(w_hi[s][:, :, :], raw[s]).then_inc(split_hi, 1)

            def drain(p, s):
                n = 2 * p + s
                act.wait_ge(projected, done(n))
                act.wait_ge(taps, done(n - 2))
                act.wait_ge(tail_kept, done(n - 2))
                nc.scalar.copy(pre[s][:, F_PAD:F_PAD + 2 * TG].rearrange("p (g t) -> p g t", g=2), psum[s][:, 0:2, 0:TG])
                nc.scalar.copy(pre[s][:, F_PAD + 2 * TG:F_SAMPLE], psum[s][:, 2, 0:TG - NS])
                nc.scalar.copy(samples(pre[s], F_SAMPLE, F_PAD, F_PAD, NL),
                               psum[s][:, 2, TG - NS:TG].rearrange("p (b l) -> p b l", b=NB)).then_inc(evacuated, 1)

            def first_tap(p, s):
                n, j = 2 * p + s, p + s * FT
                act.wait_ge(evacuated, done(n))
                act.wait_ge(state_put, done(n))
                act.wait_ge(gated, p + 1)
                nc.scalar.activation(
                    acc[s][:, 0:F_OUT], pre[s][:, 0:F_OUT], ACT.Identity,
                    scale=col[:, bass.ds(j, 1), NB * F_PAD:NB * F_PAD + 1].rearrange("p o r -> p (o r)"),
                    bias=col[:, bass.ds(j, 1), NRW - 1:NRW].rearrange("p o r -> p (o r)")).then_inc(tap0, 1)

            def pair(p, last=False):
                drain(p, 0)
                if not last:
                    high(2 * p + 2, p + 1, 0)
                first_tap(p, 0)
                act.wait_ge(taps, done(2 * p))
                nc.scalar.activation(acc[0][:, 0:F_OUT], acc[0][:, 0:F_OUT], ACT.Silu).then_inc(activated, 1)
                drain(p, 1)
                if not last:
                    high(2 * p + 3, p + 1, 1)
                first_tap(p, 1)

            def gate_high(p, x):
                act.wait_ge(gated, p + 2)
                nc.scalar.copy(g_hi[:, x, :], prod).then_inc(gate_hi, 1)

            def turn(it, last=False):
                pair(2 * it)
                act.wait_ge(d_loaded, 16 * it + 16)
                act.wait_ge(partial, NU * it + 1)
                nc.scalar.copy(d_hi[:, :, :], raw_d).then_inc(d_split_hi, 1)
                gate_high(2 * it, 0)
                pair(2 * it + 1, last)
                gate_high(2 * it + 1, 1)

            high(0, 0, 0)
            high(1, 0, 1)
            act.wait_ge(totalled, 1)
            nc.scalar.activation(root.rearrange("p (g t) -> p g t", g=NG), psum[1][:, :, 0:TG], ACT.Sqrt, bias=c["eps"][:, :],
                                 scale=1.0).then_inc(root_done, 1)
            for k in range(KT):
                act.wait_ge(value_done, k + 1)
                nc.scalar.copy(x_hi[:, k, :], value[k % 2]).then_inc(hi_done, 1)
            nc.scalar.preload_act_table(ACT.Silu)
            act.wait_ge(pads, 2)
            with act.Fori(0, FT // 2 - 1) as it:
                turn(it)
            turn(FT // 2 - 1, last=True)
            for q in range(NTG):
                act.wait_ge(tail_turned, q + 1)
                nc.scalar.copy(tail_tok[:, q * 4 * P:(q + 1) * 4 * P], psum[q % 2][0:F_TAIL, q // 2 % NG, :]).then_inc(tail_rows, 1)
            for t in range(KT):
                act.wait_ge(y_turned, t + 1)
                if t >= 2:
                    act.wait_ge(y_out[t % 2], 32 * (t // 2))
                turned = psum[t % 2][:, :, :].rearrange("p g (n d) -> p (g n) d", d=P)
                nc.scalar.copy(y[t % 2][:, 0:NT, :], turned[:, 0:NT, :])
                nc.scalar.copy(y[t % 2][0:NS, NT, :], turned[0:NS, NT, :]).then_inc(y_kept, 1)

        @block.vector
        def _(dve):
            for x in (split_lo, taps, tap1):
                dve.sem_inc(x, CREDIT)
            dve.sem_inc(gate_lo, 1)
            dve.sem_inc(gated, 1)
            dve.sem_inc(summed, 2)

            def low(n, s):
                dve.wait_ge(split_hi, done(n))
                nc.vector.tensor_tensor(w_lo[s][:, :, :], raw[s], r32(w_hi[s][:, :, :]), ALU.subtract
                                        ).then_inc(split_lo, 1)

            def tap(p, s, t):
                n, j = 2 * p + s, p + s * FT
                dve.wait_ge(tap0 if t == 1 else tap1, done(n))
                nc.vector.scalar_tensor_tensor(
                    out=acc[s][:, 0:F_OUT], in0=pre[s][:, t:t + F_OUT],
                    scalar=col[:, bass.ds(j, 1), NB * F_PAD + t:NB * F_PAD + t + 1].rearrange("p o r -> p (o r)"),
                    in1=acc[s][:, 0:F_OUT], op0=ALU.mult, op1=ALU.add).then_inc(tap1 if t == 1 else taps, 1)

            def add_partials(it, u0, u1):
                for u in range(u0, u1):
                    dve.wait_ge(partial, NU * it + (u + 2))
                    h = hT[:, u // NG, (u % NG) * TG:(u % NG + 1) * TG]
                    nc.vector.tensor_tensor(h, down[u % 2][:, 0:TG], h, ALU.add).then_inc(summed, 1)

            def gate(p):
                dve.wait_ge(activated, p + 1)
                dve.wait_ge(taps, done(2 * p + 1))
                dve.wait_ge(gate_lo, p + 1)
                nc.vector.tensor_tensor(prod[:, 0:SEQ], acc[0][:, 0:SEQ], acc[1][:, 0:SEQ], ALU.mult)
                nc.vector.tensor_tensor(prod[:, SEQ:T].rearrange("p (b l) -> p b l", b=NB), samples(acc[0], F_SAMPLE, F_PAD, 0, NL),
                                        samples(acc[1], F_SAMPLE, F_PAD, 0, NL), ALU.mult).then_inc(gated, 1)

            def gate_low(p, x):
                dve.wait_ge(gate_hi, p + 1)
                nc.vector.tensor_tensor(g_lo[:, x, :], prod, r32(g_hi[:, x, :]), ALU.subtract).then_inc(gate_lo, 1)

            def turn(it, before=None, last=False):
                add = (lambda u0, u1: add_partials(before, u0, u1)) if before is not None else (lambda u0, u1: None)
                a, b = 2 * it, 2 * it + 1
                tap(a, 0, 1)
                tap(a, 0, 2)
                low(2 * a + 2, 0)
                add(0, 4)
                tap(a, 1, 1)
                add(4, 6)
                tap(a, 1, 2)
                add(6, 8)
                low(2 * a + 3, 1)
                add(8, 10)
                gate(a)
                add(10, NU)
                gate_low(a, 0)
                dve.wait_ge(d_split_hi, it + 1)
                nc.vector.tensor_tensor(d_lo[:, :, :], raw_d, r32(d_hi[:, :, :]), ALU.subtract).then_inc(d_split_lo, 1)
                tap(b, 0, 1)
                tap(b, 0, 2)
                if not last:
                    low(2 * b + 2, 0)
                tap(b, 1, 1)
                tap(b, 1, 2)
                if not last:
                    low(2 * b + 3, 1)
                gate(b)
                gate_low(b, 1)

            def keep_rows(q):
                dve.wait_ge(rows_turned, q + 1)
                nc.vector.tensor_copy(col[:, q * Q:(q + 1) * Q, :].rearrange("p j r -> p (j r)"),
                                      down[q % 2][:, 0:Q * NRW]).then_inc(rows_kept, 1)

            def norm_low(k):
                dve.wait_ge(hi_done, k + 1)
                nc.vector.tensor_tensor(x_lo[:, k, :], value[k % 2], r32(x_hi[:, k, :]), ALU.subtract).then_inc(lo_done, 1)

            low(0, 0)
            low(1, 1)
            dve.wait_ge(root_done, 1)
            nc.vector.reciprocal(root, root).then_inc(inverted, 1)
            dve.wait_ge(inverted, 1)
            for k in range(KT):
                if k >= 2:
                    dve.wait_ge(lo_done, k - 1)
                nc.vector.scalar_tensor_tensor(out=value[k % 2], in0=hT[:, k, :], scalar=c["cols"][:, KT + k:KT + k + 1],
                                               in1=root, op0=ALU.mult, op1=ALU.mult).then_inc(value_done, 1)
                if k >= 1:
                    norm_low(k - 1)
            norm_low(KT - 1)
            for q in range(4):
                keep_rows(q)
            dve.wait_ge(rows_kept, 4)
            turn(0)
            with dve.Fori(1, FT // 2 - 1) as it:
                turn(it, it - 1)
            turn(FT // 2 - 1, FT // 2 - 2, last=True)
            add_partials(FT // 2 - 1, 0, NU)

        @block.tensor
        def _(pe):
            pe.sem_inc(projected, CREDIT)
            pe.sem_inc(partial, 1)
            def turn_rows(q):
                pe.wait_ge(rows_in, 48 * (q + 1))
                if q >= 2:
                    pe.wait_ge(rows_kept, q - 1)
                for j in range(Q):
                    mm = nc.tensor.transpose(down[q % 2][:, j * NRW:(j + 1) * NRW], rows[:, j * P:(j + 1) * P],
                                             c["ident"][0:NRW, 0:NRW])
                mm.then_inc(rows_turned, 1)

            def up_tile(n, s, before=None):
                pe.wait_ge(split_lo, done(n))
                pe.wait_ge(evacuated, done(n - 2))
                project_tile(nc, psum[s], w_hi[s], w_lo[s], x_hi, x_lo, before=before).then_inc(projected, 1)

            def up(p):
                for s in range(2):
                    up_tile(2 * p + s, s)

            def down_product(it, u0=0, u1=NU):
                pe.wait_ge(d_split_lo, it + 1)
                pe.wait_ge(gate_lo, 2 * it + 3)
                for u in range(u0, u1):
                    t, g = u // NG, u % NG
                    pe.wait_ge(summed, NU * it + (u + 1))
                    for k, (a, b) in enumerate(((d_hi, g_hi), (d_hi, g_lo), (d_lo, g_hi))):
                        for x in range(2):
                            mm = nc.tensor.matmul(down[u % 2][:, 0:TG], a[:, x, t * P:(t + 1) * P], b[:, x, g * TG:(g + 1) * TG],
                                                  start=(k + x == 0), stop=(k == 2 and x == 1))
                    mm.then_inc(partial, 1)

            for g in range(NG):
                mm = nc.tensor.matmul(psum[1][:, g, 0:TG], c["ones"][:, :], sumsq[:, g * TG:(g + 1) * TG], start=True, stop=True)
            mm.then_inc(totalled, 1)
            turn_rows(0)
            turn_rows(1)
            up_tile(0, 0, before=lambda k: pe.wait_ge(lo_done, k + 1))
            turn_rows(2)
            turn_rows(3)
            up_tile(1, 1)
            up(1)
            with pe.Fori(1, FT // 2) as it:
                up(2 * it)
                down_product(it - 1)
                up(2 * it + 1)

            def turn_tails(q0, q1):
                for q in range(q0, q1):
                    if q >= 2 * NG:
                        pe.wait_ge(tail_rows, q - 2 * NG + 1)
                    for j in range(4):
                        mm = nc.tensor.transpose(psum[q % 2][0:F_TAIL, q // 2 % NG, j * P:(j + 1) * P], tail[:, 4 * q + j, :],
                                                 c["ident"][:, :])
                    mm.then_inc(tail_turned, 1)

            last = FT // 2 - 1

            def turn_y(t):
                pe.wait_ge(summed, NU * last + NG * (t + 1) + 2)
                if t >= 2:
                    pe.wait_ge(y_kept, t - 1)
                for n in range(NT + 1):
                    rows_n = P if n < NT else NS
                    mm = nc.tensor.transpose(psum[t % 2][0:rows_n, n // 4, (n % 4) * P:(n % 4 + 1) * P],
                                             hT[:, t, n * P:n * P + rows_n], c["ident"][:, :])
                mm.then_inc(y_turned, 1)

            pe.wait_ge(tail_kept, done(2 * FT - 1))
            pe.wait_ge(evacuated, done(2 * FT - 1))
            turn_tails(0, 2 * NG)
            down_product(last, 0, 2 * NG)
            turn_tails(2 * NG, NTG)
            pe.wait_ge(tail_rows, NTG)
            turn_y(0)
            for t in range(2, KT):
                down_product(last, NG * t, NG * (t + 1))
                turn_y(t - 1)
            turn_y(KT - 1)
    m.free()


_INS = ['x_prompt', 'x_sample', 'state_gdn_conv', 'state_gdn_S', 'cache_k', 'cache_v', 'page_table', 'state_ffn_conv',
        'attn_norm_g', 'w_in', 'gdn_conv_w', 'gdn_A_log', 'gdn_dt_bias', 'gdn_out_norm_g', 'diff_q_norm_g', 'diff_k_norm_g',
        'diff_lambda_q1', 'diff_lambda_k1', 'diff_lambda_q2', 'diff_lambda_k2', 'diff_subln_g', 'w_out', 'ffn_norm_g',
        'w_up', 'ffn_conv_w', 'ffn_conv_b', 'w_down']
_OUTS = [('y_prompt', (1, SEQ, D)), ('y_sample', (NB, NL, D)), ('gdn_conv_prompt', (1, 1, G_PAD, 3 * GW)),
         ('gdn_S_prompt', (1, 1, H, DH, DH)), ('k_prompt', (1, 1, SEQ, H, DH)), ('v_prompt', (1, 1, SEQ, H, DH)),
         ('ffn_conv_prompt', (1, 1, F_PAD, 2 * FF)), ('gdn_conv_sample', (1, NB, G_PAD, 3 * GW)),
         ('gdn_S_sample', (1, NB, H, DH, DH)), ('k_sample', (1, NB, NL, H, DH)), ('v_sample', (1, NB, NL, H, DH)),
         ('ffn_conv_sample', (1, NB, F_PAD, 2 * FF))]


def kernel(**inputs):
    import numpy as _np
    import concourse.bacc as _bacc
    from concourse import mybir as _mybir
    from concourse.bass_utils import run_bass_kernel_spmd as _run

    nc = _bacc.Bacc("TRN2", target_bir_lowering=False, num_devices=1)
    arrays, ins, outs = {}, {}, {}
    for name in _INS:
        a = _np.ascontiguousarray(inputs[name])
        arrays[f"in_{name}"] = a
        ins[name] = nc.dram_tensor(f"in_{name}", a.shape, _mybir.dt.from_np(a.dtype), kind="ExternalInput").ap()
    for name, shape in _OUTS:
        outs[name] = nc.dram_tensor(f"out_{name}", shape, F32, kind="ExternalOutput").ap()
    hybrid_step(nc, ins, outs)
    r = _run(nc, [arrays], core_ids=[0])
    return tuple(r.results[0][f"out_{name}"] for name, _ in _OUTS)
```

```python
from contextlib import ExitStack

import concourse.bass as bass
from concourse import mybir

F32 = mybir.dt.float32
F32R = mybir.dt.float32r
BF16 = mybir.dt.bfloat16
I32 = mybir.dt.int32
ALU = mybir.AluOpType
ACT = mybir.ActivationFunctionType
AX = mybir.AxisListType

P = 128
D = 1024
KT = D // P
SEQ = 1024
NB = 8
NL = 4
NS = NB * NL
T = SEQ + NS
NG = 3
TG = T // NG
H = 4
DH = 128
HALF = 64
GW = H * DH
CG = 4
CF = 3
FF = 2816
FT = FF // P
COL_BA = 4 * GW
COL_DIFF = COL_BA + 2 * H
PAGE = 128
NPG = 4
PAST = NPG * PAGE
EPS = 1e-6
NEG = -1e30
LAM_INIT = 0.8 - 0.6
NLEV = 7
NT = SEQ // P
CREDIT = 2

G_PAD, F_PAD = CG - 1, CF - 1
G_SAMPLE, F_SAMPLE = G_PAD + SEQ, F_PAD + SEQ
G_BUF = G_SAMPLE + NB * (G_PAD + NL)
F_BUF = F_SAMPLE + NB * (F_PAD + NL)
G_OUT, F_OUT = G_BUF - G_PAD, F_BUF - F_PAD
G_TAIL = G_PAD * (1 + NB)
F_TAIL = F_PAD * (1 + NB)


def done(n):
    return n + 1 + CREDIT


def levels_done(turn, level, levels=NLEV):
    return levels * turn + (level + 1)


def r32(ap):
    return ap.bitcast(F32)


def over(ap, axis, shape):
    return ap.unsqueeze(axis).to_broadcast(shape)


def samples(buf, start, pad, lo, n):
    return buf[:, start:start + NB * (pad + NL)].rearrange("p (b c) -> p b c", b=NB)[:, :, lo:lo + n]


def project_tile(nc, psum, w_hi, w_lo, x_hi, x_lo, cols=P, before=None):
    for k in range(KT):
        if before is not None:
            before(k)
        for i, (w, x) in enumerate(((w_hi, x_hi), (w_hi, x_lo), (w_lo, x_hi))):
            for g in range(NG):
                mm = nc.tensor.matmul(psum[0:cols, g, 0:TG], w[:, k, 0:cols], x[:, k, g * TG:(g + 1) * TG],
                                      start=(k == 0 and i == 0), stop=(k == KT - 1 and i == 2))
    return mm


class Memory:

    def __init__(self, nc):
        self.nc, self.stack = nc, ExitStack()

    def sb(self, name, shape, dt=F32):
        return self.stack.enter_context(self.nc.sbuf_tensor(name, shape, dt))

    def ps(self, name, shape, dt=F32):
        return self.stack.enter_context(self.nc.psum_tensor(name, shape, dt))

    def free(self):
        self.stack.close()


def hybrid_step(nc, i, o):
    held = []

    def sem(name):
        held.append(nc.alloc_semaphore(name=name))
        return held[-1]

    def phase(step, *args):
        step(nc, *args, sem)
        nc.clear_and_free_semaphores(held)
        nc.all_engine_barrier()
        held.clear()

    x_scratch = nc.dram_tensor("x_scratch", (P, KT, T), F32, kind="Internal").ap()
    z_scratch = nc.dram_tensor("z_scratch", (P, H, T), F32, kind="Internal").ap()

    keep = Memory(nc)
    c = {
        "ident": keep.sb("ident", [P, P]),
        "ones": keep.sb("ones", [P, P]),
        "cols": keep.sb("cols", [P, 2 * KT]),
        "gain": keep.sb("gain", [P, 4]),
        "neglam": keep.sb("neglam", [P, 1]),
        "eps": keep.sb("eps", [P, 1]),
        "pages": keep.sb("pages", [1, NB * NPG], I32),
        "gtail": keep.sb("gtail", [P, 3 * H, G_TAIL]),
        "gcol": keep.sb("gcol", [P, 3 * H, NB * G_PAD + CG]),
    }
    feat = keep.sb("feat", [P, 5 * H, T])
    ba = keep.sb("ba", [P, NT + 1, 2 * H])
    x_split = Memory(nc)
    x_hi = x_split.sb("x_hi", [P, KT, T], F32R)
    x_lo = x_split.sb("x_lo", [P, KT, T], F32R)

    phase(setup_and_input_norm, i, c, feat, x_hi, x_lo, x_scratch)
    phase(input_projection, i, o, c, feat, ba, x_hi, x_lo, z_scratch)
    x_split.free()

    head_out = feat[:, 0:2 * H, :]
    delta_space = Memory(nc)
    delta_consts, fill = delta_constants(nc, delta_space, sem)
    phase(head_norms, i, o, c, feat, ba, fill)
    phase(delta_prompt, i, o, c, feat, ba, head_out, delta_consts)
    delta_space.free()
    phase(delta_sample, i, o, c, feat, ba, head_out)
    phase(attention_prompt, i, o, c, feat, head_out)
    phase(attention_sample, i, o, c, feat, head_out)
    hT = feat[:, 3 * H:5 * H, :]
    x_split = Memory(nc)
    x_hi = x_split.sb("hn_hi", [P, KT, T], F32R)
    x_lo = x_split.sb("hn_lo", [P, KT, T], F32R)
    phase(head_gate, c, hT, feat[:, 2 * H:3 * H, :], head_out, x_hi, x_lo, x_scratch, z_scratch)
    sumsq = feat[:, 3, :]
    phase(output_projection, i, hT, x_hi, x_lo, sumsq)
    phase(gated_mlp, i, o, c, feat, hT, x_hi, x_lo, sumsq)
    x_split.free()
    keep.free()


def ln_rows(ap):
    return ap.rearrange("a (k p) -> (a k) p", p=P)


def norm_emitters(nc, src, hi, lo, g_cols, c, m, sem, name, psum):
    sumsq = m.sb(f"{name}_sumsq", [P, T])
    square = [m.sb(f"{name}_square{s}", [P, T]) for s in range(2)]
    rstd = m.sb(f"{name}_rstd", [P, T])
    value = [m.sb(f"{name}_value{s}", [P, T]) for s in range(2)]
    squared, gathered, summed, root_done = (sem(f"{name}_{x}") for x in ("squared", "gathered", "summed", "root"))
    rstd_done, value_done, hi_done, lo_done = (sem(f"{name}_{x}") for x in ("rstd_done", "value_done", "hi_done", "lo_done"))

    def on_scalar(act):
        nc.scalar.preload_act_table(ACT.Sqrt)
        for k in range(KT):
            if k >= 2:
                act.wait_ge(gathered, k - 1)
            nc.scalar.activation(square[k % 2][:, :], src[:, k, :], ACT.Square).then_inc(squared, 1)
        act.wait_ge(summed, 1)
        nc.scalar.activation(rstd[:, :].rearrange("p (g t) -> p g t", g=NG), psum[:, :, 0:TG], ACT.Sqrt,
                             bias=c["eps"][:, 0:1], scale=1.0).then_inc(root_done, 1)
        for k in range(KT):
            act.wait_ge(value_done, k + 1)
            nc.scalar.activation(hi[:, k, :], value[k % 2][:, :], ACT.Copy).then_inc(hi_done, 1)

    def on_tensor(pe):
        pe.wait_ge(gathered, KT)
        for g in range(NG):
            mm = nc.tensor.matmul(psum[:, g, 0:TG], c["ones"][:, :], sumsq[:, g * TG:(g + 1) * TG], start=True, stop=True)
        mm.then_inc(summed, 1)

    def on_vector(dve):
        for k in range(KT):
            dve.wait_ge(squared, k + 1)
            if k == 0:
                nc.vector.tensor_copy(sumsq[:, :], square[0][:, :]).then_inc(gathered, 1)
            else:
                dve.wait_ge(gathered, k)
                nc.vector.tensor_tensor(sumsq[:, :], sumsq[:, :], square[k % 2][:, :], ALU.add).then_inc(gathered, 1)
        dve.wait_ge(root_done, 1)
        nc.vector.reciprocal(rstd[:, :], rstd[:, :]).then_inc(rstd_done, 1)
        dve.wait_ge(rstd_done, 1)
        for k in range(KT):
            if k >= 2:
                dve.wait_ge(lo_done, k - 1)
            nc.vector.scalar_tensor_tensor(out=value[k % 2][:, :], in0=src[:, k, :], scalar=g_cols[:, k:k + 1],
                                           in1=rstd[:, :], op0=ALU.mult, op1=ALU.mult).then_inc(value_done, 1)
            if k >= 1:
                split_low(k - 1, dve)
        split_low(KT - 1, dve)

    def split_low(k, dve):
        dve.wait_ge(hi_done, k + 1)
        nc.vector.tensor_tensor(lo[:, k, :], value[k % 2][:, :], r32(hi[:, k, :]), ALU.subtract).then_inc(lo_done, 1)

    return on_scalar, on_tensor, on_vector


def setup_and_input_norm(nc, i, c, feat, x_hi, x_lo, x_scratch, sem):
    m = Memory(nc)
    xT = feat[:, 0:KT, :]
    x_in = [m.sb(f"x_in{s}", [P, D]) for s in range(2)]
    rows = m.sb("rows", [20, P])
    state_rows = m.sb("state_rows", [NB * G_PAD + CG, 3 * GW])
    lam = m.sb("lam", [P, 4, HALF])
    lam_sum = m.sb("lam_sum", [P, 4])
    lam_prod = m.sb("lam_prod", [P, 2, HALF])
    turned = [m.ps(f"turned{s}", [P, KT, P]) for s in range(2)]
    total = m.ps("total", [P, NG, 512])

    params_in, x_loaded = sem("params_in"), [sem(f"x_loaded{s}") for s in range(2)]
    x_turned, x_kept = sem("x_turned"), [sem(f"x_kept{s}") for s in range(2)]
    consts_zero, consts = sem("consts_zero"), sem("consts")
    turned_cols, cols_kept, scratch_out = sem("turned_cols"), sem("cols_kept"), sem("x_scratch_out")
    lam_step = sem("lam_step")
    lam_exp = sem("lam_exp")
    n_act, n_pe, n_dve = norm_emitters(nc, xT, x_hi, x_lo, c["cols"][:, 0:KT], c, m, sem, "xn", total)

    with nc.Block() as block:
        @block.sync
        def _(sp):
            sp.dma_start(x_in[0][:, :], i["x_prompt"][0, 0:P, :]).then_inc(x_loaded[0], 16)
            sp.dma_start(x_in[1][:, :], i["x_prompt"][0, P:2 * P, :]).then_inc(x_loaded[1], 16)
            prompt_rows = i["x_prompt"].rearrange("a t d -> (a t) d")
            with sp.Fori(1, NT // 2) as it:
                for s in range(2):
                    sp.wait_ge(x_turned, 2 * it + s - 1)
                    sp.dma_start(x_in[s][:, :], prompt_rows[bass.ds(it * (2 * P) + s * P, P), :]).then_inc(x_loaded[s], 16)
            sp.wait_ge(x_turned, NT - 1)
            sp.dma_start(x_in[0][0:NS, :], i["x_sample"].rearrange("b l d -> (b l) d")).then_inc(x_loaded[0], 16)
            sp.wait_ge(x_kept[0], NT // 2 + 2)
            sp.wait_ge(x_kept[1], NT // 2 + 1)
            sp.dma_start(x_scratch, xT).then_inc(scratch_out, 16)
            sp.wait_ge(scratch_out, 16)

        @block.gpsimd
        def _(pool):
            pool.memset(c["ident"][:, :], 0.0).then_inc(consts_zero, 1)
            pool.memset(c["ones"][:, :], 1.0).then_inc(consts_zero, 1)
            pool.memset(c["eps"][:, :], D * EPS).then_inc(consts_zero, 1)
            pool.wait_ge(consts_zero, 3)
            pool.affine_select(out=c["ident"][:, :], in_=c["ident"][:, :], compare_op=ALU.not_equal, fill=1.0, base=0,
                               pattern=[[-1, P]], channel_multiplier=1).then_inc(consts, 1)

        @block.scalar
        def _(act):
            n = 0
            for dst, src in (
                (rows[0:KT, :], ln_rows(i["attn_norm_g"])),
                (rows[KT:2 * KT, :], ln_rows(i["ffn_norm_g"])),
                (rows[16:17, :], i["gdn_out_norm_g"]),
                (rows[17:18, :], i["diff_subln_g"]),
                (rows[18:19, 0:HALF], i["diff_q_norm_g"]),
                (rows[18:19, HALF:P], i["diff_q_norm_g"]),
                (rows[19:20, 0:HALF], i["diff_k_norm_g"]),
                (rows[19:20, HALF:P], i["diff_k_norm_g"]),
                (state_rows[0:NB * G_PAD, :], i["state_gdn_conv"].rearrange("a b r w -> (a b r) w")),
                (state_rows[NB * G_PAD:NB * G_PAD + CG, :], i["gdn_conv_w"].rearrange("a r w -> (a r) w")),
                (lam[:, 0, :], i["diff_lambda_q1"].to_broadcast([P, HALF])),
                (lam[:, 1, :], i["diff_lambda_k1"].to_broadcast([P, HALF])),
                (lam[:, 2, :], i["diff_lambda_q2"].to_broadcast([P, HALF])),
                (lam[:, 3, :], i["diff_lambda_k2"].to_broadcast([P, HALF])),
                (c["pages"][:, :], i["page_table"].rearrange("(o b) n -> o (b n)", o=1)),
            ):
                nc.scalar.dma_start(dst, src).then_inc(params_in, 16)
                n += 1
            nc.scalar.preload_act_table(ACT.Copy)
            act.sem_inc(x_kept[0], 1)
            with act.Fori(0, NT // 2) as it:
                act.wait_ge(x_turned, 2 * it + 1)
                nc.scalar.copy(xT[:, :, bass.ds(it * (2 * P), P)], turned[0][:, :, :]).then_inc(x_kept[0], 1)
            act.wait_ge(x_turned, NT + 1)
            nc.scalar.copy(xT[:, :, SEQ:T], turned[0][:, :, 0:NS]).then_inc(x_kept[0], 1)
            act.wait_ge(lam_step, 2)
            nc.scalar.activation(lam_sum[:, 2:4], lam_sum[:, 0:2], ACT.Exp).then_inc(lam_exp, 1)
            act.wait_ge(x_kept[0], NT // 2 + 2)
            act.wait_ge(x_kept[1], NT // 2 + 1)
            n_act(act)

        @block.tensor
        def _(pe):
            pe.wait_ge(consts, 1)
            with pe.Fori(0, NT // 2) as it:
                for s in range(2):
                    pe.wait_ge(x_loaded[s], 16 * it + 16)
                    pe.wait_ge(x_kept[s], it + 1)
                    for k in range(KT):
                        mm = nc.tensor.transpose(turned[s][:, k, :], x_in[s][:, k * P:(k + 1) * P], c["ident"][:, :])
                    mm.then_inc(x_turned, 1)
            pe.wait_ge(x_loaded[0], 16 * (NT // 2 + 1))
            pe.wait_ge(x_kept[0], NT // 2 + 1)
            for k in range(KT):
                mm = nc.tensor.transpose(turned[0][:, k, 0:NS], x_in[0][0:NS, k * P:(k + 1) * P], c["ident"][0:NS, 0:NS])
            mm.then_inc(x_turned, 1)
            pe.wait_ge(params_in, 16 * 15)
            pe.wait_ge(x_kept[1], NT // 2 + 1)
            nr = NB * G_PAD + CG
            for j in range(3 * H):
                nc.tensor.transpose(turned[1][:, :, :].rearrange("p a b -> p (a b)")[:, j * nr:(j + 1) * nr],
                                    state_rows[:, j * P:(j + 1) * P], c["ident"][0:nr, 0:nr])
            nc.tensor.transpose(turned[1][:, KT - 1, 0:20], rows[:, :], c["ident"][0:20, 0:20]).then_inc(turned_cols, 1)
            n_pe(pe)

        @block.vector
        def _(dve):
            dve.sem_inc(x_kept[1], 1)
            dve.wait_ge(params_in, 16 * 15)
            for j in range(2):
                nc.vector.tensor_tensor_reduce(out=lam_prod[:, j, :], in0=lam[:, 2 * j, :], in1=lam[:, 2 * j + 1, :], scale=1.0,
                                               scalar=0.0, op0=ALU.mult, op1=ALU.add,
                                               accum_out=lam_sum[:, j:j + 1]).then_inc(lam_step, 1)
            with dve.Fori(0, NT // 2) as it:
                dve.wait_ge(x_turned, 2 * it + 2)
                nc.vector.tensor_copy(xT[:, :, bass.ds(it * (2 * P) + P, P)], turned[1][:, :, :]).then_inc(x_kept[1], 1)
            dve.wait_ge(turned_cols, 1)
            nr = NB * G_PAD + CG
            nc.vector.tensor_copy(c["gcol"][:, :, :].rearrange("p a b -> p (a b)"),
                                  turned[1][:, :, :].rearrange("p a b -> p (a b)")[:, 0:3 * H * nr]).then_inc(cols_kept, 1)
            nc.vector.tensor_scalar(c["cols"][:, :], turned[1][:, KT - 1, 0:2 * KT], D ** 0.5, None,
                                    ALU.mult).then_inc(cols_kept, 1)
            for j, scale in enumerate((DH ** 0.5, (1.0 - LAM_INIT) * DH ** 0.5, 1.0, HALF ** 0.5)):
                nc.vector.tensor_scalar(c["gain"][:, j:j + 1], turned[1][:, KT - 1, 2 * KT + j:2 * KT + j + 1], scale, None,
                                        ALU.mult).then_inc(cols_kept, 1)
            dve.wait_ge(lam_exp, 1)
            nc.vector.tensor_tensor(c["neglam"][:, :], lam_sum[:, 3:4], lam_sum[:, 2:3], ALU.subtract).then_inc(lam_step, 1)
            dve.wait_ge(lam_step, 3)
            nc.vector.tensor_scalar(c["neglam"][:, :], c["neglam"][:, :], LAM_INIT, None, ALU.subtract)
            dve.wait_ge(cols_kept, 6)
            n_dve(dve)
    m.free()


def input_projection(nc, i, o, c, feat, ba, x_hi, x_lo, z_scratch, sem):
    m = Memory(nc)
    raw = [m.sb(f"win_raw{s}", [P, KT, P]) for s in range(2)]
    w_hi = [m.sb(f"win_hi{s}", [P, KT, P], F32R) for s in range(2)]
    w_lo = [m.sb(f"win_lo{s}", [P, KT, P], F32R) for s in range(2)]
    buf = m.sb("conv_buf", [P, 4, G_BUF])
    pre = [buf[:, s, :] for s in range(2)]
    acc = [buf[:, 2 + s, :] for s in range(2)]
    psum = [m.ps(f"proj{s}", [P, NG, 512]) for s in range(2)]
    small = m.ps("proj_small", [P, 2, 512])

    NGDN, NZ, ND, NV = 3 * H, H, 2 * H, H
    Z0, D0, V0 = NGDN, NGDN + NZ, NGDN + NZ + ND
    NTILE = V0 + NV

    loaded = [sem(f"win_loaded{s}") for s in range(2)]
    split_hi, split_lo = sem("win_split_hi"), sem("win_split_lo")
    projected, evacuated = sem("win_projected"), sem("win_evacuated")
    state_put, tail_kept = sem("g_state_put"), sem("g_tail_kept")
    tap0, taps, activated = sem("g_tap0"), sem("g_taps"), sem("g_activated")
    pads = sem("g_pads")
    z_out = [sem(f"z_out{s}") for s in range(2)]
    ba_loaded, ba_split, ba_projected, ba_kept, ba_turned = (sem(f"ba_{x}") for x in ("loaded", "split", "projected", "kept", "turned"))
    tail_turned, tail_rows, tail_out = sem("g_tail_turned"), sem("g_tail_rows"), sem("g_tail_out")
    v_turned, v_kept, v_out = sem("v_turned"), sem("v_kept"), [sem(f"v_out{s}") for s in range(2)]

    w = i["w_in"][0].rearrange("(k p) n -> p k n", p=P)
    ba_raw = m.sb("ba_raw", [P, KT, 2 * H])
    ba_hi = m.sb("ba_hi", [P, KT, 2 * H], F32R)
    ba_lo = m.sb("ba_lo", [P, KT, 2 * H], F32R)
    tail_tok = raw[0][0:G_TAIL, :, :].rearrange("p a b -> p (a b)")
    tail_tok2 = raw[1][0:G_TAIL, :, :].rearrange("p a b -> p (a b)")
    v_tok = [raw[s][:, 4:8, :].rearrange("p a b -> p (a b)") for s in range(2)]
    tail_tok3 = m.sb("tail_tok3", [G_TAIL, 512])
    ba_T = m.sb("ba_T", [2 * H, T])
    v_ps = [small[:, 1, :], psum[0][:, 0, :]]

    def pairs(eng, first, last, body):
        with eng.Fori(first // 2, last // 2) as it:
            for s in range(2):
                body(2 * it + s, s)

    with nc.Block() as block:
        @block.sync
        def _(sp):
            def load(n, s, col):
                if not isinstance(n, int) or n >= 2:
                    sp.wait_ge(split_lo, done(n - 2))
                sp.dma_start(raw[s][:, :, :], w[:, :, bass.ds(col, P)]).then_inc(loaded[s], 16)

            load(0, 0, 0)
            load(1, 1, P)
            sp.dma_start(ba_raw[:, :, :], w[:, :, COL_BA:COL_DIFF]).then_inc(ba_loaded, 16)
            with sp.Fori(1, Z0 // 2) as it:
                for s in range(2):
                    load(2 * it + s, s, it * (2 * P) + s * P)
            with sp.Fori(Z0 // 2, D0 // 2) as it:
                for s in range(2):
                    load(2 * it + s, s, it * (2 * P) + s * P)
            with sp.Fori(D0 // 2, NTILE // 2) as it:
                for s in range(2):
                    load(2 * it + s, s, it * (2 * P) + (s * P + 2 * H))
            for a, src in ((0, tail_tok[:, 0:512]), (1, tail_tok2[:, 0:512])):
                sp.wait_ge(tail_rows, a + 1)
                sp.dma_start(o["gdn_conv_prompt"][0, 0, :, a * 512:(a + 1) * 512], src[0:G_PAD, :]).then_inc(tail_out, 16)
                sp.dma_start(o["gdn_conv_sample"][0].rearrange("b r w -> (b r) w")[:, a * 512:(a + 1) * 512],
                             src[G_PAD:G_TAIL, :]).then_inc(tail_out, 16)
            sp.wait_ge(tail_rows, 3)
            sp.dma_start(o["gdn_conv_prompt"][0, 0, :, 1024:1536], tail_tok3[0:G_PAD, :]).then_inc(tail_out, 16)
            sp.dma_start(o["gdn_conv_sample"][0].rearrange("b r w -> (b r) w")[:, 1024:1536],
                         tail_tok3[G_PAD:G_TAIL, :]).then_inc(tail_out, 16)
            for t in range(NT + 1):
                sp.wait_ge(v_kept, t + 1)
                if t < NT:
                    sp.dma_start(o["v_prompt"].rearrange("a b t h d -> (a b t) (h d)")[t * P:(t + 1) * P, :],
                                 v_tok[t % 2]).then_inc(v_out[t % 2], 16)
                else:
                    sp.dma_start(o["v_sample"].rearrange("a b l h d -> (a b l) (h d)"), v_tok[t % 2][0:NS, :]).then_inc(v_out[t % 2], 16)
            sp.wait_ge(tail_out, 16 * 6)
            sp.wait_ge(v_out[0], 16 * (NT // 2 + 1))
            sp.wait_ge(v_out[1], 16 * (NT // 2))

        @block.gpsimd
        def _(pool):
            pool.sem_inc(state_put, CREDIT)
            pool.sem_inc(tail_kept, CREDIT)
            for s in range(2):
                pool.memset(pre[s][:, 0:G_PAD], 0.0).then_inc(pads, 1)

            def body(n, s):
                pool.wait_ge(taps, done(n - 2))
                nc.gpsimd.tensor_copy(samples(pre[s], G_SAMPLE, G_PAD, 0, G_PAD),
                                      c["gcol"][:, bass.ds(n, 1), 0:NB * G_PAD].rearrange("p o (b r) -> p (o b) r", r=G_PAD)
                                      ).then_inc(state_put, 1)
                pool.wait_ge(evacuated, done(n))
                nc.gpsimd.tensor_copy(c["gtail"][:, bass.ds(n, 1), 0:G_PAD], pre[s][:, SEQ:SEQ + G_PAD].unsqueeze(1))
                nc.gpsimd.tensor_copy(c["gtail"][:, bass.ds(n, 1), G_PAD:G_TAIL].rearrange("p o (b r) -> p (o b) r", r=G_PAD),
                                      samples(pre[s], G_SAMPLE, G_PAD, NL, G_PAD)).then_inc(tail_kept, 1)

            pairs(pool, 0, Z0, body)

        @block.scalar
        def _(act):
            act.sem_inc(split_hi, CREDIT)
            act.sem_inc(evacuated, CREDIT)
            act.sem_inc(tap0, CREDIT)
            act.sem_inc(activated, CREDIT)
            nc.scalar.preload_act_table(ACT.Silu)

            def high(n, s):
                act.wait_ge(loaded[s], high_loaded(n, s))
                act.wait_ge(projected, done(n - 2))
                nc.scalar.activation(w_hi[s][:, :, :], raw[s][:, :, :], ACT.Copy).then_inc(split_hi, 1)

            def high_loaded(n, s):
                return 8 * (n - s) + 16

            def drain_gdn(n, s):
                act.wait_ge(projected, done(n))
                act.wait_ge(taps, done(n - 2))
                act.wait_ge(tail_kept, done(n - 2))
                nc.scalar.copy(pre[s][:, G_PAD:G_PAD + 2 * TG].rearrange("p (g t) -> p g t", g=2), psum[s][:, 0:2, 0:TG])
                nc.scalar.copy(pre[s][:, G_PAD + 2 * TG:G_SAMPLE], psum[s][:, 2, 0:TG - NS])
                nc.scalar.copy(samples(pre[s], G_SAMPLE, G_PAD, G_PAD, NL),
                               psum[s][:, 2, TG - NS:TG].rearrange("p (b l) -> p b l", b=NB)).then_inc(evacuated, 1)
                act.wait_ge(evacuated, done(n))
                act.wait_ge(state_put, done(n))
                nc.scalar.activation(acc[s][:, 0:G_OUT], pre[s][:, 0:G_OUT], ACT.Copy,
                                     scale=c["gcol"][:, bass.ds(n, 1), NB * G_PAD:NB * G_PAD + 1].rearrange("p o r -> p (o r)")
                                     ).then_inc(tap0, 1)
                act.wait_ge(taps, done(n))
                nc.scalar.activation(feat[:, bass.ds(n, 1), 0:SEQ].rearrange("p o t -> p (o t)"), acc[s][:, 0:SEQ], ACT.Silu)
                nc.scalar.activation(feat[:, bass.ds(n, 1), SEQ:T].rearrange("p o (b l) -> p (o b) l", b=NB),
                                     samples(acc[s], G_SAMPLE, G_PAD, 0, NL), ACT.Silu).then_inc(activated, 1)

            def drain_z(n, s):
                act.wait_ge(projected, done(n))
                if n - Z0 >= 2:
                    act.wait_ge(z_out[s], 16)
                nc.scalar.activation(acc[s][:, 0:T].rearrange("p (g t) -> p g t", g=NG), psum[s][:, :, 0:TG],
                                     ACT.Silu).then_inc(evacuated, 1)
                act.wait_ge(evacuated, done(n))
                nc.scalar.dma_start(z_scratch[:, n - Z0, :], acc[s][:, 0:T]).then_inc(z_out[s], 16)

            def drain_diff(n, s):
                act.wait_ge(projected, done(n))
                nc.scalar.copy(feat[:, bass.ds(n - NZ, 1), :].rearrange("p o (g t) -> p (o g) t", g=NG),
                               psum[s][:, :, 0:TG]).then_inc(evacuated, 1)

            def drain_v(n, s):
                act.wait_ge(projected, done(n))
                if n == V0:
                    act.wait_ge(taps, done(Z0 - 1))
                    act.wait_ge(tail_kept, done(Z0 - 1))
                if n == V0 + 2:
                    act.wait_ge(z_out[0], 32)
                    act.wait_ge(z_out[1], 32)
                nc.scalar.copy(buf[:, n - V0, 0:T].rearrange("p (g t) -> p g t", g=NG), psum[s][:, :, 0:TG]).then_inc(evacuated, 1)

            high(0, 0)
            act.wait_ge(ba_loaded, 16)
            nc.scalar.activation(ba_hi[:, :, :], ba_raw[:, :, :], ACT.Copy).then_inc(ba_split, 1)

            def gdn_tile(n, s):
                high(n + 1, 1 - s)
                drain_gdn(n, s)

            def diff_tile(n, s):
                high(n + 1, 1 - s)
                drain_diff(n, s)

            pairs(act, 0, Z0, gdn_tile)
            for n in range(Z0, D0):
                high(n + 1, 1 - n % 2)
                drain_z(n, n % 2)
            pairs(act, D0, V0, diff_tile)
            for n in range(V0, NTILE):
                if n + 1 < NTILE:
                    high(n + 1, 1 - n % 2)
                drain_v(n, n % 2)
            act.wait_ge(ba_projected, 1)
            nc.scalar.copy(ba_T[:, :].rearrange("p (g t) -> p g t", g=NG), psum[0][0:2 * H, :, 0:TG]).then_inc(ba_kept, 1)

        @block.vector
        def _(dve):
            dve.sem_inc(split_lo, CREDIT)
            dve.sem_inc(taps, CREDIT)
            step = sem("g_tap_step")
            dve.sem_inc(step, 2 * CREDIT)

            def low(n, s):
                dve.wait_ge(split_hi, done(n))
                nc.vector.tensor_tensor(w_lo[s][:, :, :], raw[s][:, :, :], r32(w_hi[s][:, :, :]),
                                        ALU.subtract).then_inc(split_lo, 1)

            def gdn_tile(n, s):
                low(n + 1, 1 - s)
                dve.wait_ge(tap0, done(n))
                for j in range(1, CG):
                    if j >= 2:
                        dve.wait_ge(step, 2 * n + (2 * CREDIT + j - 1))
                    ins = nc.vector.scalar_tensor_tensor(
                        out=acc[s][:, 0:G_OUT], in0=pre[s][:, j:j + G_OUT],
                        scalar=c["gcol"][:, bass.ds(n, 1), NB * G_PAD + j:NB * G_PAD + j + 1].rearrange("p o r -> p (o r)"),
                        in1=acc[s][:, 0:G_OUT], op0=ALU.mult, op1=ALU.add)
                    ins.then_inc(step if j < CG - 1 else taps, 1)

            low(0, 0)
            dve.wait_ge(ba_split, 1)
            nc.vector.tensor_tensor(ba_lo[:, :, :], ba_raw[:, :, :], r32(ba_hi[:, :, :]), ALU.subtract).then_inc(ba_split, 1)
            pairs(dve, 0, Z0, gdn_tile)
            pairs(dve, Z0, V0, lambda n, s: low(n + 1, 1 - s))
            for n in range(V0, NTILE - 1):
                low(n + 1, 1 - n % 2)
            dve.wait_ge(ba_turned, 1)
            nc.vector.tensor_copy(ba[:, 0:NT, :], small[:, 0, 0:NT * 2 * H].rearrange("p (t c) -> p t c", c=2 * H))
            nc.vector.tensor_copy(ba[0:NS, NT, :], small[0:NS, 0, NT * 2 * H:(NT + 1) * 2 * H]).then_inc(ba_turned, 1)
            for a, dst in enumerate((tail_tok[:, 0:512], tail_tok2[:, 0:512], tail_tok3[:, :])):
                dve.wait_ge(tail_turned, a + 1)
                nc.vector.tensor_copy(dst, psum[1][0:G_TAIL, a, :]).then_inc(tail_rows, 1)
            for t in range(NT + 1):
                dve.wait_ge(v_turned, t + 1)
                if t >= 2:
                    dve.wait_ge(v_out[t % 2], 16 * (t // 2))
                n = P if t < NT else NS
                nc.vector.tensor_copy(v_tok[t % 2][0:n, :], v_ps[t % 2][0:n, :]).then_inc(v_kept, 1)

        @block.tensor
        def _(pe):
            pe.sem_inc(projected, CREDIT)

            def tile(n, s):
                pe.wait_ge(split_lo, done(n))
                pe.wait_ge(evacuated, done(n - 2))
                project_tile(nc, psum[s], w_hi[s], w_lo[s], x_hi, x_lo).then_inc(projected, 1)

            pairs(pe, 0, NTILE, tile)
            pe.wait_ge(ba_split, 2)
            pe.wait_ge(evacuated, done(NTILE - 2))
            project_tile(nc, psum[0], ba_hi, ba_lo, x_hi, x_lo, 2 * H).then_inc(ba_projected, 1)
            pe.wait_ge(ba_kept, 1)
            for t in range(NT + 1):
                n = P if t < NT else NS
                mm = nc.tensor.transpose(small[0:n, 0, t * 2 * H:(t + 1) * 2 * H], ba_T[:, t * P:t * P + n],
                                         c["ident"][0:2 * H, 0:2 * H])
            mm.then_inc(ba_turned, 1)
            pe.wait_ge(tail_kept, done(Z0 - 1))
            pe.wait_ge(evacuated, done(NTILE - 1))
            for j in range(3 * H):
                mm = nc.tensor.transpose(psum[1][0:G_TAIL, j // 4, (j % 4) * P:(j % 4 + 1) * P], c["gtail"][:, j, :],
                                         c["ident"][:, :])
                if j % 4 == 3:
                    mm.then_inc(tail_turned, 1)
            for t in range(NT + 1):
                n = P if t < NT else NS
                if t >= 2:
                    pe.wait_ge(v_kept, t - 1)
                for h in range(H):
                    mm = nc.tensor.transpose(v_ps[t % 2][0:n, h * P:(h + 1) * P], buf[:, h, t * P:t * P + n], c["ident"][:, :])
                mm.then_inc(v_turned, 1)
    m.free()


def head_scales(nc, m, sem, name, tiles, total, eps_of):
    n = len(tiles)
    R = tiles[-1][2] + (2 if tiles[-1][1] else 1)
    square = [m.sb(f"{name}_square{x}", [P, T]) for x in range(2)]
    strip = m.sb(f"{name}_strip", [P, 2, 2 * R])
    spread_by = m.sb(f"{name}_spread_by", [R, n, P])
    spread_r = m.sb(f"{name}_spread_r", [R, n, P], F32R)
    eps = m.sb(f"{name}_eps", [R, 1])
    rows = m.sb(f"{name}_rows", [R, T])
    hi, lo = m.sb(f"{name}_rows_hi", [R, T], F32R), m.sb(f"{name}_rows_lo", [R, T], F32R)
    zeroed, made, spread_made = sem(f"{name}_zeroed"), sem(f"{name}_made"), sem(f"{name}_spread_made")
    squared, summed, root_done, inverted, hi_done, lo_done = (
        sem(f"{name}_{x}") for x in ("squared", "summed", "root", "inverted", "rows_hi", "rows_lo"))
    halved = [t for t in range(n) if tiles[t][1]]
    whole = n - len(halved)

    def group(g):
        return slice(g * TG, (g + 1) * TG)

    def on_pool(pool):
        pool.memset(strip[:, :, :], 0.0).then_inc(zeroed, 1)
        pool.memset(spread_by[:, :, :], 1.0).then_inc(zeroed, 1)
        k = 2
        for first, value in eps_of:
            pool.memset(eps[0:first, :], value).then_inc(zeroed, 1)
            k += 1
            pool.wait_ge(zeroed, k)
        for j, ones in enumerate((strip[:, 0, R - 1:R], strip[0:HALF, 1, R - 1:R], strip[HALF:P, 1, R:R + 1])):
            if j:
                pool.wait_ge(made, j)
            pool.memset(ones, 1.0).then_inc(made, 1)
        pool.wait_ge(made, 3)
        views = []
        if whole:
            views.append((spread_by[:, 0:whole, :], 0, [[-1, whole], [0, P]]))
        if halved:
            views.append((spread_by[:, whole:n, :].rearrange("r t (x f) -> r (t x) f", x=2), -tiles[whole][2],
                          [[-1, 2 * (n - whole)], [0, HALF]]))
        for v, base, pattern in views:
            pool.affine_select(out=v, in_=v, compare_op=ALU.is_equal, fill=0.0, base=base, pattern=pattern,
                               channel_multiplier=1).then_inc(spread_made, 1)

    def on_scalar(act):
        nc.scalar.preload_act_table(ACT.Sqrt)
        for t in range(0, n):
            if t >= 2:
                act.wait_ge(summed, t - 1)
            nc.scalar.activation(square[t % 2][:, :], tiles[t][0], ACT.Square).then_inc(squared, 1)
        act.wait_ge(summed, n)
        act.wait_ge(zeroed, 2 + len(eps_of))
        for g in range(NG):
            nc.scalar.activation(rows[:, group(g)], total[0:R, g, 0:TG], ACT.Sqrt, bias=eps[:, :], scale=1.0).then_inc(root_done, 1)
        for g in range(NG):
            act.wait_ge(inverted, g + 1)
            nc.scalar.copy(hi[:, group(g)], rows[:, group(g)]).then_inc(hi_done, 1)

    def on_tensor(pe):
        pe.wait_ge(made, 3)
        for t, (_, two, row) in enumerate(tiles):
            pe.wait_ge(squared, t + 1)
            for g in range(NG):
                mm = nc.tensor.matmul(total[0:R, g, 0:TG], strip[:, 1 if two else 0, R - 1 - row:2 * R - 1 - row],
                                      square[t % 2][:, g * TG:(g + 1) * TG], start=(t == 0), stop=(t == n - 1))
            mm.then_inc(summed, 1)

    def on_vector(dve):
        dve.wait_ge(spread_made, (1 if whole else 0) + (1 if halved else 0))
        nc.vector.tensor_copy(spread_r[:, :, :], spread_by[:, :, :]).then_inc(lo_done, 1)
        for g in range(NG + 1):
            if g < NG:
                dve.wait_ge(root_done, g + 1)
                nc.vector.reciprocal(rows[:, group(g)], rows[:, group(g)]).then_inc(inverted, 1)
            if g >= 1:
                dve.wait_ge(hi_done, g)
                nc.vector.tensor_tensor(lo[:, group(g - 1)], rows[:, group(g - 1)], r32(hi[:, group(g - 1)]), ALU.subtract
                                        ).then_inc(lo_done, 1)

    def spread(pe, t, psum):
        for g in range(NG):
            if t == 0:
                pe.wait_ge(lo_done, g + 2)
            for k, part in enumerate((hi, lo)):
                mm = nc.tensor.matmul(psum[:, g, 0:TG], spread_r[:, t, :], part[:, g * TG:(g + 1) * TG], start=(k == 0), stop=(k == 1))
        return mm

    return on_pool, on_scalar, on_tensor, on_vector, spread


def head_norms(nc, i, o, c, feat, ba, on_pool, sem):
    m = Memory(nc)
    k_tok = [m.sb(f"k_tok{s}", [P, GW]) for s in range(2)]
    a_pos = m.sb("a_pos", [P, NT + 1, H])
    a_neg = m.sb("a_neg", [P, NT + 1, H])
    dt_bias = m.sb("dt_bias", [P, H])
    a_log = m.sb("a_log", [P, H])
    psum = [m.ps(f"h_scale{s}", [P, NG, 512]) for s in range(2)]
    k_ps = m.ps("k_ps", [P, 2, 512])

    spread_done, normed = sem("h_spread"), sem("h_normed")
    k_turned, k_kept, k_out = sem("k_turned"), sem("k_kept"), [sem(f"k_out{s}") for s in range(2)]
    rate_in, gate_act, gate_dve = sem("rate_in"), sem("gate_act"), sem("gate_dve")

    order = [(j, j, DH ** -0.5) for j in range(H)] + [(j, j, 1.0) for j in range(H, 2 * H)]
    order += [(3 * H + j, 2 * H + 2 * j, c["gain"][:, 2 + j // H:3 + j // H]) for j in range(2 * H)]
    n_pool, n_act, n_pe, n_dve, spread = head_scales(
        nc, m, sem, "h", [(feat[:, j, :], j >= 3 * H, row) for j, row, _ in order], psum[1],
        ((6 * H, HALF * EPS), (2 * H, EPS)))

    with nc.Block() as block:
        @block.sync
        def _(sp):
            sp.dma_start(dt_bias[:, :], i["gdn_dt_bias"].to_broadcast([P, H])).then_inc(rate_in, 16)
            sp.dma_start(a_log[:, :], i["gdn_A_log"].to_broadcast([P, H])).then_inc(rate_in, 16)
            for t in range(NT + 1):
                sp.wait_ge(k_kept, t + 1)
                if t < NT:
                    sp.dma_start(o["k_prompt"].rearrange("a b t h d -> (a b t) (h d)")[t * P:(t + 1) * P, :],
                                 k_tok[t % 2][:, :]).then_inc(k_out[t % 2], 16)
                else:
                    sp.dma_start(o["k_sample"].rearrange("a b l h d -> (a b l) (h d)"), k_tok[t % 2][0:NS, :]).then_inc(k_out[t % 2], 16)
            sp.wait_ge(k_out[0], 16 * (NT // 2 + 1))
            sp.wait_ge(k_out[1], 16 * (NT // 2))

        @block.gpsimd
        def _(pool):
            n_pool(pool)
            on_pool(pool)

        @block.scalar
        def _(act):
            n_act(act)
            nc.scalar.activation(ba[:, 0:NT, 0:H], ba[:, 0:NT, 0:H], ACT.Sigmoid).then_inc(gate_act, 1)
            nc.scalar.activation(ba[0:NS, NT, 0:H], ba[0:NS, NT, 0:H], ACT.Sigmoid).then_inc(gate_act, 1)
            act.wait_ge(rate_in, 32)
            nc.scalar.activation(a_log[:, :], a_log[:, :], ACT.Exp).then_inc(gate_act, 1)
            act.wait_ge(gate_dve, 4)
            nc.scalar.activation(a_neg[:, :, :], a_neg[:, :, :], ACT.Exp).then_inc(gate_act, 1)
            act.wait_ge(gate_act, 4)
            nc.scalar.activation(a_neg[:, :, :], a_neg[:, :, :], ACT.Ln, bias=c["ones"][:, 0:1], scale=1.0).then_inc(gate_act, 1)

        @block.tensor
        def _(pe):
            n_pe(pe)
            for t in range(4 * H):
                if t >= 2:
                    pe.wait_ge(normed, t - 1)
                spread(pe, t, psum[t % 2]).then_inc(spread_done, 1)
            pe.wait_ge(normed, 4 * H)
            for t in range(NT + 1):
                n = P if t < NT else NS
                if t >= 2:
                    pe.wait_ge(k_kept, t - 1)
                for h in range(H):
                    mm = nc.tensor.transpose(k_ps[0:n, t % 2, h * P:(h + 1) * P], feat[:, 4 * H + h, t * P:t * P + n],
                                             c["ident"][:, :])
                mm.then_inc(k_turned, 1)

        @block.vector
        def _(dve):
            dve.wait_ge(rate_in, 32)
            a = ba[:, :, H:2 * H]
            nc.vector.memset(a_pos[:, NT, :], 0.0).then_inc(gate_dve, 1)
            bias = over(dt_bias[:, :], 1, [P, NT, H])
            nc.vector.tensor_tensor(a_pos[:, 0:NT, :], ba[:, 0:NT, H:2 * H], bias, ALU.add).then_inc(gate_dve, 1)
            dve.wait_ge(gate_dve, 2)
            nc.vector.tensor_tensor(a_pos[0:NS, NT, :], ba[0:NS, NT, H:2 * H], dt_bias[0:NS, :], ALU.add).then_inc(gate_dve, 1)
            dve.wait_ge(gate_dve, 3)
            nc.vector.scalar_tensor_tensor(out=a_neg[:, :, :], in0=a_pos[:, :, :], scalar=-1.0, in1=a_pos[:, :, :],
                                           op0=ALU.mult, op1=ALU.min).then_inc(gate_dve, 1)

            n_dve(dve)
            for t, (j, _, gain) in enumerate(order):
                dve.wait_ge(spread_done, t + 1)
                x = feat[:, j, :].rearrange("p (g t) -> p g t", g=NG)
                nc.vector.scalar_tensor_tensor(out=x, in0=x, scalar=gain, in1=psum[t % 2][:, :, 0:TG], op0=ALU.mult,
                                               op1=ALU.mult).then_inc(normed, 1)
            for t in range(NT + 1):
                n = P if t < NT else NS
                dve.wait_ge(k_turned, t + 1)
                if t >= 2:
                    dve.wait_ge(k_out[t % 2], 16 * (t // 2))
                nc.vector.tensor_copy(k_tok[t % 2][0:n, :], k_ps[0:n, t % 2, :]).then_inc(k_kept, 1)
            dve.wait_ge(gate_act, 5)
            nc.vector.scalar_tensor_tensor(out=a_pos[:, :, :], in0=a_pos[:, :, :], scalar=0.0, in1=a_neg[:, :, :],
                                           op0=ALU.max, op1=ALU.add).then_inc(gate_dve, 1)
            dve.wait_ge(gate_dve, 5)
            nc.vector.scalar_tensor_tensor(out=a, in0=a_pos[:, :, :], scalar=-1.0, in1=over(a_log[:, :], 1, [P, NT + 1, H]),
                                           op0=ALU.mult, op1=ALU.mult)
    m.free()


def chunk_masks(nc, m, sem, n, name):
    up = m.sb(f"{name}_up", [n, n])
    far = m.sb(f"{name}_far", [n, n])
    zeroed, ready = sem(f"{name}_zeroed"), sem(f"{name}_ready")

    def emit(pool):
        blocks = n // NL if n == NS else 1
        width = n // blocks
        pool.memset(up[:, :], 1.0).then_inc(zeroed, 1)
        pool.memset(far[:, :], 0.0).then_inc(zeroed, 1)
        pool.wait_ge(zeroed, 2)
        k = 0
        for t, fill in ((up, 0.0), (far, NEG)):
            v = t[:, :].rearrange("p (b l) -> p b l", b=blocks)
            pool.affine_select(out=v, in_=v, compare_op=ALU.is_ge, fill=fill, base=0, pattern=[[width, blocks], [1, width]],
                               channel_multiplier=-1).then_inc(ready, 1)
            k += 1
            if blocks > 1:
                pool.wait_ge(ready, k)
                pool.affine_select(out=v, in_=v, compare_op=ALU.is_ge, fill=fill, base=0,
                                   pattern=[[-width, blocks], [0, width]], channel_multiplier=1).then_inc(ready, 1)
                k += 1
        return k
    return up, far, ready, emit


def level_masks(pool, mask, levels, n, made, turned=False):
    pool.memset(mask, 0.0).then_inc(made, 1)
    pool.wait_ge(made, 1)
    k = 1
    for level in range(levels):
        b = 1 << level
        v = mask[:, level, :].rearrange("p (a c) -> p a c", c=2 * b)[:, :, b:2 * b] if turned else \
            mask[:, level, :].rearrange("p (a c) -> p a c", c=2 * b)[:, :, 0:b]
        pool.memset(v, 1.0).then_inc(made, 1)
        k += 1
        pool.wait_ge(made, k)
        pool.affine_select(out=v, in_=v, compare_op=ALU.is_ge, fill=0.0, base=0 if turned else -b,
                           pattern=[[-2 * b, n // (2 * b)], [0, b]], channel_multiplier=1).then_inc(made, 1)
        k += 1
        pool.wait_ge(made, k)
        pool.affine_select(out=v, in_=v, compare_op=ALU.is_ge, fill=0.0, base=(b if turned else 2 * b) - 1,
                           pattern=[[2 * b, n // (2 * b)], [0, b]], channel_multiplier=-1).then_inc(made, 1)
        k += 1
    return k


def delta_constants(nc, m, sem):
    d = {
        "mask": m.sb("c_mask", [P, NLEV, P]),
        "join": [m.sb(f"c_join{s}", [P, NLEV - 1, H, P]) for s in range(2)],
        "state": [m.sb(f"c_S{s}", [P, H, P]) for s in range(2)],
    }
    d["up"], d["far"], _, emit_masks = chunk_masks(nc, m, sem, P, "c")
    made, zeroed = sem("c_mask_made"), sem("c_all_zero")

    def emit(pool):
        for t in (d["state"][0][:, :, :], d["join"][0][:, :, :, :], d["join"][1][:, :, :, :]):
            pool.memset(t, 0.0).then_inc(zeroed, 1)
        emit_masks(pool)
        level_masks(pool, d["mask"][:, :, :], NLEV, P, made, turned=True)
    return d, emit


def delta_prompt(nc, i, o, c, feat, ba, head_out, consts, sem):
    m = Memory(nc)

    def per_slot(name, shape):
        return [m.sb(f"{name}{s}", shape) for s in range(2)]

    W4 = [P, H, P]
    kv = per_slot("c_kv", [P, 2 * H, P])
    row_g, row_b, e_row, ET = (per_slot(n, W4) for n in ("c_row_g", "c_row_b", "c_e_row", "c_ET"))
    AT, PT, kbg, kdec, vb = (per_slot(n, W4) for n in ("c_AT", "c_PT", "c_kbg", "c_kdec", "c_vb"))
    D, DT, qg, u, wT, vn = (per_slot(n, W4) for n in ("c_D", "c_DT", "c_qg", "c_u", "c_wT", "c_vn"))
    AT_off = [[m.sb(f"c_AT_off{s}{x}", W4) for x in range(2)] for s in range(2)]
    gcum, eg, beg, beta = (per_slot(n, [P, H]) for n in ("c_gcum", "c_eg", "c_beg", "c_beta"))
    S_dec = m.sb("c_S_dec", W4)
    S, M, mask, up, far = consts["state"], consts["join"], consts["mask"], consts["up"], consts["far"]
    bank = [[m.ps(f"c_bank{s}{b}", [P, 512]) for b in range(4)] for s in range(2)]

    def heads(ap):
        return ap.rearrange("p (h t) -> p h t", h=H)

    names = ("staged slot_free rows_g rows_b DT_first beta_put R_ready B_ready KK_ready KQ_ready C_ready gcum_ready e_row_ready eg_ready arg_ready "
             "ET_ready KE_ready AT_ready PT_ready kt_turned vt_turned beg_ready kbg_ready kdec_ready vb_ready qg_ready "
             "u_product w_product u_kept w_kept wS_ready vn_ready o_ready S_product decayed S_done o_kept").split()
    S_ = {n: sem("c_" + n) for n in names}
    AT_cut, M_product, M_kept, D_product, D_kept, DT_kept = (
        [sem(f"c_{n}{s}") for s in range(2)] for n in ("AT_cut", "M_product", "M_kept", "D_product", "D_kept", "DT_kept"))
    S_out = sem("c_S_out")
    owner = {"pool": "slot_free rows_g rows_b beta_put beg_ready qg_ready",
             "tensor": "C_ready R_ready B_ready KK_ready KQ_ready kt_turned vt_turned u_product w_product wS_ready o_ready S_product",
             "scalar": "staged gcum_ready e_row_ready eg_ready ET_ready u_kept w_kept o_kept",
             "vector": "DT_first arg_ready KE_ready AT_ready PT_ready kbg_ready kdec_ready vb_ready vn_ready decayed S_done"}

    def credit(eng, who):
        for n in owner[who].split():
            eng.sem_inc(S_[n], CREDIT)

    def odd_even(ap, level, odd):
        b = 1 << level
        return ap.rearrange("p h (a c) -> p (h a) c", c=2 * b)[:, :, odd * b:(odd + 1) * b]

    with nc.Block() as block:
        @block.sync
        def _(sp):
            sp.wait_ge(S_["S_done"], done(NT - 1))
            sp.dma_start(o["gdn_S_prompt"][0, 0].rearrange("h k v -> k h v"), S[0][:, :, :]).then_inc(S_out, 16)
            sp.wait_ge(S_out, 16)

        @block.gpsimd
        def _(pool):
            credit(pool, "pool")
            with pool.Fori(0, NT // 2) as it:
                for s in range(2):
                    n = 2 * it + s
                    pool.wait_ge(S_["S_done"], done(n - 2))
                    pool.wait_ge(S_["o_kept"], done(n - 2))
                    pool.sem_inc(S_["slot_free"], 1)
                    nc.gpsimd.tensor_tensor(row_g[s][:, :, :], over(up[:, :], 1, W4),
                                            over(ba[:, bass.ds(n, 1), H:2 * H].rearrange("p o h -> p (o h)"), 2, W4),
                                            ALU.mult).then_inc(S_["rows_g"], 1)
                    nc.gpsimd.tensor_tensor(row_b[s][:, :, :], over(c["ident"][:, :], 1, W4),
                                            over(ba[:, bass.ds(n, 1), 0:H].rearrange("p o h -> p (o h)"), 2, W4),
                                            ALU.mult).then_inc(S_["rows_b"], 1)
                    nc.gpsimd.tensor_copy(beta[s][:, :], ba[:, bass.ds(n, 1), 0:H].rearrange("p o h -> p (o h)")
                                          ).then_inc(S_["beta_put"], 1)
                for level in range(NLEV):
                    for s in range(2):
                        n = 2 * it + s
                        if level == 0:
                            pool.wait_ge(S_["AT_ready"], done(n))
                        elif level >= 2:
                            if level == 2:
                                pool.wait_ge(S_["DT_first"], done(n))
                            pool.wait_ge(M_product[s], levels_done(it, level - 2))
                        nc.gpsimd.tensor_tensor(AT_off[s][level % 2][:, :, :], AT[s][:, :, :], over(mask[:, level, :], 1, W4),
                                                ALU.mult).then_inc(AT_cut[s], 1)
                    if level == 0:
                        for s in range(2):
                            n = 2 * it + s
                            pool.wait_ge(S_["beta_put"], done(n))
                            pool.wait_ge(S_["eg_ready"], done(n))
                            pool.wait_ge(S_["e_row_ready"], done(n))
                            nc.gpsimd.tensor_tensor(beg[s][:, :], eg[s][:, :], beta[s][:, :], ALU.mult).then_inc(S_["beg_ready"], 1)
                    if level == 2:
                        for s in range(2):
                            n = 2 * it + s
                            nc.gpsimd.tensor_tensor(qg[s][:, :, :], feat[:, 0:H, bass.ds(n * P, P)], e_row[s][:, :, :],
                                                    ALU.mult).then_inc(S_["qg_ready"], 1)

        @block.tensor
        def _(pe):
            credit(pe, "tensor")
            with pe.Fori(0, NT // 2) as it:
                for s in range(2):
                    n = 2 * it + s
                    b = bank[s]
                    pe.wait_ge(S_["rows_g"], done(n))
                    nc.tensor.matmul(b[3][:, 0:H], up[:, :], ba[:, bass.ds(n, 1), H:2 * H].rearrange("p o h -> p (o h)"),
                                     start=True, stop=True).then_inc(S_["C_ready"], 1)
                    nc.tensor.matmul(b[0][:, :], c["ones"][:, :], row_g[s][:, :, :], start=True, stop=True
                                     ).then_inc(S_["R_ready"], 1)
                    pe.wait_ge(S_["rows_b"], done(n))
                    nc.tensor.matmul(b[1][:, :], c["ones"][:, :], row_b[s][:, :, :], start=True, stop=True
                                     ).then_inc(S_["B_ready"], 1)
                    pe.wait_ge(S_["staged"], done(n))
                    for h in range(H):
                        mm = nc.tensor.matmul(b[2][:, h * P:(h + 1) * P], kv[s][:, h, :], kv[s][:, h, :], start=True, stop=True)
                    mm.then_inc(S_["KK_ready"], 1)
                    pe.wait_ge(S_["gcum_ready"], done(n))
                    for h in range(H):
                        mm = nc.tensor.matmul(b[3][:, h * P:(h + 1) * P], kv[s][:, h, :],
                                              feat[:, h, bass.ds(n * P, P)], start=True, stop=True)
                    mm.then_inc(S_["KQ_ready"], 1)
                for s in range(2):
                    n = 2 * it + s
                    pe.wait_ge(S_["e_row_ready"], done(n))
                    for h in range(H):
                        mm = nc.tensor.transpose(bank[s][0][:, h * P:(h + 1) * P], kv[s][:, h, :], c["ident"][:, :])
                    mm.then_inc(S_["kt_turned"], 1)
                for level in range(NLEV):
                    for s in range(2):
                        pe.wait_ge(AT_cut[s], levels_done(it, level))
                        if level > 0:
                            pe.wait_ge(D_kept[s], levels_done(it, level - 1, NLEV - 1))
                        for h in range(H):
                            if level == 0:
                                mm = nc.tensor.matmul(bank[s][2][:, h * P:(h + 1) * P], AT_off[s][0][:, h, :], c["ident"][:, :],
                                                      start=True, stop=True)
                            else:
                                mm = nc.tensor.matmul(bank[s][2][:, h * HALF:(h + 1) * HALF], AT_off[s][level % 2][:, h, :],
                                                      odd_even(D[s][:, h:h + 1, :], level, 0), start=True, stop=True)
                        mm.then_inc(M_product[s], 1)
                    if level == 0:
                        for s in range(2):
                            n = 2 * it + s
                            for h in range(H):
                                mm = nc.tensor.transpose(bank[s][1][:, h * P:(h + 1) * P], kv[s][:, H + h, :], c["ident"][:, :])
                            mm.then_inc(S_["vt_turned"], 1)
                        continue
                    for s in range(2):
                        n = 2 * it + s
                        pe.wait_ge(M_kept[s], levels_done(it, level - 1, NLEV - 1))
                        if level == 1:
                            pe.wait_ge(S_["DT_first"], done(n))
                            pe.wait_ge(S_["PT_ready"], done(n))
                        else:
                            pe.wait_ge(DT_kept[s], levels_done(it, level - 2, NLEV - 1))
                        for h in range(H):
                            if level < NLEV - 1:
                                nc.tensor.matmul(bank[s][3][:, h * HALF:(h + 1) * HALF], DT[s][:, h, :],
                                                 odd_even(M[s][:, level - 1, h:h + 1, :], level, 0), start=True, stop=True)
                            mm = nc.tensor.matmul(bank[s][3][:, (H + h) * HALF:(H + h + 1) * HALF], M[s][:, level - 1, h, :],
                                                  odd_even(DT[s][:, h:h + 1, :], level, 1), start=True, stop=True)
                        mm.then_inc(D_product[s], 1)
                for s in range(2):
                    n = 2 * it + s
                    b = bank[s]
                    pe.wait_ge(DT_kept[s], levels_done(it, NLEV - 2, NLEV - 1))
                    pe.wait_ge(S_["vb_ready"], done(n))
                    for h in range(H):
                        mm = nc.tensor.matmul(b[0][:, h * P:(h + 1) * P], DT[s][:, h, :], vb[s][:, h, :], start=True, stop=True)
                    mm.then_inc(S_["u_product"], 1)
                    for h in range(H):
                        mm = nc.tensor.matmul(b[1][:, h * P:(h + 1) * P], kbg[s][:, h, :], DT[s][:, h, :], start=True, stop=True)
                    mm.then_inc(S_["w_product"], 1)
                for s in range(2):
                    n = 2 * it + s
                    b = bank[s]
                    pe.wait_ge(S_["w_kept"], done(n))
                    pe.wait_ge(S_["S_done"], done(n - 1))
                    for h in range(H):
                        mm = nc.tensor.matmul(b[2][:, h * P:(h + 1) * P], wT[s][:, h, :], S[s][:, h, :], start=True, stop=True)
                    mm.then_inc(S_["wS_ready"], 1)
                    pe.wait_ge(S_["vn_ready"], done(n))
                    pe.wait_ge(S_["u_kept"], done(n))
                    for h in range(H):
                        mm = nc.tensor.matmul(b[0][:, h * P:(h + 1) * P], kdec[s][:, h, :], vn[s][:, h, :], start=True, stop=True)
                    mm.then_inc(S_["S_product"], 1)
                    pe.wait_ge(S_["qg_ready"], done(n))
                    for h in range(H):
                        nc.tensor.matmul(b[3][:, h * P:(h + 1) * P], S[s][:, h, :], qg[s][:, h, :], start=True, stop=False)
                        mm = nc.tensor.matmul(b[3][:, h * P:(h + 1) * P], vn[s][:, h, :], PT[s][:, h, :], start=False, stop=True)
                    mm.then_inc(S_["o_ready"], 1)

        @block.scalar
        def _(act):
            credit(act, "scalar")
            nc.scalar.preload_act_table(ACT.Exp)
            with act.Fori(0, NT // 2) as it:
                for s in range(2):
                    n = 2 * it + s
                    act.wait_ge(S_["slot_free"], done(n))
                    nc.scalar.copy(kv[s][:, :, :], feat[:, H:3 * H, bass.ds(n * P, P)]).then_inc(S_["staged"], 1)
                for s in range(2):
                    n = 2 * it + s
                    b = bank[s]
                    act.wait_ge(S_["C_ready"], done(n))
                    nc.scalar.copy(gcum[s][:, :], b[3][:, 0:H]).then_inc(S_["gcum_ready"], 1)
                    act.wait_ge(S_["gcum_ready"], done(n))
                    nc.scalar.activation(eg[s][:, :], gcum[s][:, :], ACT.Exp).then_inc(S_["eg_ready"], 1)
                    act.wait_ge(S_["arg_ready"], done(n))
                    nc.scalar.activation(ET[s][:, :, :], ET[s][:, :, :], ACT.Exp).then_inc(S_["ET_ready"], 1)
                    nc.scalar.activation(e_row[s][:, :, :], heads(b[0][:, :]), ACT.Exp).then_inc(S_["e_row_ready"], 1)
                for level in range(1, NLEV):
                    for s in range(2):
                        act.wait_ge(M_product[s], levels_done(it, level))
                        nc.scalar.copy(odd_even(M[s][:, level - 1, :, :], level, 0),
                                       bank[s][2][:, 0:H * HALF].rearrange("p (a b) -> p a b", b=1 << level)).then_inc(M_kept[s], 1)
                for s in range(2):
                    n = 2 * it + s
                    act.wait_ge(S_["w_product"], done(n))
                    nc.scalar.copy(wT[s][:, :, :], heads(bank[s][1][:, :])).then_inc(S_["w_kept"], 1)
                    nc.scalar.copy(u[s][:, :, :], heads(bank[s][0][:, :])).then_inc(S_["u_kept"], 1)
                for s in range(2):
                    n = 2 * it + s
                    act.wait_ge(S_["o_ready"], done(n))
                    nc.scalar.copy(head_out[:, 0:H, bass.ds(n * P, P)], heads(bank[s][3][:, :])).then_inc(S_["o_kept"], 1)

        @block.vector
        def _(dve):
            credit(dve, "vector")
            with dve.Fori(0, NT // 2) as it:
                for s in range(2):
                    n = 2 * it + s
                    b = bank[s]
                    dve.wait_ge(S_["R_ready"], done(n))
                    dve.wait_ge(S_["gcum_ready"], done(n))
                    for h in range(H):
                        ins = nc.vector.scalar_tensor_tensor(
                            out=ET[s][:, h, :], in0=b[0][:, h * P:(h + 1) * P], scalar=gcum[s][:, h:h + 1], in1=far[:, :],
                            op0=ALU.subtract, op1=ALU.add)
                    ins.then_inc(S_["arg_ready"], 1)
                    dve.wait_ge(S_["KK_ready"], done(n))
                    dve.wait_ge(S_["ET_ready"], done(n))
                    nc.vector.tensor_tensor(AT[s][:, :, :], heads(b[2][:, :]), ET[s][:, :, :], ALU.mult).then_inc(S_["KE_ready"], 1)
                    dve.wait_ge(S_["KE_ready"], done(n))
                    dve.wait_ge(S_["B_ready"], done(n))
                    nc.vector.tensor_tensor(AT[s][:, :, :], heads(b[1][:, :]), AT[s][:, :, :], ALU.mult).then_inc(S_["AT_ready"], 1)
                    dve.wait_ge(S_["KQ_ready"], done(n))
                    nc.vector.tensor_tensor(PT[s][:, :, :], heads(b[3][:, :]), ET[s][:, :, :], ALU.mult).then_inc(S_["PT_ready"], 1)

                def token_major(s):
                    n = 2 * it + s
                    b = bank[s]
                    dve.wait_ge(S_["kt_turned"], done(n))
                    dve.wait_ge(S_["beg_ready"], done(n))
                    nc.vector.tensor_tensor(kbg[s][:, :, :], heads(b[0][:, :]), over(beg[s][:, :], 2, W4), ALU.mult
                                            ).then_inc(S_["kbg_ready"], 1)
                    nc.vector.tensor_tensor(kdec[s][:, :, :], heads(b[0][:, :]),
                                            ET[s][:, :, P - 1:P].to_broadcast(W4), ALU.mult).then_inc(S_["kdec_ready"], 1)
                    dve.wait_ge(S_["vt_turned"], done(n))
                    nc.vector.tensor_tensor(vb[s][:, :, :], heads(b[1][:, :]),
                                            over(ba[:, bass.ds(n, 1), 0:H].rearrange("p o h -> p (o h)"), 2, W4),
                                            ALU.mult).then_inc(S_["vb_ready"], 1)

                for s in range(2):
                    dve.wait_ge(M_product[s], levels_done(it, 0))
                    nc.vector.tensor_tensor(D[s][:, :, :], over(c["ident"][:, :], 1, W4), heads(bank[s][2][:, :]),
                                            ALU.subtract).then_inc(D_kept[s], 1)
                    nc.vector.tensor_tensor(DT[s][:, :, :], over(c["ident"][:, :], 1, W4), AT_off[s][0][:, :, :],
                                            ALU.subtract).then_inc(S_["DT_first"], 1)
                for level in range(1, NLEV):
                    if level in (2, 3):
                        token_major(level - 2)
                    for s in range(2):
                        dve.wait_ge(D_product[s], levels_done(it, level - 1, NLEV - 1))
                        b = 1 << level
                        if level < NLEV - 1:
                            d = odd_even(D[s][:, :, :], level, 0)
                            nc.vector.tensor_tensor(d, d, bank[s][3][:, 0:H * HALF].rearrange("p (a b) -> p a b", b=b),
                                                    ALU.subtract).then_inc(D_kept[s], 1)
                        d = odd_even(DT[s][:, :, :], level, 1)
                        nc.vector.tensor_tensor(d, d, bank[s][3][:, H * HALF:2 * H * HALF].rearrange("p (a b) -> p a b", b=b),
                                                ALU.subtract).then_inc(DT_kept[s], 1)
                for s in range(2):
                    n = 2 * it + s
                    b = bank[s]
                    dve.wait_ge(S_["e_row_ready"], done(n))
                    dve.wait_ge(S_["S_done"], done(n - 1))
                    nc.vector.tensor_tensor(S_dec[:, :, :], S[s][:, :, :], e_row[s][:, :, P - 1:P].to_broadcast(W4),
                                            ALU.mult).then_inc(S_["decayed"], 1)
                    dve.wait_ge(S_["wS_ready"], done(n))
                    dve.wait_ge(S_["u_kept"], done(n))
                    nc.vector.tensor_tensor(vn[s][:, :, :], u[s][:, :, :], heads(b[2][:, :]), ALU.subtract
                                            ).then_inc(S_["vn_ready"], 1)
                    dve.wait_ge(S_["S_product"], done(n))
                    dve.wait_ge(S_["decayed"], done(n))
                    nc.vector.tensor_tensor(S[1 - s][:, :, :], heads(b[0][:, :]), S_dec[:, :, :], ALU.add
                                            ).then_inc(S_["S_done"], 1)
    m.free()


def delta_sample(nc, i, o, c, feat, ba, head_out, sem):
    m = Memory(nc)
    R, C = [NS, H, NS], [NS, H, DH]
    LEV = 2
    row_g, row_b, ET, AT, PT, D, DT, M = (m.sb(f"s_{n}", R) for n in ("row_g", "row_b", "ET", "AT", "PT", "D", "DT", "M"))
    kbg, kdec, vb, vn = (m.sb(f"s_{n}", C) for n in ("kbg", "kdec", "vb", "vn"))
    e_row = m.sb("s_e_row", [P, H, NS])
    wq = m.sb("s_wq", [P, H, NB, 2 * NL])
    uT, vnT, qS = (m.sb(f"s_{n}", [P, H, NS]) for n in ("uT", "vnT", "qS"))
    gcum, eg, beg, dec = (m.sb(f"s_{n}", [NS, H]) for n in ("gcum", "eg", "beg", "dec"))
    state = m.sb("s_state", [P, NB * H, DH])
    own = m.sb("s_own", [NS, NB])
    spread = [m.sb(f"s_spread{x}", [NS, NB, DH]) for x in range(2)]
    mask = m.sb("s_mask", [NS, LEV, NS])
    up, far, masks_ready, emit_masks = chunk_masks(nc, m, sem, NS, "s")
    bank = [m.ps(f"s_bank{b}", [P, 512]) for b in range(4)]
    wide = [m.ps(f"s_wide{x}", [P, NB, DH]) for x in range(2)]
    bank += [wide[1][:, 0:4, :].rearrange("p b v -> p (b v)"), wide[1][:, 4:8, :].rearrange("p b v -> p (b v)")]

    state_in, state_out = sem("s_state_in"), sem("s_state_out")
    own_made, mask_made, rows_ready, pe_done = (sem(f"s_{n}") for n in ("own_made", "mask_made", "rows_ready", "pe_done"))
    act_done, dve_done, q_put, identity_put = sem("s_act_done"), sem("s_dve_done"), sem("s_q_put"), sem("s_identity_put")
    PE = {n: k + 1 for k, n in enumerate("gcum row beta KK KQ k_turned v_turned M0 D0 M1 D1 u w wqS vn_turned o S0 S1 S2 S3".split())}
    SC = {n: k + 1 for k, n in enumerate("gcum eg e_row ET u w qS".split())}
    DV = {n: k + 1 for k, n in enumerate(
        "arg dec KE AT PT beg kbg kdec vb M0 D0 DT0 M1 DT1 vnT vn o "
        "spread0 decay0 spread1 decay1 S0 spread2 decay2 S1 spread3 decay3 S2 S3".split())}

    def cols(ap, n=NS, rows=NS):
        return ap[0:rows, 0:H * n].rearrange("p (h t) -> p h t", h=H)

    def pairs_of(ap, level, odd):
        b = 1 << level
        return ap.rearrange("p h (a c) -> p (h a) c", c=2 * b)[:, :, odd * b:(odd + 1) * b]

    b_gate = ba[0:NS, NT, 0:H]
    g_gate = ba[0:NS, NT, H:2 * H]
    q, k, v = (feat[:, x * H:(x + 1) * H, SEQ:T] for x in range(3))

    with nc.Block() as block:
        @block.sync
        def _(sp):
            sp.dma_start(state[:, :, :], i["state_gdn_S"][0].rearrange("b h k v -> k (b h) v")).then_inc(state_in, 16)
            sp.wait_ge(dve_done, DV["S3"])
            sp.dma_start(o["gdn_S_sample"][0].rearrange("b h k v -> k (b h) v"), state[:, :, :]).then_inc(state_out, 16)
            sp.wait_ge(state_out, 16)

        @block.gpsimd
        def _(pool):
            kk = emit_masks(pool)
            level_masks(pool, mask[:, :, :], LEV, NS, mask_made)
            pool.memset(own[:, :], 1.0).then_inc(own_made, 1)
            pool.wait_ge(own_made, 1)
            pool.affine_select(out=own[:, :], in_=own[:, :], compare_op=ALU.is_ge, fill=0.0, base=0, pattern=[[-NL, NB]],
                               channel_multiplier=1).then_inc(own_made, 1)
            pool.wait_ge(own_made, 2)
            pool.affine_select(out=own[:, :], in_=own[:, :], compare_op=ALU.is_ge, fill=0.0, base=NL - 1, pattern=[[NL, NB]],
                               channel_multiplier=-1).then_inc(own_made, 1)
            pool.wait_ge(masks_ready, kk)
            nc.gpsimd.tensor_tensor(row_g[:, :, :], over(up[:, :], 1, R), over(g_gate, 2, R), ALU.mult).then_inc(rows_ready, 1)
            nc.gpsimd.tensor_tensor(row_b[:, :, :], over(c["ident"][0:NS, 0:NS], 1, R), over(b_gate, 2, R), ALU.mult
                                    ).then_inc(rows_ready, 1)
            for t in (D, DT):
                nc.gpsimd.tensor_copy(t[:, :, :], over(c["ident"][0:NS, 0:NS], 1, R)).then_inc(identity_put, 1)
            pool.wait_ge(act_done, SC["e_row"])
            nc.gpsimd.tensor_tensor(wq[:, :, :, NL:2 * NL], q.rearrange("p h (b l) -> p h b l", b=NB),
                                    e_row[:, :, :].rearrange("p h (b l) -> p h b l", b=NB), ALU.mult).then_inc(q_put, 1)

        @block.tensor
        def _(pe):
            pe.wait_ge(rows_ready, 2)
            nc.tensor.matmul(bank[3][0:NS, 0:H], up[:, :], g_gate, start=True, stop=True).then_inc(pe_done, 1)
            ones = c["ones"][0:NS, :]
            nc.tensor.matmul(bank[0][:, 0:H * NS], ones, row_g[:, :, :], start=True, stop=True).then_inc(pe_done, 1)
            nc.tensor.matmul(bank[1][0:NS, 0:H * NS], ones[:, 0:NS], row_b[:, :, :], start=True, stop=True).then_inc(pe_done, 1)
            for h in range(H):
                mm = nc.tensor.matmul(cols(bank[2])[:, h, :], k[:, h, :], k[:, h, :], start=True, stop=True)
            mm.then_inc(pe_done, 1)
            pe.wait_ge(act_done, SC["gcum"])
            for h in range(H):
                mm = nc.tensor.matmul(cols(bank[3])[:, h, :], k[:, h, :], q[:, h, :], start=True, stop=True)
            mm.then_inc(pe_done, 1)
            for x, b in ((k, 4), (v, 5)):
                for h in range(H):
                    mm = nc.tensor.transpose(bank[b][0:NS, h * DH:(h + 1) * DH], x[:, h, :], c["ident"][:, :])
                mm.then_inc(pe_done, 1)
            pe.wait_ge(identity_put, 2)
            for level in range(LEV):
                pe.wait_ge(dve_done, DV["PT"] if level == 0 else DV["D0"])
                for h in range(H):
                    mm = nc.tensor.matmul(cols(bank[2])[:, h, :], AT[:, h, :], D[:, h, :], start=True, stop=True)
                mm.then_inc(pe_done, 1)
                pe.wait_ge(dve_done, DV[f"M{level}"])
                half = NS // 2
                for h in range(H):
                    if level < LEV - 1:
                        nc.tensor.matmul(bank[3][0:NS, h * half:(h + 1) * half], DT[:, h, :],
                                         pairs_of(M[:, h:h + 1, :], level, 0), start=True, stop=True)
                    mm = nc.tensor.matmul(bank[3][0:NS, (H + h) * half:(H + h + 1) * half], M[:, h, :],
                                          pairs_of(DT[:, h:h + 1, :], level, 1), start=True, stop=True)
                mm.then_inc(pe_done, 1)
            pe.wait_ge(dve_done, DV["DT1"])
            for h in range(H):
                mm = nc.tensor.matmul(cols(bank[0], NS, P)[:, h, :], vb[:, h, :], DT[:, h, :], start=True, stop=True)
            mm.then_inc(pe_done, 1)
            for h in range(H):
                mm = nc.tensor.matmul(bank[1][:, h * NS:(h + 1) * NS], kbg[:, h, :], DT[:, h, :], start=True, stop=True)
            mm.then_inc(pe_done, 1)
            pe.wait_ge(act_done, SC["w"])
            pe.wait_ge(q_put, 1)
            pe.wait_ge(state_in, 16)
            for b in range(NB):
                for h in range(H):
                    at = (h * NB + b) * 2 * NL
                    mm = nc.tensor.matmul(bank[2][:, at:at + 2 * NL], state[:, b * H + h, :], wq[:, h, b, :], start=True, stop=True)
            mm.then_inc(pe_done, 1)
            pe.wait_ge(dve_done, DV["vnT"])
            for h in range(H):
                mm = nc.tensor.transpose(bank[4][0:NS, h * DH:(h + 1) * DH], vnT[:, h, :], c["ident"][:, :])
            mm.then_inc(pe_done, 1)
            pe.wait_ge(dve_done, DV["vn"])
            for h in range(H):
                mm = nc.tensor.matmul(bank[5][:, h * NS:(h + 1) * NS], vn[:, h, :], PT[:, h, :], start=True, stop=True)
            mm.then_inc(pe_done, 1)
            for h in range(H):
                pe.wait_ge(dve_done, DV[f"spread{h}"])
                for g in range(2):
                    mm = nc.tensor.matmul(wide[h % 2][:, g * 4:g * 4 + 4, :], kdec[:, h, :], spread[h % 2][:, g * 4:g * 4 + 4, :],
                                          start=True, stop=True)
                mm.then_inc(pe_done, 1)

        @block.scalar
        def _(act):
            act.wait_ge(pe_done, PE["gcum"])
            nc.scalar.copy(gcum[:, :], bank[3][0:NS, 0:H]).then_inc(act_done, 1)
            act.wait_ge(act_done, SC["gcum"])
            nc.scalar.activation(eg[:, :], gcum[:, :], ACT.Exp).then_inc(act_done, 1)
            act.wait_ge(pe_done, PE["row"])
            nc.scalar.activation(e_row[:, :, :], cols(bank[0], NS, P), ACT.Exp).then_inc(act_done, 1)
            act.wait_ge(dve_done, DV["arg"])
            nc.scalar.activation(ET[:, :, :], ET[:, :, :], ACT.Exp).then_inc(act_done, 1)
            act.wait_ge(pe_done, PE["w"])
            nc.scalar.copy(uT[:, :, :], cols(bank[0], NS, P)).then_inc(act_done, 1)
            nc.scalar.copy(wq[:, :, :, 0:NL], cols(bank[1], NS, P).rearrange("p h (b l) -> p h b l", b=NB)).then_inc(act_done, 1)
            act.wait_ge(dve_done, DV["vnT"])
            nc.scalar.copy(qS[:, :, :].rearrange("p h (b l) -> p (h b) l", b=NB),
                           bank[2][:, 0:2 * H * NS].rearrange("p (a l) -> p a l", l=2 * NL)[:, :, NL:2 * NL]).then_inc(act_done, 1)

        @block.vector
        def _(dve):
            dve.wait_ge(masks_ready, 4)
            dve.wait_ge(mask_made, 1 + 3 * LEV)
            dve.wait_ge(act_done, SC["e_row"])
            for h in range(H):
                ins = nc.vector.scalar_tensor_tensor(out=ET[:, h, :], in0=cols(bank[0])[:, h, :], scalar=gcum[:, h:h + 1],
                                                     in1=far[:, :], op0=ALU.subtract, op1=ALU.add)
            ins.then_inc(dve_done, 1)
            dve.wait_ge(act_done, SC["ET"])
            nc.vector.tensor_reduce(out=dec[:, :], in_=ET[:, :, :].rearrange("p h (b l) -> p h b l", b=NB)[:, :, :, NL - 1],
                                    axis=AX.X, op=ALU.add).then_inc(dve_done, 1)
            dve.wait_ge(pe_done, PE["KK"])
            nc.vector.tensor_tensor(AT[:, :, :], cols(bank[2]), ET[:, :, :], ALU.mult).then_inc(dve_done, 1)
            dve.wait_ge(dve_done, DV["KE"])
            nc.vector.tensor_tensor(AT[:, :, :], cols(bank[1]), AT[:, :, :], ALU.mult).then_inc(dve_done, 1)
            dve.wait_ge(pe_done, PE["KQ"])
            nc.vector.tensor_tensor(PT[:, :, :], cols(bank[3]), ET[:, :, :], ALU.mult).then_inc(dve_done, 1)
            nc.vector.tensor_tensor(beg[:, :], eg[:, :], b_gate, ALU.mult).then_inc(dve_done, 1)
            dve.wait_ge(pe_done, PE["v_turned"])
            dve.wait_ge(dve_done, DV["beg"])
            nc.vector.tensor_tensor(kbg[:, :, :], cols(bank[4], DH), over(beg[:, :], 2, C), ALU.mult).then_inc(dve_done, 1)
            nc.vector.tensor_tensor(kdec[:, :, :], cols(bank[4], DH), over(dec[:, :], 2, C), ALU.mult).then_inc(dve_done, 1)
            nc.vector.tensor_tensor(vb[:, :, :], cols(bank[5], DH), over(b_gate, 2, C), ALU.mult).then_inc(dve_done, 1)
            for level in range(LEV):
                dve.wait_ge(pe_done, PE[f"M{level}"])
                nc.vector.tensor_tensor(M[:, :, :], cols(bank[2]), over(mask[:, level, :], 1, R), ALU.mult).then_inc(dve_done, 1)
                dve.wait_ge(pe_done, PE[f"D{level}"])
                half, b = NS // 2, 1 << level
                if level < LEV - 1:
                    d = pairs_of(D[:, :, :], level, 0)
                    nc.vector.tensor_tensor(d, d, bank[3][0:NS, 0:H * half].rearrange("p (a b) -> p a b", b=b),
                                            ALU.subtract).then_inc(dve_done, 1)
                d = pairs_of(DT[:, :, :], level, 1)
                nc.vector.tensor_tensor(d, d, bank[3][0:NS, H * half:2 * H * half].rearrange("p (a b) -> p a b", b=b),
                                        ALU.subtract).then_inc(dve_done, 1)
            dve.wait_ge(pe_done, PE["wqS"])
            dve.wait_ge(act_done, SC["u"])
            nc.vector.tensor_tensor(vnT[:, :, :].rearrange("p h (b l) -> p (h b) l", b=NB),
                                    uT[:, :, :].rearrange("p h (b l) -> p (h b) l", b=NB),
                                    bank[2][:, 0:2 * H * NS].rearrange("p (a l) -> p a l", l=2 * NL)[:, :, 0:NL],
                                    ALU.subtract).then_inc(dve_done, 1)
            dve.wait_ge(pe_done, PE["vn_turned"])
            nc.vector.tensor_copy(vn[:, :, :], cols(bank[4], DH)).then_inc(dve_done, 1)
            dve.wait_ge(pe_done, PE["o"])
            dve.wait_ge(act_done, SC["qS"])
            nc.vector.tensor_tensor(head_out[:, 0:H, SEQ:T], cols(bank[5], NS, P), qS[:, :, :], ALU.add).then_inc(dve_done, 1)
            dve.wait_ge(state_in, 16)
            def mine(h):
                return state[:, :, :].rearrange("p (b h) v -> p b h v", h=H)[:, :, h, :]

            def spread_and_decay(h):
                nc.vector.tensor_tensor(spread[h % 2][:, :, :], over(vn[:, h, :], 1, [NS, NB, DH]), over(own[:, :], 2, [NS, NB, DH]),
                                        ALU.mult).then_inc(dve_done, 1)
                last = e_row[:, h, :].rearrange("p (b l) -> p b l", b=NB)[:, :, NL - 1:NL]
                nc.vector.tensor_tensor(mine(h), mine(h), last.to_broadcast([P, NB, DH]), ALU.mult).then_inc(dve_done, 1)

            dve.wait_ge(dve_done, DV["vn"])
            spread_and_decay(0)
            spread_and_decay(1)
            for h in range(H):
                dve.wait_ge(pe_done, PE[f"S{h}"])
                dve.wait_ge(dve_done, DV[f"decay{h}"])
                nc.vector.tensor_tensor(mine(h), wide[h % 2][:, :, :], mine(h), ALU.add).then_inc(dve_done, 1)
                if h + 2 < H:
                    spread_and_decay(h + 2)
    m.free()


def attention_prompt(nc, i, o, c, feat, head_out, sem):
    m = Memory(nc)
    NE = 4
    qk = [m.sb(f"a_qk{s}", [P, 2, SEQ]) for s in range(2)]
    v = [m.sb(f"a_v{s}", [P, NT, DH]) for s in range(2)]
    e = [[m.sb(f"a_e{s}{x}", [P, SEQ]) for x in range(2)] for s in range(NE)]
    amapT = [m.sb(f"a_mapT{s}", [P, NT, P]) for s in range(2)]
    nmax, total, inv, w2 = (m.sb(f"a_{n}", [P, NE, 2]) for n in ("nmax", "total", "inv", "w2"))
    ident16 = m.sb("a_ident16", [P, P], BF16)
    far16 = m.sb("a_far16", [P, P], BF16)
    score = [m.ps(f"a_score{x}", [P, SEQ]) for x in range(3)]
    turned = m.ps("a_turned", [P, 4, P])
    out = m.ps("a_out", [P, 512])

    v_in = [sem(f"a_v_in{s}") for s in range(2)]
    made, made2 = sem("a_made"), sem("a_masks")
    qk_staged, first_staged = sem("a_qk_staged"), sem("a_first_staged")
    scored, maxed, expd = ([sem(f"a_{n}{x}") for x in range(2)] for n in ("scored", "maxed", "expd"))
    inverted, weighted, scaled, mapped = (sem(f"a_{n}") for n in ("inverted", "weighted", "scaled", "mapped"))
    block_turned, block_kept, multiplied, out_kept = (sem(f"a_{n}") for n in ("block_turned", "block_kept", "multiplied", "out_kept"))

    order = [qb for pair in zip(range(NT - 1, NT // 2 - 1, -1), range(NT // 2)) for qb in pair]
    units = [(hh, qb) for hh in range(2) for qb in order]
    NU = len(units)
    groups, g_of = [], {}
    for u, (hh, qb) in enumerate(units):
        for g in range((qb + 4) // 4):
            g_of[(u, g)] = len(groups)
            groups.append((u, g, min(4, qb + 1 - 4 * g)))
    NGR = len(groups)
    v_rows = o["v_prompt"].rearrange("a b (n p) h d -> p (a b n) h d", p=P)

    with nc.Block() as block:
        @block.sync
        def _(sp):
            sp.dma_start(v[0][:, :, :], v_rows[:, :, 0, :]).then_inc(v_in[0], 16)
            sp.dma_start(v[1][:, :, :], v_rows[:, :, 1, :]).then_inc(v_in[1], 16)
            for s in range(2):
                sp.wait_ge(multiplied, (s + 1) * NT)
                sp.dma_start(v[s][:, :, :], v_rows[:, :, 2 + s, :]).then_inc(v_in[s], 16)

        @block.gpsimd
        def _(pool):
            pool.sem_inc(qk_staged, CREDIT)
            pool.memset(ident16[:, :], 0.0).then_inc(made, 1)
            pool.memset(far16[:, :], 0.0).then_inc(made, 1)
            pool.wait_ge(made, 2)
            pool.affine_select(out=ident16[:, :], in_=ident16[:, :], compare_op=ALU.not_equal, fill=1.0, base=0,
                               pattern=[[-1, P]], channel_multiplier=1).then_inc(made2, 1)
            pool.affine_select(out=far16[:, :], in_=far16[:, :], compare_op=ALU.is_ge, fill=NEG, base=0,
                               pattern=[[-1, P]], channel_multiplier=1).then_inc(made2, 1)
            for h in range(1, H):
                if h >= 2:
                    pool.wait_ge(multiplied, (h - 1) * NT)
                nc.gpsimd.tensor_copy(qk[h % 2][:, 0, :], feat[:, 3 * H + h, 0:SEQ])
                nc.gpsimd.tensor_copy(qk[h % 2][:, 1, :], feat[:, 4 * H + h, 0:SEQ]).then_inc(qk_staged, 1)

        @block.tensor
        def _(pe):
            pe.wait_ge(made2, 2)
            pe.wait_ge(first_staged, 2)

            def scores(it, u, x):
                hh, qb = units[u]
                if x == 0 and qb == order[0]:
                    pe.wait_ge(qk_staged, CREDIT + 2 * it + hh)
                before = 2 * u + x - 3
                if before >= 0:
                    pe.wait_ge(expd[before % 2], NU * it + (before // 2 + 2))
                else:
                    pe.wait_ge(expd[0], NU * it + 1)
                    pe.wait_ge(expd[1], NU * it + 1)
                ps = score[(2 * u + x) % 3]
                lo = x * HALF
                q = qk[hh][lo:lo + HALF, 0, qb * P:(qb + 1) * P]
                n = (qb + 1) * P
                for k0 in range(0, n - P, 512):
                    k1 = min(n - P, k0 + 512)
                    nc.tensor.matmul(ps[:, k0:k1], q, qk[hh][lo:lo + HALF, 1, k0:k1], start=True, stop=True)
                nc.tensor.matmul(ps[:, n - P:n], q, qk[hh][lo:lo + HALF, 1, n - P:n], start=True, stop=False)
                nc.tensor.matmul(ps[:, n - P:n], ident16[:, :], far16[:, :], start=False, stop=True).then_inc(scored[x], 1)

            def turn(it, u, g):
                k = g_of[(u, g)]
                pe.wait_ge(block_kept, NGR * it + (k + 1))
                for j in range(groups[k][2]):
                    mm = nc.tensor.transpose(turned[:, j, :], e[u % NE][0][:, (4 * g + j) * P:(4 * g + j + 1) * P], c["ident"][:, :])
                mm.then_inc(block_turned, 1)

            def multiply(it, u, g):
                hh, qb = units[u]
                k = g_of[(u, g)]
                pe.wait_ge(block_kept, NGR * it + (k + 2))
                if g == 0:
                    if qb == order[0]:
                        pe.wait_ge(v_in[hh], 16 * it + 16)
                    pe.wait_ge(out_kept, NU * it + (u + 1))
                for j in range(groups[k][2]):
                    b = 4 * g + j
                    mm = nc.tensor.matmul(out[:, 0:P], v[hh][:, b, :], amapT[u % 2][:, b, :], start=(b == 0), stop=(b == qb))
                if b == qb:
                    mm.then_inc(multiplied, 1)

            with pe.Fori(0, H // 2) as it:
                for u in range(2):
                    scores(it, u, 0)
                    scores(it, u, 1)
                for u in range(NU):
                    ahead = [x for x in range(2) if u + 2 < NU]
                    last_group = units[u][1] // 4
                    pe.wait_ge(mapped, NU * it + (u + 1))
                    for g in range(last_group + 1):
                        turn(it, u, g)
                        for x in ahead if g == last_group else ahead[:1]:
                            scores(it, u + 2, x)
                        ahead = ahead[1:]
                        multiply(it, u, g)

        @block.scalar
        def _(act):
            act.sem_inc(expd[0], 1)
            act.sem_inc(expd[1], 1)
            act.sem_inc(block_kept, 1)
            act.sem_inc(out_kept, 1)
            nc.scalar.copy(qk[0][:, 0, :], feat[:, 3 * H, 0:SEQ]).then_inc(first_staged, 1)
            nc.scalar.preload_act_table(ACT.Exp)

            def exp_of(it, u, x):
                n = (units[u][1] + 1) * P
                act.wait_ge(maxed[x], NU * it + (u + 1))
                nc.scalar.activation(e[u % NE][x][:, 0:n], score[(2 * u + x) % 3][:, 0:n], ACT.Exp, bias=nmax[:, u % NE, x:x + 1],
                                     scale=1.0, accum_out=total[:, u % NE, x:x + 1]).then_inc(expd[x], 1)

            with act.Fori(0, H // 2) as it:
                for u in range(2):
                    exp_of(it, u, 0)
                    exp_of(it, u, 1)
                for u in range(NU):
                    hh, qb = units[u]
                    for g in range((qb + 4) // 4):
                        k = g_of[(u, g)]
                        act.wait_ge(block_turned, NGR * it + (k + 1))
                        nc.scalar.copy(amapT[u % 2][:, 4 * g:4 * g + groups[k][2], :], turned[:, 0:groups[k][2], :]
                                       ).then_inc(block_kept, 1)
                    if u + 2 < NU:
                        exp_of(it, u + 2, 0)
                    act.wait_ge(multiplied, NU * it + (u + 1))
                    nc.scalar.copy(head_out[:, bass.ds(2 * it + (H + hh), 1), qb * P:(qb + 1) * P].rearrange("p o t -> p (o t)"),
                                   out[:, 0:P]).then_inc(out_kept, 1)
                    if u + 2 < NU:
                        exp_of(it, u + 2, 1)
            act.wait_ge(v_in[0], 32)
            act.wait_ge(v_in[1], 32)

        @block.vector
        def _(dve):
            nc.vector.tensor_copy(qk[0][:, 1, :], feat[:, 4 * H, 0:SEQ]).then_inc(first_staged, 1)

            def max_of(it, u, x):
                n = (units[u][1] + 1) * P
                dve.wait_ge(scored[x], NU * it + (u + 1))
                nc.vector.tensor_reduce(out=nmax[:, u % NE, x:x + 1], in_=score[(2 * u + x) % 3][:, 0:n], axis=AX.X, op=ALU.max,
                                        negate=True).then_inc(maxed[x], 1)

            def difference(it, u):
                n = (units[u][1] + 1) * P
                s = u % NE
                for x in range(2):
                    dve.wait_ge(expd[x], NU * it + (u + 2))
                nc.vector.reciprocal(inv[:, s, :], total[:, s, :]).then_inc(inverted, 1)
                dve.wait_ge(inverted, NU * it + (u + 1))
                nc.vector.tensor_scalar(e[s][0][:, 0:n], e[s][0][:, 0:n], inv[:, s, 0:1], None, ALU.mult).then_inc(scaled, 1)
                nc.vector.tensor_tensor(w2[:, s, 0:1], inv[:, s, 1:2], c["neglam"][:, :], ALU.mult).then_inc(weighted, 1)
                dve.wait_ge(scaled, NU * it + (u + 1))
                dve.wait_ge(weighted, NU * it + (u + 1))
                nc.vector.scalar_tensor_tensor(out=e[s][0][:, 0:n], in0=e[s][1][:, 0:n], scalar=w2[:, s, 0:1],
                                               in1=e[s][0][:, 0:n], op0=ALU.mult, op1=ALU.add).then_inc(mapped, 1)

            with dve.Fori(0, H // 2) as it:
                for u in range(2):
                    max_of(it, u, 0)
                    max_of(it, u, 1)
                difference(it, 0)
                for u in range(NU):
                    if u + 1 < NU:
                        difference(it, u + 1)
                    if u + 2 < NU:
                        max_of(it, u + 2, 0)
                        max_of(it, u + 2, 1)
    m.free()


def attention_sample(nc, i, o, c, feat, head_out, sem):
    m = Memory(nc)
    NBT = 2
    SB = NB // NBT
    RW = 2 * NL
    NR = H * RW
    NK = 3
    key_in = [m.sb(f"p_key{s}", [P, NPG, GW]) for s in range(NK)]
    val_in = [m.sb(f"p_val{b}", [P, NPG, GW]) for b in range(NB)]
    v_new = m.sb("p_v_new", [NS, GW])
    keyT = [m.sb(f"p_keyT{s}", [P, H, PAST]) for s in range(2)]
    q_pad = [m.sb(f"p_q{t}", [P, H * (P + RW)]) for t in range(NBT)]
    e = [m.sb(f"p_e{t}", [P, PAST + NS]) for t in range(NBT)]
    fresh = [m.sb(f"p_fresh{t}", [P, NS]) for t in range(NBT)]
    mapT = m.sb("p_mapT", [P, NPG, P])
    mapT_new = m.sb("p_mapTn", [NS, P])
    out_rows = [e[t][:, 0:GW] for t in range(NBT)]
    stat = [m.sb(f"p_stat{t}", [P, 8]) for t in range(NBT)]
    maskT = m.sb("p_maskT", [NS, NBT, P])
    mask = m.sb("p_mask", [P, NBT, NS])
    sign_row = m.sb("p_sign_row", [1, P])
    sign = m.sb("p_sign", [P, 1])
    key_ps = m.ps("p_key_ps", [P, H, PAST])
    score = [m.ps(f"p_score{t}", [P, 512]) for t in range(NBT)]
    fresh_ps = [m.ps(f"p_fresh_ps{t}", [P, 512]) for t in range(NBT)]

    k_in, vn_in = [sem(f"p_k_in{s}") for s in range(NK)], sem("p_vn_in")
    v_in = [sem(f"p_v_in{b}") for b in range(NB)]
    made, setup_ps, setup_sb, q_put = sem("p_made"), sem("p_setup_ps"), sem("p_setup_sb"), sem("p_q_put")
    key_turned, key_kept = ([sem(f"p_{n}{x}") for x in range(2)] for n in ("key_turned", "key_kept"))
    scored, fresh_scored, masked, max_parts, maxed, expd, summed, inverse, weight, weighted, map_turned, map_kept, multiplied, out_kept, out_turned, out_added = (
        sem("p_" + n) for n in ("scored fresh_scored masked max_parts maxed expd summed inverse weight weighted map_turned "
                                "map_kept multiplied out_kept out_turned out_added").split())

    pool_k = i["cache_k"][0].rearrange("n p h d -> n p (h d)")
    pool_v = i["cache_v"][0].rearrange("n p h d -> n p (h d)")
    n_pool = i["cache_k"].shape[1]

    def load(queue, dst, src, b, signal):
        for j in range(NPG):
            page = queue.value_load(c["pages"][0:1, b * NPG + j:b * NPG + j + 1], min_val=0, max_val=n_pool - 1)
            queue.dma_start(dst[:, j, :], src[bass.ds(page, 1)].rearrange("o p w -> (o p) w")).then_inc(signal, 16)

    with nc.Block() as block:
        @block.sync
        def _(sp):
            sp.dma_start(v_new[:, :], o["v_sample"].rearrange("a b l h d -> (a b l) (h d)")).then_inc(vn_in, 16)
            for b in range(NB):
                if b >= NK:
                    sp.wait_ge(key_turned[1], b - NK + 1)
                load(sp, key_in[b % NK], pool_k, b, k_in[b % NK])

        @block.gpsimd
        def _(pool):
            for t in (q_pad[0][:, :], q_pad[1][:, :], maskT[:, :, :]):
                pool.memset(t, 0.0).then_inc(made, 1)
            pool.wait_ge(made, 3)
            for t in range(NBT):
                for x in range(2):
                    lo = x * HALF
                    dst = q_pad[t][lo:lo + HALF, :].rearrange("p (h r) -> p h r", h=H)[:, :, 0:P].rearrange(
                        "p h (s r) -> p h s r", s=SB)[:, :, :, x * NL:(x + 1) * NL]
                    src = feat[lo:lo + HALF, 3 * H:4 * H, SEQ + t * SB * NL:SEQ + (t + 1) * SB * NL]
                    ins = nc.gpsimd.tensor_copy(dst, src.rearrange("p h (s l) -> p h s l", s=SB))
                ins.then_inc(q_put, 1)
            v = maskT[:, :, :].rearrange("p t (s g l) -> p (t s) g l", s=SB, l=NL)
            pool.affine_select(out=v, in_=v, compare_op=ALU.is_ge, fill=NEG, base=0,
                               pattern=[[-NL, NB], [0, NR // NL], [0, NL]], channel_multiplier=1).then_inc(made, 1)
            pool.wait_ge(made, 4)
            pool.affine_select(out=v, in_=v, compare_op=ALU.is_ge, fill=NEG, base=0,
                               pattern=[[NL, NB], [0, NR // NL], [1, NL]], channel_multiplier=-1).then_inc(made, 1)
            rows = sign_row[:, :].rearrange("p (a x l) -> p a x l", x=2, l=NL)
            pool.memset(rows[:, :, 0, :], 1.0).then_inc(made, 1)
            nc.gpsimd.tensor_copy(rows[:, :, 1, :], over(c["neglam"][0:1, 0:1], 2, [1, P // RW, NL])).then_inc(made, 1)
            for b in range(NB):
                load(pool, val_in[b], pool_v, b, v_in[b])

        @block.tensor
        def _(pe):
            pe.wait_ge(made, 7)
            for t in range(NBT):
                nc.tensor.transpose(fresh_ps[1][:, t * NS:(t + 1) * NS], maskT[:, t, :], c["ident"][0:NS, 0:NS])
            nc.tensor.matmul(fresh_ps[0][:, 0:1], sign_row[:, :], c["ones"][0:1, 0:1], start=True, stop=True).then_inc(setup_ps, 1)

            def turn_keys(b):
                s = b % NK
                pe.wait_ge(k_in[s], NPG * 16 * (b // NK + 1))
                for x in range(2):
                    if b:
                        pe.wait_ge(key_kept[x], b)
                    for h in (2 * x, 2 * x + 1):
                        for j in range(NPG):
                            mm = nc.tensor.transpose(key_ps[:, h, j * PAGE:(j + 1) * PAGE], key_in[s][:, j, h * DH:(h + 1) * DH],
                                                     c["ident"][:, :])
                    mm.then_inc(key_turned[x], 1)

            def score_keys(b):
                t, r = b // SB, (b % SB) * NR
                for x in range(2):
                    pe.wait_ge(key_kept[x], b + 1)
                pe.wait_ge(q_put, t + 1)
                for h in range(H):
                    mm = nc.tensor.matmul(score[t][r:r + NR, :], q_pad[t][:, h * P + r:h * P + r + NR], keyT[b % 2][:, h, :],
                                          start=(h == 0), stop=(h == H - 1))
                mm.then_inc(scored, 1)

            def score_fresh(t):
                pe.wait_ge(setup_sb, 2)
                for h in range(H):
                    mm = nc.tensor.matmul(fresh_ps[t][:, 0:NS], q_pad[t][:, h * P:(h + 1) * P], feat[:, 4 * H + h, SEQ:T],
                                          start=(h == 0), stop=(h == H - 1))
                mm.then_inc(fresh_scored, 1)

            def turn_map(t):
                pe.wait_ge(weighted, t + 1)
                for j in range(NPG):
                    nc.tensor.transpose(score[t][:, j * P:(j + 1) * P], e[t][:, j * PAGE:(j + 1) * PAGE], c["ident"][:, :])
                nc.tensor.transpose(fresh_ps[t][0:NS, 0:P], e[t][:, PAST:PAST + NS], c["ident"][:, :]).then_inc(map_turned, 1)

            def multiply(b):
                t, s = b // SB, b % SB
                pe.wait_ge(map_kept, t + 1)
                pe.wait_ge(v_in[b], NPG * 16)
                at = slice(s * NR, (s + 1) * NR)
                for j in range(NPG):
                    nc.tensor.matmul(score[t][at, :], mapT[:, j, at], val_in[b][:, j, :], start=(j == 0), stop=False)
                mm = nc.tensor.matmul(score[t][at, :], mapT_new[:, at], v_new[:, :], start=False, stop=True)
                mm.then_inc(multiplied, 1)

            def turn_out(t):
                pe.wait_ge(out_kept, t + 1)
                for h in range(H):
                    mm = nc.tensor.transpose(fresh_ps[t][:, h * P:(h + 1) * P], out_rows[t][:, h * DH:(h + 1) * DH], c["ident"][:, :])
                mm.then_inc(out_turned, 1)

            turn_keys(0)
            for b in range(NB):
                if b + 1 < NB:
                    turn_keys(b + 1)
                score_keys(b)
                if b % SB == SB - 1:
                    score_fresh(b // SB)
                if b == SB + 1:
                    turn_map(0)
                    pe.wait_ge(vn_in, 16)
                if b >= SB + 2:
                    multiply(2 * (b - SB - 2))
                    multiply(2 * (b - SB - 2) + 1)
            turn_map(1)
            turn_out(0)
            for b in range(SB, NB):
                multiply(b)
            turn_out(1)

        @block.scalar
        def _(act):
            nc.scalar.preload_act_table(ACT.Exp)

            def exps(t):
                act.wait_ge(maxed, t + 1)
                nc.scalar.activation(e[t][:, 0:PAST], score[t][:, :], ACT.Exp, bias=stat[t][:, 2:3], scale=1.0,
                                     accum_out=stat[t][:, 3:4])
                nc.scalar.activation(e[t][:, PAST:PAST + NS], fresh[t][:, :], ACT.Exp, bias=stat[t][:, 2:3], scale=1.0,
                                     accum_out=stat[t][:, 4:5]).then_inc(expd, 1)

            for b in range(NB):
                act.wait_ge(key_turned[0], b + 1)
                if b >= 2:
                    act.wait_ge(scored, b - 1)
                nc.scalar.copy(keyT[b % 2][:, 0:2, :], key_ps[:, 0:2, :]).then_inc(key_kept[0], 1)
                if b == SB:
                    exps(0)
            exps(1)
            for t in range(NBT):
                act.wait_ge(multiplied, (t + 1) * SB)
                nc.scalar.copy(out_rows[t], score[t][:, :]).then_inc(out_kept, 1)

        @block.vector
        def _(dve):
            dve.wait_ge(setup_ps, 1)
            nc.vector.tensor_copy(mask[:, :, :].rearrange("p t k -> p (t k)"), fresh_ps[1][:, 0:NBT * NS]).then_inc(setup_sb, 1)
            nc.vector.tensor_copy(sign[:, :], fresh_ps[0][:, 0:1]).then_inc(setup_sb, 1)

            def maxes(t):
                dve.wait_ge(fresh_scored, t + 1)
                nc.vector.tensor_tensor(fresh[t][:, :], fresh_ps[t][:, 0:NS], mask[:, t, :], ALU.add).then_inc(masked, 1)
                nc.vector.tensor_reduce(out=stat[t][:, 0:1], in_=score[t][:, :], axis=AX.X, op=ALU.max)
                dve.wait_ge(masked, t + 1)
                nc.vector.tensor_reduce(out=stat[t][:, 1:2], in_=fresh[t][:, :], axis=AX.X, op=ALU.max).then_inc(max_parts, 1)
                dve.wait_ge(max_parts, t + 1)
                nc.vector.tensor_reduce(out=stat[t][:, 2:3], in_=stat[t][:, 0:2], axis=AX.X, op=ALU.max, negate=True).then_inc(maxed, 1)

            def weigh(t):
                dve.wait_ge(expd, t + 1)
                nc.vector.tensor_tensor(stat[t][:, 5:6], stat[t][:, 3:4], stat[t][:, 4:5], ALU.add).then_inc(summed, 1)
                dve.wait_ge(summed, t + 1)
                nc.vector.reciprocal(stat[t][:, 6:7], stat[t][:, 5:6]).then_inc(inverse, 1)
                dve.wait_ge(inverse, t + 1)
                nc.vector.tensor_tensor(stat[t][:, 7:8], stat[t][:, 6:7], sign[:, :], ALU.mult).then_inc(weight, 1)
                dve.wait_ge(weight, t + 1)
                nc.vector.tensor_scalar(e[t][:, :], e[t][:, :], stat[t][:, 7:8], None, ALU.mult).then_inc(weighted, 1)

            def keep_map(t):
                dve.wait_ge(map_turned, t + 1)
                nc.vector.tensor_copy(mapT[:, :, :].rearrange("p j r -> p (j r)"), score[t][:, :])
                nc.vector.tensor_copy(mapT_new[:, :], fresh_ps[t][0:NS, 0:P]).then_inc(map_kept, 1)

            def add_rows(t):
                dve.wait_ge(out_turned, t + 1)
                for h in range(H):
                    own = fresh_ps[t][:, h * P:(h + 1) * P].rearrange("p (s a x l) -> p s a l x", s=SB, x=2, l=NL)[:, :, h]
                    dst = head_out[:, H + h, SEQ + t * SB * NL:SEQ + (t + 1) * SB * NL].rearrange("p (s l) -> p s l", l=NL)
                    nc.vector.tensor_reduce(out=dst, in_=own, axis=AX.X, op=ALU.add).then_inc(out_added, 1)

            for b in range(NB):
                dve.wait_ge(key_turned[1], b + 1)
                if b >= 2:
                    dve.wait_ge(scored, b - 1)
                nc.vector.tensor_copy(keyT[b % 2][:, 2:4, :], key_ps[:, 2:4, :]).then_inc(key_kept[1], 1)
                if b == SB:
                    maxes(0)
                if b == SB + 1:
                    weigh(0)
                if b == SB + 2:
                    keep_map(0)
            maxes(1)
            weigh(1)
            keep_map(1)
            add_rows(0)
            add_rows(1)
    m.free()


def head_gate(nc, c, hT, zT, head_out, hi, lo, x_scratch, z_scratch, sem):
    m = Memory(nc)
    psum = [m.ps(f"o_scale{s}", [P, NG, 512]) for s in range(2)]
    spread_done, normed, gated, hi_done, lo_done, x_in, z_in = (
        sem(f"o_{x}") for x in ("spread", "normed", "gated", "hi", "lo", "x_in", "z_in"))
    n_pool, n_act, n_pe, n_dve, spread = head_scales(
        nc, m, sem, "o", [(head_out[:, t, :], False, t) for t in range(2 * H)], psum[1], ((2 * H, DH * EPS),))

    with nc.Block() as block:
        @block.sync
        def _(sp):
            sp.dma_start(zT, z_scratch).then_inc(z_in, 16)
            sp.dma_start(hT, x_scratch).then_inc(x_in, 16)
            sp.wait_ge(x_in, 16)

        @block.gpsimd
        def _(pool):
            n_pool(pool)

        @block.scalar
        def _(act):
            n_act(act)
            for t in range(2 * H):
                if t < H:
                    act.wait_ge(gated, t + 1)
                else:
                    act.wait_ge(normed, t + 1)
                nc.scalar.copy(hi[:, t, :], head_out[:, t, :]).then_inc(hi_done, 1)

        @block.tensor
        def _(pe):
            n_pe(pe)
            for t in range(2 * H):
                if t >= 2:
                    pe.wait_ge(normed, t - 1)
                spread(pe, t, psum[t % 2]).then_inc(spread_done, 1)

        @block.vector
        def _(dve):
            def low(t):
                dve.wait_ge(hi_done, t + 1)
                nc.vector.tensor_tensor(lo[:, t, :], head_out[:, t, :], r32(hi[:, t, :]), ALU.subtract).then_inc(lo_done, 1)

            n_dve(dve)
            dve.wait_ge(z_in, 16)
            for t in range(2 * H):
                dve.wait_ge(spread_done, t + 1)
                x = head_out[:, t, :].rearrange("p (g t) -> p g t", g=NG)
                nc.vector.scalar_tensor_tensor(out=x, in0=x, scalar=c["gain"][:, t // H:t // H + 1], in1=psum[t % 2][:, :, 0:TG],
                                               op0=ALU.mult, op1=ALU.mult).then_inc(normed, 1)
                if t < H:
                    dve.wait_ge(normed, t + 1)
                    nc.vector.tensor_tensor(head_out[:, t, :], head_out[:, t, :], zT[:, t, :], ALU.mult).then_inc(gated, 1)
                if t >= 1:
                    low(t - 1)
            low(2 * H - 1)
    m.free()


def output_projection(nc, i, hT, x_hi, x_lo, sumsq, sem):
    m = Memory(nc)
    raw = [m.sb(f"wo_raw{s}", [P, KT, P]) for s in range(2)]
    w_hi = [m.sb(f"wo_hi{s}", [P, KT, P], F32R) for s in range(2)]
    w_lo = [m.sb(f"wo_lo{s}", [P, KT, P], F32R) for s in range(2)]
    psum = [m.ps(f"wo_ps{s}", [P, NG, 512]) for s in range(2)]
    square = [m.sb(f"wo_square{s}", [P, T]) for s in range(2)]
    sum_zero, squared, gathered = sem("wo_sum_zero"), sem("wo_squared"), sem("wo_gathered")
    loaded = [sem(f"wo_loaded{s}") for s in range(2)]
    split_hi, split_lo, projected, added = (sem(f"wo_{x}") for x in ("split_hi", "split_lo", "projected", "added"))
    w = i["w_out"][0].rearrange("(k p) n -> p k n", p=P)

    with nc.Block() as block:
        @block.sync
        def _(sp):
            sp.dma_start(raw[0][:, :, :], w[:, :, 0:P]).then_inc(loaded[0], 16)
            sp.dma_start(raw[1][:, :, :], w[:, :, P:2 * P]).then_inc(loaded[1], 16)
            with sp.Fori(1, KT // 2) as it:
                for s in range(2):
                    sp.wait_ge(split_lo, done(2 * it + s - 2))
                    sp.dma_start(raw[s][:, :, :], w[:, :, bass.ds(it * (2 * P) + s * P, P)]).then_inc(loaded[s], 16)

        @block.scalar
        def _(act):
            act.sem_inc(split_hi, CREDIT)
            act.sem_inc(squared, CREDIT)

            def high(n, s):
                act.wait_ge(loaded[s], 8 * (n - s) + 16)
                act.wait_ge(projected, done(n - 2))
                nc.scalar.copy(w_hi[s][:, :, :], raw[s][:, :, :]).then_inc(split_hi, 1)

            def square_of(n, s):
                act.wait_ge(added, done(n))
                act.wait_ge(gathered, done(n - 2))
                nc.scalar.activation(square[s][:, :], hT[:, bass.ds(n, 1), :].rearrange("p o t -> p (o t)"), ACT.Square
                                     ).then_inc(squared, 1)

            high(0, 0)
            high(1, 1)
            with act.Fori(0, KT // 2 - 1) as it:
                for s in range(2):
                    square_of(2 * it + s, s)
                    high(2 * it + (s + 2), s)
            square_of(KT - 2, 0)
            square_of(KT - 1, 1)

        @block.gpsimd
        def _(pool):
            pool.memset(sumsq, 0.0).then_inc(sum_zero, 1)

        @block.tensor
        def _(pe):
            pe.sem_inc(projected, CREDIT)
            with pe.Fori(0, KT // 2) as it:
                for s in range(2):
                    pe.wait_ge(split_lo, done(2 * it + s))
                    pe.wait_ge(added, done(2 * it + s - 2))
                    project_tile(nc, psum[s], w_hi[s], w_lo[s], x_hi, x_lo).then_inc(projected, 1)

        @block.vector
        def _(dve):
            dve.sem_inc(split_lo, CREDIT)
            dve.sem_inc(added, CREDIT)

            def low(n, s):
                dve.wait_ge(split_hi, done(n))
                nc.vector.tensor_tensor(w_lo[s][:, :, :], raw[s][:, :, :], r32(w_hi[s][:, :, :]), ALU.subtract
                                        ).then_inc(split_lo, 1)

            def add(n, s):
                dve.wait_ge(projected, done(n))
                h = hT[:, bass.ds(n, 1), :].rearrange("p o (g t) -> p (o g) t", g=NG)
                nc.vector.tensor_tensor(h, psum[s][:, :, 0:TG], h, ALU.add).then_inc(added, 1)

            def gather(n, s):
                dve.wait_ge(squared, done(n))
                dve.wait_ge(gathered, done(n - 1))
                nc.vector.tensor_tensor(sumsq, sumsq, square[s][:, :], ALU.add).then_inc(gathered, 1)

            dve.sem_inc(gathered, CREDIT)
            low(0, 0)
            low(1, 1)
            dve.wait_ge(sum_zero, 1)
            with dve.Fori(0, KT // 2 - 1) as it:
                for s in range(2):
                    add(2 * it + s, s)
                    low(2 * it + (s + 2), s)
                    gather(2 * it + s, s)
            for s in range(2):
                add(KT - 2 + s, s)
            for s in range(2):
                gather(KT - 2 + s, s)
    m.free()


def gated_mlp(nc, i, o, c, feat, hT, x_hi, x_lo, sumsq, sem):
    m = Memory(nc)
    w_hi = [m.sb(f"up_hi{s}", [P, KT, P], F32R) for s in range(2)]
    w_lo = [m.sb(f"up_lo{s}", [P, KT, P], F32R) for s in range(2)]
    d_hi, d_lo = m.sb("dn_hi", [P, 2, D], F32R), m.sb("dn_lo", [P, 2, D], F32R)
    spare = feat[:, 0:3 * H, :].rearrange("p a t -> p (a t)")
    pre = [spare[:, s * F_BUF:(s + 1) * F_BUF] for s in range(2)]
    acc = [spare[:, (2 + s) * F_BUF:(3 + s) * F_BUF] for s in range(2)]
    prod = spare[:, 4 * F_BUF:4 * F_BUF + T]
    NRW = NB * F_PAD + CF + 1
    at = 4 * F_BUF + T
    col = spare[:, at:at + 2 * FT * NRW].rearrange("p (j r) -> p j r", r=NRW)
    at += 2 * FT * NRW
    tail = spare[:, at:at + 2 * FT * F_TAIL].rearrange("p (j r) -> p j r", r=F_TAIL)
    at += 2 * FT * F_TAIL
    raw = []
    for s in range(2):
        raw.append(spare[:, at:at + D].rearrange("p (k f) -> p k f", k=KT))
        at += D
    raw_d = spare[:, at:at + 2 * D].rearrange("p (x d) -> p x d", x=2)
    at += 2 * D
    Q = 11
    rows = spare[0:NRW, at:at + Q * P]
    tail_tok = spare[0:F_TAIL, at - 4 * D:at - 4 * D + 2 * FF]
    y = [spare[:, s * (NT + 1) * P:(s + 1) * (NT + 1) * P].rearrange("p (n d) -> p n d", d=P) for s in range(2)]
    g_hi, g_lo = m.sb("f_g_hi", [P, 2, T], F32R), m.sb("f_g_lo", [P, 2, T], F32R)
    psum = [m.ps(f"f_up{s}", [P, NG, 512]) for s in range(2)]
    root = prod
    value = [pre[s][:, F_PAD:F_PAD + T] for s in range(2)]
    down = [m.ps(f"f_down{s}", [P, 512]) for s in range(2)]

    loaded = [sem(f"up_loaded{s}") for s in range(2)]
    d_loaded, rows_in, rows_turned, rows_kept = sem("dn_loaded"), sem("f_rows_in"), sem("f_rows_turned"), sem("f_rows_kept")
    pads, state_put, tail_kept = sem("f_pads"), sem("f_state_put"), sem("f_tail_kept")
    split_hi, split_lo = sem("up_split_hi"), sem("up_split_lo")
    projected, evacuated, tap0, tap1, taps = (sem(f"f_{x}") for x in ("projected", "evacuated", "tap0", "tap1", "taps"))
    activated, gated, gate_hi, gate_lo = (sem(f"f_{x}") for x in ("activated", "gated", "gate_hi", "gate_lo"))
    d_split_hi, d_split_lo, partial, summed = (sem(f"dn_{x}") for x in ("split_hi", "split_lo", "partial", "summed"))
    tail_turned, tail_rows, tail_out = sem("f_tail_turned"), sem("f_tail_rows"), sem("f_tail_out")
    totalled, root_done, inverted, value_done, hi_done, lo_done = (
        sem(f"hn_{x}") for x in ("totalled", "root", "inverted", "value", "hi", "lo"))
    y_turned, y_kept, y_out = sem("y_turned"), sem("y_kept"), [sem(f"y_out{s}") for s in range(2)]

    w = i["w_up"][0].rearrange("(k p) n -> p k n", p=P)
    w_d = i["w_down"][0]
    NU = KT * NG
    NTG = 2 * FT // 4

    with nc.Block() as block:
        @block.sync
        def _(sp):
            sp.dma_start(raw[0], w[:, :, 0:P]).then_inc(loaded[0], 16)
            sp.dma_start(raw[1], w[:, :, FF:FF + P]).then_inc(loaded[1], 16)
            for q in range(4):
                if q:
                    sp.wait_ge(rows_turned, q)
                a, b = q * Q * P, (q + 1) * Q * P
                sp.dma_start(rows[0:NB * F_PAD, :], i["state_ffn_conv"][0].rearrange("b r w -> (b r) w")[:, a:b]).then_inc(rows_in, 16)
                sp.dma_start(rows[NB * F_PAD:NB * F_PAD + CF, :], i["ffn_conv_w"][0, :, a:b]).then_inc(rows_in, 16)
                sp.dma_start(rows[NB * F_PAD + CF:NRW, :], i["ffn_conv_b"][:, a:b]).then_inc(rows_in, 16)
            sp.dma_start(raw_d, w_d[0:2 * P, :].rearrange("(x p) d -> p x d", x=2)).then_inc(d_loaded, 16)

            def load_pair(p):
                for s in range(2):
                    sp.wait_ge(split_lo, done(2 * p + s - 2))
                    sp.dma_start(raw[s], w[:, :, bass.ds(p * P + s * FF, P)]).then_inc(loaded[s], 16)

            load_pair(1)
            with sp.Fori(1, FT // 2) as it:
                sp.wait_ge(d_split_lo, it)
                sp.dma_start(raw_d, w_d[bass.ds(it * (2 * P), 2 * P), :].rearrange("(x p) d -> p x d", x=2)).then_inc(d_loaded, 16)
                load_pair(2 * it)
                load_pair(2 * it + 1)
            sp.wait_ge(tail_rows, NTG)
            sp.dma_start(o["ffn_conv_prompt"].rearrange("a b r w -> (a b r) w"), tail_tok[0:F_PAD, :]).then_inc(tail_out, 16)
            sp.dma_start(o["ffn_conv_sample"].rearrange("a b r w -> (a b r) w"), tail_tok[F_PAD:F_TAIL, :]).then_inc(tail_out, 16)
            for t in range(KT):
                sp.wait_ge(y_kept, t + 1)
                cols = slice(t * P, (t + 1) * P)
                sp.dma_start(o["y_prompt"].rearrange("a (n p) d -> p (a n) d", p=P)[:, :, cols], y[t % 2][:, 0:NT, :]
                             ).then_inc(y_out[t % 2], 16)
                sp.dma_start(o["y_sample"].rearrange("b l d -> (b l) d")[:, cols], y[t % 2][0:NS, NT, :]).then_inc(y_out[t % 2], 16)
            sp.wait_ge(tail_out, 32)
            for s in range(2):
                sp.wait_ge(y_out[s], 32 * KT // 2)

        @block.gpsimd
        def _(pool):
            pool.sem_inc(state_put, CREDIT)
            pool.sem_inc(tail_kept, CREDIT)
            for s in range(2):
                pool.memset(pre[s][:, 0:F_PAD], 0.0).then_inc(pads, 1)
            pool.wait_ge(rows_kept, 4)
            with pool.Fori(0, FT) as it:
                for s in range(2):
                    n, j = 2 * it + s, it + s * FT
                    pool.wait_ge(taps, done(n - 2))
                    nc.gpsimd.tensor_copy(samples(pre[s], F_SAMPLE, F_PAD, 0, F_PAD),
                                          col[:, bass.ds(j, 1), 0:NB * F_PAD].rearrange("p o (b r) -> p (o b) r", r=F_PAD)
                                          ).then_inc(state_put, 1)
                for s in range(2):
                    n, j = 2 * it + s, it + s * FT
                    pool.wait_ge(evacuated, done(n))
                    nc.gpsimd.tensor_copy(tail[:, bass.ds(j, 1), 0:F_PAD], pre[s][:, SEQ:SEQ + F_PAD].unsqueeze(1))
                    nc.gpsimd.tensor_copy(tail[:, bass.ds(j, 1), F_PAD:F_TAIL].rearrange("p o (b r) -> p (o b) r", r=F_PAD),
                                          samples(pre[s], F_SAMPLE, F_PAD, NL, F_PAD)).then_inc(tail_kept, 1)

        @block.scalar
        def _(act):
            act.sem_inc(split_hi, CREDIT)
            act.sem_inc(evacuated, CREDIT)
            act.sem_inc(tap0, CREDIT)
            nc.scalar.preload_act_table(ACT.Sqrt)

            def high(n, turn, s):
                act.wait_ge(loaded[s], 16 * turn + 16)
                act.wait_ge(projected, done(n - 2))
                nc.scalar.copy(w_hi[s][:, :, :], raw[s]).then_inc(split_hi, 1)

            def drain(p, s):
                n = 2 * p + s
                act.wait_ge(projected, done(n))
                act.wait_ge(taps, done(n - 2))
                act.wait_ge(tail_kept, done(n - 2))
                nc.scalar.copy(pre[s][:, F_PAD:F_PAD + 2 * TG].rearrange("p (g t) -> p g t", g=2), psum[s][:, 0:2, 0:TG])
                nc.scalar.copy(pre[s][:, F_PAD + 2 * TG:F_SAMPLE], psum[s][:, 2, 0:TG - NS])
                nc.scalar.copy(samples(pre[s], F_SAMPLE, F_PAD, F_PAD, NL),
                               psum[s][:, 2, TG - NS:TG].rearrange("p (b l) -> p b l", b=NB)).then_inc(evacuated, 1)

            def first_tap(p, s):
                n, j = 2 * p + s, p + s * FT
                act.wait_ge(evacuated, done(n))
                act.wait_ge(state_put, done(n))
                act.wait_ge(gated, p + 1)
                nc.scalar.activation(
                    acc[s][:, 0:F_OUT], pre[s][:, 0:F_OUT], ACT.Identity,
                    scale=col[:, bass.ds(j, 1), NB * F_PAD:NB * F_PAD + 1].rearrange("p o r -> p (o r)"),
                    bias=col[:, bass.ds(j, 1), NRW - 1:NRW].rearrange("p o r -> p (o r)")).then_inc(tap0, 1)

            def pair(p, last=False):
                drain(p, 0)
                if not last:
                    high(2 * p + 2, p + 1, 0)
                first_tap(p, 0)
                act.wait_ge(taps, done(2 * p))
                nc.scalar.activation(acc[0][:, 0:F_OUT], acc[0][:, 0:F_OUT], ACT.Silu).then_inc(activated, 1)
                drain(p, 1)
                if not last:
                    high(2 * p + 3, p + 1, 1)
                first_tap(p, 1)

            def gate_high(p, x):
                act.wait_ge(gated, p + 2)
                nc.scalar.copy(g_hi[:, x, :], prod).then_inc(gate_hi, 1)

            def turn(it, last=False):
                pair(2 * it)
                act.wait_ge(d_loaded, 16 * it + 16)
                act.wait_ge(partial, NU * it + 1)
                nc.scalar.copy(d_hi[:, :, :], raw_d).then_inc(d_split_hi, 1)
                gate_high(2 * it, 0)
                pair(2 * it + 1, last)
                gate_high(2 * it + 1, 1)

            high(0, 0, 0)
            high(1, 0, 1)
            act.wait_ge(totalled, 1)
            nc.scalar.activation(root.rearrange("p (g t) -> p g t", g=NG), psum[1][:, :, 0:TG], ACT.Sqrt, bias=c["eps"][:, :],
                                 scale=1.0).then_inc(root_done, 1)
            for k in range(KT):
                act.wait_ge(value_done, k + 1)
                nc.scalar.copy(x_hi[:, k, :], value[k % 2]).then_inc(hi_done, 1)
            nc.scalar.preload_act_table(ACT.Silu)
            act.wait_ge(pads, 2)
            with act.Fori(0, FT // 2 - 1) as it:
                turn(it)
            turn(FT // 2 - 1, last=True)
            for q in range(NTG):
                act.wait_ge(tail_turned, q + 1)
                nc.scalar.copy(tail_tok[:, q * 4 * P:(q + 1) * 4 * P], psum[q % 2][0:F_TAIL, q // 2 % NG, :]).then_inc(tail_rows, 1)
            for t in range(KT):
                act.wait_ge(y_turned, t + 1)
                if t >= 2:
                    act.wait_ge(y_out[t % 2], 32 * (t // 2))
                turned = psum[t % 2][:, :, :].rearrange("p g (n d) -> p (g n) d", d=P)
                nc.scalar.copy(y[t % 2][:, 0:NT, :], turned[:, 0:NT, :])
                nc.scalar.copy(y[t % 2][0:NS, NT, :], turned[0:NS, NT, :]).then_inc(y_kept, 1)

        @block.vector
        def _(dve):
            for x in (split_lo, taps, tap1):
                dve.sem_inc(x, CREDIT)
            dve.sem_inc(gate_lo, 1)
            dve.sem_inc(gated, 1)
            dve.sem_inc(summed, 2)

            def low(n, s):
                dve.wait_ge(split_hi, done(n))
                nc.vector.tensor_tensor(w_lo[s][:, :, :], raw[s], r32(w_hi[s][:, :, :]), ALU.subtract
                                        ).then_inc(split_lo, 1)

            def tap(p, s, t):
                n, j = 2 * p + s, p + s * FT
                dve.wait_ge(tap0 if t == 1 else tap1, done(n))
                nc.vector.scalar_tensor_tensor(
                    out=acc[s][:, 0:F_OUT], in0=pre[s][:, t:t + F_OUT],
                    scalar=col[:, bass.ds(j, 1), NB * F_PAD + t:NB * F_PAD + t + 1].rearrange("p o r -> p (o r)"),
                    in1=acc[s][:, 0:F_OUT], op0=ALU.mult, op1=ALU.add).then_inc(tap1 if t == 1 else taps, 1)

            def add_partials(it, u0, u1):
                for u in range(u0, u1):
                    dve.wait_ge(partial, NU * it + (u + 2))
                    h = hT[:, u // NG, (u % NG) * TG:(u % NG + 1) * TG]
                    nc.vector.tensor_tensor(h, down[u % 2][:, 0:TG], h, ALU.add).then_inc(summed, 1)

            def gate(p):
                dve.wait_ge(activated, p + 1)
                dve.wait_ge(taps, done(2 * p + 1))
                dve.wait_ge(gate_lo, p + 1)
                nc.vector.tensor_tensor(prod[:, 0:SEQ], acc[0][:, 0:SEQ], acc[1][:, 0:SEQ], ALU.mult)
                nc.vector.tensor_tensor(prod[:, SEQ:T].rearrange("p (b l) -> p b l", b=NB), samples(acc[0], F_SAMPLE, F_PAD, 0, NL),
                                        samples(acc[1], F_SAMPLE, F_PAD, 0, NL), ALU.mult).then_inc(gated, 1)

            def gate_low(p, x):
                dve.wait_ge(gate_hi, p + 1)
                nc.vector.tensor_tensor(g_lo[:, x, :], prod, r32(g_hi[:, x, :]), ALU.subtract).then_inc(gate_lo, 1)

            def turn(it, before=None, last=False):
                add = (lambda u0, u1: add_partials(before, u0, u1)) if before is not None else (lambda u0, u1: None)
                a, b = 2 * it, 2 * it + 1
                tap(a, 0, 1)
                tap(a, 0, 2)
                low(2 * a + 2, 0)
                add(0, 4)
                tap(a, 1, 1)
                add(4, 6)
                tap(a, 1, 2)
                add(6, 8)
                low(2 * a + 3, 1)
                add(8, 10)
                gate(a)
                add(10, NU)
                gate_low(a, 0)
                dve.wait_ge(d_split_hi, it + 1)
                nc.vector.tensor_tensor(d_lo[:, :, :], raw_d, r32(d_hi[:, :, :]), ALU.subtract).then_inc(d_split_lo, 1)
                tap(b, 0, 1)
                tap(b, 0, 2)
                if not last:
                    low(2 * b + 2, 0)
                tap(b, 1, 1)
                tap(b, 1, 2)
                if not last:
                    low(2 * b + 3, 1)
                gate(b)
                gate_low(b, 1)

            def keep_rows(q):
                dve.wait_ge(rows_turned, q + 1)
                nc.vector.tensor_copy(col[:, q * Q:(q + 1) * Q, :].rearrange("p j r -> p (j r)"),
                                      down[q % 2][:, 0:Q * NRW]).then_inc(rows_kept, 1)

            def norm_low(k):
                dve.wait_ge(hi_done, k + 1)
                nc.vector.tensor_tensor(x_lo[:, k, :], value[k % 2], r32(x_hi[:, k, :]), ALU.subtract).then_inc(lo_done, 1)

            low(0, 0)
            low(1, 1)
            dve.wait_ge(root_done, 1)
            nc.vector.reciprocal(root, root).then_inc(inverted, 1)
            dve.wait_ge(inverted, 1)
            for k in range(KT):
                if k >= 2:
                    dve.wait_ge(lo_done, k - 1)
                nc.vector.scalar_tensor_tensor(out=value[k % 2], in0=hT[:, k, :], scalar=c["cols"][:, KT + k:KT + k + 1],
                                               in1=root, op0=ALU.mult, op1=ALU.mult).then_inc(value_done, 1)
                if k >= 1:
                    norm_low(k - 1)
            norm_low(KT - 1)
            for q in range(4):
                keep_rows(q)
            dve.wait_ge(rows_kept, 4)
            turn(0)
            with dve.Fori(1, FT // 2 - 1) as it:
                turn(it, it - 1)
            turn(FT // 2 - 1, FT // 2 - 2, last=True)
            add_partials(FT // 2 - 1, 0, NU)

        @block.tensor
        def _(pe):
            pe.sem_inc(projected, CREDIT)
            pe.sem_inc(partial, 1)
            def turn_rows(q):
                pe.wait_ge(rows_in, 48 * (q + 1))
                if q >= 2:
                    pe.wait_ge(rows_kept, q - 1)
                for j in range(Q):
                    mm = nc.tensor.transpose(down[q % 2][:, j * NRW:(j + 1) * NRW], rows[:, j * P:(j + 1) * P],
                                             c["ident"][0:NRW, 0:NRW])
                mm.then_inc(rows_turned, 1)

            def up_tile(n, s, before=None):
                pe.wait_ge(split_lo, done(n))
                pe.wait_ge(evacuated, done(n - 2))
                project_tile(nc, psum[s], w_hi[s], w_lo[s], x_hi, x_lo, before=before).then_inc(projected, 1)

            def up(p):
                for s in range(2):
                    up_tile(2 * p + s, s)

            def down_product(it, u0=0, u1=NU):
                pe.wait_ge(d_split_lo, it + 1)
                pe.wait_ge(gate_lo, 2 * it + 3)
                for u in range(u0, u1):
                    t, g = u // NG, u % NG
                    pe.wait_ge(summed, NU * it + (u + 1))
                    for k, (a, b) in enumerate(((d_hi, g_hi), (d_hi, g_lo), (d_lo, g_hi))):
                        for x in range(2):
                            mm = nc.tensor.matmul(down[u % 2][:, 0:TG], a[:, x, t * P:(t + 1) * P], b[:, x, g * TG:(g + 1) * TG],
                                                  start=(k + x == 0), stop=(k == 2 and x == 1))
                    mm.then_inc(partial, 1)

            for g in range(NG):
                mm = nc.tensor.matmul(psum[1][:, g, 0:TG], c["ones"][:, :], sumsq[:, g * TG:(g + 1) * TG], start=True, stop=True)
            mm.then_inc(totalled, 1)
            turn_rows(0)
            turn_rows(1)
            up_tile(0, 0, before=lambda k: pe.wait_ge(lo_done, k + 1))
            turn_rows(2)
            turn_rows(3)
            up_tile(1, 1)
            up(1)
            with pe.Fori(1, FT // 2) as it:
                up(2 * it)
                down_product(it - 1)
                up(2 * it + 1)

            def turn_tails(q0, q1):
                for q in range(q0, q1):
                    if q >= 2 * NG:
                        pe.wait_ge(tail_rows, q - 2 * NG + 1)
                    for j in range(4):
                        mm = nc.tensor.transpose(psum[q % 2][0:F_TAIL, q // 2 % NG, j * P:(j + 1) * P], tail[:, 4 * q + j, :],
                                                 c["ident"][:, :])
                    mm.then_inc(tail_turned, 1)

            last = FT // 2 - 1

            def turn_y(t):
                pe.wait_ge(summed, NU * last + NG * (t + 1) + 2)
                if t >= 2:
                    pe.wait_ge(y_kept, t - 1)
                for n in range(NT + 1):
                    rows_n = P if n < NT else NS
                    mm = nc.tensor.transpose(psum[t % 2][0:rows_n, n // 4, (n % 4) * P:(n % 4 + 1) * P],
                                             hT[:, t, n * P:n * P + rows_n], c["ident"][:, :])
                mm.then_inc(y_turned, 1)

            pe.wait_ge(tail_kept, done(2 * FT - 1))
            pe.wait_ge(evacuated, done(2 * FT - 1))
            turn_tails(0, 2 * NG)
            down_product(last, 0, 2 * NG)
            turn_tails(2 * NG, NTG)
            pe.wait_ge(tail_rows, NTG)
            turn_y(0)
            for t in range(2, KT):
                down_product(last, NG * t, NG * (t + 1))
                turn_y(t - 1)
            turn_y(KT - 1)
    m.free()


_INS = ['x_prompt', 'x_sample', 'state_gdn_conv', 'state_gdn_S', 'cache_k', 'cache_v', 'page_table', 'state_ffn_conv',
        'attn_norm_g', 'w_in', 'gdn_conv_w', 'gdn_A_log', 'gdn_dt_bias', 'gdn_out_norm_g', 'diff_q_norm_g', 'diff_k_norm_g',
        'diff_lambda_q1', 'diff_lambda_k1', 'diff_lambda_q2', 'diff_lambda_k2', 'diff_subln_g', 'w_out', 'ffn_norm_g',
        'w_up', 'ffn_conv_w', 'ffn_conv_b', 'w_down']
_OUTS = [('y_prompt', (1, SEQ, D)), ('y_sample', (NB, NL, D)), ('gdn_conv_prompt', (1, 1, G_PAD, 3 * GW)),
         ('gdn_S_prompt', (1, 1, H, DH, DH)), ('k_prompt', (1, 1, SEQ, H, DH)), ('v_prompt', (1, 1, SEQ, H, DH)),
         ('ffn_conv_prompt', (1, 1, F_PAD, 2 * FF)), ('gdn_conv_sample', (1, NB, G_PAD, 3 * GW)),
         ('gdn_S_sample', (1, NB, H, DH, DH)), ('k_sample', (1, NB, NL, H, DH)), ('v_sample', (1, NB, NL, H, DH)),
         ('ffn_conv_sample', (1, NB, F_PAD, 2 * FF))]


def kernel(**inputs):
    import numpy as _np
    import concourse.bacc as _bacc
    from concourse import mybir as _mybir
    from concourse.bass_utils import run_bass_kernel_spmd as _run

    nc = _bacc.Bacc("TRN2", target_bir_lowering=False, num_devices=1)
    arrays, ins, outs = {}, {}, {}
    for name in _INS:
        a = _np.ascontiguousarray(inputs[name])
        arrays[f"in_{name}"] = a
        ins[name] = nc.dram_tensor(f"in_{name}", a.shape, _mybir.dt.from_np(a.dtype), kind="ExternalInput").ap()
    for name, shape in _OUTS:
        outs[name] = nc.dram_tensor(f"out_{name}", shape, F32, kind="ExternalOutput").ap()
    hybrid_step(nc, ins, outs)
    r = _run(nc, [arrays], core_ids=[0])
    return tuple(r.results[0][f"out_{name}"] for name, _ in _OUTS)
```
